# Optimizing a Trainium2 kernel written in Bass

```python
import math
import jax, jax.numpy as jnp
from jax import lax
import numpy as np

D_MODEL = 1024
BATCH = 1
SEQ = 256
DEPTH = 2

CHUNK = 64
Q_BLOCK = 128
N_A_LAYERS = DEPTH // 2
N_B_LAYERS = DEPTH - N_A_LAYERS
SSM_GROUP = 16
SSM_GROUPS = D_MODEL // SSM_GROUP
SSM_STATE = 64
DT_MIN = 0.001
DT_MAX = 0.1
N_HEADS = 16
QK_NOPE_DIM = 64
QK_ROPE_DIM = 32
V_HEAD_DIM = 64
Q_LORA_RANK = 256
KV_LORA_RANK = 256
ROPE_THETA = 10000.0
ATTN_SCALE = 1.0 / math.sqrt(QK_NOPE_DIM + QK_ROPE_DIM)
D_FF = ((8 * D_MODEL + 3 * 256 - 1) // (3 * 256)) * 256
EPS = 1e-6


def rms_norm(x, g):
    xf = x.astype(jnp.float32)
    y = xf * lax.rsqrt(jnp.mean(xf * xf, axis=-1, keepdims=True) + EPS)
    return (y * g.astype(jnp.float32)).astype(x.dtype)

def modulate(h, shift, scale):
    return h * (1.0 + scale[:, None, :]) + shift[:, None, :]

def rope_cos_sin(positions):
    inv = 1.0 / (ROPE_THETA ** (jnp.arange(0, QK_ROPE_DIM, 2, dtype=jnp.float32) / QK_ROPE_DIM))
    ang = positions.astype(jnp.float32)[..., None] * inv
    return jnp.cos(ang), jnp.sin(ang)

def apply_rope(x, cos, sin):
    shape = cos.shape[:2] + (1,) * (x.ndim - 3) + cos.shape[-1:]
    cos = cos.reshape(shape)
    sin = sin.reshape(shape)
    x1, x2 = jnp.split(x.astype(jnp.float32), 2, axis=-1)
    return jnp.concatenate([x1 * cos - x2 * sin, x1 * sin + x2 * cos], axis=-1).astype(x.dtype)

def _complex_linear_combine(e1, e2):
    a1r, a1i, b1r, b1i = e1
    a2r, a2i, b2r, b2i = e2
    ar = a1r * a2r - a1i * a2i
    ai = a1r * a2i + a1i * a2r
    br = a2r * b1r - a2i * b1i + b2r
    bi = a2r * b1i + a2i * b1r + b2i
    return (ar, ai, br, bi)

def s5_mixer(h, lam_re, lam_im, log_dt, b_re, b_im, c_re, c_im, d_skip, w_glu, b_glu):
    bsz, s_len, d = h.shape
    f32 = jnp.float32
    lr = lam_re.astype(f32)
    li = lam_im.astype(f32)
    dt = jnp.exp(log_dt.astype(f32))[:, None]
    mag = jnp.exp(lr * dt)
    ab_re = mag * jnp.cos(li * dt)
    ab_im = mag * jnp.sin(li * dt)
    den = lr * lr + li * li
    nr = ab_re - 1.0
    ni = ab_im
    f_re = (nr * lr + ni * li) / den
    f_im = (ni * lr - nr * li) / den
    br = b_re.astype(f32)
    bi = b_im.astype(f32)
    bb_re = f_re[..., None] * br - f_im[..., None] * bi
    bb_im = f_re[..., None] * bi + f_im[..., None] * br
    cr = c_re.astype(f32)
    ci = c_im.astype(f32)

    n_chunks = s_len // CHUNK
    u = h.astype(f32).reshape(bsz, n_chunks, CHUNK, SSM_GROUPS, SSM_GROUP).transpose(1, 0, 2, 3, 4)

    def chunk_step(carry, u_c):
        s_re, s_im = carry
        bu_re = jnp.einsum('blgp,gnp->blgn', u_c, bb_re)
        bu_im = jnp.einsum('blgp,gnp->blgn', u_c, bb_im)
        a_re = jnp.broadcast_to(ab_re, bu_re.shape)
        a_im = jnp.broadcast_to(ab_im, bu_im.shape)
        pa_re, pa_im, loc_re, loc_im = lax.associative_scan(
            _complex_linear_combine, (a_re, a_im, bu_re, bu_im), axis=1)
        st_re = loc_re + pa_re * s_re[:, None] - pa_im * s_im[:, None]
        st_im = loc_im + pa_re * s_im[:, None] + pa_im * s_re[:, None]
        y = jnp.einsum('blgn,gpn->blgp', st_re, cr) - jnp.einsum('blgn,gpn->blgp', st_im, ci)
        return (st_re[:, -1], st_im[:, -1]), y

    init = (jnp.zeros((bsz, SSM_GROUPS, SSM_STATE), f32), jnp.zeros((bsz, SSM_GROUPS, SSM_STATE), f32))
    _, y = lax.scan(chunk_step, init, u)
    y = y.transpose(1, 0, 2, 3, 4).reshape(bsz, s_len, d)
    y = (y + d_skip.astype(f32) * h.astype(f32)).astype(h.dtype)
    g = jax.nn.gelu(y)
    return g * jax.nn.sigmoid(g @ w_glu + b_glu)

def shared_mla_kv(hk, cos, sin, w_kv_a, kv_a_norm_g, w_kv_b, k_nope_norm_g, k_rope_norm_g):
    bsz, s_len, _ = hk.shape
    kv_a = hk @ w_kv_a
    c_kv, k_rope = jnp.split(kv_a, [KV_LORA_RANK], axis=-1)
    c_kv = rms_norm(c_kv, kv_a_norm_g)
    kv = (c_kv @ w_kv_b).reshape(bsz, s_len, N_HEADS, QK_NOPE_DIM + V_HEAD_DIM)
    k_nope, v = jnp.split(kv, [QK_NOPE_DIM], axis=-1)
    k_nope = rms_norm(k_nope, k_nope_norm_g)
    k_rope = apply_rope(rms_norm(k_rope, k_rope_norm_g), cos, sin)
    return k_nope, k_rope, v

def mla_attention(h, cos, sin, k_nope, k_rope, v, w_dq, q_norm_g, w_uq, q_nope_norm_g, q_rope_norm_g, w_o):
    bsz, s_len, _ = h.shape
    q = rms_norm(h @ w_dq, q_norm_g) @ w_uq
    q = q.reshape(bsz, s_len, N_HEADS, QK_NOPE_DIM + QK_ROPE_DIM)
    q_nope, q_rope = jnp.split(q, [QK_NOPE_DIM], axis=-1)
    q_nope = rms_norm(q_nope, q_nope_norm_g)
    q_rope = apply_rope(rms_norm(q_rope, q_rope_norm_g), cos, sin)
    n_blocks = s_len // Q_BLOCK
    qn_b = q_nope.reshape(bsz, n_blocks, Q_BLOCK, N_HEADS, QK_NOPE_DIM).transpose(1, 0, 2, 3, 4)
    qr_b = q_rope.reshape(bsz, n_blocks, Q_BLOCK, N_HEADS, QK_ROPE_DIM).transpose(1, 0, 2, 3, 4)
    key_chunk = jnp.arange(s_len) // CHUNK

    def block_attn(args):
        qn, qr, blk = args
        s = (jnp.einsum('bqhd,bkhd->bhqk', qn, k_nope, preferred_element_type=jnp.float32)
             + jnp.einsum('bqhr,bkr->bhqk', qr, k_rope, preferred_element_type=jnp.float32)) * ATTN_SCALE
        q_chunk = (blk * Q_BLOCK + jnp.arange(Q_BLOCK)) // CHUNK
        mask = q_chunk[:, None] >= key_chunk[None, :]
        s = jnp.where(mask[None, None], s, -1e30)
        p = jax.nn.softmax(s, axis=-1)
        return jnp.einsum('bhqk,bkhd->bqhd', p.astype(v.dtype), v)

    o = lax.map(block_attn, (qn_b, qr_b, jnp.arange(n_blocks)))
    o = o.transpose(1, 0, 2, 3, 4).reshape(bsz, s_len, N_HEADS * V_HEAD_DIM)
    return o @ w_o

def swiglu(h, w_gate, w_up, w_down):
    return (jax.nn.silu(h @ w_gate) * (h @ w_up)) @ w_down

def first_inputs(seed: int = 0) -> dict:
    key = jax.random.key(seed)
    ks = iter(jax.random.split(key, 48))
    f32 = jnp.float32
    D, F, G, N, P = D_MODEL, D_FF, SSM_GROUPS, SSM_STATE, SSM_GROUP
    NA, NB = N_A_LAYERS, N_B_LAYERS

    def nrm(shape, scale):
        return jax.random.normal(next(ks), shape, f32) * scale

    def gain(shape):
        return 1.0 + 0.02 * jax.random.normal(next(ks), shape, f32)

    x = jax.random.normal(next(ks), (BATCH, SEQ, D), f32)
    c = jax.random.normal(next(ks), (BATCH, D), f32)
    offsets = jax.random.randint(next(ks), (BATCH, 1), 0, 4096, dtype=jnp.int32)
    positions = offsets + jnp.arange(SEQ, dtype=jnp.int32)[None, :]

    n_idx = jnp.arange(N, dtype=f32)
    inputs = {
        "x": x, "c": c, "positions": positions,
        "ada_w": nrm((DEPTH, D, 6 * D), 0.5 * D ** -0.5),
        "ada_b": nrm((DEPTH, 6 * D), 0.02),
        "norm1_g": gain((DEPTH, D)),
        "norm2_g": gain((DEPTH, D)),
        "ffn_w_gate": nrm((DEPTH, D, F), D ** -0.5),
        "ffn_w_up": nrm((DEPTH, D, F), D ** -0.5),
        "ffn_w_down": nrm((DEPTH, F, D), F ** -0.5),
        "s5_lam_re": -0.5 + 0.01 * jax.random.normal(next(ks), (NA, G, N), f32),
        "s5_lam_im": math.pi * n_idx[None, None, :] + 0.01 * jax.random.normal(next(ks), (NA, G, N), f32),
        "s5_log_dt": jax.random.uniform(next(ks), (NA, G), f32, math.log(DT_MIN), math.log(DT_MAX)),
        "s5_b_re": nrm((NA, G, N, P), P ** -0.5),
        "s5_b_im": nrm((NA, G, N, P), P ** -0.5),
        "s5_c_re": nrm((NA, G, P, N), N ** -0.5),
        "s5_c_im": nrm((NA, G, P, N), N ** -0.5),
        "s5_d": nrm((NA, D), 1.0),
        "s5_w_glu": nrm((NA, D, D), D ** -0.5),
        "s5_b_glu": nrm((NA, D), 0.02),
        "kv_ada_w": nrm((D, 2 * D), 0.5 * D ** -0.5),
        "kv_ada_b": nrm((2 * D,), 0.02),
        "kv_norm_g": gain((D,)),
        "w_kv_a": nrm((D, KV_LORA_RANK + QK_ROPE_DIM), D ** -0.5),
        "kv_a_norm_g": gain((KV_LORA_RANK,)),
        "w_kv_b": nrm((KV_LORA_RANK, N_HEADS * (QK_NOPE_DIM + V_HEAD_DIM)), KV_LORA_RANK ** -0.5),
        "k_nope_norm_g": gain((QK_NOPE_DIM,)),
        "k_rope_norm_g": gain((QK_ROPE_DIM,)),
        "mla_w_dq": nrm((NB, D, Q_LORA_RANK), D ** -0.5),
        "mla_q_norm_g": gain((NB, Q_LORA_RANK)),
        "mla_w_uq": nrm((NB, Q_LORA_RANK, N_HEADS * (QK_NOPE_DIM + QK_ROPE_DIM)), Q_LORA_RANK ** -0.5),
        "mla_q_nope_norm_g": gain((NB, QK_NOPE_DIM)),
        "mla_q_rope_norm_g": gain((NB, QK_ROPE_DIM)),
        "mla_w_o": nrm((NB, N_HEADS * V_HEAD_DIM, D), (N_HEADS * V_HEAD_DIM) ** -0.5),
    }
    return inputs

def first_block(x, c, positions, ada_w, ada_b, norm1_g, norm2_g, ffn_w_gate, ffn_w_up, ffn_w_down,
              s5_lam_re, s5_lam_im, s5_log_dt, s5_b_re, s5_b_im, s5_c_re, s5_c_im, s5_d, s5_w_glu, s5_b_glu,
              kv_ada_w, kv_ada_b, kv_norm_g, w_kv_a, kv_a_norm_g, w_kv_b, k_nope_norm_g, k_rope_norm_g,
              mla_w_dq, mla_q_norm_g, mla_w_uq, mla_q_nope_norm_g, mla_q_rope_norm_g, mla_w_o):
    cos, sin = rope_cos_sin(positions)
    c_act = jax.nn.silu(c)
    k_nope = k_rope = v = None
    for l in range(DEPTH):
        shift1, scale1, gate1, shift2, scale2, gate2 = jnp.split(c_act @ ada_w[l] + ada_b[l], 6, axis=-1)
        if l == N_A_LAYERS:
            k_shift, k_scale = jnp.split(c_act @ kv_ada_w + kv_ada_b, 2, axis=-1)
            hk = modulate(rms_norm(x, kv_norm_g), k_shift, k_scale)
            k_nope, k_rope, v = shared_mla_kv(hk, cos, sin, w_kv_a, kv_a_norm_g, w_kv_b,
                                              k_nope_norm_g, k_rope_norm_g)
        h = modulate(rms_norm(x, norm1_g[l]), shift1, scale1)
        if l < N_A_LAYERS:
            mix = s5_mixer(h, s5_lam_re[l], s5_lam_im[l], s5_log_dt[l], s5_b_re[l], s5_b_im[l],
                           s5_c_re[l], s5_c_im[l], s5_d[l], s5_w_glu[l], s5_b_glu[l])
        else:
            j = l - N_A_LAYERS
            mix = mla_attention(h, cos, sin, k_nope, k_rope, v, mla_w_dq[j], mla_q_norm_g[j], mla_w_uq[j],
                                mla_q_nope_norm_g[j], mla_q_rope_norm_g[j], mla_w_o[j])
        x = x + gate1[:, None, :] * mix
        h = modulate(rms_norm(x, norm2_g[l]), shift2, scale2)
        x = x + gate2[:, None, :] * swiglu(h, ffn_w_gate[l], ffn_w_up[l], ffn_w_down[l])
    return x


HEAD_DIM = 64
MEM_LEN = 256
MEM_HEADS = 4
MEM_W = MEM_HEADS * HEAD_DIM
MIX_W = D_MODEL
BR_W = MIX_W - MEM_W
A_HEADS = BR_W // HEAD_DIM
B_HEADS = BR_W // (2 * HEAD_DIM)
LORA_W = 64
LORA_A = 64
N_A = DEPTH // 2
N_B = DEPTH - N_A
A_SHIFT = 3 * BR_W + LORA_W + LORA_A
A_IN = A_SHIFT + BR_W + 2 * MEM_W
B_IN = 2 * BR_W + 2 * MEM_W
NORM_EPS = 1e-6
LNX_EPS = 64e-5


def rms_norm_2(x, g):
    xf = x.astype(jnp.float32)
    y = xf * lax.rsqrt(jnp.mean(xf * xf, axis=-1, keepdims=True) + NORM_EPS)
    return (y * g.astype(jnp.float32)).astype(x.dtype)

def token_shift(z):
    return jnp.pad(z, ((0, 0), (1, 0), (0, 0)))[:, :-1]

def alibi_slopes(n):
    def pow2(m):
        start = 2.0 ** (-8.0 / m)
        return [start ** (i + 1) for i in range(m)]
    if math.log2(n).is_integer():
        s = pow2(n)
    else:
        c = 2 ** int(math.floor(math.log2(n)))
        s = pow2(c) + pow2(2 * c)[0::2][: n - c]
    return jnp.asarray(np.array(s, dtype=np.float32))

def rwkv7_time_mix(z, mu, w0, w2, a0, a2, k_k, k_a, r_k, lnx_w, lnx_b):
    B, S, _ = z.shape
    z = z.astype(jnp.float32)
    z = z + (token_shift(z) - z) * mu
    r, k, v, wd, ad = jnp.split(z, [BR_W, 2 * BR_W, 3 * BR_W, 3 * BR_W + LORA_W], axis=-1)
    w = -jax.nn.softplus(-(w0 + jnp.tanh(wd) @ w2)) - 0.5
    decay = jnp.exp(-jnp.exp(w))
    a = jax.nn.sigmoid(a0 + ad @ a2)
    heads = lambda t: t.reshape(B, S, A_HEADS, HEAD_DIM)
    kk = heads(k * k_k)
    kk = kk * lax.rsqrt(jnp.maximum(jnp.sum(kk * kk, axis=-1, keepdims=True), 1e-12))
    k = k * (1.0 + (a - 1.0) * k_a)
    r, k, v, decay, a = heads(r), heads(k), heads(v), heads(decay), heads(a)

    def step(state, inp):
        r_t, w_t, k_t, v_t, kk_t, a_t = inp
        sa = jnp.einsum('bhvk,bhk->bhv', state, -kk_t)
        state = (state * w_t[:, :, None, :]
                 + sa[..., None] * (kk_t * a_t)[:, :, None, :]
                 + v_t[..., None] * k_t[:, :, None, :])
        y_t = jnp.einsum('bhvk,bhk->bhv', state, r_t)
        return state, y_t

    tm = lambda t: jnp.moveaxis(t, 1, 0)
    state0 = jnp.zeros((B, A_HEADS, HEAD_DIM, HEAD_DIM), jnp.float32)
    _, y = lax.scan(step, state0, (tm(r), tm(decay), tm(k), tm(v), tm(kk), tm(a)))
    y = jnp.moveaxis(y, 0, 1)
    mean = jnp.mean(y, axis=-1, keepdims=True)
    var = jnp.mean(jnp.square(y - mean), axis=-1, keepdims=True)
    y = ((y - mean) * lax.rsqrt(var + LNX_EPS)).reshape(B, S, BR_W) * lnx_w + lnx_b
    bonus = jnp.sum(r * k * r_k, axis=-1, keepdims=True) * v
    return y + bonus.reshape(B, S, BR_W)

def diff_attention(q, k_sh, v_sh, lq1, lk1, lq2, lk2, subln, lam_init):
    B, S, _ = q.shape
    q = q.reshape(B, S, B_HEADS, 2, HEAD_DIM) * (HEAD_DIM ** -0.5)
    k = k_sh.reshape(B, S, B_HEADS, 2, HEAD_DIM)
    v = v_sh.reshape(B, S, B_HEADS, 2 * HEAD_DIM)
    lq1f, lk1f = lq1.astype(jnp.float32), lk1.astype(jnp.float32)
    lq2f, lk2f = lq2.astype(jnp.float32), lk2.astype(jnp.float32)
    lam = jnp.exp(jnp.sum(lq1f * lk1f)) - jnp.exp(jnp.sum(lq2f * lk2f)) + lam_init
    slopes = alibi_slopes(B_HEADS)
    pos = jnp.arange(S)
    nb = S // Q_BLOCK
    qb = jnp.moveaxis(q.reshape(B, nb, Q_BLOCK, B_HEADS, 2, HEAD_DIM), 1, 0)

    def block(args):
        q_blk, i = args
        t = i * Q_BLOCK + jnp.arange(Q_BLOCK)
        s = jnp.einsum('bqhcd,bkhcd->bhcqk', q_blk, k, preferred_element_type=jnp.float32)
        dist = jnp.abs(t[:, None] - pos[None, :]).astype(jnp.float32)
        bias = -slopes[:, None, None] * dist
        allowed = (pos[None, :] // CHUNK) <= (t[:, None] // CHUNK)
        s = jnp.where(allowed, s + bias[None, :, None], -jnp.inf)
        p = jax.nn.softmax(s, axis=-1)
        attn = (p[:, :, 0] - lam * p[:, :, 1]).astype(v.dtype)
        return jnp.einsum('bhqk,bkhe->bqhe', attn, v)

    o = lax.map(block, (qb, jnp.arange(nb)))
    o = jnp.moveaxis(o, 0, 1).reshape(B, S, B_HEADS, 2 * HEAD_DIM)
    o = rms_norm_2(o, subln) * (1.0 - lam_init)
    return o.reshape(B, S, BR_W)

def memory_cross_attention(q, mem_n, w_mem_kv):
    B, S, _ = q.shape
    k, v = jnp.split(mem_n @ w_mem_kv, 2, axis=-1)
    k = k.reshape(B, -1, MEM_HEADS, HEAD_DIM)
    v = v.reshape(B, -1, MEM_HEADS, HEAD_DIM)
    q = q.reshape(B, S, MEM_HEADS, HEAD_DIM)
    s = jnp.einsum('bshd,bmhd->bhsm', q, k, preferred_element_type=jnp.float32) * (HEAD_DIM ** -0.5)
    p = jax.nn.softmax(s, axis=-1).astype(v.dtype)
    o = jnp.einsum('bhsm,bmhd->bshd', p, v)
    return o.reshape(B, S, MEM_W)

def second_inputs(seed: int = 0) -> dict:
    key = jax.random.key(seed)
    ks = jax.random.split(key, 32)
    nrm = lambda k, shape, scale: scale * jax.random.normal(k, shape, jnp.float32)
    gain = lambda k, shape: 1.0 + 0.05 * jax.random.normal(k, shape, jnp.float32)
    return {
        'x': jax.random.normal(ks[0], (BATCH, SEQ, D_MODEL), jnp.float32),
        'mem': jax.random.normal(ks[1], (BATCH, MEM_LEN, D_MODEL), jnp.float32),
        'pre_norm': gain(ks[2], (DEPTH, D_MODEL)),
        'post_norm': gain(ks[3], (DEPTH, D_MODEL)),
        'w_out': nrm(ks[4], (DEPTH, MIX_W, D_MODEL), MIX_W ** -0.5),
        'mem_norm': gain(ks[5], (DEPTH, D_MODEL)),
        'w_mem_kv': nrm(ks[6], (DEPTH, D_MODEL, 2 * MEM_W), D_MODEL ** -0.5),
        'a_w_in': nrm(ks[7], (N_A, D_MODEL, A_IN), D_MODEL ** -0.5),
        'a_shift_mu': jax.random.uniform(ks[8], (N_A, A_SHIFT), jnp.float32),
        'a_w0': jax.random.uniform(ks[9], (N_A, BR_W), jnp.float32, minval=-6.0, maxval=0.0),
        'a_w2': nrm(ks[10], (N_A, LORA_W, BR_W), 0.5 * LORA_W ** -0.5),
        'a_a0': nrm(ks[11], (N_A, BR_W), 0.1),
        'a_a2': nrm(ks[12], (N_A, LORA_A, BR_W), 0.5 * LORA_A ** -0.5),
        'a_k_k': 0.85 + 0.05 * jax.random.normal(ks[13], (N_A, BR_W), jnp.float32),
        'a_k_a': gain(ks[14], (N_A, BR_W)),
        'a_r_k': nrm(ks[15], (N_A, A_HEADS, HEAD_DIM), 0.1),
        'a_lnx_w': gain(ks[16], (N_A, BR_W)),
        'a_lnx_b': nrm(ks[17], (N_A, BR_W), 0.02),
        'kv_norm': gain(ks[18], (D_MODEL,)),
        'w_kv': nrm(ks[19], (D_MODEL, 2 * BR_W), D_MODEL ** -0.5),
        'b_w_in': nrm(ks[20], (N_B, D_MODEL, B_IN), D_MODEL ** -0.5),
        'b_lam_q1': nrm(ks[21], (N_B, HEAD_DIM), 0.1),
        'b_lam_k1': nrm(ks[22], (N_B, HEAD_DIM), 0.1),
        'b_lam_q2': nrm(ks[23], (N_B, HEAD_DIM), 0.1),
        'b_lam_k2': nrm(ks[24], (N_B, HEAD_DIM), 0.1),
        'b_subln': gain(ks[25], (N_B, 2 * HEAD_DIM)),
    }

def second_block(x, mem, pre_norm, post_norm, w_out, mem_norm, w_mem_kv,
              a_w_in, a_shift_mu, a_w0, a_w2, a_a0, a_a2, a_k_k, a_k_a, a_r_k, a_lnx_w, a_lnx_b,
              kv_norm, w_kv,
              b_w_in, b_lam_q1, b_lam_k1, b_lam_q2, b_lam_k2, b_subln):
    k_sh = None
    v_sh = None
    for l in range(DEPTH):
        h = rms_norm_2(x, pre_norm[l])
        mem_n = rms_norm_2(mem, mem_norm[l])
        if l < N_A:
            i = l
            proj = h @ a_w_in[i]
            z, gate, q_mem, g_mem = jnp.split(
                proj, [A_SHIFT, A_SHIFT + BR_W, A_SHIFT + BR_W + MEM_W], axis=-1)
            y_br = rwkv7_time_mix(z, a_shift_mu[i], a_w0[i], a_w2[i], a_a0[i], a_a2[i],
                                  a_k_k[i], a_k_a[i], a_r_k[i], a_lnx_w[i], a_lnx_b[i])
        else:
            if l == N_A:
                k_sh, v_sh = jnp.split(rms_norm_2(x, kv_norm) @ w_kv, 2, axis=-1)
            i = l - N_A
            proj = h @ b_w_in[i]
            q, gate, q_mem, g_mem = jnp.split(
                proj, [BR_W, 2 * BR_W, 2 * BR_W + MEM_W], axis=-1)
            lam_init = 0.8 - 0.6 * math.exp(-0.3 * l)
            y_br = diff_attention(q, k_sh, v_sh, b_lam_q1[i], b_lam_k1[i], b_lam_q2[i],
                                  b_lam_k2[i], b_subln[i], lam_init)
        y_mem = memory_cross_attention(q_mem, mem_n, w_mem_kv[l])
        y = jnp.concatenate([(y_br * jax.nn.silu(gate.astype(jnp.float32))).astype(x.dtype),
                             y_mem * jax.nn.silu(g_mem)], axis=-1) @ w_out[l]
        x = x + rms_norm_2(y, post_norm[l])
    return x


def setup_inputs(seed=0):
    out = dict(first_inputs(seed))
    for name, value in second_inputs(seed + 1).items():
        if name != "x":
            out[name + "_2"] = value
    return out


def reference(
    x, c, positions, ada_w, ada_b, norm1_g, norm2_g, ffn_w_gate, ffn_w_up, ffn_w_down,
    s5_lam_re, s5_lam_im, s5_log_dt, s5_b_re, s5_b_im, s5_c_re, s5_c_im, s5_d, s5_w_glu,
    s5_b_glu, kv_ada_w, kv_ada_b, kv_norm_g, w_kv_a, kv_a_norm_g, w_kv_b, k_nope_norm_g,
    k_rope_norm_g, mla_w_dq, mla_q_norm_g, mla_w_uq, mla_q_nope_norm_g, mla_q_rope_norm_g,
    mla_w_o, mem_2, pre_norm_2, post_norm_2, w_out_2, mem_norm_2, w_mem_kv_2, a_w_in_2,
    a_shift_mu_2, a_w0_2, a_w2_2, a_a0_2, a_a2_2, a_k_k_2, a_k_a_2, a_r_k_2, a_lnx_w_2,
    a_lnx_b_2, kv_norm_2, w_kv_2, b_w_in_2, b_lam_q1_2, b_lam_k1_2, b_lam_q2_2, b_lam_k2_2,
    b_subln_2,
):
    x = first_block(
        x, c, positions, ada_w, ada_b, norm1_g, norm2_g, ffn_w_gate, ffn_w_up, ffn_w_down,
        s5_lam_re, s5_lam_im, s5_log_dt, s5_b_re, s5_b_im, s5_c_re, s5_c_im, s5_d, s5_w_glu,
        s5_b_glu, kv_ada_w, kv_ada_b, kv_norm_g, w_kv_a, kv_a_norm_g, w_kv_b, k_nope_norm_g,
        k_rope_norm_g, mla_w_dq, mla_q_norm_g, mla_w_uq, mla_q_nope_norm_g, mla_q_rope_norm_g,
        mla_w_o,
    )
    return second_block(
        x, mem_2, pre_norm_2, post_norm_2, w_out_2, mem_norm_2, w_mem_kv_2, a_w_in_2,
        a_shift_mu_2, a_w0_2, a_w2_2, a_a0_2, a_a2_2, a_k_k_2, a_k_a_2, a_r_k_2, a_lnx_w_2,
        a_lnx_b_2, kv_norm_2, w_kv_2, b_w_in_2, b_lam_q1_2, b_lam_k1_2, b_lam_q2_2, b_lam_k2_2,
        b_subln_2,
    )


_drawn_inputs = setup_inputs


def setup_inputs(seed=0):
    import zlib

    import numpy as np

    out = dict(_drawn_inputs(seed))
    spreads = {}
    factors = {'norm1_g': 7.839,
     'norm2_g': 2.709,
     's5_lam_re': 200.0,
     's5_b_glu': 8.0,
     'kv_ada_b': 3.423,
     'kv_norm_g': 8.0,
     'kv_a_norm_g': 8.0,
     'k_nope_norm_g': 8.0,
     'k_rope_norm_g': 8.0,
     'mla_q_norm_g': 8.0,
     'mla_q_nope_norm_g': 8.0,
     'mla_q_rope_norm_g': 8.0,
     'mem_norm_2': 8.0,
     'a_lnx_b_2': 22.008,
     'b_lam_k1_2': 25.53,
     'post_norm_2': 2.799,
     'a_w2_2': 8.0,
     'a_a0_2': 8.0,
     'a_a2_2': 3.308,
     'a_k_k_2': 8.0,
     'a_k_a_2': 8.0,
     'a_r_k_2': 2.908,
     'a_lnx_w_2': 8.0,
     'kv_norm_2': 8.0,
     'b_lam_q2_2': 2.921,
     'b_lam_k2_2': 32.109,
     'b_subln_2': 22.161}
    for name, (base, spread) in spreads.items():
        noise = np.random.default_rng([zlib.crc32(name.encode()), seed]).standard_normal(out[name].shape)
        drawn = base * np.exp(spread * noise) if base else spread * noise
        out[name] = __import__('jax').numpy.asarray(drawn.astype(out[name].dtype))
    for name, factor in factors.items():
        out[name] = (out[name] * factor).astype(out[name].dtype)
    return out
```

```python
from contextlib import ExitStack
import math

import numpy as np

import concourse.bass as bass
from concourse import mybir

F32 = mybir.dt.float32
I32 = mybir.dt.int32
ALU = mybir.AluOpType
ACT = mybir.ActivationFunctionType
AX_X = mybir.AxisListType.X

P = 128
T = 256
D = 1024
KC = D // P
FF = 2816
EPS = 1e-6
NEG = -1e30

G5, P5, N5 = 64, 16, 64
L5 = 8
C5 = T // L5
J5 = G5 // 2
BJ = 4
NB5 = J5 // BJ

H1, DN, DR, DV = 16, 64, 32, 64
DQK = DN + DR
RKV = RQ = 256
SCALE1 = 1.0 / math.sqrt(DQK)
THETA = 10000.0
CHUNK = 64

HD = 64
MW = 256
BR = 768
NBR = BR // P
A_SHIFT = 3 * BR + 128
A_IN = A_SHIFT + BR + 2 * MW
B_IN = 2 * BR + 2 * MW
HB = 6
LNX_EPS = 64e-5
CR = 64
NCR = T // CR
NU = NBR * NCR
LAM_INIT = 0.8 - 0.6 * math.exp(-0.3)

RING = 4
PANEL = 2048
ARING = 2
ARENA = 30000
TWO_PI = 2.0 * math.pi
ROUND = 1.5 * 2.0 ** 23
PI2_A = 6.28125
PI2_B = float((np.float32(TWO_PI - PI2_A).view(np.uint32) & np.uint32(0xFFFFF000)).view(np.float32))
PI2_C = float(np.float32(TWO_PI - PI2_A - PI2_B))


def alibi_slopes(n):
    def pow2(m):
        start = 2.0 ** (-8.0 / m)
        return [start ** (i + 1) for i in range(m)]
    if math.log2(n).is_integer():
        return pow2(n)
    c = 2 ** int(math.floor(math.log2(n)))
    return pow2(c) + pow2(2 * c)[0::2][: n - c]


def shape_constants():
    p = np.arange(P)
    parts = {}
    parts["ident"] = np.eye(P)
    parts["ones"] = np.ones((P, P))
    half = (p[:, None] // 64) == (p[None, :] // 64)
    parts["half"] = half * 1.0
    m = np.zeros((P, P))
    m[:DN, :DN] = 1.0 / DN
    m[DN:DQK, DN:DQK] = 1.0 / DR
    parts["qk_mean"] = m
    r = np.zeros((P, P))
    for j in range(DR // 2):
        r[DN + DR // 2 + j, DN + j] = -1.0
        r[DN + j, DN + DR // 2 + j] = 1.0
    parts["rotate"] = r
    parts["diag16"] = ((p[:, None] % P5) == np.arange(P5)[None, :]) * 1.0
    f = np.zeros((P, 1))
    inv = 1.0 / (np.float32(THETA) ** (np.arange(0, DR, 2, dtype=np.float32) / np.float32(DR)))
    f[DN:DQK, 0] = np.concatenate([inv, inv])
    parts["inv_freq"] = f
    mask = np.zeros((P, 2, T))
    for b in range(2):
        q = (b * P + p) // CHUNK
        mask[:, b, :] = np.where(q[:, None] >= (np.arange(T) // CHUNK)[None, :], 0.0, NEG)
    parts["chunk_mask"] = mask.reshape(P, -1)
    t = np.arange(CR)
    row = p % CR
    parts["strict_t"] = (row[:, None] < t[None, :]) * 1.0
    parts["causal_t"] = (row[:, None] <= t[None, :]) * 1.0
    parts["eye64"] = (row[:, None] == t[None, :]) * 1.0
    lev = []
    for l in range(6):
        b = 1 << l
        hi, lo = t[None, :], row[:, None]
        lev.append(((hi // (2 * b)) == (lo // (2 * b))) & ((hi // b) % 2 == 1) & ((lo // b) % 2 == 0))
    parts["levels_t"] = np.concatenate(lev, axis=1) * 1.0
    parts["level0"] = (((row[:, None] // 2) == (t[None, :] // 2)) & (row[:, None] % 2 == 1) & (t[None, :] % 2 == 0)) * 1.0
    parts["restart"] = np.broadcast_to((np.arange(T) % CR != 0) * 1.0, (P, T))
    bias = np.zeros((P, HB, 2, T), np.float32)
    for h, s in enumerate(np.array(alibi_slopes(HB), np.float32)):
        for b in range(2):
            dist = np.abs((b * P + p)[:, None] - np.arange(T)[None, :]).astype(np.float32)
            bias[:, h, b, :] = -s * dist + mask[:, b, :].astype(np.float32)
    parts["alibi"] = bias.reshape(P, -1)
    at, cols = {}, 0
    for n, a in parts.items():
        at[n] = (cols, a.shape[1])
        cols += a.shape[1]
    return at, np.concatenate([np.asarray(a, np.float32) for a in parts.values()], axis=1)


CONST_AT, CONSTANTS = shape_constants()
CONST_KEEP = CONST_AT["chunk_mask"][0]
CONST_MASK = CONST_AT["strict_t"][0]
CONST_ALIBI = CONST_AT["alibi"][0]


def vector_rows():
    tiles = [
        [("c", 8), ("ada_b", 96), ("kv_ada_b", 16)],
        [("norm1_g", 16), ("norm2_g", 16), ("s5_b_glu", 8), ("kv_norm_g", 8), ("kv_a_norm_g", 2),
         ("mla_q_norm_g", 2), ("pre_norm_2", 16), ("post_norm_2", 16), ("mem_norm_2", 16), ("kv_norm_2", 8),
         ("b_subln_2", 1)],
        [("a_shift_mu_2", 19), ("a_w0_2", 6), ("a_a0_2", 6), ("a_k_k_2", 6), ("a_k_a_2", 6), ("a_r_k_2", 6),
         ("a_lnx_w_2", 6), ("a_lnx_b_2", 6), ("q_gain", 1), ("k_gain", 1),
         ("b_lam_q1_2", 1), ("b_lam_k1_2", 1), ("b_lam_q2_2", 1), ("b_lam_k2_2", 1)],
    ]
    at, counts = {}, []
    for i, rows in enumerate(tiles):
        n = 0
        for name, k in rows:
            at[name] = (i, n, k)
            n += k
        counts.append(n)
    return at, counts


def blocks_kernel(nc, a, constants, out):
    ctx = ExitStack()
    with ctx:
        def sb(name, n):
            return ctx.enter_context(nc.sbuf_tensor(name, [P, n], F32))

        const_sb = sb("const_sb", CONST_KEEP)
        rows = sb("rows", 3 * P)
        vec = sb("vec", 3 * P)
        ada = sb("ada", 7 * 16)
        c_act = sb("c_act", KC)
        gains = sb("gains", 8 * KC)
        xT = sb("xT", KC * T)
        hT = sb("hT", KC * T)
        sq = sb("sq", KC * T)
        stat = sb("stat", 4 * T)
        ring = sb("ring", RING * PANEL)
        aring = sb("aring", ARING * PANEL)
        acc = sb("acc", PANEL)
        arena = sb("arena", ARENA)
        psum = ctx.enter_context(nc.psum_tensor("psum", [P, 8, 512], F32))

        sems = {}

        def done(name):
            if name not in sems:
                sems[name] = ctx.enter_context(nc.semaphore(name))
            return sems[name]

        filled = [done(f"bank{b}_filled") for b in range(8)]
        emptied = [done(f"bank{b}_emptied") for b in range(8)]
        panel_landed = [done(f"panel{i}_landed") for i in range(RING)]
        ada_landed = [done(f"ada_panel{i}_landed") for i in range(ARING)]

        turns = {"a": 0, "b": 0}
        use = {}
        made = {}

        class Program:

            def __init__(self, name):
                self.name, self.n, self.last = name + "_step", 0, None

            def step(self):
                self.n += 1
                self.last = (done(self.name), self.n)
                return done(self.name), 1

            def signals(self, name):
                made[name] = made.get(name, 0) + 1
                self.last = (done(name), made[name])
                return done(name), 1

            def empties(self, key):
                b, n = use[key]
                self.last = (emptied[b], n)
                return emptied[b], 1

        def next_bank(key, pool="a"):
            q = turns[pool]
            turns[pool] += 1
            b, n = (0 if pool == "a" else 4) + q % 4, q // 4
            use[key] = (b, n + 1)
            return emptied[b], n

        def fills(key):
            return filled[use[key][0]], 1

        def filled_at(key):
            b, n = use[key]
            return filled[b], n

        def emptied_at(key):
            b, n = use[key]
            return emptied[b], n

        def bank_of(key):
            return psum[:, use[key][0], :]

        def carve(base, n):
            return arena[:, base:base + n]

        def con(name):
            at, n = CONST_AT[name]
            return const_sb[:, at:at + n]

        ident, ones, half = con("ident"), con("ones"), con("half")
        VEC_AT, VEC_N = vector_rows()
        VEC_LOADS = [sum(2 if n in ("q_gain", "k_gain") else 1 for n, x in VEC_AT.items() if x[0] == i)
                     for i in range(3)]

        def col(name, j):
            i, r, _ = VEC_AT[name]
            return vec[:, i * P + r + j:i * P + r + j + 1]

        def cols(name, j, k):
            i, r, _ = VEC_AT[name]
            return vec[:, i * P + r + j:i * P + r + j + k]

        def ada_cols(layer, which):
            if layer == "kv":
                return ada[:, 96 + which * 8:96 + which * 8 + 8]
            return ada[:, layer * 48 + which * 8:layer * 48 + which * 8 + 8]

        xT3 = xT[:, :].rearrange("p (k t) -> p k t", t=T)
        hT3 = hT[:, :].rearrange("p (k t) -> p k t", t=T)
        sq3 = sq[:, :].rearrange("p (k t) -> p k t", t=T)

        o = 0
        CA_N = J5 * 9 * P5
        xC_in = ring[0:C5, 0:8 * D].rearrange("c (s d) -> c s d", d=D)
        xC = carve(0, 8 * D)[0:C5, :].rearrange("c (g s q) -> c g s q", s=L5, q=P5)
        ca_re = carve(0, CA_N).rearrange("p (j k q) -> p j k q", k=9, q=P5)
        ca_im = carve(CA_N, CA_N).rearrange("p (j k q) -> p j k q", k=9, q=P5)
        gC = carve(0, 8 * D)[0:C5, :].rearrange("c (t d) -> c t d", d=D)
        o = 2 * CA_N
        toep = carve(o, G5 * P).rearrange("p (g n) -> p g n", n=P)
        raw = carve(o, 4 * 2048)[0:J5, :].rearrange("j (m r n) -> j m r n", m=4, r=2)
        o += G5 * P
        wT = carve(o, BJ * 2 * P).rearrange("p (j i n) -> p j i n", i=2, n=P)
        o += BJ * 2 * P
        aB = carve(o, BJ * 2 * P).rearrange("p (i j n) -> p i j n", i=2, n=P)
        o += BJ * 2 * P
        kern = carve(o, 2 * BJ * P).rearrange("p (g n) -> p g n", n=P)
        lam_rows = carve(o, 3 * P)[0:J5, :].rearrange("j (m n) -> j m n", n=P)
        group_rows = carve(o + 3 * P, 4 * P5)[0:G5, :].rearrange("g (m n) -> g m n", n=P5)
        group_rep = carve(o + 3 * P + 64, 4 * P)[0:G5, :].rearrange("g (m n) -> g m n", n=P)
        o += 2 * BJ * P
        bb_rep = carve(o, 2 * BJ * P).rearrange("p (i j n) -> p i j n", i=2, n=P)
        st = carve(o, (C5 + 1) * 64).rearrange("p (c i j) -> p c i j", i=2, j=J5)
        o += (C5 + 1) * 64
        powr = carve(o, 9 * J5).rearrange("p (k j) -> p k j", j=J5)
        powi = carve(o + 9 * J5, 9 * J5).rearrange("p (k j) -> p k j", j=J5)
        prv = carve(o + 18 * J5, 16 * J5).rearrange("p (i j s) -> p i j s", i=2, s=L5)
        o += 34 * J5
        small = carve(o, 24 * J5).rearrange("p (m j) -> p m j", j=J5)
        o += 24 * J5
        bb = carve(o, 2 * J5 * P5).rearrange("p (i j q) -> p i j q", i=2, q=P5)
        ct = carve(o + 1024, 2 * J5 * P5).rearrange("p (i j q) -> p i j q", i=2, q=P5)
        bt = carve(o + 2048, 2 * J5 * P5).rearrange("p (i j q) -> p i j q", i=2, q=P5)
        o += 3072
        step4 = carve(o, 4 * J5).rearrange("p (e i j) -> p e i j", e=2, i=2)
        part4 = carve(o + 4 * J5, 4 * J5).rearrange("p (e i j) -> p e i j", e=2, i=2)
        part2 = carve(o + 8 * J5, 2 * J5).rearrange("p (e j) -> p e j", e=2)
        o += 10 * J5
        grp = carve(o, 4 * G5).rearrange("p (m g) -> p m g", g=G5)
        gmod = carve(o + 4 * G5, 2 * G5).rearrange("p (m g) -> p m g", g=G5)
        o += 6 * G5
        ss = carve(o, 24)[0:C5, :].rearrange("c (m s) -> c m s", s=L5)
        o += 24
        tmp5 = carve(o, 1280)
        pick = tmp5
        o += 1280
        assert o <= ARENA, o
        U = hT[:, :].rearrange("p (g c) -> p g c", c=C5)
        BU = sq[:, :].rearrange("p (c i j) -> p c i j", i=2, j=J5)
        gS = sq[:, :].rearrange("p (g c) -> p g c", c=C5)

        def y5_part(i):
            return gS[:, 32 * (i // 2) + i % 2:32 * (i // 2) + 32:2, :]

        xN = sq[:, :].rearrange("p (b d) -> p b d", d=D)

        class Carver:
            def __init__(self, base=0):
                self.o = base

            def __call__(self, n):
                self.o += n
                assert self.o <= ARENA, self.o
                return carve(self.o - n, n)

        hid = carve(ARENA - FF // P * T, FF // P * T).rearrange("p (n t) -> p n t", t=T)
        m1 = Carver()
        h2 = m1(KC * T).rearrange("p (k t) -> p k t", t=T)
        latent = [m1(2 * T).rearrange("p (k t) -> p k t", t=T) for _ in range(2)]
        qh = m1(H1 * T).rearrange("p (h t) -> p h t", t=T)
        kh = m1(H1 * T).rearrange("p (h t) -> p h t", t=T)
        v1 = m1(2 * D).rearrange("p (b n) -> p b n", n=D)
        o1 = m1(KC * T).rearrange("p (k t) -> p k t", t=T)
        wide = m1(H1 * T)
        krope = m1(T)
        krope_sq = m1(T)
        angle = m1(6 * T).rearrange("p (m t) -> p m t", t=T)
        pos_i = angle[:, 5, :].bitcast(I32)
        turn = m1(2 * 2 * T).rearrange("p (m t) -> p m t", t=2 * T)
        mask1 = m1(2 * T).rearrange("p (b t) -> p b t", t=T)
        pslots = m1(4 * T).rearrange("p (i t) -> p i t", t=T)
        tslots = m1(4 * T).rearrange("p (i t) -> p i t", t=T)
        soft = m1(3 * 32).rearrange("p (m u) -> p m u", u=32)
        inv_freq = con("inv_freq")

        e2 = Carver()
        mem_nat = aring[:, 0:2 * D].rearrange("p (b d) -> p b d", d=D)
        memT = aring[:, 2 * D:4 * D].rearrange("p (k t) -> p k t", t=T)
        mem_sq = acc[:, :].rearrange("p (k t) -> p k t", t=T)
        memn = [mem_sq, aring[:, 0:2 * D].rearrange("p (k t) -> p k t", t=T)]
        k_mem = [e2(2 * T).rearrange("p (m t) -> p m t", t=T) for _ in range(2)]
        v_mem = [e2(2 * MW).rearrange("p (b n) -> p b n", n=MW) for _ in range(2)]
        gateT = e2(KC * T).rearrange("p (k t) -> p k t", t=T)
        q_mem = e2(2 * T).rearrange("p (m t) -> p m t", t=T)
        pslots2 = e2(4 * T).rearrange("p (i t) -> p i t", t=T)
        tslots2 = aring[:, 2 * NBR * T:2 * NBR * T + 4 * T].rearrange("p (i t) -> p i t", t=T)
        soft2 = e2(5 * 32).rearrange("p (m u) -> p m u", u=32)
        sums2 = e2(64).rearrange("p (m u) -> p m u", u=32)
        columns2 = e2(64)
        r7 = Carver(e2.o)
        lora_in = r7(T)
        w2a2 = r7(BR)
        masks7 = r7(CONST_ALIBI - CONST_MASK)
        NB = NBR * T

        def con7(name):
            at, n = CONST_AT[name]
            return masks7[:, at - CONST_MASK:at - CONST_MASK + n]

        def tokens(x):
            return x.rearrange("p (i t) -> p i t", t=T)

        def units(x):
            return x.rearrange("p (u t) -> p u t", t=CR)

        ar7 = r7(2 * NB).rearrange("p (x i t) -> p x i t", x=2, t=T)
        at7, rt7 = ar7[:, 0], ar7[:, 1]
        k7, a7, v7, cum7, grow7, sig7, kk7, tmp7 = [tokens(r7(NB)) for _ in range(8)]
        lt7, x7, y7 = [units(r7(NB)) for _ in range(3)]
        lrb7, lak7 = [units(aring[:, i * NB:(i + 1) * NB]) for i in range(2)]
        v_tok = units(hT[:, 0:NB])
        k_tok = units(acc[:, 0:NB])
        flat = lambda x: x.rearrange("p i t -> p (i t)")
        b_tok, lt_t7, lt_m7 = units(flat(kk7)), units(flat(sig7)), units(flat(grow7))
        lrk7 = units(r7(NB))
        yT7 = tokens(x7.rearrange("p u t -> p (u t)"))
        yc7 = tokens(lt7.rearrange("p u t -> p (u t)"))
        chain = sq[:, 0:4 * NBR * CR].rearrange("p (n i t) -> p n i t", n=4, t=CR)
        state7, rhs7, sa7 = [chain[:, 0], chain[:, 1]], chain[:, 2], chain[:, 3]
        shifted = sq[:, 0:4 * (T + 1)].rearrange("p (s m t) -> p s m t", s=2, t=T + 1)
        y_sq7 = tokens(flat(sig7))
        yP = sq3
        out_sq = [ar7.rearrange("p x i t -> p (x i t)")[:, 0:KC * T].rearrange("p (k t) -> p k t", t=T)]

        f2 = Carver(e2.o)
        alibi = f2(HB * 2 * T).rearrange("p (h b t) -> p h b t", b=2, t=T)
        kT, qT = [tokens(f2(NB)) for _ in range(2)]
        v_sh = f2(2 * BR).rearrange("p (b n) -> p b n", n=BR)
        h_kv = f2(KC * T).rearrange("p (k t) -> p k t", t=T)
        out_sq.append(f2(KC * T).rearrange("p (k t) -> p k t", t=T))
        o_sq = tokens(f2(NB))
        both = f2(3 * 2 * T).rearrange("p (s c t) -> p s c t", c=2, t=T)
        out_rows = f2(2 * D).rearrange("p (b d) -> p b d", d=D)
        ND = 2 * HB

        def head(u):
            h = u // 2
            return slice(h % 2 * HD, h % 2 * HD + HD), h // 2, slice(u % 2 * P, u % 2 * P + P)

        def memory(l):
            def query(u):
                r, c, t = head(u)
                return q_mem[r, c, t]

            def key(u):
                r, c, _ = head(u)
                return k_mem[l][r, c, :]

            def dst(u):
                r, c, t = head(u)
                return hT3[r, NBR + c, t]
            return Attention(
                f"memory{l}", 2 * MW // HD, query, key, lambda u: T, HD ** -0.5, lambda u: None,
                lambda u, kb: v_mem[l][:, kb, u // 2 * HD:u // 2 * HD + HD], dst, lambda u: (u // 2 % 2 * HD, HD),
                (pslots2, tslots2, soft2))

        NGU = FF // P
        NDN = NGU // 2
        UPDATES = [None, ("dn", 0), ("wo1",), ("dn", 1)]

        class Attention:

            def __init__(self, name, n, query, key, keys, scale, bias, value, dst, width, buffers):
                self.pslots, self.tslots, self.soft = buffers
                self.name, self.n, self.query, self.key, self.keys = name, n, query, key, keys
                self.scale, self.bias, self.value, self.dst, self.width = scale, bias, value, dst, width

        mla = Attention(
            "mla", 2 * H1,
            lambda u: qh[0:DQK, u // 2, (u % 2) * P:(u % 2 + 1) * P],
            lambda u: kh[0:DQK, u // 2, 0:P * (u % 2 + 1)],
            lambda u: P * (u % 2 + 1), SCALE1,
            lambda u: mask1[:, u % 2, 0:P * (u % 2 + 1)],
            lambda u, kb: v1[:, kb, (u // 2) * DV:(u // 2 + 1) * DV],
            lambda u: o1[(u // 2 % 2) * DV:(u // 2 % 2 + 1) * DV, u // 4, (u % 2) * P:(u % 2 + 1) * P],
            lambda u: ((u // 2 % 2) * DV, DV), (pslots, tslots, soft))

        weights = []

        def in_columns(name, w, n_cols):
            rows_ = w.rearrange("(k p) n -> p k n", p=P)
            for i in range((n_cols + 255) // 256):
                m = min(256, n_cols - 256 * i)
                weights.append((rows_[:, :, 256 * i:256 * i + m], (rows_.shape[1], m), (*name, i)))

        def swiglu_weights(l):
            wg, wu = [a[x][l].rearrange("(k p) n -> p k n", p=P) for x in ("ffn_w_gate", "ffn_w_up")]
            wd = a["ffn_w_down"][l].rearrange("(j k p) n -> j p k n", k=2, p=P)
            for j in range(NDN + 1):
                if j < NDN:
                    for w in (wg, wu):
                        weights.append((w[:, :, j * 256:(j + 1) * 256], (KC, 256), ("gu", l, 2 * j + 1)))
                if j:
                    weights.append((wd[j - 1], (2, D), ("down", l, j - 1) if j < NDN else ("dn", l, 3)))

        in_columns(("glu",), a["s5_w_glu"][0], D)
        swiglu_weights(0)
        weights.append((a["w_kv_a"][:, 0:RKV].rearrange("(k p) n -> p k n", p=P), (KC, RKV), "ckv"))
        weights.append((a["w_kv_a"][:, RKV:].rearrange("(k p) n -> p k n", p=P), (KC, DR), "krope"))
        in_columns(("cq",), a["mla_w_dq"][0], RQ)
        for i in range(2):
            weights.append((a["w_kv_b"].rearrange("(k p) n -> p k n", p=P)[:, :, i * D:(i + 1) * D], (2, D),
                            ("v1", i, 1)))
        for i in range(2):
            weights.append((a["mla_w_uq"][0].rearrange("(k p) n -> p k n", p=P)[:, :, i * 8 * DQK:(i + 1) * 8 * DQK],
                            (2, 8 * DQK), ("q", 4 * i + 3)))
        in_columns(("wo1",), a["mla_w_o"][0], D)
        swiglu_weights(1)
        for l in range(2):
            in_columns(("k_mem", l), a["w_mem_kv_2"][l][:, 0:MW], MW)
            in_columns(("v_mem", l), a["w_mem_kv_2"][l][:, MW:], MW)
        in_columns(("a_in",), a["a_w_in_2"][0], A_IN)
        in_columns(("out", 0), a["w_out_2"][0], D)
        in_columns(("k_sh",), a["w_kv_2"][:, 0:BR], BR)
        in_columns(("v_sh",), a["w_kv_2"][:, BR:], BR)
        in_columns(("b_in",), a["b_w_in_2"][0], B_IN)
        in_columns(("out", 1), a["w_out_2"][1], D)

        def slot(i):
            shape = weights[i][1]
            n = shape[0] * shape[1]
            at = (i % RING) * PANEL
            return ring[:, at:at + n].rearrange("p (k n) -> p k n", n=shape[1])

        block = ctx.enter_context(nc.Block())

        @block.tensor
        def _(eng):
            pe = Program("tensor")

            def mm(dst, w, x, first=True, last=True):
                return eng.matmul(dst, w, x, start=first, stop=last)

            def panel():
                i = taken[0]
                taken[0] += 1
                return slot(i), (panel_landed[i % RING], 16 * (i // RING + 1))

            taken = [0]

            for i in range(3):
                eng.wait_ge(done(f"vectors{i}_landed"), 16 * VEC_LOADS[i])
                if i == 0:
                    eng.wait_ge(done("const_landed"), 16)
                eng.wait_ge(*next_bank(("vec", i)))
                ps = bank_of(("vec", i))
                eng.transpose(ps[:, 0:VEC_N[i]], rows[0:VEC_N[i], i * P:(i + 1) * P], ident[0:VEC_N[i], 0:VEC_N[i]])\
                    .then_inc(*fills(("vec", i)))

            eng.wait_ge(done("x_landed"), 16)
            for i in range(4):
                eng.wait_ge(*next_bank(("xT", i)))
                ps = bank_of(("xT", i)).rearrange("p (k b t) -> p k b t", k=2, b=2)
                for k in range(2):
                    for b in range(2):
                        last = eng.transpose(ps[:, k, b, :], xN[:, b, (2 * i + k) * P:(2 * i + k + 1) * P], ident)
                last.then_inc(*fills(("xT", i)))

            eng.wait_ge(done("s5_landed"), 16 * 11)
            eng.wait_ge(*next_bank("lam"))
            ps = bank_of("lam").rearrange("p (m j) -> p m j", j=J5)
            for m in range(2):
                mm(ps[:, m, :], lam_rows[:, m, :], ident[0:J5, 0:J5])
            for r in range(2):
                last = mm(ps[r * N5:(r + 1) * N5, 2, :], lam_rows[:, 2, r:r + 1].to_broadcast([J5, N5]),
                          ident[0:J5, 0:J5])
            last.then_inc(*fills("lam"))
            eng.wait_ge(done("group_rows_ready"), 1)
            eng.wait_ge(*next_bank("grp"))
            ps = bank_of("grp").rearrange("p (m g) -> p m g", g=G5)
            for m in range(4):
                last = mm(ps[:, m, :], group_rep[:, m, :], ident[0:G5, 0:G5])
            last.then_inc(*fills("grp"))
            for m in range(4):
                eng.wait_ge(*next_bank(("raw", m), "b"))
                ps = bank_of(("raw", m)).rearrange("p (q j) -> p q j", j=J5)
                for q in range(P5):
                    if m < 2:
                        src = raw[:, m, :, :].rearrange("j r (n q) -> j (r n) q", q=P5)[:, :, q]
                        last = eng.transpose(ps[:, q, :], src, ident[0:J5, 0:J5])
                    else:
                        for r in range(2):
                            last = mm(ps[r * N5:(r + 1) * N5, q, :], raw[:, m, r, q * N5:(q + 1) * N5],
                                      ident[0:J5, 0:J5])
                last.then_inc(*fills(("raw", m)))

            eng.wait_ge(done("xc_scaled"), 8)
            for i in range(4):
                eng.wait_ge(*next_bank(("U", i)))
                ps = bank_of(("U", i)).rearrange("p (g c) -> p g c", c=C5)
                for g in range(16):
                    gg = 16 * i + g
                    last = eng.transpose(ps[:, g, :], xC[:, gg, :, :].rearrange("c s q -> c (s q)"), ident[0:C5, 0:C5])
                last.then_inc(*fills(("U", i)))

            def ada_columns(blk):
                eng.wait_ge(done("ada_used"), 8 * (blk + 1))
                eng.wait_ge(*next_bank(("ada", blk), "b" if blk < 3 else "a"))
                ps = bank_of(("ada", blk))
                for j in range(16):
                    last = mm(ps[:, j:j + 1], acc[:, j * P:(j + 1) * P], ones[:, 0:1])
                last.then_inc(*fills(("ada", blk)))

            eng.wait_ge(done("ada_used"), 8)
            for i in range(4):
                eng.wait_ge(*next_bank(("ada0", i), "b"))
                ps = bank_of(("ada0", i))
                mm(ps, ones, acc[:, i * 512:(i + 1) * 512]).then_inc(*fills(("ada0", i)))

            for b in range(NB5):
                eng.wait_ge(done("ab_ready"), 2 * (b + 1))
                for i in range(2):
                    eng.wait_ge(*next_bank(("w", b, i)))
                    ps = bank_of(("w", b, i)).rearrange("p (j n) -> p j n", n=P)
                    for j in range(BJ):
                        last = eng.transpose(ps[:, j, :], aB[:, i, j, :], ident)
                    last.then_inc(*fills(("w", b, i)))
                eng.wait_ge(done("ca_ready"), 2 * (b + 1))
                eng.wait_ge(done("bb_rep_ready"), 2 * (b + 1))
                for i in range(2):
                    eng.wait_ge(*next_bank(("kern", b, i), "b"))
                    ps = bank_of(("kern", b, i)).rearrange("p (g n) -> p g n", n=P)
                    for g in range(4):
                        j, r = BJ * b + g, i * N5
                        for m, c in ((0, ca_re), (1, ca_im)):
                            w = bb_rep[r:r + N5, m, j % BJ, :]
                            last = mm(ps[:, g, :], w, c[r:r + N5, j, 0:L5, :], m == 0, m == 1)
                    last.then_inc(*fills(("kern", b, i)))
                eng.wait_ge(*emptied_at(("w", b, 0)))
                eng.wait_ge(*emptied_at(("w", b, 1)))
                if b == 0:
                    eng.wait_ge(done("u_ready"), 1)
                eng.wait_ge(*next_bank(("bu", b)))
                ps = bank_of(("bu", b)).rearrange("p (j i c) -> p j i c", j=BJ, i=2)[:, :, :, 0:C5]
                for j in range(BJ):
                    for i in range(2):
                        for r in range(2):
                            last = mm(ps[r * N5:(r + 1) * N5, j, i, :], wT[:, j, i, r * N5:(r + 1) * N5],
                                      U[:, 2 * (BJ * b + j) + r, :])
                last.then_inc(*fills(("bu", b)))
                if b == 3:
                    ada_columns(1)
                if b == 7:
                    ada_columns(2)

            eng.wait_ge(done("toeplitz_landed"), 16 * 64)
            eng.wait_ge(done("states_ready"), 1)
            for i in range(4):
                eng.wait_ge(*next_bank(("y5", i)))
                ps = bank_of(("y5", i)).rearrange("p (g c) -> p g c", c=C5)
                for g in range(16):
                    j, r = 16 * (i // 2) + g, (i % 2) * N5
                    gg = 2 * j + i % 2
                    mm(ps[:, g, :], toep[:, gg, :], U[:, gg, :], True, False)
                    mm(ps[:, g, :], ca_re[r:r + N5, j, 1:9, :], st[r:r + N5, 0:C5, 0, j], False, False)
                    last = mm(ps[:, g, :], ca_im[r:r + N5, j, 1:9, :], st[r:r + N5, 0:C5, 1, j], False, True)
                last.then_inc(*fills(("y5", i)))
            for i in range(16):
                eng.wait_ge(done("gelu_ready"), 2 * (i // 8) + 2)
                eng.wait_ge(*next_bank(("gc", i), "b"))
                ps = bank_of(("gc", i)).rearrange("p (g n) -> p g n", n=P)
                for g in range(4):
                    last = eng.transpose(ps[0:C5, g, :], gS[:, 4 * i + g, :], ident)
                last.then_inc(*fills(("gc", i)))
            for i in range(12, 16):
                eng.wait_ge(*emptied_at(("gc", i)))
            for i in range(4):
                eng.wait_ge(*next_bank(("gt", i)))
                ps = bank_of(("gt", i)).rearrange("p (k t c) -> p k t c", k=2, t=L5)
                for k in range(2):
                    for t in range(L5):
                        last = eng.transpose(ps[:, k, t, :], gC[:, t, (2 * i + k) * P:(2 * i + k + 1) * P],
                                             ident[0:C5, 0:C5])
                last.then_inc(*fills(("gt", i)))

            for i in range(4):
                eng.wait_ge(*emptied_at(("gt", i)))
            for i in range(4):
                w, landed = panel()
                eng.wait_ge(*landed)
                eng.wait_ge(*next_bank(("glu", i)))
                ps = bank_of(("glu", i)).rearrange("p (m t) -> p m t", t=T)
                for m in range(2):
                    for k in range(KC):
                        last = mm(ps[:, m, :], w[:, k, m * P:(m + 1) * P], hT3[:, k, :], k == 0, k == KC - 1)
                last.then_inc(*fills(("glu", i)))

            def mean_square(key, chunks, src, sig, count):
                eng.wait_ge(*next_bank(key))
                ps = bank_of(key)
                for k in range(chunks):
                    eng.wait_ge(done(sig), count(k))
                    last = mm(ps[:, 0:T], ones, src[:, k, :], k == 0, k == chunks - 1)
                last.then_inc(*fills(key))

            def project(name, x, n_cols, chunks=KC, ready=None, pool="a"):
                for i in range((n_cols + 255) // 256):
                    m = min(256, n_cols - 256 * i)
                    w, landed = panel()
                    eng.wait_ge(*landed)
                    key = (*name, i) if isinstance(name, tuple) else (name, i)
                    eng.wait_ge(*next_bank(key, pool))
                    ps = bank_of(key).rearrange("p (m t) -> p m t", t=T)
                    for j in range(m // P):
                        for k in range(chunks):
                            if ready and i == 0 and j == 0:
                                eng.wait_ge(done(ready[0]), ready[1] + k + 1)
                            last = mm(ps[:, j, :], w[:, k, j * P:(j + 1) * P], x[:, k, :], k == 0, k == chunks - 1)
                    last.then_inc(*fills(key))

            def swiglu(l, h_base, extra):
                for i in range(4):
                    eng.wait_ge(*next_bank(("dn", l, i), "b"))
                dn = [bank_of(("dn", l, i)).rearrange("p (m t) -> p m t", t=T) for i in range(4)]

                def down(j):
                    w, landed = panel()
                    eng.wait_ge(*landed)
                    for kk in range(2):
                        eng.wait_ge(*emptied_at(("gu", l, 2 * j + kk)))
                        for c in range(KC):
                            last = eng.matmul(dn[c // 2][:, c % 2, :], w[:, kk, c * P:(c + 1) * P],
                                              hid[:, 2 * j + kk, :], start=(j == 0 and kk == 0 and c % 2 == 0),
                                              stop=(j == NDN - 1 and kk == 1), skip_group_check=True)
                            if j == NDN - 1 and kk == 1 and c % 2:
                                last.then_inc(*fills(("dn", l, c // 2)))
                    if j < NDN - 1:
                        last.then_inc(*pe.signals("down_used"))

                for j in range(NDN):
                    g, landed = panel()
                    eng.wait_ge(*landed)
                    u, landed = panel()
                    eng.wait_ge(*landed)
                    for m in range(2):
                        c = 2 * j + m
                        eng.wait_ge(*next_bank(("gu", l, c)))
                        ps = bank_of(("gu", l, c)).rearrange("p (m t) -> p m t", t=T)
                        for i, w in enumerate((g, u)):
                            for k in range(KC):
                                if c == 0 and i == 0:
                                    eng.wait_ge(done("h_ready"), h_base + k + 1)
                                last = mm(ps[:, i, :], w[:, k, m * P:(m + 1) * P], hT3[:, k, :], k == 0, k == KC - 1)
                        last.then_inc(*fills(("gu", l, c)))
                    extra(j)
                    if j:
                        down(j - 1)
                down(NDN - 1)

            def attend(at):
                def scores(u):
                    key = ("s", at.name, u)
                    eng.wait_ge(*next_bank(key))
                    ps = bank_of(key)
                    mm(ps[:, 0:at.keys(u)], at.query(u), at.key(u)).then_inc(*fills(key))

                def transposes(u):
                    key = ("pt", at.name, u)
                    eng.wait_ge(done("prob_" + at.name), u + 1)
                    eng.wait_ge(*next_bank(key, "b"))
                    ps = bank_of(key).rearrange("p (b q) -> p b q", q=P)
                    for kb in range(at.keys(u) // P):
                        last = eng.transpose(ps[:, kb, :], at.pslots[:, u % 4, kb * P:(kb + 1) * P], ident)
                    last.then_inc(*fills(key))

                def values(u):
                    key = ("o", at.name, u)
                    eng.wait_ge(*emptied_at(("pt", at.name, u)))
                    eng.wait_ge(*next_bank(key, "b"))
                    ps = bank_of(key)
                    r, m = at.width(u)
                    nb = at.keys(u) // P
                    for kb in range(nb):
                        last = mm(ps[r:r + m, 0:P], at.value(u, kb), at.tslots[:, u % 4, kb * P:(kb + 1) * P],
                                  kb == 0, kb == nb - 1)
                    last.then_inc(*fills(key))

                for u in range(at.n + 2):
                    if u < at.n:
                        scores(u)
                    if 1 <= u <= at.n:
                        transposes(u - 1)
                    if u >= 2:
                        values(u - 2)

            mean_square(("ms", 1), KC, sq3, "squares", lambda k: 2 * 0 + k // 4 + 1)
            swiglu(0, 0, lambda j: ada_columns({2: 3, 4: 4, 7: 5}[j]) if j in (2, 4, 7) else None)
            ada_columns(6)
            mean_square(("ms", 2), KC, sq3, "squares", lambda k: 2 * 1 + k // 4 + 1)
            w, landed = panel()
            eng.wait_ge(*landed)
            eng.wait_ge(*next_bank("ckv"))
            ps = bank_of("ckv").rearrange("p (m t) -> p m t", t=T)
            for m in range(2):
                for k in range(KC):
                    if m == 0:
                        eng.wait_ge(done("h_ready"), KC + k + 1)
                    last = mm(ps[:, m, :], w[:, k, m * P:(m + 1) * P], hT3[:, k, :], k == 0, k == KC - 1)
            last.then_inc(*fills("ckv"))
            w, landed = panel()
            eng.wait_ge(*landed)
            eng.wait_ge(*next_bank("krope"))
            ps = bank_of("krope")
            for k in range(KC):
                last = mm(ps[DN:DQK, 0:T], w[:, k, :], hT3[:, k, :], k == 0, k == KC - 1)
            last.then_inc(*fills("krope"))
            project("cq", h2, RQ, ready=("h_ready", 2 * KC))
            mean_square("ms_ckv", 2, sq3, "ckv_squares", lambda k: 1)
            mean_square("ms_cq", 2, sq3[:, 2:4, :], "cq_squares", lambda k: 1)
            eng.wait_ge(done("ckv_ready"), 2)
            for hh in range(2):
                w, landed = panel()
                eng.wait_ge(*landed)
                for i in range(4):
                    key = ("kn", 4 * hh + i)
                    eng.wait_ge(*next_bank(key))
                    ps = bank_of(key).rearrange("p (m t) -> p m t", t=T)
                    for m in range(2):
                        h = 2 * i + m
                        for k in range(2):
                            last = mm(ps[0:DN, m, :], w[:, k, h * P:h * P + DN], latent[0][:, k, :], k == 0, k == 1)
                    last.then_inc(*fills(key))
                for b in range(2):
                    key = ("v1", hh, b)
                    eng.wait_ge(*next_bank(key, "b"))
                    ps = bank_of(key)
                    for k in range(2):
                        last = mm(ps, latent[0][:, k, b * P:(b + 1) * P],
                                  w[:, k, :].rearrange("p (h n) -> p h n", n=P)[:, :, DN:P], k == 0, k == 1)
                    last.then_inc(*fills(key))
            for i in range(8):
                key = ("km", i)
                eng.wait_ge(*emptied_at(("kn", i)))
                eng.wait_ge(done("k_squares"), i + 1)
                eng.wait_ge(*next_bank(key))
                ps = bank_of(key)
                mm(ps[0:DN, :], con("qk_mean")[0:DN, 0:DN], wide[0:DN, i * 512:(i + 1) * 512]).then_inc(*fills(key))
            eng.wait_ge(done("krope_squares"), 1)
            eng.wait_ge(*next_bank("krope_m"))
            ps = bank_of("krope_m")
            mm(ps[DN:DQK, 0:T], con("qk_mean")[DN:DQK, DN:DQK], krope_sq[DN:DQK, :]).then_inc(*fills("krope_m"))
            eng.wait_ge(done("cq_ready"), 2)
            for hh in range(2):
                w, landed = panel()
                eng.wait_ge(*landed)
                for i in range(4):
                    key = ("q", 4 * hh + i)
                    eng.wait_ge(*next_bank(key, "b"))
                    ps = bank_of(key).rearrange("p (m t) -> p m t", t=T)
                    for m in range(2):
                        h = 2 * i + m
                        for k in range(2):
                            last = mm(ps[0:DQK, m, :], w[:, k, h * DQK:(h + 1) * DQK], latent[1][:, k, :], k == 0, k == 1)
                    last.then_inc(*fills(key))
            eng.wait_ge(done("krope_normed"), 1)
            eng.wait_ge(*next_bank("krope_r"))
            ps = bank_of("krope_r")
            mm(ps[DN:DQK, 0:T], con("rotate")[DN:DQK, DN:DQK], krope[DN:DQK, :]).then_inc(*fills("krope_r"))
            for i in range(8):
                key = ("qm", i)
                eng.wait_ge(done("q_squares"), i + 1)
                eng.wait_ge(*next_bank(key))
                ps = bank_of(key)
                mm(ps[0:DQK, :], con("qk_mean")[0:DQK, 0:DQK], wide[0:DQK, i * 512:(i + 1) * 512])\
                    .then_inc(*fills(key))
            for i in range(8):
                key = ("qr", i)
                eng.wait_ge(done("q_normed"), i + 1)
                eng.wait_ge(*next_bank(key, "b"))
                ps = bank_of(key)
                mm(ps[DN:DQK, :], con("rotate")[DN:DQK, DN:DQK], qh[DN:DQK, 2 * i:2 * i + 2, :].rearrange("p h t -> p (h t)"))\
                    .then_inc(*fills(key))
            eng.wait_ge(done("qk_ready"), 1)
            attend(mla)
            eng.wait_ge(*emptied_at(("o", "mla", mla.n - 1)))
            project("wo1", o1, D)
            mean_square(("ms", 3), KC, sq3, "squares", lambda k: 2 * 2 + k // 4 + 1)
            swiglu(1, 3 * KC, lambda j: None)
            eng.wait_ge(done("mem_landed"), 16)
            for i in range(4):
                eng.wait_ge(*next_bank(("memT", i)))
                ps = bank_of(("memT", i)).rearrange("p (k b t) -> p k b t", k=2, b=2)
                for k in range(2):
                    for b in range(2):
                        last = eng.transpose(ps[:, k, b, :], mem_nat[:, b, (2 * i + k) * P:(2 * i + k + 1) * P], ident)
                last.then_inc(*fills(("memT", i)))
            mean_square("ms_mem", KC, mem_sq, "mem_squares", lambda k: 1)
            for l in range(2):
                project(("k_mem", l), memn[l], MW,
                        ready=("memn_ready", KC * l))
                w, landed = panel()
                eng.wait_ge(*landed)
                eng.wait_ge(*next_bank(("v_mem", l, 0)))
                ps = bank_of(("v_mem", l, 0)).rearrange("p (b n) -> p b n", n=MW)
                for b in range(2):
                    for k in range(KC):
                        last = mm(ps[:, b, :], memn[l][:, k, b * P:(b + 1) * P], w[:, k, :], k == 0, k == KC - 1)
                last.then_inc(*fills(("v_mem", l, 0)))

            mean_square(("ms", 4), KC, sq3, "squares", lambda k: 2 * 3 + k // 4 + 1)
            project("a_in", hT3, A_IN, ready=("h_scaled", 4 * KC))
            eng.wait_ge(done("w2_landed"), 32)
            eng.wait_ge(done("tanh_ready"), 1)
            eng.wait_ge(*emptied_at(("a_in", 9)))
            for i in range(NBR // 2):
                for r, key, pool in ((0, "decay", "a"), (64, "rate", "b")):
                    eng.wait_ge(*next_bank((key, i), pool))
                    ps = bank_of((key, i)).rearrange("p (m t) -> p m t", t=T)
                    for m in range(2):
                        c = 2 * i + m
                        last = mm(ps[:, m, :], w2a2[r:r + 64, c * P:(c + 1) * P], lora_in[r:r + 64, :])
                    last.then_inc(*fills((key, i)))
            for i in range(NBR // 2):
                eng.wait_ge(done("kk_squares"), 2 * i + 2)
                eng.wait_ge(*next_bank(("kks", i)))
                ps = bank_of(("kks", i))
                mm(ps, half, flat(tmp7[:, 2 * i:2 * i + 2, :])).then_inc(*fills(("kks", i)))
            HEADS = [(u, p * HD, p * CR) for u in range(8) for p in range(2)]

            def chunk(x, u, r):
                return x[r:r + HD, u // NCR, u % NCR * CR:(u % NCR + 1) * CR]

            eng.wait_ge(done("scaled7"), 3)
            for g in range(NU // 8):
                eng.wait_ge(*next_bank(("l", g)))
                ps = bank_of(("l", g)).rearrange("p (u t) -> p u t", t=CR)
                for uu in range(8):
                    for r in (0, HD):
                        u = 8 * g + uu
                        last = mm(ps[r:r + CR, uu, :], chunk(at7, u, r), chunk(a7, u, r))
                last.then_inc(*fills(("l", g)))
                for h in range(2):
                    for key, x in (("lb", a7), ("lk", k7)):
                        eng.wait_ge(*next_bank((key, g, h), "b"))
                        ps = bank_of((key, g, h)).rearrange("p (u x t) -> p u x t", x=2, t=CR)
                        for uu in range(4):
                            for r in (0, HD):
                                u = 8 * g + 4 * h + uu
                                last = mm(ps[r:r + CR, uu, :, :], chunk(x, u, r),
                                          ar7[r:r + HD, :, u // NCR, u % NCR * CR:(u % NCR + 1) * CR])
                        last.then_inc(*fills((key, g, h)))
            for key, x in (("b_tok", a7), ("k_tok", k7), ("v_tok", v7)):
                for g in range(NU // 8):
                    eng.wait_ge(*next_bank((key, g)))
                    ps = bank_of((key, g)).rearrange("p (u t) -> p u t", t=CR)
                    for uu in range(8):
                        for r in (0, HD):
                            last = mm(ps[r:r + CR, uu, :], chunk(x, 8 * g + uu, r), ident[r:r + HD, r:r + HD])
                    last.then_inc(*fills((key, g)))
            for l in range(1, 6):
                for g in range(NU // 8):
                    eng.wait_ge(done("level_mask"), l)
                    if l == 1:
                        eng.wait_ge(done("inverse_ready"), 2 * g + 2)
                    else:
                        eng.wait_ge(*emptied_at(("lx", l - 1, g)))
                        eng.wait_ge(*emptied_at(("ly", l - 1, g)))
                    eng.wait_ge(*next_bank(("lt", l, g)))
                    ps = bank_of(("lt", l, g)).rearrange("p (u t) -> p u t", t=CR)
                    for uu in range(8):
                        for r in (0, HD):
                            u, rr = 8 * g + uu, slice(r, r + CR)
                            last = mm(ps[rr, uu, :], lt_m7[rr, u, :], x7[rr, u, :])
                    last.then_inc(*fills(("lt", l, g)))
                for g in range(NU // 8):
                    eng.wait_ge(*emptied_at(("lt", l, g)))
                    for key, w, x in (("lx", y7, lt_t7), ("ly", lt_t7, y7)):
                        if key == "lx" and l == 5:
                            continue
                        eng.wait_ge(*next_bank((key, l, g), "b"))
                        ps = bank_of((key, l, g)).rearrange("p (u t) -> p u t", t=CR)
                        for uu in range(8):
                            for r in (0, HD):
                                u, rr = 8 * g + uu, slice(r, r + CR)
                                last = mm(ps[rr, uu, :], w[rr, u, :], x[rr, u, :])
                        last.then_inc(*fills((key, l, g)))
            for g in range(3):
                eng.wait_ge(*emptied_at(("ly", 5, g)))
                eng.wait_ge(*emptied_at(("b_tok", g)))
                eng.wait_ge(*emptied_at(("k_tok", g)))
                eng.wait_ge(*emptied_at(("v_tok", g)))
            for c in range(NCR):
                S = state7[c % 2]
                if c == 1:
                    eng.wait_ge(*emptied_at(("state", 0)))
                elif c:
                    eng.wait_ge(done("state_ready"), c - 1)
                eng.wait_ge(*next_bank(("rhs", c)))
                ps = bank_of(("rhs", c)).rearrange("p (i t) -> p i t", t=CR)[:, 0:NBR, :]
                for i in range(NBR):
                    for r in (0, HD):
                        u, rr = NCR * i + c, slice(r, r + CR)
                        if c:
                            mm(ps[rr, i, :], chunk(at7, u, r), S[rr, i, :], True, False)
                        last = mm(ps[rr, i, :], lak7[rr, u, :], v_tok[rr, u, :], c == 0, True)
                last.then_inc(*fills(("rhs", c)))
                eng.wait_ge(*emptied_at(("rhs", c)))
                eng.wait_ge(*next_bank(("sa", c), "b"))
                ps = bank_of(("sa", c)).rearrange("p (i t) -> p i t", t=CR)[:, 0:NBR, :]
                for i in range(NBR):
                    for r in (0, HD):
                        u, rr = NCR * i + c, slice(r, r + CR)
                        last = mm(ps[rr, i, :], y7[rr, u, :], rhs7[rr, i, :])
                last.then_inc(*fills(("sa", c)))
                eng.wait_ge(*emptied_at(("sa", c)))
                if c < NCR - 1:
                    eng.wait_ge(*next_bank(("state", c)))
                    ps = bank_of(("state", c)).rearrange("p (i t) -> p i t", t=CR)[:, 0:NBR, :]
                    for i in range(NBR):
                        for r in (0, HD):
                            u, rr = NCR * i + c, slice(r, r + CR)
                            mm(ps[rr, i, :], b_tok[rr, u, :], sa7[rr, i, :], True, False)
                            last = mm(ps[rr, i, :], k_tok[rr, u, :], v_tok[rr, u, :], False, True)
                    last.then_inc(*fills(("state", c)))
                eng.wait_ge(*next_bank(("y7", c), "b"))
                ps = bank_of(("y7", c)).rearrange("p (i t) -> p i t", t=CR)[:, 0:NBR, :]
                for i in range(NBR):
                    for r in (0, HD):
                        u, rr = NCR * i + c, slice(r, r + CR)
                        if c:
                            mm(ps[rr, i, :], S[rr, i, :], chunk(rt7, u, r), True, False)
                        mm(ps[rr, i, :], sa7[rr, i, :], lrb7[rr, u, :], c == 0, False)
                        last = mm(ps[rr, i, :], v_tok[rr, u, :], lrk7[rr, u, :], False, True)
                last.then_inc(*fills(("y7", c)))
            attend(memory(0))
            eng.wait_ge(*emptied_at(("y7", NCR - 1)))
            for i in range(3):
                eng.wait_ge(*next_bank(("mean7", i)))
                ps = bank_of(("mean7", i))
                mm(ps, half, flat(yT7[:, 2 * i:2 * i + 2, :])).then_inc(*fills(("mean7", i)))
            for i in range(3):
                eng.wait_ge(*next_bank(("bonus", i), "b"))
                ps = bank_of(("bonus", i))
                mm(ps, half, flat(tmp7[:, 2 * i:2 * i + 2, :])).then_inc(*fills(("bonus", i)))
            for i in range(3):
                eng.wait_ge(done("y7_squares"), i + 1)
                eng.wait_ge(*next_bank(("var7", i)))
                ps = bank_of(("var7", i))
                mm(ps, half, flat(y_sq7[:, 2 * i:2 * i + 2, :])).then_inc(*fills(("var7", i)))

            def output(l):
                project(("out", l), hT3, D, ready=("mixed", KC * l))
                mean_square(("ms_out", l), KC, out_sq[l], "out_squares", lambda k: 4 * l + k // 2 + 1)

            output(0)
            mean_square(("ms", 5), KC, sq3, "squares", lambda k: 2 * 4 + k // 4 + 1)
            project("k_sh", h_kv, BR, ready=("h_scaled", 5 * KC))
            for i in range(3):
                w, landed = panel()
                eng.wait_ge(*landed)
                eng.wait_ge(*next_bank(("v_sh", i)))
                ps = bank_of(("v_sh", i)).rearrange("p (b n) -> p b n", n=256)
                for b in range(2):
                    for k in range(KC):
                        last = mm(ps[:, b, :], h_kv[:, k, b * P:(b + 1) * P], w[:, k, :], k == 0, k == KC - 1)
                last.then_inc(*fills(("v_sh", i)))
            project("b_in", hT3, B_IN, ready=("h_scaled", 6 * KC))
            eng.wait_ge(done("lam_products"), 2)
            eng.wait_ge(*next_bank("lam2"))
            ps = bank_of("lam2")
            mm(ps[:, 0:2], ones, columns2[:, 32:34]).then_inc(*fills("lam2"))
            for i in range(3):
                eng.wait_ge(*emptied_at(("v_sh", i)))
                eng.wait_ge(*emptied_at(("b_in", i)))
            for u in range(ND + 2):
                if u < ND:
                    h, b = u // 2, u % 2
                    for c in range(2):
                        r = slice(c * HD, (c + 1) * HD)
                        eng.wait_ge(*next_bank(("ds", u, c)))
                        ps = bank_of(("ds", u, c))
                        mm(ps[:, 0:P * (b + 1)], qT[r, h, b * P:(b + 1) * P], kT[r, h, 0:P * (b + 1)])\
                            .then_inc(*fills(("ds", u, c)))
                if 1 <= u <= ND:
                    w = u - 1
                    eng.wait_ge(done("prob_diff"), w + 1)
                    eng.wait_ge(*next_bank(("dpt", w), "b"))
                    ps = bank_of(("dpt", w)).rearrange("p (b q) -> p b q", q=P)
                    for kb in range(w % 2 + 1):
                        last = eng.transpose(ps[:, kb, :], both[:, w % 3, 0, kb * P:(kb + 1) * P], ident)
                    last.then_inc(*fills(("dpt", w)))
                if u >= 2:
                    w = u - 2
                    eng.wait_ge(*emptied_at(("dpt", w)))
                    eng.wait_ge(*next_bank(("do", w), "b"))
                    ps = bank_of(("do", w))
                    for kb in range(w % 2 + 1):
                        last = mm(ps[:, 0:P], v_sh[:, kb, w // 2 * P:(w // 2 + 1) * P], tslots2[:, w % 4, kb * P:(kb + 1) * P],
                                  kb == 0, kb == w % 2)
                    last.then_inc(*fills(("do", w)))
            attend(memory(1))
            for i in range(3):
                eng.wait_ge(done("o_squares"), i + 1)
                eng.wait_ge(*next_bank(("sub", i)))
                ps = bank_of(("sub", i))
                mm(ps, ones, flat(o_sq[:, 2 * i:2 * i + 2, :])).then_inc(*fills(("sub", i)))
            output(1)
            eng.wait_ge(done("post_added"), 2 * KC)
            for i in range(4):
                eng.wait_ge(*next_bank(("rows", i)))
                ps = bank_of(("rows", i)).rearrange("p (k n) -> p k n", n=P)
                for k in range(4):
                    last = eng.transpose(ps[:, k, :], xT3[:, i % 2 * 4 + k, i // 2 * P:(i // 2 + 1) * P], ident)
                last.then_inc(*fills(("rows", i)))

        @block.sync
        def _(sp):
            sp.dma_start(xN, a["x"][0].rearrange("(b p) d -> p b d", p=P)).then_inc(done("x_landed"), 16)
            sp.dma_start(xC_in, a["x"][0].rearrange("(c s) d -> c s d", s=L5)).then_inc(done("xc_landed"), 16)

            def load(i):
                if i >= RING:
                    key = weights[i - RING][2]
                    if key[0] == "down":
                        sp.wait_ge(done("down_used"), (NDN - 1) * key[1] + key[2] + 1)
                    else:
                        sp.wait_ge(*filled_at(key))
                sp.dma_start(slot(i), weights[i][0]).then_inc(panel_landed[i % RING], 16)

            first = RING
            sp.wait_ge(done("xc_scaled"), 8)
            for i in range(first):
                load(i)
            sp.wait_ge(done("toeplitz_clear"), 1)
            for b in range(NB5):
                for i in range(2):
                    kb, kn = use[("kern", b, i)]
                    sp.wait_ge(emptied[kb], kn)
                for s in range(L5):
                    sp.dma_start(toep[s * P5:(s + 1) * P5, 8 * b:8 * b + 8, s * P5:P],
                                 kern[s * P5:(s + 1) * P5, :, 0:P - s * P5]).then_inc(done("toeplitz_landed"), 16)
            for i in range(first, len(weights)):
                load(i)
            for i in range(4):
                b, n = use[("rows", i)]
                sp.wait_ge(emptied[b], n)
                sp.dma_start(out[0][i // 2 * P:(i // 2 + 1) * P, i % 2 * 512:i % 2 * 512 + 512],
                             out_rows[:, i // 2, i % 2 * 512:i % 2 * 512 + 512]).then_inc(done("out_written"), 16)
            sp.wait_ge(done("out_written"), 16 * 4)

        @block.vector
        def _(eng):
            v = Program("vector")
            V = nc.vector

            def tt(dst, x, y, op):
                return V.tensor_tensor(dst, x, y, op)

            def ts(dst, x, s1, s2, op0, op1=ALU.bypass):
                return V.tensor_scalar(dst, x, s1, s2, op0, op1)

            def stt(dst, x, s, y, op0, op1):
                return V.scalar_tensor_tensor(dst, x, s, y, op0, op1)

            ada_next = [0]

            def ada_panel():
                i = ada_next[0]
                ada_next[0] += 1
                blk, k = i // 8, i % 8
                eng.wait_ge(ada_landed[i % ARING], 16 * (i // ARING + 1))
                w = aring[:, (i % ARING) * PANEL:(i % ARING + 1) * PANEL]
                if i == 0:
                    eng.wait_ge(done("c_act_ready"), 1)
                if k == 0:
                    if blk:
                        eng.wait_ge(*filled_at(("ada", blk - 1) if blk > 1 else ("ada0", 3)))
                    ts(acc[:, :], w, c_act[:, 0:1], None, ALU.mult).then_inc(*v.signals("ada_used"))
                else:
                    eng.wait_ge(done("ada_used"), i)
                    stt(acc[:, :], w, c_act[:, k:k + 1], acc[:, :], ALU.mult, ALU.add).then_inc(*v.signals("ada_used"))

            def ada_bias(blk):
                eng.wait_ge(*filled_at(("ada", blk)))
                ps = bank_of(("ada", blk))
                name, at = ("ada_b", 16 * blk) if blk < 6 else ("kv_ada_b", 0)
                tt(ada[:, blk * 16:blk * 16 + 16], ps[:, 0:16], cols(name, at, 16), ALU.add)\
                    .then_inc(*v.empties(("ada", blk)))

            V.memset(rows[:, :], 0.0).then_inc(*v.signals("rows_clear"))
            for i in range(3):
                eng.wait_ge(*filled_at(("vec", i)))
                ps = bank_of(("vec", i))
                V.tensor_copy(vec[:, i * P:i * P + VEC_N[i]], ps[:, 0:VEC_N[i]]).then_inc(*v.empties(("vec", i)))

            eng.wait_ge(done("s5_landed"), 16 * 11)
            for m in range(4):
                V.tensor_copy(group_rep[:, m, :].rearrange("g (s q) -> g s q", q=P5),
                              group_rows[:, m, :].unsqueeze(1).to_broadcast([G5, L5, P5]))\
                    .then_inc(*(v.signals("group_rows_ready") if m == 3 else v.step()))
            eng.wait_ge(done("xc_squares"), 8)
            ts(ss[:, 1, :], ss[:, 0, :], 1.0 / D, EPS, ALU.mult, ALU.add).then_inc(*v.signals("xc_mean"))
            eng.wait_ge(done("xc_root"), 1)
            V.reciprocal(ss[:, 0, :], ss[:, 2, :]).then_inc(*v.step())
            eng.wait_ge(*v.last)
            for s in range(L5):
                ts(xC[:, :, s, :], xC_in[:, s, :].rearrange("c (g q) -> c g q", q=P5), ss[:, 0, s:s + 1], None, ALU.mult)\
                    .then_inc(*v.signals("xc_scaled"))

            eng.wait_ge(*filled_at("lam"))
            ps = bank_of("lam").rearrange("p (m j) -> p m j", j=J5)
            V.tensor_copy(small[:, 0:3, :], ps[:, 0:3, :]).then_inc(*v.empties("lam"))
            lr, li, dt = small[:, 0, :], small[:, 1, :], small[:, 3, :]
            eng.wait_ge(*v.last)
            V.tensor_copy(small[:, 4, :], small[:, 2, :]).then_inc(*v.signals("log_dt_ready"))
            eng.wait_ge(done("dt_ready"), 1)
            tt(small[:, 5, :], lr, dt, ALU.mult).then_inc(*v.signals("decay_ready"))
            tt(small[:, 6, :], li, dt, ALU.mult).then_inc(*v.step())
            eng.wait_ge(*v.last)
            ts(small[:, 7, :], small[:, 6, :], 1.0 / TWO_PI, ROUND, ALU.mult, ALU.add).then_inc(*v.step())
            eng.wait_ge(*v.last)
            ts(small[:, 8, :], small[:, 7, :], -ROUND, None, ALU.add).then_inc(*v.step())
            for part in (PI2_A, PI2_B, PI2_C):
                eng.wait_ge(*v.last)
                stt(small[:, 6, :], small[:, 8, :], -part, small[:, 6, :], ALU.mult, ALU.add).then_inc(*v.step())
            eng.wait_ge(*v.last)
            ts(small[:, 6, :], small[:, 6, :], math.pi * (1 - 1e-7), -math.pi * (1 - 1e-7), ALU.min, ALU.max)\
                .then_inc(*v.step())
            eng.wait_ge(*v.last)
            ts(small[:, 7, :], small[:, 6, :], math.pi / 2, None, ALU.add).then_inc(*v.step())
            eng.wait_ge(*v.last)
            ts(small[:, 8, :], small[:, 7, :], math.pi, -TWO_PI, ALU.is_gt, ALU.mult).then_inc(*v.step())
            eng.wait_ge(*v.last)
            tt(small[:, 7, :], small[:, 7, :], small[:, 8, :], ALU.add).then_inc(*v.step())
            eng.wait_ge(*v.last)
            ts(small[:, 7, :], small[:, 7, :], math.pi * (1 - 1e-7), -math.pi * (1 - 1e-7), ALU.min, ALU.max)\
                .then_inc(*v.signals("angles_ready"))
            eng.wait_ge(done("poles_ready"), 3)
            tt(powr[:, 1, :], small[:, 9, :], small[:, 11, :], ALU.mult).then_inc(*v.step())
            tt(powi[:, 1, :], small[:, 9, :], small[:, 10, :], ALU.mult).then_inc(*v.step())
            V.memset(powr[:, 0, :], 1.0).then_inc(*v.step())
            V.memset(powi[:, 0, :], 0.0).then_inc(*v.step())
            eng.wait_ge(*v.last)
            tt(small[:, 12, :], lr, lr, ALU.mult).then_inc(*v.step())
            tt(small[:, 13, :], li, li, ALU.mult).then_inc(*v.step())
            ts(small[:, 14, :], powr[:, 1, :], -1.0, None, ALU.add).then_inc(*v.step())
            eng.wait_ge(*v.last)
            tt(small[:, 12, :], small[:, 12, :], small[:, 13, :], ALU.add).then_inc(*v.step())
            eng.wait_ge(*v.last)
            V.reciprocal(small[:, 13, :], small[:, 12, :]).then_inc(*v.step())
            tt(small[:, 15, :], small[:, 14, :], lr, ALU.mult).then_inc(*v.step())
            tt(small[:, 16, :], powi[:, 1, :], li, ALU.mult).then_inc(*v.step())
            tt(small[:, 17, :], powi[:, 1, :], lr, ALU.mult).then_inc(*v.step())
            tt(small[:, 18, :], small[:, 14, :], li, ALU.mult).then_inc(*v.step())
            eng.wait_ge(*v.last)
            tt(small[:, 15, :], small[:, 15, :], small[:, 16, :], ALU.add).then_inc(*v.step())
            tt(small[:, 17, :], small[:, 17, :], small[:, 18, :], ALU.subtract).then_inc(*v.step())
            eng.wait_ge(*v.last)
            tt(small[:, 19, :], small[:, 15, :], small[:, 13, :], ALU.mult).then_inc(*v.step())
            tt(small[:, 20, :], small[:, 17, :], small[:, 13, :], ALU.mult).then_inc(*v.step())
            for m in (1, 2, 4):
                pr = powr[:, m, :].unsqueeze(1).to_broadcast([P, m, J5])
                pi = powi[:, m, :].unsqueeze(1).to_broadcast([P, m, J5])
                xr, xi = powr[:, 1:m + 1, :], powi[:, 1:m + 1, :]
                q = [tmp5[:, n * 128:n * 128 + m * J5].rearrange("p (k j) -> p k j", j=J5) for n in range(4)]
                eng.wait_ge(*v.last)
                tt(q[0], xr, pr, ALU.mult).then_inc(*v.step())
                tt(q[1], xi, pi, ALU.mult).then_inc(*v.step())
                tt(q[2], xr, pi, ALU.mult).then_inc(*v.step())
                tt(q[3], xi, pr, ALU.mult).then_inc(*v.step())
                eng.wait_ge(*v.last)
                tt(powr[:, m + 1:2 * m + 1, :], q[0], q[1], ALU.subtract).then_inc(*v.step())
                tt(powi[:, m + 1:2 * m + 1, :], q[2], q[3], ALU.add).then_inc(*v.step())
            eng.wait_ge(*v.last)
            for s in range(L5):
                V.tensor_copy(prv[:, 0, :, s], powr[:, L5 - 1 - s, :]).then_inc(*v.step())
                V.tensor_copy(prv[:, 1, :, s], powi[:, L5 - 1 - s, :]).then_inc(*v.step())
            V.tensor_copy(step4[:, 0, 0, :], powr[:, L5, :]).then_inc(*v.step())
            ts(step4[:, 0, 1, :], powi[:, L5, :], -1.0, None, ALU.mult).then_inc(*v.step())
            V.tensor_copy(step4[:, 1, 0, :], powi[:, L5, :]).then_inc(*v.step())
            V.tensor_copy(step4[:, 1, 1, :], powr[:, L5, :]).then_inc(*v.step())
            for m in range(4):
                eng.wait_ge(*emptied_at(("raw", m)))
            fr = small[:, 19, :].unsqueeze(2).to_broadcast([P, J5, P5])
            fi = small[:, 20, :].unsqueeze(2).to_broadcast([P, J5, P5])
            q = [tmp5[:, n * 512:(n + 1) * 512].rearrange("p (j q) -> p j q", q=P5) for n in range(2)]
            for i, (f0, f1, op) in enumerate(((fr, fi, ALU.subtract), (fi, fr, ALU.add))):
                eng.wait_ge(*v.last)
                tt(q[0], bt[:, 0, :, :], f0, ALU.mult).then_inc(*v.step())
                tt(q[1], bt[:, 1, :, :], f1, ALU.mult).then_inc(*v.step())
                eng.wait_ge(*v.last)
                tt(bb[:, i, :, :], q[0], q[1], op).then_inc(*v.signals("bb_ready"))
            V.memset(toep, 0.0).then_inc(*v.signals("toeplitz_clear"))
            eng.wait_ge(*filled_at("grp"))
            ps = bank_of("grp").rearrange("p (m g) -> p m g", g=G5)
            V.tensor_copy(grp, ps[:, 0:4, :]).then_inc(*v.empties("grp"))

            for k in range(8):
                ada_panel()
            for i in range(4):
                eng.wait_ge(*filled_at(("ada0", i)))
                ps = bank_of(("ada0", i)).rearrange("p (g q) -> p g q", q=P5)
                pk = pick[:, 0:512].rearrange("p (g q) -> p g q", q=P5)
                eng.wait_ge(*v.last)
                tt(pk, ps, con("diag16").unsqueeze(1).to_broadcast([P, 32, P5]), ALU.mult)\
                    .then_inc(*v.empties(("ada0", i)))
                eng.wait_ge(*v.last)
                V.tensor_reduce(gmod[:, i // 2, (i % 2) * 32:(i % 2) * 32 + 32], pk, AX_X, ALU.add).then_inc(*v.step())
            eng.wait_ge(*v.last)
            tt(gmod, gmod, grp[:, 1:3, :], ALU.add).then_inc(*v.step())
            eng.wait_ge(*v.last)
            stt(gmod[:, 1, :], gmod[:, 1, :], 1.0, grp[:, 0, :], ALU.add, ALU.mult).then_inc(*v.step())
            for i in range(4):
                eng.wait_ge(*emptied_at(("U", i)))
            eng.wait_ge(*v.last)
            tt(U, U, gmod[:, 1, :].unsqueeze(2).to_broadcast([P, G5, C5]), ALU.mult).then_inc(*v.step())
            eng.wait_ge(*v.last)
            tt(U, U, gmod[:, 0, :].unsqueeze(2).to_broadcast([P, G5, C5]), ALU.add).then_inc(*v.signals("u_ready"))

            for b in range(NB5):
                js = slice(b * BJ, (b + 1) * BJ)
                if b:
                    eng.wait_ge(*filled_at(("w", b - 1, 1)))
                for i, (n0, n1, op) in enumerate(((0, 1, ALU.subtract), (1, 0, ALU.add))):
                    w0 = prv[:, n0, js, :].unsqueeze(3).to_broadcast([P, BJ, L5, P5])
                    w1 = prv[:, n1, js, :].unsqueeze(3).to_broadcast([P, BJ, L5, P5])
                    q = [tmp5[:, n * 512:(n + 1) * 512].rearrange("p (j s q) -> p j s q", s=L5, q=P5)
                         for n in range(2)]
                    eng.wait_ge(*v.last)
                    tt(q[0], w0, bb[:, 0, js, :].unsqueeze(2).to_broadcast([P, BJ, L5, P5]), ALU.mult)\
                        .then_inc(*v.step())
                    tt(q[1], w1, bb[:, 1, js, :].unsqueeze(2).to_broadcast([P, BJ, L5, P5]), ALU.mult)\
                        .then_inc(*v.step())
                    eng.wait_ge(*v.last)
                    tt(aB[:, i, :, :].rearrange("p j (s q) -> p j s q", q=P5), q[0], q[1], op)\
                        .then_inc(*v.signals("ab_ready"))
                for i, (n0, n1) in enumerate(((0, 1), (1, 0))):
                    w0 = (powr, powi)[n0][:, :, js].rearrange("p k j -> p j k").unsqueeze(3).to_broadcast([P, BJ, 9, P5])
                    w1 = (powr, powi)[n1][:, :, js].rearrange("p k j -> p j k").unsqueeze(3).to_broadcast([P, BJ, 9, P5])
                    q = [tmp5[:, n * 576:(n + 1) * 576].rearrange("p (j k q) -> p j k q", k=9, q=P5)
                         for n in range(2)]
                    eng.wait_ge(*v.last)
                    tt(q[0], w0, ct[:, 0, js, :].unsqueeze(2).to_broadcast([P, BJ, 9, P5]), ALU.mult)\
                        .then_inc(*v.step())
                    tt(q[1], w1, ct[:, 1, js, :].unsqueeze(2).to_broadcast([P, BJ, 9, P5]), ALU.mult)\
                        .then_inc(*v.step())
                    eng.wait_ge(*v.last)
                    if i == 0:
                        tt(ca_re[:, js, :, :], q[0], q[1], ALU.subtract).then_inc(*v.signals("ca_ready"))
                    else:
                        f = [tmp5[:, n * 576:(n + 1) * 576] for n in range(2)]
                        stt(ca_im[:, js, :, :].rearrange("p j k q -> p (j k q)"), f[0], -1.0, f[1], ALU.mult,
                            ALU.subtract)\
                            .then_inc(*v.signals("ca_ready"))
                ada_panel()
                ada_panel()
                if b == 4:
                    ada_bias(1)
            ada_bias(2)

            for b in range(4, NB5):
                eng.wait_ge(*emptied_at(("bu", b)))
            V.memset(st[:, 0, :, :], 0.0).then_inc(*v.step())
            for c in range(C5 - 1):
                eng.wait_ge(*v.last)
                tt(part4, step4, st[:, c, :, :].unsqueeze(1).to_broadcast([P, 2, 2, J5]), ALU.mult).then_inc(*v.step())
                eng.wait_ge(*v.last)
                tt(part2, part4[:, :, 0, :], BU[:, c, :, :], ALU.add).then_inc(*v.step())
                eng.wait_ge(*v.last)
                tt(st[:, c + 1, :, :], part2, part4[:, :, 1, :], ALU.add)\
                    .then_inc(*(v.signals("states_ready") if c == C5 - 2 else v.step()))
            eng.wait_ge(*v.last)
            tt(gS, U, grp[:, 3, :].unsqueeze(2).to_broadcast([P, G5, C5]), ALU.mult).then_inc(*v.step())
            eng.wait_ge(*v.last)
            for i in range(4):
                eng.wait_ge(*filled_at(("y5", i)))
                ps = bank_of(("y5", i))
                x = y5_part(i)
                tt(x, x, ps.rearrange("p (g c) -> p g c", c=C5), ALU.add).then_inc(*v.empties(("y5", i)))
            for i in range(0, 16, 2):
                eng.wait_ge(*filled_at(("gc", i)))
                ps = bank_of(("gc", i))[0:C5, :].rearrange("c (g t q) -> c t g q", g=4, t=L5)
                dst = gC[:, :, i * 64:(i + 1) * 64].rearrange("c t (g q) -> c t g q", q=P5)
                if i == 0:
                    eng.wait_ge(*filled_at(("y5", 3)))
                V.tensor_copy(dst, ps).then_inc(*v.empties(("gc", i)))
            for i in range(4):
                eng.wait_ge(*emptied_at(("glu", i)))
                for m in range(2):
                    k = 2 * i + m
                    tt(sq3[:, k, :], sq3[:, k, :], hT3[:, k, :], ALU.mult).then_inc(*v.step())
                    eng.wait_ge(*v.last)
                    stt(xT3[:, k, :], sq3[:, k, :], ada_cols(0, 2)[:, k:k + 1], xT3[:, k, :], ALU.mult, ALU.add)\
                        .then_inc(*v.signals("x_ready"))

            def inverse_root(key, n, width=T, rows=slice(0, P), dst=None, tag="root"):
                x = stat[rows, 0:width]
                eng.wait_ge(*filled_at(key))
                ps = bank_of(key)
                ts(x, ps[rows, 0:width], 1.0 / n, EPS, ALU.mult, ALU.add).then_inc(*v.empties(key))
                eng.wait_ge(done("root_ready"), roots[0] + 1)
                roots[0] += 1
                V.reciprocal(stat[rows, 2 * T:2 * T + width], stat[rows, T:T + width]).then_inc(*v.step())
                eng.wait_ge(*v.last)

            roots = [0]
            rstd = stat[:, 2 * T:3 * T]

            def scale_chunks(dst, gain, sig, chunks=KC, src=xT3):
                for k in range(chunks):
                    stt(dst[:, k, :], src[:, k, :], gain[:, k:k + 1], rstd, ALU.mult, ALU.mult)\
                        .then_inc(*v.signals(sig))

            def modulation(slot, layer, which, gain):
                g = gains[:, slot * KC:(slot + 1) * KC]
                stt(g, ada_cols(layer, which), 1.0, gain, ALU.add, ALU.mult).then_inc(*v.step())
                eng.wait_ge(*v.last)
                return g

            def swiglu(l, extra):
                for c in range(NGU):
                    eng.wait_ge(*filled_at(("gu", l, c)))
                    ps = bank_of(("gu", l, c))
                    eng.wait_ge(done("silu_ready"), l * NGU + c + 1)
                    tt(hid[:, c, :], hid[:, c, :], ps[:, T:2 * T], ALU.mult).then_inc(*v.empties(("gu", l, c)))
                    extra(c)
                for c in range(KC):
                    eng.wait_ge(*filled_at(("dn", l, c // 2)))
                    ps = bank_of(("dn", l, c // 2)).rearrange("p (m t) -> p m t", t=T)
                    stt(xT3[:, c, :], ps[:, c % 2, :], ada_cols(l, 5)[:, c:c + 1], xT3[:, c, :], ALU.mult, ALU.add)\
                        .then_inc(*(v.empties(("dn", l, c // 2)) if c % 2 else v.step()))

            def attend(at, combine=None):
                for u in range(at.n + 1):
                    if u < at.n:
                        key = ("s", at.name, u)
                        eng.wait_ge(*filled_at(key))
                        ps = bank_of(key)
                        w = at.keys(u)
                        x = at.pslots[:, u % 4, 0:w]
                        if u >= 4:
                            eng.wait_ge(*filled_at(("pt", at.name, u - 4)))
                        bias = at.bias(u)
                        if bias is None:
                            ts(x, ps[:, 0:w], at.scale, None, ALU.mult).then_inc(*v.empties(key))
                        else:
                            stt(x, ps[:, 0:w], at.scale, bias, ALU.mult, ALU.add).then_inc(*v.empties(key))
                        eng.wait_ge(*v.last)
                        V.tensor_reduce(at.soft[:, 0, u:u + 1], x, AX_X, ALU.max, negate=True)\
                            .then_inc(*v.signals("max_" + at.name))
                    if u:
                        u -= 1
                        eng.wait_ge(done("exp_" + at.name), u + 1)
                        V.reciprocal(at.soft[:, 2, u:u + 1], at.soft[:, 1, u:u + 1]).then_inc(*v.step())
                        eng.wait_ge(*v.last)
                        x = at.pslots[:, u % 4, 0:at.keys(u)]
                        ts(x, x, at.soft[:, 2, u:u + 1], None, ALU.mult).then_inc(*v.signals("prob_" + at.name))

            g = modulation(0, 0, 4, cols("norm2_g", 0, KC))
            inverse_root(("ms", 1), D)
            scale_chunks(hT3, g, "h_scaled")

            def ada_beside(c):
                for _ in range(2 if c < 10 else 1):
                    ada_panel()
                if c in (5, 9, 15):
                    ada_bias({5: 3, 9: 4, 15: 5}[c])
            swiglu(0, ada_beside)
            ada_bias(6)
            eng.wait_ge(*v.last)
            gk = modulation(1, "kv", 1, cols("kv_norm_g", 0, KC))
            gq = modulation(2, 1, 1, cols("norm1_g", KC, KC))
            inverse_root(("ms", 2), D)
            scale_chunks(hT3, gk, "h_scaled")
            scale_chunks(h2, gq, "h_scaled")
            eng.wait_ge(done("positions_landed"), 16)
            rr = slice(DN, DQK)
            ang = angle[rr, :, :]
            V.tensor_copy(ang[:, 0, :], pos_i[rr, :]).then_inc(*v.step())
            eng.wait_ge(*v.last)
            ts(ang[:, 0, :], ang[:, 0, :], inv_freq[rr, :], None, ALU.mult).then_inc(*v.step())
            eng.wait_ge(*v.last)
            ts(ang[:, 1, :], ang[:, 0, :], 1.0 / TWO_PI, ROUND, ALU.mult, ALU.add).then_inc(*v.step())
            eng.wait_ge(*v.last)
            ts(ang[:, 1, :], ang[:, 1, :], -ROUND, None, ALU.add).then_inc(*v.step())
            for part in (PI2_A, PI2_B, PI2_C):
                eng.wait_ge(*v.last)
                stt(ang[:, 0, :], ang[:, 1, :], -part, ang[:, 0, :], ALU.mult, ALU.add).then_inc(*v.step())
            eng.wait_ge(*v.last)
            ts(ang[:, 0, :], ang[:, 0, :], math.pi * (1 - 1e-7), -math.pi * (1 - 1e-7), ALU.min, ALU.max)\
                .then_inc(*v.step())
            eng.wait_ge(*v.last)
            ts(ang[:, 1, :], ang[:, 0, :], math.pi / 2, None, ALU.add).then_inc(*v.step())
            eng.wait_ge(*v.last)
            ts(ang[:, 2, :], ang[:, 1, :], math.pi, -TWO_PI, ALU.is_gt, ALU.mult).then_inc(*v.step())
            eng.wait_ge(*v.last)
            tt(ang[:, 1, :], ang[:, 1, :], ang[:, 2, :], ALU.add).then_inc(*v.step())
            eng.wait_ge(*v.last)
            ts(ang[:, 1, :], ang[:, 1, :], math.pi * (1 - 1e-7), -math.pi * (1 - 1e-7), ALU.min, ALU.max)\
                .then_inc(*v.signals("rotary_angles"))
            for i, (x, gain) in enumerate((("ckv", "kv_a_norm_g"), ("cq", "mla_q_norm_g"))):
                eng.wait_ge(*emptied_at("ckv" if i == 0 else ("cq", 0)))
                tt(sq3[:, 2 * i:2 * i + 2, :], latent[i], latent[i], ALU.mult).then_inc(*v.signals(x + "_squares"))
                inverse_root("ms_" + x, RKV)
                scale_chunks(latent[i], cols(gain, 0, 2), x + "_ready", 2, latent[i])
            eng.wait_ge(*emptied_at("krope"))
            tt(krope_sq[rr, :], krope[rr, :], krope[rr, :], ALU.mult).then_inc(*v.signals("krope_squares"))
            for i in range(8):
                eng.wait_ge(*filled_at(("km", i)))
                ps = bank_of(("km", i))
                w = wide[0:DN, i * 512:(i + 1) * 512]
                ts(w, ps[0:DN, :], EPS, None, ALU.add).then_inc(*v.empties(("km", i)))
            eng.wait_ge(*filled_at("krope_m"))
            ps = bank_of("krope_m")
            ts(stat[rr, 0:T], ps[rr, 0:T], EPS, None, ALU.add).then_inc(*v.empties("krope_m"))
            eng.wait_ge(done("root_ready"), roots[0] + 1)
            roots[0] += 1
            V.reciprocal(stat[rr, 2 * T:3 * T], stat[rr, T:2 * T]).then_inc(*v.step())
            eng.wait_ge(*v.last)
            stt(krope[rr, :], krope[rr, :], col("k_gain", 0)[rr], stat[rr, 2 * T:3 * T], ALU.mult, ALU.mult)\
                .then_inc(*v.signals("krope_normed"))
            eng.wait_ge(done("k_root"), 1)
            w = wide[0:DN, :]
            V.reciprocal(w, w).then_inc(*v.step())
            eng.wait_ge(*v.last)
            kf = kh[0:DN, :, :].rearrange("p h t -> p (h t)")
            stt(kf, kf, col("k_gain", 0)[0:DN], w, ALU.mult, ALU.mult).then_inc(*v.signals("k_normed"))
            eng.wait_ge(done("rotary_ready"), 1)
            eng.wait_ge(*filled_at("krope_r"))
            ps = bank_of("krope_r")
            sin, cos = turn[rr, 0, :], turn[rr, 1, :]
            tt(stat[rr, 0:T], ps[rr, 0:T], sin[:, 0:T], ALU.mult).then_inc(*v.empties("krope_r"))
            tt(krope[rr, :], krope[rr, :], cos[:, 0:T], ALU.mult).then_inc(*v.step())
            eng.wait_ge(*v.last)
            tt(krope[rr, :], krope[rr, :], stat[rr, 0:T], ALU.add).then_inc(*v.step())
            eng.wait_ge(*v.last)
            V.tensor_copy(kh[rr, :, :], krope[rr, :].unsqueeze(1).to_broadcast([DR, H1, T])).then_inc(*v.step())
            for i in range(8):
                eng.wait_ge(*filled_at(("qm", i)))
                ps = bank_of(("qm", i))
                w = wide[0:DQK, i * 512:(i + 1) * 512]
                ts(w, ps[0:DQK, :], EPS, None, ALU.add).then_inc(*v.empties(("qm", i)))
            for i in range(8):
                eng.wait_ge(done("q_root"), i + 1)
                w = wide[0:DQK, i * 512:(i + 1) * 512]
                V.reciprocal(w, w).then_inc(*v.step())
                eng.wait_ge(*v.last)
                x = qh[0:DQK, 2 * i:2 * i + 2, :].rearrange("p h t -> p (h t)")
                stt(x, x, col("q_gain", 0)[0:DQK], w, ALU.mult, ALU.mult).then_inc(*v.signals("q_normed"))
            for i in range(8):
                eng.wait_ge(*filled_at(("qr", i)))
                ps = bank_of(("qr", i))
                x = qh[rr, 2 * i:2 * i + 2, :].rearrange("p h t -> p (h t)")
                y = wide[rr, i * 512:(i + 1) * 512]
                tt(y, ps[rr, :], sin, ALU.mult).then_inc(*v.empties(("qr", i)))
                tt(x, x, cos, ALU.mult).then_inc(*v.step())
                eng.wait_ge(*v.last)
                tt(x, x, y, ALU.add).then_inc(*(v.signals("qk_ready") if i == 7 else v.step()))
            eng.wait_ge(done("mask_landed"), 16)
            attend(mla)
            for c in range(KC):
                eng.wait_ge(*filled_at(("wo1", c // 2)))
                ps = bank_of(("wo1", c // 2)).rearrange("p (m t) -> p m t", t=T)
                stt(xT3[:, c, :], ps[:, c % 2, :], ada_cols(1, 2)[:, c:c + 1], xT3[:, c, :], ALU.mult, ALU.add)\
                    .then_inc(*(v.empties(("wo1", c // 2)) if c % 2 else v.step()))
            g = modulation(0, 1, 4, cols("norm2_g", KC, KC))
            inverse_root(("ms", 3), D)
            scale_chunks(hT3, g, "h_scaled")
            swiglu(1, lambda c: None)
            inverse_root("ms_mem", D)
            for l in range(2):
                scale_chunks(memn[l], cols("mem_norm_2", l * KC, KC), "memn_ready", src=memT)
            eng.wait_ge(*v.last)
            keep = columns2[:, 0:19]
            ts(keep, cols("a_shift_mu_2", 0, 19), -1.0, 1.0, ALU.mult, ALU.add).then_inc(*v.step())
            keep_k = columns2[:, 19:25]
            ts(keep_k, cols("a_k_a_2", 0, 6), -1.0, 1.0, ALU.mult, ALU.add).then_inc(*v.step())
            inverse_root(("ms", 4), D)
            V.memset(shifted[:, :, :, 0:1], 0.0).then_inc(*v.signals("shift_clear"))
            scale_chunks(hT3, cols("pre_norm_2", 0, KC), "h_scaled")
            for c in range(19):
                key = ("a_in", c // 2)
                eng.wait_ge(*filled_at(key))
                ps = bank_of(key).rearrange("p (m t) -> p m t", t=T)
                eng.wait_ge(done("shift_ready"), min(c // 2 * 2 + 2, 19))
                dst = (rt7[:, c, :] if c < 6 else k7[:, c - 6, :] if c < 12 else v7[:, c - 12, :] if c < 18 else lora_in)
                stt(dst, ps[:, c % 2, :], keep[:, c:c + 1], shifted[:, c // 2 % 2, c % 2, 0:T], ALU.mult, ALU.add)\
                    .then_inc(*(v.signals("lora_shifted") if c == 18 else v.empties(key) if c % 2 else v.step()))
            for i in range(3):
                key = ("kks", i)
                eng.wait_ge(*filled_at(key))
                ps = bank_of(key)
                ts(flat(tmp7[:, 2 * i:2 * i + 2, :]), ps, 1e-12, None, ALU.max).then_inc(*v.empties(key))
            for c in range(NBR):
                ts(kk7[:, c, :], k7[:, c, :], col("a_k_k_2", c), None, ALU.mult).then_inc(*v.step())
            eng.wait_ge(done("kk_root"), 1)
            V.reciprocal(flat(tmp7), flat(tmp7)).then_inc(*v.step())
            eng.wait_ge(*v.last)
            tt(kk7, kk7, tmp7, ALU.mult).then_inc(*v.step())
            eng.wait_ge(done("masks7_landed"), 16)
            for c in range(NBR):
                eng.wait_ge(*emptied_at(("decay", c // 2)))
                V.tensor_tensor_scan(cum7[:, c, :], con7("restart"), sig7[:, c, :], 0.0, ALU.mult, ALU.add)\
                    .then_inc(*v.step())
            eng.wait_ge(*v.last)
            tt(at7, cum7, sig7, ALU.subtract).then_inc(*v.signals("cum_ready"))
            eng.wait_ge(*emptied_at(("rate", 2)))
            eng.wait_ge(*v.last)
            for c in range(NBR):
                ts(tmp7[:, c, :], a7[:, c, :], col("a_k_a_2", c), keep_k[:, c:c + 1], ALU.mult, ALU.add)\
                    .then_inc(*v.step())
            eng.wait_ge(*v.last)
            tt(k7, k7, tmp7, ALU.mult).then_inc(*v.step())
            tt(a7, a7, kk7, ALU.mult).then_inc(*v.step())
            eng.wait_ge(*v.last)
            for c in range(NBR):
                stt(tmp7[:, c, :], rt7[:, c, :], col("a_r_k_2", c), k7[:, c, :], ALU.mult, ALU.mult)\
                    .then_inc(*v.step())
            eng.wait_ge(*v.last)
            eng.wait_ge(done("exp7"), 3)
            tt(a7, a7, grow7, ALU.mult).then_inc(*v.signals("scaled7"))
            tt(k7, k7, grow7, ALU.mult).then_inc(*v.step())
            stt(flat(at7), flat(kk7), -1.0, flat(at7), ALU.mult, ALU.mult).then_inc(*v.signals("scaled7"))
            tt(rt7, rt7, cum7, ALU.mult).then_inc(*v.signals("scaled7"))
            def spread(name, n, i=0):
                return con7(name)[:, i * CR:(i + 1) * CR].unsqueeze(1).to_broadcast([P, n, CR])

            for g in range(NU // 8):
                us = slice(8 * g, 8 * g + 8)
                key = ("l", g)
                eng.wait_ge(done("masks7_landed"), 16)
                eng.wait_ge(*filled_at(key))
                ps = bank_of(key).rearrange("p (u t) -> p u t", t=CR)
                tt(x7[:, us, :], ps, spread("level0", 8), ALU.mult).then_inc(*v.empties(key))
                for h in range(2):
                    for key, s_dst, c_dst in (("lb", lt7, lrb7), ("lk", lak7, lrk7)):
                        key = (key, g, h)
                        eng.wait_ge(*filled_at(key))
                        ps = bank_of(key).rearrange("p (u x t) -> p u x t", x=2, t=CR)
                        uh = slice(8 * g + 4 * h, 8 * g + 4 * h + 4)
                        tt(s_dst[:, uh, :], ps[:, :, 0, :], spread("strict_t", 4), ALU.mult).then_inc(*v.step())
                        tt(c_dst[:, uh, :], ps[:, :, 1, :], spread("causal_t", 4), ALU.mult).then_inc(*v.empties(key))
                eng.wait_ge(*v.last)
                tt(y7[:, us, :], lt7[:, us, :], spread("levels_t", 8), ALU.mult).then_inc(*v.step())
                tt(x7[:, us, :], x7[:, us, :], spread("eye64", 8), ALU.add).then_inc(*v.signals("inverse_ready"))
                eng.wait_ge(*v.last)
                tt(y7[:, us, :], y7[:, us, :], spread("eye64", 8), ALU.add).then_inc(*v.signals("inverse_ready"))
            for l in range(1, 6):
                if l > 1:
                    eng.wait_ge(*filled_at(("lt", l - 1, 2)))
                eng.wait_ge(*v.last)
                tt(lt_m7, lt7, spread("levels_t", NU, l), ALU.mult).then_inc(*v.signals("level_mask"))
                for g in range(NU // 8):
                    us = slice(8 * g, 8 * g + 8)
                    pair = [(key, x) for key, x in (("lx", x7), ("ly", y7)) if not (key == "lx" and l == 5)]
                    for key, _ in pair:
                        eng.wait_ge(*filled_at((key, l, g)))
                    for key, x in pair:
                        b, _ = use[(key, l, g)]
                        b = psum[:, b, :].rearrange("p (u t) -> p u t", t=CR)
                        tt(x[:, us, :], x[:, us, :], b, ALU.add).then_inc(*v.empties((key, l, g)))
            for c in range(NCR - 1):
                key = ("state", c)
                eng.wait_ge(*filled_at(key))
                ps = bank_of(key).rearrange("p (i t) -> p i t", t=CR)[:, 0:NBR, :]
                end = cum7[:, :, CR * (c + 1) - 1:CR * (c + 1)].to_broadcast([P, NBR, CR])
                S, S1 = state7[c % 2], state7[(c + 1) % 2]
                if c:
                    eng.wait_ge(*filled_at(("y7", c - 1)))
                    tt(S1, ps, S, ALU.add).then_inc(*v.empties(key))
                    eng.wait_ge(*v.last)
                    tt(S1, S1, end, ALU.mult).then_inc(*v.signals("state_ready"))
                else:
                    tt(S1, ps, end, ALU.mult).then_inc(*v.empties(key))
            attend(memory(0))
            for i in range(3):
                key, two = ("mean7", i), slice(2 * i, 2 * i + 2)
                eng.wait_ge(*filled_at(key))
                ps = bank_of(key)
                stt(flat(yc7[:, two, :]), ps, -1.0 / HD, flat(yT7[:, two, :]), ALU.mult, ALU.add)\
                    .then_inc(*v.empties(key))
            for i in range(3):
                key, two = ("var7", i), slice(2 * i, 2 * i + 2)
                eng.wait_ge(*filled_at(key))
                ps = bank_of(key)
                ts(flat(y_sq7[:, two, :]), ps, 1.0 / HD, LNX_EPS, ALU.mult, ALU.add).then_inc(*v.empties(key))
            eng.wait_ge(done("y7_root"), 1)
            V.reciprocal(flat(y_sq7), flat(y_sq7)).then_inc(*v.step())
            eng.wait_ge(*v.last)
            tt(yc7, yc7, y_sq7, ALU.mult).then_inc(*v.step())
            eng.wait_ge(*v.last)
            for c in range(NBR):
                ts(yc7[:, c, :], yc7[:, c, :], col("a_lnx_w_2", c), col("a_lnx_b_2", c), ALU.mult, ALU.add)\
                    .then_inc(*v.step())
            for i in range(3):
                key, two = ("bonus", i), slice(2 * i, 2 * i + 2)
                eng.wait_ge(*filled_at(key))
                ps = bank_of(key)
                tt(flat(v7[:, two, :]), flat(v7[:, two, :]), ps, ALU.mult).then_inc(*v.empties(key))
                eng.wait_ge(*v.last)
                tt(yc7[:, two, :], yc7[:, two, :], v7[:, two, :], ALU.add).then_inc(*v.step())
                eng.wait_ge(*v.last)
                for c in (2 * i, 2 * i + 1):
                    tt(hT3[:, c, :], yc7[:, c, :], gateT[:, c, :], ALU.mult).then_inc(*v.signals("mixed"))

            def finish(l):
                at = memory(l)
                eng.wait_ge(*emptied_at(("o", at.name, at.n - 1)))
                for c in range(NBR, KC):
                    tt(hT3[:, c, :], hT3[:, c, :], gateT[:, c, :], ALU.mult).then_inc(*v.signals("mixed"))
                inverse_root(("ms_out", l), D)
                for c in range(KC):
                    stt(yP[:, c, :], yP[:, c, :], cols("post_norm_2", l * KC, KC)[:, c:c + 1], rstd, ALU.mult, ALU.mult)\
                        .then_inc(*v.step())
                    eng.wait_ge(*v.last)
                    tt(xT3[:, c, :], xT3[:, c, :], yP[:, c, :], ALU.add).then_inc(*v.signals("post_added"))

            finish(0)
            for i in range(2):
                tt(columns2[:, 32 + i:33 + i], col(f"b_lam_q{i + 1}_2", 0), col(f"b_lam_k{i + 1}_2", 0), ALU.mult)\
                    .then_inc(*v.signals("lam_products"))
            subln = columns2[:, 37:38]
            ts(subln, col("b_subln_2", 0), 1.0 - LAM_INIT, None, ALU.mult).then_inc(*v.step())
            inverse_root(("ms", 5), D)
            scale_chunks(h_kv, cols("kv_norm_2", 0, KC), "h_scaled")
            scale_chunks(hT3, cols("pre_norm_2", KC, KC), "h_scaled")
            minus_lam = columns2[:, 36:37]
            eng.wait_ge(*emptied_at("lam2"))
            stt(minus_lam, columns2[:, 34:35], -1.0, columns2[:, 35:36], ALU.mult, ALU.add).then_inc(*v.step())
            eng.wait_ge(*v.last)
            ts(minus_lam, minus_lam, -LAM_INIT, None, ALU.add).then_inc(*v.step())
            eng.wait_ge(done("alibi_landed"), 16)
            for u in range(ND + 1):
                if u < ND:
                    h, b = u // 2, u % 2
                    w = P * (b + 1)
                    if u >= 3:
                        eng.wait_ge(*filled_at(("dpt", u - 3)))
                    for c in range(2):
                        x = both[:, u % 3, c, 0:w]
                        eng.wait_ge(*filled_at(("ds", u, c)))
                        ps = bank_of(("ds", u, c))
                        stt(x, ps[:, 0:w], HD ** -0.5, alibi[:, h, b, 0:w], ALU.mult, ALU.add)\
                            .then_inc(*v.empties(("ds", u, c)))
                    eng.wait_ge(*v.last)
                    V.tensor_reduce(soft2[:, 0:2, u], both[:, u % 3, :, 0:w], AX_X, ALU.max, negate=True)\
                        .then_inc(*v.signals("max_diff"))
                if u:
                    u -= 1
                    w = P * (u % 2 + 1)
                    eng.wait_ge(done("exp_diff"), 2 * u + 2)
                    V.reciprocal(soft2[:, 2:4, u], sums2[:, 0:2, u]).then_inc(*v.step())
                    eng.wait_ge(*v.last)
                    tt(soft2[:, 3, u:u + 1], soft2[:, 3, u:u + 1], minus_lam, ALU.mult).then_inc(*v.step())
                    x = both[:, u % 3, :, 0:w]
                    ts(x[:, 0], x[:, 0], soft2[:, 2, u:u + 1], None, ALU.mult).then_inc(*v.step())
                    eng.wait_ge(*v.last)
                    stt(x[:, 0], x[:, 1], soft2[:, 3, u:u + 1], x[:, 0], ALU.mult, ALU.add)\
                        .then_inc(*v.signals("prob_diff"))
            attend(memory(1))
            for i in range(3):
                key, two = ("sub", i), slice(2 * i, 2 * i + 2)
                eng.wait_ge(*filled_at(key))
                ps = bank_of(key)
                ts(flat(o_sq[:, two, :]), ps, 1.0 / P, EPS, ALU.mult, ALU.add).then_inc(*v.empties(key))
            eng.wait_ge(done("sub_root"), 1)
            V.reciprocal(flat(o_sq), flat(o_sq)).then_inc(*v.step())
            for h in range(HB):
                eng.wait_ge(*v.last)
                stt(hT3[:, h, :], hT3[:, h, :], subln, o_sq[:, h, :], ALU.mult, ALU.mult).then_inc(*v.step())
                eng.wait_ge(*v.last)
                tt(hT3[:, h, :], hT3[:, h, :], gateT[:, h, :], ALU.mult).then_inc(*v.signals("mixed"))
            finish(1)
            for i in range(0, 4, 2):
                eng.wait_ge(*filled_at(("rows", i)))
                ps = bank_of(("rows", i))
                V.tensor_copy(out_rows[:, i // 2, 0:512], ps).then_inc(*v.empties(("rows", i)))

        @block.scalar
        def _(eng):
            s = Program("scalar")

            def act(dst, x, f, **k):
                return eng.activation(dst, x, f, **k)

            def vector_sources(name, n):
                if name in ("q_gain", "k_gain"):
                    x, y = {"q_gain": (a["mla_q_nope_norm_g"][0], a["mla_q_rope_norm_g"][0]),
                            "k_gain": (a["k_nope_norm_g"], a["k_rope_norm_g"])}[name]
                    return [(x.rearrange("(o n) -> o n", o=1), 0, DN), (y.rearrange("(o n) -> o n", o=1), DN, DQK)]
                x = a[name]
                if name == "a_r_k_2":
                    x = x.rearrange("l h n -> l (h n)")
                if len(x.shape) == 2:
                    x = x.rearrange("l n -> (l n)")
                if name.startswith("b_lam"):
                    return [(x.rearrange("(o n) -> o n", o=1), 0, HD)]
                return [(x.rearrange("(r p) -> r p", p=P), 0, P)]

            def load_s5():
                groups = [a["norm1_g"][0], a["ada_b"][0, 0:D], a["ada_b"][0, D:2 * D], a["s5_d"][0]]
                loads = [(lam_rows[:, 0, :], a["s5_lam_re"][0].rearrange("(j r) n -> j (r n)", r=2)),
                         (lam_rows[:, 1, :], a["s5_lam_im"][0].rearrange("(j r) n -> j (r n)", r=2)),
                         (lam_rows[:, 2, 0:2], a["s5_log_dt"][0].rearrange("(j r) -> j r", r=2))]
                loads += [(group_rows[:, m, :], x.rearrange("(g q) -> g q", q=P5)) for m, x in enumerate(groups)]
                loads += [(raw[:, m, :, :].rearrange("j r n -> j (r n)"),
                           a[x][0].rearrange("(j r) n q -> j (r n q)", r=2))
                          for m, x in enumerate(("s5_b_re", "s5_b_im", "s5_c_re", "s5_c_im"))]
                for dst, src in loads:
                    eng.dma_start(dst, src).then_inc(done("s5_landed"), 16)

            eng.dma_start(const_sb[:, :], constants[:, 0:CONST_KEEP]).then_inc(done("const_landed"), 16)
            eng.wait_ge(done("rows_clear"), 1)
            for name, (tile, r, n) in VEC_AT.items():
                for src, lo, hi in vector_sources(name, n):
                    eng.dma_start(rows[r:r + n, tile * P + lo:tile * P + hi], src)\
                       .then_inc(done(f"vectors{tile}_landed"), 16)
                if name == "kv_ada_b":
                    load_s5()
            eng.wait_ge(*emptied_at(("vec", 0)))
            act(c_act[:, :], cols("c", 0, KC), ACT.Silu).then_inc(*s.signals("c_act_ready"))
            for i in range(4):
                eng.wait_ge(*filled_at(("xT", i)))
                ps = bank_of(("xT", i))
                act(xT[:, i * 512:(i + 1) * 512], ps, ACT.Copy).then_inc(*s.empties(("xT", i)))
            eng.wait_ge(done("xc_landed"), 16)
            for t in range(L5):
                if t:
                    eng.wait_ge(*s.last)
                else:
                    eng.wait_ge(*filled_at(("xT", 3)))
                act(sq[0:C5, 0:D], xC_in[:, t, :], ACT.Square, accum_out=ss[:, 0, t:t + 1])\
                    .then_inc(*s.signals("xc_squares"))
            eng.wait_ge(done("xc_mean"), 1)
            act(ss[:, 2, :], ss[:, 1, :], ACT.Sqrt).then_inc(*s.signals("xc_root"))
            eng.wait_ge(done("log_dt_ready"), 1)
            act(small[:, 3, :], small[:, 4, :], ACT.Exp).then_inc(*s.signals("dt_ready"))
            eng.wait_ge(done("decay_ready"), 1)
            act(small[:, 9, :], small[:, 5, :], ACT.Exp).then_inc(*s.signals("poles_ready"))
            eng.wait_ge(done("angles_ready"), 1)
            act(small[:, 10, :], small[:, 6, :], ACT.Sin).then_inc(*s.signals("poles_ready"))
            act(small[:, 11, :], small[:, 7, :], ACT.Sin).then_inc(*s.signals("poles_ready"))
            for m, dst in enumerate((bt[:, 0], bt[:, 1], ct[:, 0], ct[:, 1])):
                eng.wait_ge(*filled_at(("raw", m)))
                ps = bank_of(("raw", m)).rearrange("p (q j) -> p j q", j=J5)
                act(dst, ps, ACT.Copy).then_inc(*s.empties(("raw", m)))
            for i in range(4):
                eng.wait_ge(*filled_at(("U", i)))
                ps = bank_of(("U", i))
                act(hT[:, i * 512:(i + 1) * 512], ps, ACT.Copy).then_inc(*s.empties(("U", i)))
            for b in range(NB5):
                for i in range(2):
                    if b == 0:
                        eng.wait_ge(done("bb_ready"), 2)
                    else:
                        eng.wait_ge(*filled_at(("kern", b - 1, 1)))
                    act(bb_rep[:, i, :, :].rearrange("p j (s q) -> p j s q", q=P5),
                        bb[:, i, b * BJ:(b + 1) * BJ, :].unsqueeze(2).to_broadcast([P, BJ, L5, P5]), ACT.Copy)\
                        .then_inc(*s.signals("bb_rep_ready"))
                for i in range(2):
                    eng.wait_ge(*filled_at(("w", b, i)))
                    ps = bank_of(("w", b, i)).rearrange("p (j n) -> p j n", n=P)
                    if b:
                        eng.wait_ge(*filled_at(("bu", b - 1)))
                    act(wT[:, :, i, :], ps, ACT.Copy).then_inc(*s.empties(("w", b, i)))
                for i in range(2):
                    eng.wait_ge(*filled_at(("kern", b, i)))
                    ps = bank_of(("kern", b, i))
                    if b:
                        eng.wait_ge(done("toeplitz_landed"), 16 * 8 * b)
                    act(kern[:, i::2, :], ps.rearrange("p (g n) -> p g n", n=P), ACT.Copy)\
                        .then_inc(*s.empties(("kern", b, i)))
                eng.wait_ge(*filled_at(("bu", b)))
                ps = bank_of(("bu", b)).rearrange("p (j i c) -> p c i j", j=BJ, i=2)[:, 0:C5]
                act(BU[:, :, :, b * BJ:(b + 1) * BJ], ps, ACT.Copy).then_inc(*s.empties(("bu", b)))
            for i in range(4):
                eng.wait_ge(*emptied_at(("y5", i)))
                x = y5_part(i)
                act(x, x, ACT.Gelu_apprx_tanh).then_inc(*s.signals("gelu_ready"))
            for i in range(1, 16, 2):
                eng.wait_ge(*filled_at(("gc", i)))
                ps = bank_of(("gc", i))[0:C5, :].rearrange("c (g t q) -> c t g q", g=4, t=L5)
                dst = gC[:, :, i * 64:(i + 1) * 64].rearrange("c t (g q) -> c t g q", q=P5)
                act(dst, ps, ACT.Copy).then_inc(*s.empties(("gc", i)))
            for i in range(4):
                eng.wait_ge(*filled_at(("gt", i)))
                ps = bank_of(("gt", i)).rearrange("p (k t c) -> p k c t", k=2, t=L5)
                for k in range(2):
                    act(hT3[:, 2 * i + k, :].rearrange("p (c t) -> p c t", t=L5), ps[:, k], ACT.Copy)\
                        .then_inc(*(s.empties(("gt", i)) if k else s.step()))
            for i in range(4):
                eng.wait_ge(*filled_at(("glu", i)))
                ps = bank_of(("glu", i)).rearrange("p (m t) -> p m t", t=T)
                for m in range(2):
                    k = 2 * i + m
                    act(sq3[:, k, :], ps[:, m, :], ACT.Sigmoid, bias=col("s5_b_glu", k))\
                        .then_inc(*(s.empties(("glu", i)) if m else s.step()))

            def squares(r):
                for i in range(2):
                    for pair in (2 * i, 2 * i + 1):
                        if r == 0:
                            eng.wait_ge(done("x_ready"), 2 * (pair + 1))
                        elif r >= len(UPDATES):
                            eng.wait_ge(done("post_added"), KC * (r - len(UPDATES)) + 2 * (pair + 1))
                        else:
                            key = UPDATES[r]
                            eng.wait_ge(*emptied_at((*key, pair)))
                    act(sq[:, i * 4 * T:(i + 1) * 4 * T], xT[:, i * 4 * T:(i + 1) * 4 * T], ACT.Square)\
                        .then_inc(*s.signals("squares"))

            def root(key, width=T, rows=slice(0, P)):
                eng.wait_ge(*emptied_at(key))
                act(stat[rows, T:T + width], stat[rows, 0:width], ACT.Sqrt).then_inc(*s.signals("root_ready"))

            def shift(dst, layer, which, base):
                for k in range(KC):
                    eng.wait_ge(done("h_scaled"), base + k + 1)
                    act(dst[:, k, :], dst[:, k, :], ACT.Identity, bias=ada_cols(layer, which)[:, k:k + 1])\
                        .then_inc(*s.signals("h_ready"))

            def swiglu(l):
                for c in range(NGU):
                    eng.wait_ge(*filled_at(("gu", l, c)))
                    ps = bank_of(("gu", l, c))
                    act(hid[:, c, :], ps[:, 0:T], ACT.Silu).then_inc(*s.signals("silu_ready"))

            def attend(at):
                for u in range(at.n + 3):
                    if u < at.n:
                        eng.wait_ge(done("max_" + at.name), u + 1)
                        x = at.pslots[:, u % 4, 0:at.keys(u)]
                        act(x, x, ACT.Exp, bias=at.soft[:, 0, u:u + 1], accum_out=at.soft[:, 1, u:u + 1])\
                            .then_inc(*s.signals("exp_" + at.name))
                    if 1 <= u <= at.n:
                        w = u - 1
                        eng.wait_ge(*filled_at(("pt", at.name, w)))
                        ps = bank_of(("pt", at.name, w))
                        if w >= 4:
                            eng.wait_ge(*filled_at(("o", at.name, w - 4)))
                        act(at.tslots[:, w % 4, 0:at.keys(w)], ps[:, 0:at.keys(w)], ACT.Copy)\
                            .then_inc(*s.empties(("pt", at.name, w)))
                    if 2 <= u <= at.n + 1:
                        w = u - 2
                        eng.wait_ge(*filled_at(("o", at.name, w)))
                        ps = bank_of(("o", at.name, w))
                        r, m = at.width(w)
                        act(at.dst(w), ps[r:r + m, 0:P], ACT.Copy).then_inc(*s.empties(("o", at.name, w)))

            squares(0)
            root(("ms", 1))
            shift(hT3, 0, 3, 0)
            swiglu(0)
            squares(1)
            eng.dma_start(pos_i[DN:DQK, :], a["positions"][0].partition_broadcast(DR)).then_inc(done("positions_landed"), 16)
            eng.dma_start(mask1, constants[:, CONST_KEEP:CONST_MASK].rearrange("p (b t) -> p b t", t=T))\
               .then_inc(done("mask_landed"), 16)
            root(("ms", 2))
            shift(hT3, "kv", 0, KC)
            shift(h2, 1, 0, 2 * KC)
            eng.wait_ge(*filled_at("ckv"))
            ps = bank_of("ckv")
            act(latent[0].rearrange("p k t -> p (k t)"), ps, ACT.Copy).then_inc(*s.empties("ckv"))
            eng.wait_ge(*filled_at("krope"))
            ps = bank_of("krope")
            act(krope[DN:DQK, :], ps[DN:DQK, 0:T], ACT.Copy).then_inc(*s.empties("krope"))
            eng.wait_ge(*filled_at(("cq", 0)))
            ps = bank_of(("cq", 0))
            act(latent[1].rearrange("p k t -> p (k t)"), ps, ACT.Copy).then_inc(*s.empties(("cq", 0)))
            root("ms_ckv")
            root("ms_cq")
            for i in range(8):
                eng.wait_ge(*filled_at(("kn", i)))
                ps = bank_of(("kn", i))
                act(wide[0:DN, i * 512:(i + 1) * 512], ps[0:DN, :], ACT.Square).then_inc(*s.signals("k_squares"))
                act(kh[0:DN, 2 * i:2 * i + 2, :].rearrange("p h t -> p (h t)"), ps[0:DN, :], ACT.Copy)\
                    .then_inc(*s.empties(("kn", i)))
                if i % 4 == 3:
                    for b in range(2):
                        key = ("v1", i // 4, b)
                        eng.wait_ge(*filled_at(key))
                        ps = bank_of(key)
                        act(v1[:, b, (i // 4) * 512:(i // 4 + 1) * 512], ps, ACT.Copy).then_inc(*s.empties(key))
            eng.wait_ge(*emptied_at("krope_m"))
            act(stat[DN:DQK, T:2 * T], stat[DN:DQK, 0:T], ACT.Sqrt).then_inc(*s.signals("root_ready"))
            for i in range(8):
                eng.wait_ge(*emptied_at(("km", i)))
            act(wide[0:DN, :], wide[0:DN, :], ACT.Sqrt).then_inc(*s.signals("k_root"))
            eng.wait_ge(done("rotary_angles"), 1)
            rr = slice(DN, DQK)
            act(turn[rr, 0:2, 0:T], angle[rr, 0:2, :], ACT.Sin).then_inc(*s.step())
            eng.wait_ge(*s.last)
            act(turn[rr, 0:2, T:2 * T], turn[rr, 0:2, 0:T], ACT.Copy).then_inc(*s.signals("rotary_ready"))
            eng.wait_ge(done("k_normed"), 1)
            for i in range(8):
                eng.wait_ge(*filled_at(("q", i)))
                ps = bank_of(("q", i))
                act(wide[0:DQK, i * 512:(i + 1) * 512], ps[0:DQK, :], ACT.Square).then_inc(*s.signals("q_squares"))
                act(qh[0:DQK, 2 * i:2 * i + 2, :].rearrange("p h t -> p (h t)"), ps[0:DQK, :], ACT.Copy)\
                    .then_inc(*s.empties(("q", i)))
            for i in range(8):
                eng.wait_ge(*emptied_at(("qm", i)))
                w = wide[0:DQK, i * 512:(i + 1) * 512]
                act(w, w, ACT.Sqrt).then_inc(*s.signals("q_root"))
            attend(mla)
            squares(2)
            root(("ms", 3))
            shift(hT3, 1, 3, 3 * KC)
            swiglu(1)
            eng.wait_ge(done("ada_used"), 56)
            eng.dma_start(mem_nat, a["mem_2"][0].rearrange("(b p) d -> p b d", p=P)).then_inc(done("mem_landed"), 16)
            eng.wait_ge(*emptied_at(("ada", 6)))
            for i in range(4):
                eng.wait_ge(*filled_at(("memT", i)))
                ps = bank_of(("memT", i))
                act(memT[:, 2 * i:2 * i + 2, :].rearrange("p k t -> p (k t)"), ps, ACT.Copy)\
                    .then_inc(*s.empties(("memT", i)))
            eng.wait_ge(*s.last)
            act(flat(mem_sq), flat(memT), ACT.Square).then_inc(*s.signals("mem_squares"))
            root("ms_mem")
            for l in range(2):
                for dst, key in ((k_mem[l], ("k_mem", l, 0)), (v_mem[l], ("v_mem", l, 0))):
                    eng.wait_ge(*filled_at(key))
                    ps = bank_of(key)
                    act(flat(dst), ps, ACT.Copy).then_inc(*s.empties(key))
            squares(3)
            for r, x in ((0, "a_w2_2"), (64, "a_a2_2")):
                eng.dma_start(w2a2[r:r + 64, :], a[x][0]).then_inc(done("w2_landed"), 16)
            eng.dma_start(masks7, constants[:, CONST_MASK:CONST_ALIBI]).then_inc(done("masks7_landed"), 16)
            root(("ms", 4))
            eng.wait_ge(done("shift_clear"), 1)
            for c in range(A_IN // P):
                i, m = c // 2, c % 2
                key = ("a_in", i)
                eng.wait_ge(*filled_at(key))
                ps = bank_of(key).rearrange("p (m t) -> p m t", t=T)[:, m, :]
                if c < 19:
                    if m == 0 and i > 1:
                        eng.wait_ge(*emptied_at(("a_in", i - 2)))
                    act(shifted[:, i % 2, m, 1:T + 1], ps, ACT.Identity, scale=col("a_shift_mu_2", c))\
                        .then_inc(*s.signals("shift_ready"))
                    if c == 18:
                        eng.wait_ge(done("lora_shifted"), 1)
                elif c < 19 + NBR or c >= 27:
                    k = c - 19 if c < 25 else c - 21
                    act(gateT[:, k, :], ps, ACT.Silu).then_inc(*(s.empties(key) if m or c == 28 else s.step()))
                else:
                    act(q_mem[:, c - 25, :], ps, ACT.Copy).then_inc(*(s.empties(key) if m else s.step()))
            act(lora_in[0:64, :], lora_in[0:64, :], ACT.Tanh).then_inc(*s.signals("tanh_ready"))
            eng.wait_ge(*emptied_at(("a_in", 5)))
            for c in range(NBR):
                act(tmp7[:, c, :], k7[:, c, :], ACT.Square, scale=col("a_k_k_2", c)).then_inc(*s.signals("kk_squares"))
            for i in range(NBR // 2):
                for key, bias, dst in ((("decay", i), "a_w0_2", sig7), (("rate", i), "a_a0_2", a7)):
                    eng.wait_ge(*filled_at(key))
                    ps = bank_of(key).rearrange("p (m t) -> p m t", t=T)
                    for m in range(2):
                        act(dst[:, 2 * i + m, :], ps[:, m, :], ACT.Sigmoid, bias=col(bias, 2 * i + m))\
                            .then_inc(*(s.empties(key) if m else s.step()))
            for i in range(3):
                eng.wait_ge(*emptied_at(("kks", i)))
            act(flat(tmp7), flat(tmp7), ACT.Sqrt).then_inc(*s.signals("kk_root"))
            eng.wait_ge(done("cum_ready"), 1)
            act(flat(grow7), flat(cum7), ACT.Exp, scale=math.exp(-0.5)).then_inc(*s.signals("exp7"))
            eng.wait_ge(*s.last)
            act(flat(cum7), flat(cum7), ACT.Exp, scale=-math.exp(-0.5)).then_inc(*s.signals("exp7"))
            act(flat(at7), flat(at7), ACT.Exp, scale=-math.exp(-0.5)).then_inc(*s.signals("exp7"))
            for name, dst in (("b_tok", b_tok), ("k_tok", k_tok), ("v_tok", v_tok)):
                for g in range(3):
                    key = (name, g)
                    eng.wait_ge(*filled_at(key))
                    ps = bank_of(key)
                    act(flat(dst[:, 8 * g:8 * g + 8, :]), ps, ACT.Copy).then_inc(*s.empties(key))
            for l in range(1, 6):
                for g in range(3):
                    key = ("lt", l, g)
                    eng.wait_ge(*filled_at(key))
                    ps = bank_of(key)
                    act(flat(lt_t7[:, 8 * g:8 * g + 8, :]), ps, ACT.Copy).then_inc(*s.empties(key))
            for c in range(NCR):
                for name, dst in (("rhs", rhs7), ("sa", sa7)):
                    eng.wait_ge(*filled_at((name, c)))
                    ps = bank_of((name, c))
                    act(flat(dst), ps[:, 0:NBR * CR], ACT.Copy).then_inc(*s.empties((name, c)))
                eng.wait_ge(*filled_at(("y7", c)))
                ps = bank_of(("y7", c)).rearrange("p (i t) -> p i t", t=CR)[:, 0:NBR, :]
                act(yT7[:, :, c * CR:(c + 1) * CR], ps, ACT.Copy).then_inc(*s.empties(("y7", c)))
            attend(memory(0))
            for i in range(3):
                eng.wait_ge(*emptied_at(("mean7", i)))
                act(flat(y_sq7[:, 2 * i:2 * i + 2, :]), flat(yc7[:, 2 * i:2 * i + 2, :]), ACT.Square)\
                    .then_inc(*s.signals("y7_squares"))
            for i in range(3):
                eng.wait_ge(*emptied_at(("var7", i)))
            act(flat(y_sq7), flat(y_sq7), ACT.Sqrt).then_inc(*s.signals("y7_root"))

            def output(l):
                for i in range(4):
                    key = ("out", l, i)
                    eng.wait_ge(*filled_at(key))
                    ps = bank_of(key)
                    act(flat(out_sq[l][:, 2 * i:2 * i + 2, :]), ps, ACT.Square).then_inc(*s.signals("out_squares"))
                    act(flat(yP[:, 2 * i:2 * i + 2, :]), ps, ACT.Copy).then_inc(*s.empties(key))
                root(("ms_out", l))

            output(0)
            squares(4)
            eng.dma_start(alibi, constants[:, CONST_ALIBI:].rearrange("p (h b t) -> p h b t", b=2, t=T))\
               .then_inc(done("alibi_landed"), 16)
            root(("ms", 5))
            for i in range(3):
                eng.wait_ge(*filled_at(("k_sh", i)))
                ps = bank_of(("k_sh", i))
                act(flat(kT[:, 2 * i:2 * i + 2, :]), ps, ACT.Copy).then_inc(*s.empties(("k_sh", i)))
            for i in range(3):
                eng.wait_ge(*filled_at(("v_sh", i)))
                ps = bank_of(("v_sh", i)).rearrange("p (b n) -> p b n", n=256)
                act(v_sh[:, :, i * 256:(i + 1) * 256], ps, ACT.Copy).then_inc(*s.empties(("v_sh", i)))
            for i in range(8):
                eng.wait_ge(*filled_at(("b_in", i)))
                ps = bank_of(("b_in", i))
                dst, f = ((qT[:, 2 * i:2 * i + 2, :], ACT.Copy) if i < 3 else
                          (gateT[:, 2 * i - 6:2 * i - 4, :], ACT.Silu) if i < 6 else
                          (q_mem, ACT.Copy) if i == 6 else (gateT[:, 6:8, :], ACT.Silu))
                act(flat(dst), ps, f).then_inc(*s.empties(("b_in", i)))
            eng.wait_ge(*filled_at("lam2"))
            ps = bank_of("lam2")
            act(columns2[:, 34:36], ps[:, 0:2], ACT.Exp).then_inc(*s.empties("lam2"))
            for u in range(ND + 3):
                if u < ND:
                    eng.wait_ge(done("max_diff"), u + 1)
                    for c in range(2):
                        x = both[:, u % 3, c, 0:P * (u % 2 + 1)]
                        act(x, x, ACT.Exp, bias=soft2[:, c, u:u + 1], accum_out=sums2[:, c, u:u + 1])\
                            .then_inc(*s.signals("exp_diff"))
                if 1 <= u <= ND:
                    w = u - 1
                    eng.wait_ge(*filled_at(("dpt", w)))
                    ps = bank_of(("dpt", w))
                    if w >= 4:
                        eng.wait_ge(*filled_at(("do", w - 4)))
                    n = P * (w % 2 + 1)
                    act(tslots2[:, w % 4, 0:n], ps[:, 0:n], ACT.Copy).then_inc(*s.empties(("dpt", w)))
                if 2 <= u <= ND + 1:
                    w = u - 2
                    eng.wait_ge(*filled_at(("do", w)))
                    ps = bank_of(("do", w))
                    act(hT3[:, w // 2, w % 2 * P:(w % 2 + 1) * P], ps[:, 0:P], ACT.Copy)\
                        .then_inc(*s.empties(("do", w)))
            attend(memory(1))
            eng.wait_ge(*emptied_at(("do", ND - 1)))
            for i in range(3):
                two = slice(2 * i, 2 * i + 2)
                act(flat(o_sq[:, two, :]), flat(hT3[:, two, :]), ACT.Square).then_inc(*s.signals("o_squares"))
            for i in range(3):
                eng.wait_ge(*emptied_at(("sub", i)))
            act(flat(o_sq), flat(o_sq), ACT.Sqrt).then_inc(*s.signals("sub_root"))
            output(1)
            for i in range(1, 4, 2):
                eng.wait_ge(*filled_at(("rows", i)))
                ps = bank_of(("rows", i))
                act(out_rows[:, i // 2, 512:1024], ps, ACT.Copy).then_inc(*s.empties(("rows", i)))

        @block.gpsimd
        def _(eng):
            g = Program("gpsimd")
            w = [a["ada_w"][l].rearrange("(k p) n -> k p n", p=P) for l in range(2)]
            kv = a["kv_ada_w"].rearrange("(k p) n -> k p n", p=P)
            src = [w[l][k, :, m * PANEL:(m + 1) * PANEL] for l in range(2) for m in range(3) for k in range(KC)]
            src += [kv[k] for k in range(KC)]
            for i, x in enumerate(src):
                if i >= ARING:
                    eng.wait_ge(done("ada_used"), i - ARING + 1)
                eng.dma_start(aring[:, (i % ARING) * PANEL:(i % ARING + 1) * PANEL], x).then_inc(ada_landed[i % ARING], 16)


def kernel(**inputs):
    import concourse.bacc as bacc
    from concourse.bass_utils import run_bass_kernel_spmd

    nc = bacc.Bacc("TRN2", target_bir_lowering=False, num_devices=1)
    arrays = {"in_" + name: np.ascontiguousarray(x) for name, x in inputs.items()}
    arrays["in_constants"] = CONSTANTS
    drams = {name: nc.dram_tensor(name, x.shape, mybir.dt.from_np(x.dtype), kind="ExternalInput").ap()
             for name, x in arrays.items()}
    constants = drams.pop("in_constants")
    out = nc.dram_tensor("out_0", (1, T, D), F32, kind="ExternalOutput").ap()
    blocks_kernel(nc, {name[3:]: x for name, x in drams.items()}, constants, out)
    r = run_bass_kernel_spmd(nc, [arrays], core_ids=[0])
    return r.results[0]["out_0"]
```

```python
from contextlib import ExitStack
import math

import numpy as np

import concourse.bass as bass
from concourse import mybir

F32 = mybir.dt.float32
I32 = mybir.dt.int32
ALU = mybir.AluOpType
ACT = mybir.ActivationFunctionType
AX_X = mybir.AxisListType.X

P = 128
T = 256
D = 1024
KC = D // P
FF = 2816
EPS = 1e-6
NEG = -1e30

G5, P5, N5 = 64, 16, 64
L5 = 8
C5 = T // L5
J5 = G5 // 2
BJ = 4
NB5 = J5 // BJ

H1, DN, DR, DV = 16, 64, 32, 64
DQK = DN + DR
RKV = RQ = 256
SCALE1 = 1.0 / math.sqrt(DQK)
THETA = 10000.0
CHUNK = 64

HD = 64
MW = 256
BR = 768
NBR = BR // P
A_SHIFT = 3 * BR + 128
A_IN = A_SHIFT + BR + 2 * MW
B_IN = 2 * BR + 2 * MW
HB = 6
LNX_EPS = 64e-5
CR = 64
NCR = T // CR
NU = NBR * NCR
LAM_INIT = 0.8 - 0.6 * math.exp(-0.3)

SLOTS = 6
LAG = 3
RING = 4
PANEL = 2048
ARING = 2
ARENA = 30000
TWO_PI = 2.0 * math.pi
ROUND = 1.5 * 2.0 ** 23
PI2_A = 6.28125
PI2_B = float((np.float32(TWO_PI - PI2_A).view(np.uint32) & np.uint32(0xFFFFF000)).view(np.float32))
PI2_C = float(np.float32(TWO_PI - PI2_A - PI2_B))


def alibi_slopes(n):
    def pow2(m):
        start = 2.0 ** (-8.0 / m)
        return [start ** (i + 1) for i in range(m)]
    if math.log2(n).is_integer():
        return pow2(n)
    c = 2 ** int(math.floor(math.log2(n)))
    return pow2(c) + pow2(2 * c)[0::2][: n - c]


def shape_constants():
    p = np.arange(P)
    parts = {}
    parts["ident"] = np.eye(P)
    parts["ones"] = np.ones((P, P))
    half = (p[:, None] // 64) == (p[None, :] // 64)
    parts["half"] = half * 1.0
    parts["diag16"] = ((p[:, None] % P5) == np.arange(P5)[None, :]) * 1.0
    inv = 1.0 / (np.float32(THETA) ** (np.arange(0, DR, 2, dtype=np.float32) / np.float32(DR)))
    parts["inv_freq"] = np.broadcast_to(inv[None, :], (P, DR // 2))
    mask = np.zeros((P, 2, T))
    for b in range(2):
        q = (b * P + p) // CHUNK
        mask[:, b, :] = np.where(q[:, None] >= (np.arange(T) // CHUNK)[None, :], 0.0, NEG)
    parts["chunk_mask"] = mask.reshape(P, -1)
    t = np.arange(CR)
    row = p % CR
    parts["strict_t"] = (row[:, None] < t[None, :]) * 1.0
    parts["causal_t"] = (row[:, None] <= t[None, :]) * 1.0
    parts["eye64"] = (row[:, None] == t[None, :]) * 1.0
    lev = []
    for l in range(6):
        b = 1 << l
        hi, lo = t[None, :], row[:, None]
        lev.append(((hi // (2 * b)) == (lo // (2 * b))) & ((hi // b) % 2 == 1) & ((lo // b) % 2 == 0))
    parts["levels_t"] = np.concatenate(lev, axis=1) * 1.0
    parts["level0"] = (((row[:, None] // 2) == (t[None, :] // 2)) & (row[:, None] % 2 == 1) & (t[None, :] % 2 == 0)) * 1.0
    parts["restart"] = np.broadcast_to((np.arange(T) % CR != 0) * 1.0, (P, T))
    bias = np.zeros((P, HB, 2, T), np.float32)
    for h, s in enumerate(np.array(alibi_slopes(HB), np.float32)):
        for b in range(2):
            dist = np.abs((b * P + p)[:, None] - np.arange(T)[None, :]).astype(np.float32)
            bias[:, h, b, :] = -s * dist + mask[:, b, :].astype(np.float32)
    parts["alibi"] = bias.reshape(P, -1)
    at, cols = {}, 0
    for n, a in parts.items():
        at[n] = (cols, a.shape[1])
        cols += a.shape[1]
    return at, np.concatenate([np.asarray(a, np.float32) for a in parts.values()], axis=1)


CONST_AT, CONSTANTS = shape_constants()
CONST_KEEP = CONST_AT["chunk_mask"][0]
CONST_MASK = CONST_AT["strict_t"][0]
CONST_ALIBI = CONST_AT["alibi"][0]


def vector_rows():
    tiles = [
        [("c", 8), ("ada_b", 96), ("kv_ada_b", 16)],
        [("norm1_g", 16), ("norm2_g", 16), ("s5_b_glu", 8), ("kv_norm_g", 8), ("kv_a_norm_g", 2),
         ("mla_q_norm_g", 2), ("pre_norm_2", 16), ("post_norm_2", 16), ("mem_norm_2", 16), ("kv_norm_2", 8),
         ("b_subln_2", 1)],
        [("a_shift_mu_2", 19), ("a_w0_2", 6), ("a_a0_2", 6), ("a_k_k_2", 6), ("a_k_a_2", 6), ("a_r_k_2", 6),
         ("a_lnx_w_2", 6), ("a_lnx_b_2", 6),
         ("b_lam_q1_2", 1), ("b_lam_k1_2", 1), ("b_lam_q2_2", 1), ("b_lam_k2_2", 1)],
    ]
    at, counts = {}, []
    for i, rows in enumerate(tiles):
        n = 0
        for name, k in rows:
            at[name] = (i, n, k)
            n += k
        counts.append(n)
    return at, counts


def blocks_kernel(nc, a, constants, out):
    ctx = ExitStack()
    with ctx:
        def sb(name, n):
            return ctx.enter_context(nc.sbuf_tensor(name, [P, n], F32))

        const_sb = sb("const_sb", CONST_KEEP)
        rows = sb("rows", 3 * P)
        vec = sb("vec", 3 * P)
        ada = sb("ada", 7 * 16)
        c_act = sb("c_act", KC)
        gains = sb("gains", 8 * KC)
        xT = sb("xT", KC * T)
        hT = sb("hT", KC * T)
        sq = sb("sq", KC * T)
        stat = sb("stat", 4 * T)
        ring = sb("ring", RING * PANEL)
        aring = sb("aring", ARING * PANEL)
        acc = sb("acc", PANEL)
        arena = sb("arena", ARENA)
        psum = ctx.enter_context(nc.psum_tensor("psum", [P, 8, 512], F32))

        sems = {}

        def done(name):
            if name not in sems:
                sems[name] = ctx.enter_context(nc.semaphore(name))
            return sems[name]

        filled = [done(f"bank{b}_filled") for b in range(8)]
        emptied = [done(f"bank{b}_emptied") for b in range(8)]
        panel_landed = [done(f"panel{i}_landed") for i in range(RING)]
        ada_landed = [done(f"ada_panel{i}_landed") for i in range(ARING)]

        turns = {"a": 0, "b": 0}
        use = {}
        made = {}

        class Program:

            def __init__(self, name):
                self.name, self.n, self.last = name + "_step", 0, None

            def step(self):
                self.n += 1
                self.last = (done(self.name), self.n)
                return done(self.name), 1

            def signals(self, name):
                made[name] = made.get(name, 0) + 1
                self.last = (done(name), made[name])
                return done(name), 1

            def empties(self, key):
                b, n = use[key]
                self.last = (emptied[b], n)
                return emptied[b], 1

        def next_bank(key, pool="a"):
            q = turns[pool]
            turns[pool] += 1
            b, n = (0 if pool == "a" else 4) + q % 4, q // 4
            use[key] = (b, n + 1)
            return emptied[b], n

        def fills(key):
            return filled[use[key][0]], 1

        def filled_at(key):
            b, n = use[key]
            return filled[b], n

        def emptied_at(key):
            b, n = use[key]
            return emptied[b], n

        def bank_of(key):
            return psum[:, use[key][0], :]

        def carve(base, n):
            return arena[:, base:base + n]

        def con(name):
            at, n = CONST_AT[name]
            return const_sb[:, at:at + n]

        ident, ones, half = con("ident"), con("ones"), con("half")
        VEC_AT, VEC_N = vector_rows()
        VEC_LOADS = [sum(x[0] == i for x in VEC_AT.values()) for i in range(3)]

        def col(name, j):
            i, r, _ = VEC_AT[name]
            return vec[:, i * P + r + j:i * P + r + j + 1]

        def cols(name, j, k):
            i, r, _ = VEC_AT[name]
            return vec[:, i * P + r + j:i * P + r + j + k]

        def ada_cols(layer, which):
            if layer == "kv":
                return ada[:, 96 + which * 8:96 + which * 8 + 8]
            return ada[:, layer * 48 + which * 8:layer * 48 + which * 8 + 8]

        xT3 = xT[:, :].rearrange("p (k t) -> p k t", t=T)
        hT3 = hT[:, :].rearrange("p (k t) -> p k t", t=T)
        sq3 = sq[:, :].rearrange("p (k t) -> p k t", t=T)

        o = 0
        CA_N = J5 * 9 * P5
        xC_in = ring[0:C5, 0:8 * D].rearrange("c (s d) -> c s d", d=D)
        xC = carve(0, 8 * D)[0:C5, :].rearrange("c (g s q) -> c g s q", s=L5, q=P5)
        ca_re = carve(0, CA_N).rearrange("p (j k q) -> p j k q", k=9, q=P5)
        ca_im = carve(CA_N, CA_N).rearrange("p (j k q) -> p j k q", k=9, q=P5)
        o = 2 * CA_N
        toep = carve(o, G5 * P).rearrange("p (g n) -> p g n", n=P)
        raw = carve(o, 4 * 2048)[0:J5, :].rearrange("j (m r n) -> j m r n", m=4, r=2)
        o += G5 * P
        gC = carve(o, 8 * D)[0:C5, :].rearrange("c (t d) -> c t d", d=D)
        wT = carve(o, BJ * 2 * P).rearrange("p (j i n) -> p j i n", i=2, n=P)
        o += BJ * 2 * P
        aB = carve(o, BJ * 2 * P).rearrange("p (i j n) -> p i j n", i=2, n=P)
        o += BJ * 2 * P
        kern = carve(o, 2 * 2 * BJ * P)[0:P5, :].rearrange("q (i g n) -> q i g n", i=2, n=P)
        lam_rows = carve(o, 3 * P)[0:J5, :].rearrange("j (m n) -> j m n", n=P)
        group_rows = carve(o + 3 * P, 4 * P5)[0:G5, :].rearrange("g (m n) -> g m n", n=P5)
        group_rep = carve(o + 3 * P + 64, 4 * P)[0:G5, :].rearrange("g (m n) -> g m n", n=P)
        o += 4 * BJ * P
        bb = carve(o, 2 * J5 * P5).rearrange("p (i j q) -> p i j q", i=2, q=P5)
        ct = carve(o + 1024, 2 * J5 * P5).rearrange("p (i j q) -> p i j q", i=2, q=P5)
        bt = carve(o + 2048, 2 * J5 * P5).rearrange("p (i j q) -> p i j q", i=2, q=P5)
        tmp_c = carve(o + 2048, 2 * BJ * 9 * P5)
        o += 2048 + 2 * BJ * 9 * P5
        tmp5 = carve(o, 1024)
        pick = tmp5
        o += 1024
        st = carve(o, (C5 + 1) * 64).rearrange("p (c i j) -> p c i j", i=2, j=J5)
        o += (C5 + 1) * 64
        powr = carve(o, 9 * J5).rearrange("p (k j) -> p k j", j=J5)
        powi = carve(o + 9 * J5, 9 * J5).rearrange("p (k j) -> p k j", j=J5)
        prv = carve(o + 18 * J5, 16 * J5).rearrange("p (i j s) -> p i j s", i=2, s=L5)
        o += 34 * J5
        negi = carve(o, 9 * J5).rearrange("p (k j) -> p k j", j=J5)
        o += 9 * J5
        small = stat[:, 0:24 * J5].rearrange("p (m j) -> p m j", j=J5)
        skip = stat[0:P5, 24 * J5:24 * J5 + 8 * P5].rearrange("q (g p) -> q g p", p=P5)
        step4 = rows[:, 0:4 * J5].rearrange("p (e i j) -> p e i j", e=2, i=2)
        part4 = rows[:, 4 * J5:8 * J5].rearrange("p (e i j) -> p e i j", e=2, i=2)
        part2 = rows[:, 8 * J5:10 * J5].rearrange("p (e j) -> p e j", e=2)
        grp = carve(o, 4 * G5).rearrange("p (m g) -> p m g", g=G5)
        gmod = carve(o + 4 * G5, 2 * G5).rearrange("p (m g) -> p m g", g=G5)
        o += 6 * G5
        ss = carve(o, 24)[0:C5, :].rearrange("c (m s) -> c m s", s=L5)
        o += 24
        assert o <= ARENA, o
        U = hT[:, :].rearrange("p (g c) -> p g c", c=C5)
        BU = sq[:, :].rearrange("p (c i j) -> p c i j", i=2, j=J5)
        xN = sq[:, :].rearrange("p (b d) -> p b d", d=D)

        class Carver:
            def __init__(self, base=0):
                self.o = base

            def __call__(self, n):
                self.o += n
                assert self.o <= ARENA, self.o
                return carve(self.o - n, n)

        NGU = FF // P
        NDN = NGU // 2
        hid = carve(ARENA - FF // P * T, FF // P * T).rearrange("p (n t) -> p n t", t=T)
        m1 = Carver(2 * (2 * T + 2 * MW))
        h2 = m1(KC * T).rearrange("p (k t) -> p k t", t=T)
        latent = [m1(2 * T).rearrange("p (k t) -> p k t", t=T) for _ in range(2)]
        latent_tok = [m1(2 * RKV).rearrange("p (b n) -> p b n", n=RKV) for _ in range(2)]
        krope_tok = m1(2 * DR).rearrange("p (b n) -> p b n", n=DR)
        k_tok1, q_tok1 = [m1(2 * H1 * DQK).rearrange("p (b h n) -> p b h n", b=2, n=DQK) for _ in range(2)]
        v1 = m1(2 * D).rearrange("p (b n) -> p b n", n=D)
        qh = m1(H1 * T).rearrange("p (h t) -> p h t", t=T)
        kh = m1(H1 * T).rearrange("p (h t) -> p h t", t=T)
        k_sq = kh[:, :, :].rearrange("p h t -> p (h t)")[:, 0:2 * H1 * DN].rearrange("p (b h n) -> p b h n", b=2, n=DN)
        q_sq = qh[:, :, :].rearrange("p h t -> p (h t)")[:, 0:2 * H1 * DQK].rearrange("p (b h n) -> p b h n", b=2, n=DQK)
        o1 = m1(KC * T).rearrange("p (k t) -> p k t", t=T)
        gain_rows = m1(2 * DQK).rearrange("p (m n) -> p m n", n=DQK)
        angle = m1(4 * DR).rearrange("p (m b n) -> p m b n", b=2, n=DR // 2)
        pos_i = m1(2)
        pos_f = m1(2)
        turned = m1(2 * H1 * DR).rearrange("p (m h n) -> p m h n", m=2, n=DR)
        latent_ss = m1(3 * 6).rearrange("p (m n) -> p m n", n=6)
        head_ss = m1(3 * 96).rearrange("p (m b n) -> p m b n", b=2, n=48)
        mask1 = m1(2 * T).rearrange("p (b t) -> p b t", t=T)
        pslots = m1(SLOTS * T).rearrange("p (i t) -> p i t", t=T)
        tslots = m1(4 * T).rearrange("p (i t) -> p i t", t=T)
        soft = m1(3 * 32).rearrange("p (m u) -> p m u", u=32)

        e2 = Carver()
        mem_nat = aring[:, 0:2 * D].rearrange("p (b d) -> p b d", d=D)
        memT = aring[:, 2 * D:4 * D].rearrange("p (k t) -> p k t", t=T)
        mem_sq = acc[:, :].rearrange("p (k t) -> p k t", t=T)
        memn = [mem_sq, aring[:, 0:2 * D].rearrange("p (k t) -> p k t", t=T)]
        k_mem = [e2(2 * T).rearrange("p (m t) -> p m t", t=T) for _ in range(2)]
        v_mem = [e2(2 * MW).rearrange("p (b n) -> p b n", n=MW) for _ in range(2)]
        gateT = e2(KC * T).rearrange("p (k t) -> p k t", t=T)
        q_mem = e2(2 * T).rearrange("p (m t) -> p m t", t=T)
        pslots2 = e2(SLOTS * T).rearrange("p (i t) -> p i t", t=T)
        tslots2 = aring[:, 2 * NBR * T:2 * NBR * T + 4 * T].rearrange("p (i t) -> p i t", t=T)
        soft2 = e2(5 * 32).rearrange("p (m u) -> p m u", u=32)
        sums2 = e2(64).rearrange("p (m u) -> p m u", u=32)
        columns2 = e2(64)
        r7 = Carver(e2.o)
        lora_in = r7(T)
        w2a2 = r7(BR)
        masks7 = r7(CONST_ALIBI - CONST_MASK)
        NB = NBR * T

        def con7(name):
            at, n = CONST_AT[name]
            return masks7[:, at - CONST_MASK:at - CONST_MASK + n]

        def tokens(x):
            return x.rearrange("p (i t) -> p i t", t=T)

        def units(x):
            return x.rearrange("p (u t) -> p u t", t=CR)

        ar7 = r7(2 * NB).rearrange("p (x i t) -> p x i t", x=2, t=T)
        at7, rt7 = ar7[:, 0], ar7[:, 1]
        k7, a7, v7, cum7, grow7, sig7, kk7, tmp7 = [tokens(r7(NB)) for _ in range(8)]
        lt7, x7, y7 = [units(r7(NB)) for _ in range(3)]
        lrb7, lak7 = [units(aring[:, i * NB:(i + 1) * NB]) for i in range(2)]
        v_tok = units(hT[:, 0:NB])
        k_tok = units(acc[:, 0:NB])
        flat = lambda x: x.rearrange("p i t -> p (i t)")
        b_tok, lt_t7, lt_m7 = units(flat(kk7)), units(flat(sig7)), units(flat(grow7))
        lrk7 = units(r7(NB))
        yT7 = tokens(x7.rearrange("p u t -> p (u t)"))
        yc7 = tokens(lt7.rearrange("p u t -> p (u t)"))
        chain = sq[:, 0:4 * NBR * CR].rearrange("p (n i t) -> p n i t", n=4, t=CR)
        state7, rhs7, sa7 = [chain[:, 0], chain[:, 1]], chain[:, 2], chain[:, 3]
        shifted = sq[:, 0:4 * (T + 1)].rearrange("p (s m t) -> p s m t", s=2, t=T + 1)
        y_sq7 = tokens(flat(sig7))
        yP = sq3
        out_sq = [ar7.rearrange("p x i t -> p (x i t)")[:, 0:KC * T].rearrange("p (k t) -> p k t", t=T)]

        f2 = Carver(e2.o)
        alibi = f2(HB * 2 * T).rearrange("p (h b t) -> p h b t", b=2, t=T)
        kT, qT = [tokens(f2(NB)) for _ in range(2)]
        v_sh = f2(2 * BR).rearrange("p (b n) -> p b n", n=BR)
        h_kv = f2(KC * T).rearrange("p (k t) -> p k t", t=T)
        out_sq.append(f2(KC * T).rearrange("p (k t) -> p k t", t=T))
        o_sq = tokens(f2(NB))
        both = f2(3 * 2 * T).rearrange("p (s c t) -> p s c t", c=2, t=T)
        out_rows = f2(2 * D).rearrange("p (b d) -> p b d", d=D)
        ND = 2 * HB

        def head(u):
            h = u // 2
            return slice(h % 2 * HD, h % 2 * HD + HD), h // 2, slice(u % 2 * P, u % 2 * P + P)

        def memory(l):
            def query(u):
                r, c, t = head(u)
                return q_mem[r, c, t]

            def key(u):
                r, c, _ = head(u)
                return k_mem[l][r, c, :]

            def dst(u):
                r, c, t = head(u)
                return hT3[r, NBR + c, t]
            return Attention(
                f"memory{l}", 2 * MW // HD, query, key, lambda u: T, HD ** -0.5, lambda u: None,
                lambda u, kb: v_mem[l][:, kb, u // 2 * HD:u // 2 * HD + HD], dst, lambda u: (u // 2 % 2 * HD, HD),
                (pslots2, tslots2, soft2))

        UPDATES = [None, ("dn", 0), ("wo1",), ("dn", 1)]

        class Attention:

            def __init__(self, name, n, query, key, keys, scale, bias, value, dst, width, buffers):
                self.pslots, self.tslots, self.soft = buffers
                self.name, self.n, self.query, self.key, self.keys = name, n, query, key, keys
                self.scale, self.bias, self.value, self.dst, self.width = scale, bias, value, dst, width

        mla = Attention(
            "mla", 2 * H1,
            lambda u: qh[0:DQK, u // 2, (u % 2) * P:(u % 2 + 1) * P],
            lambda u: kh[0:DQK, u // 2, 0:P * (u % 2 + 1)],
            lambda u: P * (u % 2 + 1), SCALE1,
            lambda u: mask1[:, u % 2, 0:P * (u % 2 + 1)],
            lambda u, kb: v1[:, kb, (u // 2) * DV:(u // 2 + 1) * DV],
            lambda u: o1[(u // 2 % 2) * DV:(u // 2 % 2 + 1) * DV, u // 4, (u % 2) * P:(u % 2 + 1) * P],
            lambda u: ((u // 2 % 2) * DV, DV), (pslots, tslots, soft))

        taken = [0]
        weights = []

        def in_columns(name, w, n_cols):
            rows_ = w.rearrange("(k p) n -> p k n", p=P)
            for i in range((n_cols + 255) // 256):
                m = min(256, n_cols - 256 * i)
                weights.append((rows_[:, :, 256 * i:256 * i + m], (rows_.shape[1], m), (*name, i)))

        def swiglu_weights(l):
            wg, wu = [a[x][l].rearrange("(k p) n -> p k n", p=P) for x in ("ffn_w_gate", "ffn_w_up")]
            wd = a["ffn_w_down"][l].rearrange("(j k p) n -> j p k n", k=2, p=P)
            for j in range(NDN + 1):
                if j < NDN:
                    for w in (wg, wu):
                        weights.append((w[:, :, j * 256:(j + 1) * 256], (KC, 256), ("gu", l, 2 * j + 1)))
                if j:
                    weights.append((wd[j - 1], (2, D), ("down", l, j - 1) if j < NDN else ("dn", l, 3)))

        in_columns(("glu",), a["s5_w_glu"][0], D)
        swiglu_weights(0)
        w_kva = a["w_kv_a"].rearrange("(k p) n -> p k n", p=P)
        weights.append((w_kva[:, :, 0:RKV], (KC, RKV), ("kva", 1)))
        weights.append((w_kva[:, :, RKV:], (KC, DR), ("kva", 1)))
        weights.append((a["mla_w_dq"][0].rearrange("(k p) n -> p k n", p=P), (KC, RQ), ("cqt", 1)))

        def memory_weights(l):
            in_columns(("k_mem", l), a["w_mem_kv_2"][l][:, 0:MW], MW)
            in_columns(("v_mem", l), a["w_mem_kv_2"][l][:, MW:], MW)

        memory_weights(0)
        for i in range(2):
            weights.append((a["w_kv_b"].rearrange("(k p) n -> p k n", p=P)[:, :, i * D:(i + 1) * D], (2, D),
                            ("kv", i, 1, 1)))
        for i in range(2):
            weights.append((a["mla_w_uq"][0].rearrange("(k p) n -> p k n", p=P)[:, :, i * 8 * DQK:(i + 1) * 8 * DQK],
                            (2, 8 * DQK), ("q1", i, 1, 1)))
        memory_weights(1)
        in_columns(("wo1",), a["mla_w_o"][0], D)
        swiglu_weights(1)
        in_columns(("a_in",), a["a_w_in_2"][0], A_IN)
        in_columns(("out", 0), a["w_out_2"][0], D)
        in_columns(("k_sh",), a["w_kv_2"][:, 0:BR], BR)
        in_columns(("v_sh",), a["w_kv_2"][:, BR:], BR)
        in_columns(("b_in",), a["b_w_in_2"][0], B_IN)
        in_columns(("out", 1), a["w_out_2"][1], D)

        def slot(i):
            shape = weights[i][1]
            n = shape[0] * shape[1]
            at = (i % RING) * PANEL
            return ring[:, at:at + n].rearrange("p (k n) -> p k n", n=shape[1])

        block = ctx.enter_context(nc.Block())

        @block.tensor
        def _(eng):
            pe = Program("tensor")

            def mm(dst, w, x, first=True, last=True):
                return eng.matmul(dst, w, x, start=first, stop=last)

            def panel():
                i = taken[0]
                taken[0] += 1
                return slot(i), (panel_landed[i % RING], 16 * (i // RING + 1))

            for i in range(3):
                eng.wait_ge(done(f"vectors{i}_landed"), 16 * VEC_LOADS[i])
                if i == 0:
                    eng.wait_ge(done("const_landed"), 16)
                eng.wait_ge(*next_bank(("vec", i)))
                ps = bank_of(("vec", i))
                eng.transpose(ps[:, 0:VEC_N[i]], rows[0:VEC_N[i], i * P:(i + 1) * P], ident[0:VEC_N[i], 0:VEC_N[i]])\
                    .then_inc(*fills(("vec", i)))

            eng.wait_ge(done("x_landed"), 16)
            for i in range(4):
                eng.wait_ge(*next_bank(("xT", i)))
                ps = bank_of(("xT", i)).rearrange("p (k b t) -> p k b t", k=2, b=2)
                for k in range(2):
                    for b in range(2):
                        last = eng.transpose(ps[:, k, b, :], xN[:, b, (2 * i + k) * P:(2 * i + k + 1) * P], ident)
                last.then_inc(*fills(("xT", i)))

            eng.wait_ge(done("s5_landed"), 16 * 11)
            eng.wait_ge(*next_bank("lam"))
            ps = bank_of("lam").rearrange("p (m j) -> p m j", j=J5)
            for m in range(2):
                mm(ps[:, m, :], lam_rows[:, m, :], ident[0:J5, 0:J5])
            for r in range(2):
                last = mm(ps[r * N5:(r + 1) * N5, 2, :], lam_rows[:, 2, r:r + 1].to_broadcast([J5, N5]),
                          ident[0:J5, 0:J5])
            last.then_inc(*fills("lam"))
            eng.wait_ge(done("group_rows_ready"), 1)
            eng.wait_ge(*next_bank("grp"))
            ps = bank_of("grp").rearrange("p (m g) -> p m g", g=G5)
            for m in range(4):
                last = mm(ps[:, m, :], group_rep[:, m, :], ident[0:G5, 0:G5])
            last.then_inc(*fills("grp"))
            for m in range(4):
                eng.wait_ge(*next_bank(("raw", m), "b"))
                ps = bank_of(("raw", m)).rearrange("p (q j) -> p q j", j=J5)
                for q in range(P5):
                    if m < 2:
                        src = raw[:, m, :, :].rearrange("j r (n q) -> j (r n) q", q=P5)[:, :, q]
                        last = eng.transpose(ps[:, q, :], src, ident[0:J5, 0:J5])
                    else:
                        for r in range(2):
                            last = mm(ps[r * N5:(r + 1) * N5, q, :], raw[:, m, r, q * N5:(q + 1) * N5],
                                      ident[0:J5, 0:J5])
                last.then_inc(*fills(("raw", m)))

            eng.wait_ge(done("xc_scaled"), 8)
            for i in range(4):
                eng.wait_ge(*next_bank(("U", i)))
                ps = bank_of(("U", i)).rearrange("p (g c) -> p g c", c=C5)
                for g in range(16):
                    gg = 16 * i + g
                    last = eng.transpose(ps[:, g, :], xC[:, gg, :, :].rearrange("c s q -> c (s q)"), ident[0:C5, 0:C5])
                last.then_inc(*fills(("U", i)))

            def ada_columns(blk):
                eng.wait_ge(done("ada_used"), 8 * (blk + 1))
                eng.wait_ge(*next_bank(("ada", blk), "b" if blk < 3 else "a"))
                ps = bank_of(("ada", blk))
                for j in range(16):
                    last = mm(ps[:, j:j + 1], acc[:, j * P:(j + 1) * P], ones[:, 0:1])
                last.then_inc(*fills(("ada", blk)))

            eng.wait_ge(done("ada_used"), 8)
            for i in range(4):
                eng.wait_ge(*next_bank(("ada0", i), "b"))
                ps = bank_of(("ada0", i))
                mm(ps, ones, acc[:, i * 512:(i + 1) * 512]).then_inc(*fills(("ada0", i)))

            for b in range(NB5):
                eng.wait_ge(done("ab_ready"), 2 * (b + 1))
                for i in range(2):
                    eng.wait_ge(*next_bank(("w", b, i)))
                    ps = bank_of(("w", b, i)).rearrange("p (j n) -> p j n", n=P)
                    for j in range(BJ):
                        last = eng.transpose(ps[:, j, :], aB[:, i, j, :], ident)
                    last.then_inc(*fills(("w", b, i)))
                eng.wait_ge(done("ca_ready"), 2 * (b + 1))
                for i in range(2):
                    eng.wait_ge(*next_bank(("kern", b, i), "b"))
                for g in range(4):
                    j = BJ * b + g
                    for m, c in ((0, ca_re), (1, ca_im)):
                        for i in range(2):
                            n5 = slice(i * N5, (i + 1) * N5)
                            ps = bank_of(("kern", b, i)).rearrange("p (g n) -> p g n", n=P)
                            last = mm(ps[64 * i:64 * i + P5, g, :], bb[n5, m, j, :], c[n5, j, 0:L5, :], m == 0, m == 1)
                            if g == 3 and m == 1:
                                last.then_inc(*fills(("kern", b, i)))
                eng.wait_ge(*emptied_at(("w", b, 0)))
                eng.wait_ge(*emptied_at(("w", b, 1)))
                if b == 0:
                    eng.wait_ge(done("u_ready"), 1)
                eng.wait_ge(*next_bank(("bu", b)))
                ps = bank_of(("bu", b)).rearrange("p (j i c) -> p j i c", j=BJ, i=2)[:, :, :, 0:C5]
                for j in range(BJ):
                    for i in range(2):
                        for r in range(2):
                            last = mm(ps[r * N5:(r + 1) * N5, j, i, :], wT[:, j, i, r * N5:(r + 1) * N5],
                                      U[:, 2 * (BJ * b + j) + r, :])
                last.then_inc(*fills(("bu", b)))
            ada_columns(1)

            for i in range(2):
                eng.wait_ge(done(f"toeplitz{i}_landed"), 16 * L5 * NB5 // 2)
            eng.wait_ge(done("states_ready"), 1)
            for q in range(8):
                for r in range(2):
                    eng.wait_ge(*next_bank(("y5", 2 * q + r), "ab"[r]))
                ps = [bank_of(("y5", 2 * q + r))[64 * r:64 * r + C5, :].rearrange("c (m n) -> c m n", n=P)
                      for r in range(2)]
                for m in range(4):
                    j = 4 * q + m
                    for r in range(2):
                        mm(ps[r][:, m, :], U[:, 2 * j + r, :], toep[:, 2 * j + r, :], True, False)
                    for i, c in enumerate((ca_re, ca_im)):
                        for r in range(2):
                            n5 = slice(r * N5, (r + 1) * N5)
                            last = mm(ps[r][:, m, :], st[n5, 0:C5, i, j], c[n5, j, 1:9, :], False, i == 1)
                            if m == 3 and i == 1:
                                last.then_inc(*fills(("y5", 2 * q + r)))
            for i in range(4):
                eng.wait_ge(*emptied_at(("y5", 4 * i + 3)))
                eng.wait_ge(*next_bank(("gt", i)))
                ps = bank_of(("gt", i)).rearrange("p (k t c) -> p k t c", k=2, t=L5)
                for k in range(2):
                    for t in range(L5):
                        last = eng.transpose(ps[:, k, t, :], gC[:, t, (2 * i + k) * P:(2 * i + k + 1) * P],
                                             ident[0:C5, 0:C5])
                last.then_inc(*fills(("gt", i)))

            ada_columns(2)
            for i in range(4):
                eng.wait_ge(*emptied_at(("gt", i)))
            for i in range(4):
                w, landed = panel()
                eng.wait_ge(*landed)
                eng.wait_ge(*next_bank(("glu", i)))
                ps = bank_of(("glu", i)).rearrange("p (m t) -> p m t", t=T)
                for m in range(2):
                    for k in range(KC):
                        last = mm(ps[:, m, :], w[:, k, m * P:(m + 1) * P], hT3[:, k, :], k == 0, k == KC - 1)
                last.then_inc(*fills(("glu", i)))

            def mean_square(key, chunks, src, sig, count, pool="a"):
                eng.wait_ge(*next_bank(key, pool))
                ps = bank_of(key)
                for k in range(chunks):
                    eng.wait_ge(done(sig), count(k))
                    last = mm(ps[:, 0:T], ones, src[:, k, :], k == 0, k == chunks - 1)
                last.then_inc(*fills(key))

            def project(name, x, n_cols, chunks=KC, ready=None, pool="a"):
                for i in range((n_cols + 255) // 256):
                    m = min(256, n_cols - 256 * i)
                    w, landed = panel()
                    eng.wait_ge(*landed)
                    key = (*name, i) if isinstance(name, tuple) else (name, i)
                    eng.wait_ge(*next_bank(key, pool))
                    ps = bank_of(key).rearrange("p (m t) -> p m t", t=T)
                    for j in range(m // P):
                        for k in range(chunks):
                            if ready and i == 0 and j == 0:
                                eng.wait_ge(done(ready[0]), ready[1] + k + 1)
                            last = mm(ps[:, j, :], w[:, k, j * P:(j + 1) * P], x[:, k, :], k == 0, k == chunks - 1)
                    last.then_inc(*fills(key))

            def swiglu(l, h_base, extra):
                for i in range(4):
                    eng.wait_ge(*next_bank(("dn", l, i), "b"))
                dn = [bank_of(("dn", l, i)).rearrange("p (m t) -> p m t", t=T) for i in range(4)]

                def down(j):
                    w, landed = panel()
                    eng.wait_ge(*landed)
                    for kk in range(2):
                        eng.wait_ge(*emptied_at(("gu", l, 2 * j + kk)))
                        for c in range(KC):
                            last = eng.matmul(dn[c // 2][:, c % 2, :], w[:, kk, c * P:(c + 1) * P],
                                              hid[:, 2 * j + kk, :], start=(j == 0 and kk == 0 and c % 2 == 0),
                                              stop=(j == NDN - 1 and kk == 1), skip_group_check=True)
                            if j == NDN - 1 and kk == 1 and c % 2:
                                last.then_inc(*fills(("dn", l, c // 2)))
                    if j < NDN - 1:
                        last.then_inc(*pe.signals("down_used"))

                for j in range(NDN):
                    g, landed = panel()
                    eng.wait_ge(*landed)
                    u, landed = panel()
                    eng.wait_ge(*landed)
                    for m in range(2):
                        c = 2 * j + m
                        eng.wait_ge(*next_bank(("gu", l, c)))
                        ps = bank_of(("gu", l, c)).rearrange("p (m t) -> p m t", t=T)
                        for i, w in enumerate((g, u)):
                            for k in range(KC):
                                if c == 0 and i == 0:
                                    eng.wait_ge(done("h_ready"), h_base + k + 1)
                                last = mm(ps[:, i, :], w[:, k, m * P:(m + 1) * P], hT3[:, k, :], k == 0, k == KC - 1)
                        last.then_inc(*fills(("gu", l, c)))
                    extra(j)
                    if j:
                        down(j - 1)
                down(NDN - 1)

            def attend(at):
                def scores(u):
                    key = ("s", at.name, u)
                    eng.wait_ge(*next_bank(key))
                    ps = bank_of(key)
                    mm(ps[:, 0:at.keys(u)], at.query(u), at.key(u)).then_inc(*fills(key))

                def transposes(u):
                    key = ("pt", at.name, u)
                    eng.wait_ge(done("prob_" + at.name), u + 1)
                    eng.wait_ge(*next_bank(key, "b"))
                    ps = bank_of(key).rearrange("p (b q) -> p b q", q=P)
                    for kb in range(at.keys(u) // P):
                        last = eng.transpose(ps[:, kb, :], at.pslots[:, u % SLOTS, kb * P:(kb + 1) * P], ident)
                    last.then_inc(*fills(key))

                def values(u):
                    key = ("o", at.name, u)
                    eng.wait_ge(*emptied_at(("pt", at.name, u)))
                    eng.wait_ge(*next_bank(key, "b"))
                    ps = bank_of(key)
                    r, m = at.width(u)
                    nb = at.keys(u) // P
                    for kb in range(nb):
                        last = mm(ps[r:r + m, 0:P], at.value(u, kb), at.tslots[:, u % 4, kb * P:(kb + 1) * P],
                                  kb == 0, kb == nb - 1)
                    last.then_inc(*fills(key))

                for u in range(at.n + LAG + 1):
                    if u < at.n:
                        scores(u)
                    if LAG <= u < at.n + LAG:
                        transposes(u - LAG)
                    if u > LAG:
                        values(u - LAG - 1)

            mean_square(("ms", 1), KC, sq3, "squares", lambda k: 2 * 0 + k // 4 + 1)
            swiglu(0, 0, lambda j: ada_columns({2: 3, 4: 4, 7: 5}[j]) if j in (2, 4, 7) else None)
            ada_columns(6)
            eng.wait_ge(done("mem_landed"), 16)
            for i in range(4):
                eng.wait_ge(*next_bank(("memT", i)))
                ps = bank_of(("memT", i)).rearrange("p (k b t) -> p k b t", k=2, b=2)
                for k in range(2):
                    for b in range(2):
                        last = eng.transpose(ps[:, k, b, :], mem_nat[:, b, (2 * i + k) * P:(2 * i + k + 1) * P], ident)
                last.then_inc(*fills(("memT", i)))

            def memory_kv(l):
                project(("k_mem", l), memn[l], MW, ready=("memn_ready", KC * l))
                w, landed = panel()
                eng.wait_ge(*landed)
                eng.wait_ge(*next_bank(("v_mem", l, 0)))
                ps = bank_of(("v_mem", l, 0)).rearrange("p (b n) -> p b n", n=MW)
                for b in range(2):
                    for k in range(KC):
                        last = mm(ps[:, b, :], memn[l][:, k, b * P:(b + 1) * P], w[:, k, :], k == 0, k == KC - 1)
                last.then_inc(*fills(("v_mem", l, 0)))

            mean_square(("ms", 2), KC, sq3, "squares", lambda k: 2 * 1 + k // 4 + 1)
            for b in range(2):
                eng.wait_ge(*next_bank(("kva", b)))
            w, landed = panel()
            eng.wait_ge(*landed)
            for b in range(2):
                ps = bank_of(("kva", b))
                for k in range(KC):
                    if b == 0:
                        eng.wait_ge(done("h_ready"), KC + k + 1)
                    mm(ps[:, 0:RKV], hT3[:, k, b * P:(b + 1) * P], w[:, k, :], k == 0, k == KC - 1)
            w, landed = panel()
            eng.wait_ge(*landed)
            for b in range(2):
                ps = bank_of(("kva", b))
                for k in range(KC):
                    last = mm(ps[:, RKV:RKV + DR], hT3[:, k, b * P:(b + 1) * P], w[:, k, :], k == 0, k == KC - 1)
                last.then_inc(*fills(("kva", b)))
            w, landed = panel()
            eng.wait_ge(*landed)
            for b in range(2):
                eng.wait_ge(*next_bank(("cqt", b)))
                ps = bank_of(("cqt", b))
                for k in range(KC):
                    if b == 0:
                        eng.wait_ge(done("h_ready"), 2 * KC + k + 1)
                    last = mm(ps[:, 0:RQ], h2[:, k, b * P:(b + 1) * P], w[:, k, :], k == 0, k == KC - 1)
                last.then_inc(*fills(("cqt", b)))
            mean_square("ms_mem", KC, mem_sq, "mem_squares", lambda k: 1, "b")
            for i, (name, src) in enumerate((("ckvT", "kva"), ("cqT", "cqt"))):
                if i == 0:
                    memory_kv(0)
                eng.wait_ge(*next_bank(name, "b"))
                ps = bank_of(name).rearrange("p (k b t) -> p k b t", k=2, b=2)
                for b in range(2):
                    eng.wait_ge(*emptied_at((src, b)))
                    for k in range(2):
                        last = eng.transpose(ps[:, k, b, :], latent_tok[i][:, b, k * P:(k + 1) * P], ident)
                last.then_inc(*fills(name))
            eng.wait_ge(*emptied_at("ckvT"))
            for name, x, width, pool in (("kv", latent[0], 4 * P, "a"), ("q1", latent[1], 4 * DQK, "b")):
                if name == "q1":
                    eng.wait_ge(*emptied_at("cqT"))
                for hh in range(2):
                    w, landed = panel()
                    eng.wait_ge(*landed)
                    for b in range(2):
                        for n in range(2):
                            key = (name, hh, b, n)
                            eng.wait_ge(*next_bank(key, pool))
                            ps = bank_of(key)
                            for k in range(2):
                                last = mm(ps[:, 0:width], x[:, k, b * P:(b + 1) * P], w[:, k, n * width:(n + 1) * width],
                                          k == 0, k == 1)
                            last.then_inc(*fills(key))
            memory_kv(1)
            for name, x, pool in (("kT1", k_tok1, "a"), ("qT1", q_tok1, "b")):
                for b in range(2):
                    eng.wait_ge(done(name + "_ready"), b + 1)
                    for g in range(H1 // 4):
                        key = (name, b, g)
                        eng.wait_ge(*next_bank(key, pool))
                        ps = bank_of(key).rearrange("p (h t) -> p h t", t=P)
                        for h in range(4):
                            last = eng.transpose(ps[0:DQK, h, :], x[:, b, 4 * g + h, :], ident)
                        last.then_inc(*fills(key))
            for name in ("kT1", "qT1"):
                for g in range(H1 // 4):
                    eng.wait_ge(*emptied_at((name, 1, g)))
            attend(mla)
            eng.wait_ge(*emptied_at(("o", "mla", mla.n - 1)))
            project("wo1", o1, D)
            mean_square(("ms", 3), KC, sq3, "squares", lambda k: 2 * 2 + k // 4 + 1)
            swiglu(1, 3 * KC, lambda j: None)
            mean_square(("ms", 4), KC, sq3, "squares", lambda k: 2 * 3 + k // 4 + 1)
            project("a_in", hT3, A_IN, ready=("h_scaled", 4 * KC))
            eng.wait_ge(done("w2_landed"), 32)
            eng.wait_ge(done("tanh_ready"), 1)
            eng.wait_ge(*emptied_at(("a_in", 9)))
            for i in range(NBR // 2):
                for r, key, pool in ((0, "decay", "a"), (64, "rate", "b")):
                    eng.wait_ge(*next_bank((key, i), pool))
                    ps = bank_of((key, i)).rearrange("p (m t) -> p m t", t=T)
                    for m in range(2):
                        c = 2 * i + m
                        last = mm(ps[:, m, :], w2a2[r:r + 64, c * P:(c + 1) * P], lora_in[r:r + 64, :])
                    last.then_inc(*fills((key, i)))
            for i in range(NBR // 2):
                eng.wait_ge(done("kk_squares"), 2 * i + 2)
                eng.wait_ge(*next_bank(("kks", i)))
                ps = bank_of(("kks", i))
                mm(ps, half, flat(tmp7[:, 2 * i:2 * i + 2, :])).then_inc(*fills(("kks", i)))
            HEADS = [(u, p * HD, p * CR) for u in range(8) for p in range(2)]

            def chunk(x, u, r):
                return x[r:r + HD, u // NCR, u % NCR * CR:(u % NCR + 1) * CR]

            eng.wait_ge(done("scaled7"), 3)
            for g in range(NU // 8):
                eng.wait_ge(*next_bank(("l", g)))
                ps = bank_of(("l", g)).rearrange("p (u t) -> p u t", t=CR)
                for uu in range(8):
                    for r in (0, HD):
                        u = 8 * g + uu
                        last = mm(ps[r:r + CR, uu, :], chunk(at7, u, r), chunk(a7, u, r))
                last.then_inc(*fills(("l", g)))
                for h in range(2):
                    for key, x in (("lb", a7), ("lk", k7)):
                        eng.wait_ge(*next_bank((key, g, h), "b"))
                        ps = bank_of((key, g, h)).rearrange("p (u x t) -> p u x t", x=2, t=CR)
                        for uu in range(4):
                            for r in (0, HD):
                                u = 8 * g + 4 * h + uu
                                last = mm(ps[r:r + CR, uu, :, :], chunk(x, u, r),
                                          ar7[r:r + HD, :, u // NCR, u % NCR * CR:(u % NCR + 1) * CR])
                        last.then_inc(*fills((key, g, h)))
            for key, x in (("b_tok", a7), ("k_tok", k7), ("v_tok", v7)):
                for g in range(NU // 8):
                    eng.wait_ge(*next_bank((key, g)))
                    ps = bank_of((key, g)).rearrange("p (u t) -> p u t", t=CR)
                    for uu in range(8):
                        for r in (0, HD):
                            last = mm(ps[r:r + CR, uu, :], chunk(x, 8 * g + uu, r), ident[r:r + HD, r:r + HD])
                    last.then_inc(*fills((key, g)))
            for l in range(1, 6):
                for g in range(NU // 8):
                    eng.wait_ge(done("level_mask"), l)
                    if l == 1:
                        eng.wait_ge(done("inverse_ready"), 2 * g + 2)
                    else:
                        eng.wait_ge(*emptied_at(("lx", l - 1, g)))
                        eng.wait_ge(*emptied_at(("ly", l - 1, g)))
                    eng.wait_ge(*next_bank(("lt", l, g)))
                    ps = bank_of(("lt", l, g)).rearrange("p (u t) -> p u t", t=CR)
                    for uu in range(8):
                        for r in (0, HD):
                            u, rr = 8 * g + uu, slice(r, r + CR)
                            last = mm(ps[rr, uu, :], lt_m7[rr, u, :], x7[rr, u, :])
                    last.then_inc(*fills(("lt", l, g)))
                for g in range(NU // 8):
                    eng.wait_ge(*emptied_at(("lt", l, g)))
                    for key, w, x in (("lx", y7, lt_t7), ("ly", lt_t7, y7)):
                        if key == "lx" and l == 5:
                            continue
                        eng.wait_ge(*next_bank((key, l, g), "b"))
                        ps = bank_of((key, l, g)).rearrange("p (u t) -> p u t", t=CR)
                        for uu in range(8):
                            for r in (0, HD):
                                u, rr = 8 * g + uu, slice(r, r + CR)
                                last = mm(ps[rr, uu, :], w[rr, u, :], x[rr, u, :])
                        last.then_inc(*fills((key, l, g)))
            for g in range(3):
                eng.wait_ge(*emptied_at(("ly", 5, g)))
                eng.wait_ge(*emptied_at(("b_tok", g)))
                eng.wait_ge(*emptied_at(("k_tok", g)))
                eng.wait_ge(*emptied_at(("v_tok", g)))
            for c in range(NCR):
                S = state7[c % 2]
                if c == 1:
                    eng.wait_ge(*emptied_at(("state", 0)))
                elif c:
                    eng.wait_ge(done("state_ready"), c - 1)
                eng.wait_ge(*next_bank(("rhs", c)))
                ps = bank_of(("rhs", c)).rearrange("p (i t) -> p i t", t=CR)[:, 0:NBR, :]
                for i in range(NBR):
                    for r in (0, HD):
                        u, rr = NCR * i + c, slice(r, r + CR)
                        if c:
                            mm(ps[rr, i, :], chunk(at7, u, r), S[rr, i, :], True, False)
                        last = mm(ps[rr, i, :], lak7[rr, u, :], v_tok[rr, u, :], c == 0, True)
                last.then_inc(*fills(("rhs", c)))
                eng.wait_ge(*emptied_at(("rhs", c)))
                eng.wait_ge(*next_bank(("sa", c), "b"))
                ps = bank_of(("sa", c)).rearrange("p (i t) -> p i t", t=CR)[:, 0:NBR, :]
                for i in range(NBR):
                    for r in (0, HD):
                        u, rr = NCR * i + c, slice(r, r + CR)
                        last = mm(ps[rr, i, :], y7[rr, u, :], rhs7[rr, i, :])
                last.then_inc(*fills(("sa", c)))
                eng.wait_ge(*emptied_at(("sa", c)))
                if c < NCR - 1:
                    eng.wait_ge(*next_bank(("state", c)))
                    ps = bank_of(("state", c)).rearrange("p (i t) -> p i t", t=CR)[:, 0:NBR, :]
                    for i in range(NBR):
                        for r in (0, HD):
                            u, rr = NCR * i + c, slice(r, r + CR)
                            mm(ps[rr, i, :], b_tok[rr, u, :], sa7[rr, i, :], True, False)
                            last = mm(ps[rr, i, :], k_tok[rr, u, :], v_tok[rr, u, :], False, True)
                    last.then_inc(*fills(("state", c)))
                eng.wait_ge(*next_bank(("y7", c), "b"))
                ps = bank_of(("y7", c)).rearrange("p (i t) -> p i t", t=CR)[:, 0:NBR, :]
                for i in range(NBR):
                    for r in (0, HD):
                        u, rr = NCR * i + c, slice(r, r + CR)
                        if c:
                            mm(ps[rr, i, :], S[rr, i, :], chunk(rt7, u, r), True, False)
                        mm(ps[rr, i, :], sa7[rr, i, :], lrb7[rr, u, :], c == 0, False)
                        last = mm(ps[rr, i, :], v_tok[rr, u, :], lrk7[rr, u, :], False, True)
                last.then_inc(*fills(("y7", c)))
            attend(memory(0))
            eng.wait_ge(*emptied_at(("y7", NCR - 1)))
            for i in range(3):
                eng.wait_ge(*next_bank(("mean7", i)))
                ps = bank_of(("mean7", i))
                mm(ps, half, flat(yT7[:, 2 * i:2 * i + 2, :])).then_inc(*fills(("mean7", i)))
            for i in range(3):
                eng.wait_ge(*next_bank(("bonus", i), "b"))
                ps = bank_of(("bonus", i))
                mm(ps, half, flat(tmp7[:, 2 * i:2 * i + 2, :])).then_inc(*fills(("bonus", i)))
            for i in range(3):
                eng.wait_ge(done("y7_squares"), i + 1)
                eng.wait_ge(*next_bank(("var7", i)))
                ps = bank_of(("var7", i))
                mm(ps, half, flat(y_sq7[:, 2 * i:2 * i + 2, :])).then_inc(*fills(("var7", i)))

            def output(l):
                project(("out", l), hT3, D, ready=("mixed", KC * l))
                mean_square(("ms_out", l), KC, out_sq[l], "out_squares", lambda k: 4 * l + k // 2 + 1)

            output(0)
            mean_square(("ms", 5), KC, sq3, "squares", lambda k: 2 * 4 + k // 4 + 1)
            project("k_sh", h_kv, BR, ready=("h_scaled", 5 * KC))
            for i in range(3):
                w, landed = panel()
                eng.wait_ge(*landed)
                eng.wait_ge(*next_bank(("v_sh", i)))
                ps = bank_of(("v_sh", i)).rearrange("p (b n) -> p b n", n=256)
                for b in range(2):
                    for k in range(KC):
                        last = mm(ps[:, b, :], h_kv[:, k, b * P:(b + 1) * P], w[:, k, :], k == 0, k == KC - 1)
                last.then_inc(*fills(("v_sh", i)))
            project("b_in", hT3, B_IN, ready=("h_scaled", 6 * KC))
            eng.wait_ge(done("lam_products"), 2)
            eng.wait_ge(*next_bank("lam2"))
            ps = bank_of("lam2")
            mm(ps[:, 0:2], ones, columns2[:, 32:34]).then_inc(*fills("lam2"))
            for i in range(3):
                eng.wait_ge(*emptied_at(("v_sh", i)))
                eng.wait_ge(*emptied_at(("b_in", i)))
            for u in range(ND + 2):
                if u < ND:
                    h, b = u // 2, u % 2
                    for c in range(2):
                        r = slice(c * HD, (c + 1) * HD)
                        eng.wait_ge(*next_bank(("ds", u, c)))
                        ps = bank_of(("ds", u, c))
                        mm(ps[:, 0:P * (b + 1)], qT[r, h, b * P:(b + 1) * P], kT[r, h, 0:P * (b + 1)])\
                            .then_inc(*fills(("ds", u, c)))
                if 1 <= u <= ND:
                    w = u - 1
                    eng.wait_ge(done("prob_diff"), w + 1)
                    eng.wait_ge(*next_bank(("dpt", w), "b"))
                    ps = bank_of(("dpt", w)).rearrange("p (b q) -> p b q", q=P)
                    for kb in range(w % 2 + 1):
                        last = eng.transpose(ps[:, kb, :], both[:, w % 3, 0, kb * P:(kb + 1) * P], ident)
                    last.then_inc(*fills(("dpt", w)))
                if u >= 2:
                    w = u - 2
                    eng.wait_ge(*emptied_at(("dpt", w)))
                    eng.wait_ge(*next_bank(("do", w), "b"))
                    ps = bank_of(("do", w))
                    for kb in range(w % 2 + 1):
                        last = mm(ps[:, 0:P], v_sh[:, kb, w // 2 * P:(w // 2 + 1) * P], tslots2[:, w % 4, kb * P:(kb + 1) * P],
                                  kb == 0, kb == w % 2)
                    last.then_inc(*fills(("do", w)))
            attend(memory(1))
            for i in range(3):
                eng.wait_ge(done("o_squares"), i + 1)
                eng.wait_ge(*next_bank(("sub", i)))
                ps = bank_of(("sub", i))
                mm(ps, ones, flat(o_sq[:, 2 * i:2 * i + 2, :])).then_inc(*fills(("sub", i)))
            output(1)
            eng.wait_ge(done("post_added"), 2 * KC)
            for i in range(4):
                eng.wait_ge(*next_bank(("rows", i)))
                ps = bank_of(("rows", i)).rearrange("p (k n) -> p k n", n=P)
                for k in range(4):
                    last = eng.transpose(ps[:, k, :], xT3[:, i % 2 * 4 + k, i // 2 * P:(i // 2 + 1) * P], ident)
                last.then_inc(*fills(("rows", i)))

        @block.sync
        def _(sp):
            sp.dma_start(xN, a["x"][0].rearrange("(b p) d -> p b d", p=P)).then_inc(done("x_landed"), 16)
            sp.dma_start(xC_in, a["x"][0].rearrange("(c s) d -> c s d", s=L5)).then_inc(done("xc_landed"), 16)

            def load(i):
                if i >= RING:
                    key = weights[i - RING][2]
                    if key[0] == "down":
                        sp.wait_ge(done("down_used"), (NDN - 1) * key[1] + key[2] + 1)
                    else:
                        sp.wait_ge(*filled_at(key))
                sp.dma_start(slot(i), weights[i][0]).then_inc(panel_landed[i % RING], 16)

            first = RING
            sp.wait_ge(done("xc_scaled"), 8)
            for i in range(first):
                load(i)
            sp.wait_ge(done("toeplitz_clear"), 1)
            for b in range(NB5):
                sp.wait_ge(done("kern_ready"), b + 1)
                for s in range(L5):
                    sp.dma_start(toep[s * P5:(s + 1) * P5, 8 * b:8 * b + 8, s * P5:P],
                                 kern[:, b % 2, :, 0:P - s * P5]).then_inc(done(f"toeplitz{b % 2}_landed"), 16)
            for i in range(first, len(weights)):
                load(i)
            for i in range(4):
                b, n = use[("rows", i)]
                sp.wait_ge(emptied[b], n)
                sp.dma_start(out[0][i // 2 * P:(i // 2 + 1) * P, i % 2 * 512:i % 2 * 512 + 512],
                             out_rows[:, i // 2, i % 2 * 512:i % 2 * 512 + 512]).then_inc(done("out_written"), 16)
            sp.wait_ge(done("out_written"), 16 * 4)

        @block.vector
        def _(eng):
            v = Program("vector")
            V = nc.vector

            def tt(dst, x, y, op):
                return V.tensor_tensor(dst, x, y, op)

            def ts(dst, x, s1, s2, op0, op1=ALU.bypass):
                return V.tensor_scalar(dst, x, s1, s2, op0, op1)

            def stt(dst, x, s, y, op0, op1):
                return V.scalar_tensor_tensor(dst, x, s, y, op0, op1)

            ada_next = [0]

            def ada_panel():
                i = ada_next[0]
                ada_next[0] += 1
                blk, k = i // 8, i % 8
                eng.wait_ge(ada_landed[i % ARING], 16 * (i // ARING + 1))
                w = aring[:, (i % ARING) * PANEL:(i % ARING + 1) * PANEL]
                if i == 0:
                    eng.wait_ge(done("c_act_ready"), 1)
                if k == 0:
                    if blk:
                        eng.wait_ge(*filled_at(("ada", blk - 1) if blk > 1 else ("ada0", 3)))
                    ts(acc[:, :], w, c_act[:, 0:1], None, ALU.mult).then_inc(*v.signals("ada_used"))
                else:
                    eng.wait_ge(done("ada_used"), i)
                    stt(acc[:, :], w, c_act[:, k:k + 1], acc[:, :], ALU.mult, ALU.add).then_inc(*v.signals("ada_used"))

            def ada_bias(blk):
                eng.wait_ge(*filled_at(("ada", blk)))
                ps = bank_of(("ada", blk))
                name, at = ("ada_b", 16 * blk) if blk < 6 else ("kv_ada_b", 0)
                tt(ada[:, blk * 16:blk * 16 + 16], ps[:, 0:16], cols(name, at, 16), ALU.add)\
                    .then_inc(*v.empties(("ada", blk)))

            V.memset(rows[:, :], 0.0).then_inc(*v.signals("rows_clear"))
            for i in range(3):
                eng.wait_ge(*filled_at(("vec", i)))
                ps = bank_of(("vec", i))
                V.tensor_copy(vec[:, i * P:i * P + VEC_N[i]], ps[:, 0:VEC_N[i]]).then_inc(*v.empties(("vec", i)))

            eng.wait_ge(done("s5_landed"), 16 * 11)
            for m in range(4):
                V.tensor_copy(group_rep[:, m, :].rearrange("g (s q) -> g s q", q=P5),
                              group_rows[:, m, :].unsqueeze(1).to_broadcast([G5, L5, P5]))\
                    .then_inc(*(v.signals("group_rows_ready") if m == 3 else v.step()))
            eng.wait_ge(done("xc_squares"), 8)
            ts(ss[:, 1, :], ss[:, 0, :], 1.0 / D, EPS, ALU.mult, ALU.add).then_inc(*v.signals("xc_mean"))
            eng.wait_ge(done("xc_root"), 1)
            V.reciprocal(ss[:, 0, :], ss[:, 2, :]).then_inc(*v.step())
            eng.wait_ge(*v.last)
            for s in range(L5):
                ts(xC[:, :, s, :], xC_in[:, s, :].rearrange("c (g q) -> c g q", q=P5), ss[:, 0, s:s + 1], None, ALU.mult)\
                    .then_inc(*v.signals("xc_scaled"))

            eng.wait_ge(*filled_at("lam"))
            ps = bank_of("lam").rearrange("p (m j) -> p m j", j=J5)
            V.tensor_copy(small[:, 0:3, :], ps[:, 0:3, :]).then_inc(*v.empties("lam"))
            lr, li, dt = small[:, 0, :], small[:, 1, :], small[:, 3, :]
            eng.wait_ge(*v.last)
            V.tensor_copy(small[:, 4, :], small[:, 2, :]).then_inc(*v.signals("log_dt_ready"))
            eng.wait_ge(done("dt_ready"), 1)
            tt(small[:, 5, :], lr, dt, ALU.mult).then_inc(*v.signals("decay_ready"))
            tt(small[:, 6, :], li, dt, ALU.mult).then_inc(*v.step())
            eng.wait_ge(*v.last)
            ts(small[:, 7, :], small[:, 6, :], 1.0 / TWO_PI, ROUND, ALU.mult, ALU.add).then_inc(*v.step())
            eng.wait_ge(*v.last)
            ts(small[:, 8, :], small[:, 7, :], -ROUND, None, ALU.add).then_inc(*v.step())
            for part in (PI2_A, PI2_B, PI2_C):
                eng.wait_ge(*v.last)
                stt(small[:, 6, :], small[:, 8, :], -part, small[:, 6, :], ALU.mult, ALU.add).then_inc(*v.step())
            eng.wait_ge(*v.last)
            ts(small[:, 6, :], small[:, 6, :], math.pi * (1 - 1e-7), -math.pi * (1 - 1e-7), ALU.min, ALU.max)\
                .then_inc(*v.step())
            eng.wait_ge(*v.last)
            ts(small[:, 7, :], small[:, 6, :], math.pi / 2, None, ALU.add).then_inc(*v.step())
            eng.wait_ge(*v.last)
            ts(small[:, 8, :], small[:, 7, :], math.pi, -TWO_PI, ALU.is_gt, ALU.mult).then_inc(*v.step())
            eng.wait_ge(*v.last)
            tt(small[:, 7, :], small[:, 7, :], small[:, 8, :], ALU.add).then_inc(*v.step())
            eng.wait_ge(*v.last)
            ts(small[:, 7, :], small[:, 7, :], math.pi * (1 - 1e-7), -math.pi * (1 - 1e-7), ALU.min, ALU.max)\
                .then_inc(*v.signals("angles_ready"))
            eng.wait_ge(done("poles_ready"), 3)
            tt(powr[:, 1, :], small[:, 9, :], small[:, 11, :], ALU.mult).then_inc(*v.step())
            tt(powi[:, 1, :], small[:, 9, :], small[:, 10, :], ALU.mult).then_inc(*v.step())
            V.memset(powr[:, 0, :], 1.0).then_inc(*v.step())
            V.memset(powi[:, 0, :], 0.0).then_inc(*v.step())
            eng.wait_ge(*v.last)
            tt(small[:, 12, :], lr, lr, ALU.mult).then_inc(*v.step())
            tt(small[:, 13, :], li, li, ALU.mult).then_inc(*v.step())
            ts(small[:, 14, :], powr[:, 1, :], -1.0, None, ALU.add).then_inc(*v.step())
            eng.wait_ge(*v.last)
            tt(small[:, 12, :], small[:, 12, :], small[:, 13, :], ALU.add).then_inc(*v.step())
            eng.wait_ge(*v.last)
            V.reciprocal(small[:, 13, :], small[:, 12, :]).then_inc(*v.step())
            tt(small[:, 15, :], small[:, 14, :], lr, ALU.mult).then_inc(*v.step())
            tt(small[:, 16, :], powi[:, 1, :], li, ALU.mult).then_inc(*v.step())
            tt(small[:, 17, :], powi[:, 1, :], lr, ALU.mult).then_inc(*v.step())
            tt(small[:, 18, :], small[:, 14, :], li, ALU.mult).then_inc(*v.step())
            eng.wait_ge(*v.last)
            tt(small[:, 15, :], small[:, 15, :], small[:, 16, :], ALU.add).then_inc(*v.step())
            tt(small[:, 17, :], small[:, 17, :], small[:, 18, :], ALU.subtract).then_inc(*v.step())
            eng.wait_ge(*v.last)
            tt(small[:, 19, :], small[:, 15, :], small[:, 13, :], ALU.mult).then_inc(*v.step())
            tt(small[:, 20, :], small[:, 17, :], small[:, 13, :], ALU.mult).then_inc(*v.step())
            for m in (1, 2, 4):
                pr = powr[:, m, :].unsqueeze(1).to_broadcast([P, m, J5])
                pi = powi[:, m, :].unsqueeze(1).to_broadcast([P, m, J5])
                xr, xi = powr[:, 1:m + 1, :], powi[:, 1:m + 1, :]
                q = [tmp5[:, n * 128:n * 128 + m * J5].rearrange("p (k j) -> p k j", j=J5) for n in range(4)]
                eng.wait_ge(*v.last)
                tt(q[0], xr, pr, ALU.mult).then_inc(*v.step())
                tt(q[1], xi, pi, ALU.mult).then_inc(*v.step())
                tt(q[2], xr, pi, ALU.mult).then_inc(*v.step())
                tt(q[3], xi, pr, ALU.mult).then_inc(*v.step())
                eng.wait_ge(*v.last)
                tt(powr[:, m + 1:2 * m + 1, :], q[0], q[1], ALU.subtract).then_inc(*v.step())
                tt(powi[:, m + 1:2 * m + 1, :], q[2], q[3], ALU.add).then_inc(*v.step())
            eng.wait_ge(*v.last)
            ts(negi, powi, -1.0, None, ALU.mult).then_inc(*v.signals("powers_ready"))
            for s in range(L5):
                V.tensor_copy(prv[:, 0, :, s], powr[:, L5 - 1 - s, :]).then_inc(*v.step())
                V.tensor_copy(prv[:, 1, :, s], powi[:, L5 - 1 - s, :]).then_inc(*v.step())
            V.tensor_copy(step4[:, 0, 0, :], powr[:, L5, :]).then_inc(*v.step())
            ts(step4[:, 0, 1, :], powi[:, L5, :], -1.0, None, ALU.mult).then_inc(*v.step())
            V.tensor_copy(step4[:, 1, 0, :], powi[:, L5, :]).then_inc(*v.step())
            V.tensor_copy(step4[:, 1, 1, :], powr[:, L5, :]).then_inc(*v.step())
            for m in range(4):
                eng.wait_ge(*emptied_at(("raw", m)))
            fr = small[:, 19, :].unsqueeze(2).to_broadcast([P, J5, P5])
            fi = small[:, 20, :].unsqueeze(2).to_broadcast([P, J5, P5])
            q = [tmp5[:, n * 512:(n + 1) * 512].rearrange("p (j q) -> p j q", q=P5) for n in range(2)]
            for i, (f0, f1, op) in enumerate(((fr, fi, ALU.subtract), (fi, fr, ALU.add))):
                eng.wait_ge(*v.last)
                tt(q[0], bt[:, 0, :, :], f0, ALU.mult).then_inc(*v.step())
                tt(q[1], bt[:, 1, :, :], f1, ALU.mult).then_inc(*v.step())
                eng.wait_ge(*v.last)
                tt(bb[:, i, :, :], q[0], q[1], op).then_inc(*v.signals("bb_ready"))
            eng.wait_ge(*filled_at("grp"))
            ps = bank_of("grp").rearrange("p (m g) -> p m g", g=G5)
            V.tensor_copy(grp, ps[:, 0:4, :]).then_inc(*v.empties("grp"))
            for k in range(8):
                ada_panel()
            for i in range(4):
                eng.wait_ge(*filled_at(("ada0", i)))
                ps = bank_of(("ada0", i)).rearrange("p (g q) -> p g q", q=P5)
                pk = pick[:, 0:512].rearrange("p (g q) -> p g q", q=P5)
                eng.wait_ge(*v.last)
                tt(pk, ps, con("diag16").unsqueeze(1).to_broadcast([P, 32, P5]), ALU.mult)\
                    .then_inc(*v.empties(("ada0", i)))
                eng.wait_ge(*v.last)
                V.tensor_reduce(gmod[:, i // 2, (i % 2) * 32:(i % 2) * 32 + 32], pk, AX_X, ALU.add).then_inc(*v.step())
            eng.wait_ge(*v.last)
            tt(gmod, gmod, grp[:, 1:3, :], ALU.add).then_inc(*v.step())
            eng.wait_ge(*v.last)
            stt(gmod[:, 1, :], gmod[:, 1, :], 1.0, grp[:, 0, :], ALU.add, ALU.mult).then_inc(*v.step())
            for i in range(4):
                eng.wait_ge(*emptied_at(("U", i)))
            eng.wait_ge(*v.last)
            tt(U, U, gmod[:, 1, :].unsqueeze(2).to_broadcast([P, G5, C5]), ALU.mult).then_inc(*v.step())
            eng.wait_ge(*v.last)
            tt(U, U, gmod[:, 0, :].unsqueeze(2).to_broadcast([P, G5, C5]), ALU.add).then_inc(*v.signals("u_ready"))

            def add_skip(b):
                for i in range(2):
                    eng.wait_ge(*emptied_at(("kern", b, i)))
                x = kern[:, b % 2, :, 0:P5]
                eng.wait_ge(*v.last)
                tt(skip, grp[0:P5, 3, 8 * b:8 * b + 8].unsqueeze(2).to_broadcast([P5, 8, P5]),
                   con("diag16")[0:P5].unsqueeze(1).to_broadcast([P5, 8, P5]), ALU.mult).then_inc(*v.step())
                eng.wait_ge(*v.last)
                tt(x, x, skip, ALU.add).then_inc(*v.signals("kern_ready"))

            for b in range(NB5):
                js = slice(b * BJ, (b + 1) * BJ)
                if b:
                    eng.wait_ge(*filled_at(("w", b - 1, 1)))
                for i, (n0, n1, op) in enumerate(((0, 1, ALU.subtract), (1, 0, ALU.add))):
                    w0 = prv[:, n0, js, :].unsqueeze(3).to_broadcast([P, BJ, L5, P5])
                    w1 = prv[:, n1, js, :].unsqueeze(3).to_broadcast([P, BJ, L5, P5])
                    q = [tmp5[:, n * 512:(n + 1) * 512].rearrange("p (j s q) -> p j s q", s=L5, q=P5)
                         for n in range(2)]
                    eng.wait_ge(*v.last)
                    tt(q[0], w0, bb[:, 0, js, :].unsqueeze(2).to_broadcast([P, BJ, L5, P5]), ALU.mult)\
                        .then_inc(*v.step())
                    tt(q[1], w1, bb[:, 1, js, :].unsqueeze(2).to_broadcast([P, BJ, L5, P5]), ALU.mult)\
                        .then_inc(*v.step())
                    eng.wait_ge(*v.last)
                    tt(aB[:, i, :, :].rearrange("p j (s q) -> p j s q", q=P5), q[0], q[1], op)\
                        .then_inc(*v.signals("ab_ready"))
                ada_panel()
                if b:
                    add_skip(b - 1)
            add_skip(NB5 - 1)

            for b in range(4, NB5):
                eng.wait_ge(*emptied_at(("bu", b)))
            V.memset(st[:, 0, :, :], 0.0).then_inc(*v.step())
            for c in range(C5 - 1):
                eng.wait_ge(*v.last)
                tt(part4, step4, st[:, c, :, :].unsqueeze(1).to_broadcast([P, 2, 2, J5]), ALU.mult).then_inc(*v.step())
                eng.wait_ge(*v.last)
                tt(part2, part4[:, :, 0, :], BU[:, c, :, :], ALU.add).then_inc(*v.step())
                eng.wait_ge(*v.last)
                tt(st[:, c + 1, :, :], part2, part4[:, :, 1, :], ALU.add)\
                    .then_inc(*(v.signals("states_ready") if c == C5 - 2 else v.step()))
            ada_bias(1)
            for k in range(8):
                ada_panel()
            ada_bias(2)
            for i in range(4):
                eng.wait_ge(*emptied_at(("glu", i)))
                for m in range(2):
                    k = 2 * i + m
                    tt(sq3[:, k, :], sq3[:, k, :], hT3[:, k, :], ALU.mult).then_inc(*v.step())
                    eng.wait_ge(*v.last)
                    stt(xT3[:, k, :], sq3[:, k, :], ada_cols(0, 2)[:, k:k + 1], xT3[:, k, :], ALU.mult, ALU.add)\
                        .then_inc(*v.signals("x_ready"))

            def inverse_root(key, n, width=T, rows=slice(0, P), dst=None, tag="root"):
                x = stat[rows, 0:width]
                eng.wait_ge(*filled_at(key))
                ps = bank_of(key)
                ts(x, ps[rows, 0:width], 1.0 / n, EPS, ALU.mult, ALU.add).then_inc(*v.empties(key))
                eng.wait_ge(done("root_ready"), roots[0] + 1)
                roots[0] += 1
                V.reciprocal(stat[rows, 2 * T:2 * T + width], stat[rows, T:T + width]).then_inc(*v.step())
                eng.wait_ge(*v.last)

            roots = [0]
            rstd = stat[:, 2 * T:3 * T]

            def scale_chunks(dst, gain, sig, chunks=KC, src=xT3):
                for k in range(chunks):
                    stt(dst[:, k, :], src[:, k, :], gain[:, k:k + 1], rstd, ALU.mult, ALU.mult)\
                        .then_inc(*v.signals(sig))

            def modulation(slot, layer, which, gain):
                g = gains[:, slot * KC:(slot + 1) * KC]
                stt(g, ada_cols(layer, which), 1.0, gain, ALU.add, ALU.mult).then_inc(*v.step())
                eng.wait_ge(*v.last)
                return g

            def swiglu(l, extra):
                for c in range(NGU):
                    eng.wait_ge(*filled_at(("gu", l, c)))
                    ps = bank_of(("gu", l, c))
                    eng.wait_ge(done("silu_ready"), l * NGU + c + 1)
                    tt(hid[:, c, :], hid[:, c, :], ps[:, T:2 * T], ALU.mult).then_inc(*v.empties(("gu", l, c)))
                    extra(c)
                for c in range(KC):
                    eng.wait_ge(*filled_at(("dn", l, c // 2)))
                    ps = bank_of(("dn", l, c // 2)).rearrange("p (m t) -> p m t", t=T)
                    stt(xT3[:, c, :], ps[:, c % 2, :], ada_cols(l, 5)[:, c:c + 1], xT3[:, c, :], ALU.mult, ALU.add)\
                        .then_inc(*(v.empties(("dn", l, c // 2)) if c % 2 else v.step()))

            def attend(at, combine=None):
                for u in range(at.n + 1):
                    if u < at.n:
                        key = ("s", at.name, u)
                        eng.wait_ge(*filled_at(key))
                        ps = bank_of(key)
                        w = at.keys(u)
                        x = at.pslots[:, u % SLOTS, 0:w]
                        if u >= SLOTS:
                            eng.wait_ge(*filled_at(("pt", at.name, u - SLOTS)))
                        bias = at.bias(u)
                        if bias is None:
                            ts(x, ps[:, 0:w], at.scale, None, ALU.mult).then_inc(*v.empties(key))
                        else:
                            stt(x, ps[:, 0:w], at.scale, bias, ALU.mult, ALU.add).then_inc(*v.empties(key))
                        eng.wait_ge(*v.last)
                        V.tensor_reduce(at.soft[:, 0, u:u + 1], x, AX_X, ALU.max, negate=True)\
                            .then_inc(*v.signals("max_" + at.name))
                    if u:
                        u -= 1
                        eng.wait_ge(done("exp_" + at.name), u + 1)
                        V.reciprocal(at.soft[:, 2, u:u + 1], at.soft[:, 1, u:u + 1]).then_inc(*v.step())
                        eng.wait_ge(*v.last)
                        x = at.pslots[:, u % SLOTS, 0:at.keys(u)]
                        ts(x, x, at.soft[:, 2, u:u + 1], None, ALU.mult).then_inc(*v.signals("prob_" + at.name))

            g = modulation(0, 0, 4, cols("norm2_g", 0, KC))
            inverse_root(("ms", 1), D)
            scale_chunks(hT3, g, "h_scaled")

            def ada_beside(c):
                for _ in range(2 if c < 10 else 1):
                    ada_panel()
                if c in (5, 9, 15):
                    ada_bias({5: 3, 9: 4, 15: 5}[c])
            swiglu(0, ada_beside)
            ada_bias(6)
            eng.wait_ge(*v.last)
            gk = modulation(1, "kv", 1, cols("kv_norm_g", 0, KC))
            gq = modulation(2, 1, 1, cols("norm1_g", KC, KC))
            inverse_root(("ms", 2), D)
            scale_chunks(hT3, gk, "h_scaled")
            scale_chunks(h2, gq, "h_scaled")
            eng.wait_ge(done("positions_landed"), 16)
            V.tensor_copy(pos_f, pos_i.bitcast(I32)).then_inc(*v.step())
            eng.wait_ge(*v.last)
            for b in range(2):
                ts(angle[:, 0, b, :], con("inv_freq"), pos_f[:, b:b + 1], None, ALU.mult).then_inc(*v.step())
            ang = [angle[:, i, :, :] for i in range(3)]
            eng.wait_ge(*v.last)
            ts(ang[1], ang[0], 1.0 / TWO_PI, ROUND, ALU.mult, ALU.add).then_inc(*v.step())
            eng.wait_ge(*v.last)
            ts(ang[1], ang[1], -ROUND, None, ALU.add).then_inc(*v.step())
            for part in (PI2_A, PI2_B, PI2_C):
                eng.wait_ge(*v.last)
                stt(ang[0], ang[1], -part, ang[0], ALU.mult, ALU.add).then_inc(*v.step())
            eng.wait_ge(*v.last)
            ts(ang[0], ang[0], math.pi * (1 - 1e-7), -math.pi * (1 - 1e-7), ALU.min, ALU.max).then_inc(*v.step())
            eng.wait_ge(*v.last)
            ts(ang[1], ang[0], math.pi / 2, None, ALU.add).then_inc(*v.step())
            eng.wait_ge(*v.last)
            ts(ang[2], ang[1], math.pi, -TWO_PI, ALU.is_gt, ALU.mult).then_inc(*v.step())
            eng.wait_ge(*v.last)
            tt(ang[1], ang[1], ang[2], ALU.add).then_inc(*v.step())
            eng.wait_ge(*v.last)
            ts(ang[1], ang[1], math.pi * (1 - 1e-7), -math.pi * (1 - 1e-7), ALU.min, ALU.max)\
                .then_inc(*v.signals("rotary_angles"))
            eng.wait_ge(done("latent_squares"), 6)
            for i, n in enumerate((RKV, DR, RQ)):
                x = slice(2 * i, 2 * i + 2)
                ts(latent_ss[:, 1, x], latent_ss[:, 0, x], 1.0 / n, EPS, ALU.mult, ALU.add)\
                    .then_inc(*v.signals("latent_mean"))
            eng.wait_ge(done("latent_root"), 1)
            V.reciprocal(latent_ss[:, 0, :], latent_ss[:, 2, :]).then_inc(*v.signals("latent_rstd"))
            inverse_root("ms_mem", D)
            for l in range(2):
                scale_chunks(memn[l], cols("mem_norm_2", l * KC, KC), "memn_ready", src=memT)

            def turn(x, n, b, tells=None):
                x4 = x.rearrange("p h (s m) -> p h s m", s=2)
                t = [turned[:, i, 0:n, :].rearrange("p h (s m) -> p h s m", s=2) for i in range(2)]
                for i in range(2):
                    f = angle[:, i, b, :].unsqueeze(1).unsqueeze(1).to_broadcast([P, n, 2, DR // 2])
                    tt(t[i], x4, f, ALU.mult).then_inc(*v.step())
                eng.wait_ge(*v.last)
                tt(x4[:, :, 0, :], t[1][:, :, 0, :], t[0][:, :, 1, :], ALU.subtract).then_inc(*v.step())
                tt(x4[:, :, 1, :], t[1][:, :, 1, :], t[0][:, :, 0, :], ALU.add)\
                    .then_inc(*(v.signals(tells) if tells else v.step()))
                eng.wait_ge(*v.last)

            def over_tokens(x, n):
                return x.unsqueeze(1).to_broadcast([P, n, x.shape[1]])

            eng.wait_ge(done("gain_rows_landed"), 16 * 4)
            eng.wait_ge(done("rotary_ready"), 1)
            eng.wait_ge(*emptied_at(("kva", 1)))
            tt(krope_tok, krope_tok, over_tokens(gain_rows[:, 0, DN:], 2), ALU.mult).then_inc(*v.step())
            eng.wait_ge(*v.last)
            for b in range(2):
                turn(krope_tok[:, b:b + 1, :], 1, b)
                V.tensor_copy(k_tok1[:, b, :, DN:], krope_tok[:, b:b + 1, :].to_broadcast([P, H1, DR]))\
                    .then_inc(*v.step())
            for hh in range(2):
                for b in range(2):
                    hs = slice(8 * hh, 8 * hh + 8)
                    eng.wait_ge(*emptied_at(("kv", hh, b, 1)))
                    V.tensor_reduce(head_ss[:, 0, b, hs], k_sq[:, b, hs, :], AX_X, ALU.add).then_inc(*v.step())
            eng.wait_ge(*v.last)
            ts(head_ss[:, 1, :, 0:H1], head_ss[:, 0, :, 0:H1], 1.0 / DN, EPS, ALU.mult, ALU.add)\
                .then_inc(*v.signals("k1_mean"))
            eng.wait_ge(done("k1_root"), 1)
            V.reciprocal(head_ss[:, 0, :, 0:H1], head_ss[:, 2, :, 0:H1]).then_inc(*v.step())
            for b in range(2):
                x = k_tok1[:, b, :, 0:DN]
                eng.wait_ge(*v.last)
                tt(x, x, head_ss[:, 0, b, 0:H1].unsqueeze(2).to_broadcast([P, H1, DN]), ALU.mult).then_inc(*v.step())
                eng.wait_ge(*v.last)
                tt(x, x, over_tokens(gain_rows[:, 0, 0:DN], H1), ALU.mult).then_inc(*v.signals("kT1_ready"))
            for hh in range(2):
                for b in range(2):
                    hs = slice(8 * hh, 8 * hh + 8)
                    eng.wait_ge(*emptied_at(("q1", hh, b, 1)))
                    for at, lo, hi in ((H1, 0, DN), (2 * H1, DN, DQK)):
                        V.tensor_reduce(head_ss[:, 0, b, at + 8 * hh:at + 8 * hh + 8], q_sq[:, b, hs, lo:hi], AX_X, ALU.add)\
                            .then_inc(*v.step())
            eng.wait_ge(*v.last)
            for at, n in ((H1, DN), (2 * H1, DR)):
                ts(head_ss[:, 1, :, at:at + H1], head_ss[:, 0, :, at:at + H1], 1.0 / n, EPS, ALU.mult, ALU.add)\
                    .then_inc(*v.signals("q1_mean"))
            eng.wait_ge(done("q1_root"), 1)
            V.reciprocal(head_ss[:, 0, :, H1:], head_ss[:, 2, :, H1:]).then_inc(*v.step())
            eng.wait_ge(*v.last)
            for b in range(2):
                for at, lo, hi in ((H1, 0, DN), (2 * H1, DN, DQK)):
                    x = q_tok1[:, b, :, lo:hi]
                    tt(x, x, head_ss[:, 0, b, at:at + H1].unsqueeze(2).to_broadcast([P, H1, hi - lo]), ALU.mult)\
                        .then_inc(*v.step())
                eng.wait_ge(*v.last)
                x = q_tok1[:, b, :, :]
                tt(x, x, over_tokens(gain_rows[:, 1, :], H1), ALU.mult).then_inc(*v.step())
                eng.wait_ge(*v.last)
                turn(q_tok1[:, b, :, DN:], H1, b, "qT1_ready")
            for b in range(2):
                for g in range(H1 // 4):
                    key = ("qT1", b, g)
                    eng.wait_ge(*filled_at(key))
                    ps = bank_of(key).rearrange("p (h t) -> p h t", t=P)
                    V.tensor_copy(qh[0:DQK, 4 * g:4 * g + 4, b * P:(b + 1) * P], ps[0:DQK]).then_inc(*v.empties(key))
            eng.wait_ge(done("mask_landed"), 16)
            attend(mla)
            for c in range(KC):
                eng.wait_ge(*filled_at(("wo1", c // 2)))
                ps = bank_of(("wo1", c // 2)).rearrange("p (m t) -> p m t", t=T)
                stt(xT3[:, c, :], ps[:, c % 2, :], ada_cols(1, 2)[:, c:c + 1], xT3[:, c, :], ALU.mult, ALU.add)\
                    .then_inc(*(v.empties(("wo1", c // 2)) if c % 2 else v.step()))
            g = modulation(0, 1, 4, cols("norm2_g", KC, KC))
            inverse_root(("ms", 3), D)
            scale_chunks(hT3, g, "h_scaled")
            swiglu(1, lambda c: None)
            eng.wait_ge(*v.last)
            keep = columns2[:, 0:19]
            ts(keep, cols("a_shift_mu_2", 0, 19), -1.0, 1.0, ALU.mult, ALU.add).then_inc(*v.step())
            keep_k = columns2[:, 19:25]
            ts(keep_k, cols("a_k_a_2", 0, 6), -1.0, 1.0, ALU.mult, ALU.add).then_inc(*v.step())
            inverse_root(("ms", 4), D)
            V.memset(shifted[:, :, :, 0:1], 0.0).then_inc(*v.signals("shift_clear"))
            scale_chunks(hT3, cols("pre_norm_2", 0, KC), "h_scaled")
            for c in range(19):
                key = ("a_in", c // 2)
                eng.wait_ge(*filled_at(key))
                ps = bank_of(key).rearrange("p (m t) -> p m t", t=T)
                eng.wait_ge(done("shift_ready"), min(c // 2 * 2 + 2, 19))
                dst = (rt7[:, c, :] if c < 6 else k7[:, c - 6, :] if c < 12 else v7[:, c - 12, :] if c < 18 else lora_in)
                stt(dst, ps[:, c % 2, :], keep[:, c:c + 1], shifted[:, c // 2 % 2, c % 2, 0:T], ALU.mult, ALU.add)\
                    .then_inc(*(v.signals("lora_shifted") if c == 18 else v.empties(key) if c % 2 else v.step()))
            for i in range(3):
                key = ("kks", i)
                eng.wait_ge(*filled_at(key))
                ps = bank_of(key)
                ts(flat(tmp7[:, 2 * i:2 * i + 2, :]), ps, 1e-12, None, ALU.max).then_inc(*v.empties(key))
            for c in range(NBR):
                ts(kk7[:, c, :], k7[:, c, :], col("a_k_k_2", c), None, ALU.mult).then_inc(*v.step())
            eng.wait_ge(done("kk_root"), 1)
            V.reciprocal(flat(tmp7), flat(tmp7)).then_inc(*v.step())
            eng.wait_ge(*v.last)
            tt(kk7, kk7, tmp7, ALU.mult).then_inc(*v.step())
            eng.wait_ge(done("masks7_landed"), 16)
            for c in range(NBR):
                eng.wait_ge(*emptied_at(("decay", c // 2)))
                V.tensor_tensor_scan(cum7[:, c, :], con7("restart"), sig7[:, c, :], 0.0, ALU.mult, ALU.add)\
                    .then_inc(*v.step())
            eng.wait_ge(*v.last)
            tt(at7, cum7, sig7, ALU.subtract).then_inc(*v.signals("cum_ready"))
            eng.wait_ge(*emptied_at(("rate", 2)))
            eng.wait_ge(*v.last)
            for c in range(NBR):
                ts(tmp7[:, c, :], a7[:, c, :], col("a_k_a_2", c), keep_k[:, c:c + 1], ALU.mult, ALU.add)\
                    .then_inc(*v.step())
            eng.wait_ge(*v.last)
            tt(k7, k7, tmp7, ALU.mult).then_inc(*v.step())
            tt(a7, a7, kk7, ALU.mult).then_inc(*v.step())
            eng.wait_ge(*v.last)
            for c in range(NBR):
                stt(tmp7[:, c, :], rt7[:, c, :], col("a_r_k_2", c), k7[:, c, :], ALU.mult, ALU.mult)\
                    .then_inc(*v.step())
            eng.wait_ge(*v.last)
            eng.wait_ge(done("exp7"), 3)
            tt(a7, a7, grow7, ALU.mult).then_inc(*v.signals("scaled7"))
            tt(k7, k7, grow7, ALU.mult).then_inc(*v.step())
            stt(flat(at7), flat(kk7), -1.0, flat(at7), ALU.mult, ALU.mult).then_inc(*v.signals("scaled7"))
            tt(rt7, rt7, cum7, ALU.mult).then_inc(*v.signals("scaled7"))
            def spread(name, n, i=0):
                return con7(name)[:, i * CR:(i + 1) * CR].unsqueeze(1).to_broadcast([P, n, CR])

            for g in range(NU // 8):
                us = slice(8 * g, 8 * g + 8)
                key = ("l", g)
                eng.wait_ge(done("masks7_landed"), 16)
                eng.wait_ge(*filled_at(key))
                ps = bank_of(key).rearrange("p (u t) -> p u t", t=CR)
                tt(x7[:, us, :], ps, spread("level0", 8), ALU.mult).then_inc(*v.empties(key))
                for h in range(2):
                    for key, s_dst, c_dst in (("lb", lt7, lrb7), ("lk", lak7, lrk7)):
                        key = (key, g, h)
                        eng.wait_ge(*filled_at(key))
                        ps = bank_of(key).rearrange("p (u x t) -> p u x t", x=2, t=CR)
                        uh = slice(8 * g + 4 * h, 8 * g + 4 * h + 4)
                        tt(s_dst[:, uh, :], ps[:, :, 0, :], spread("strict_t", 4), ALU.mult).then_inc(*v.step())
                        tt(c_dst[:, uh, :], ps[:, :, 1, :], spread("causal_t", 4), ALU.mult).then_inc(*v.empties(key))
                eng.wait_ge(*v.last)
                tt(y7[:, us, :], lt7[:, us, :], spread("levels_t", 8), ALU.mult).then_inc(*v.step())
                tt(x7[:, us, :], x7[:, us, :], spread("eye64", 8), ALU.add).then_inc(*v.signals("inverse_ready"))
                eng.wait_ge(*v.last)
                tt(y7[:, us, :], y7[:, us, :], spread("eye64", 8), ALU.add).then_inc(*v.signals("inverse_ready"))
            for l in range(1, 6):
                if l > 1:
                    eng.wait_ge(*filled_at(("lt", l - 1, 2)))
                eng.wait_ge(*v.last)
                tt(lt_m7, lt7, spread("levels_t", NU, l), ALU.mult).then_inc(*v.signals("level_mask"))
                for g in range(NU // 8):
                    us = slice(8 * g, 8 * g + 8)
                    pair = [(key, x) for key, x in (("lx", x7), ("ly", y7)) if not (key == "lx" and l == 5)]
                    for key, _ in pair:
                        eng.wait_ge(*filled_at((key, l, g)))
                    for key, x in pair:
                        b, _ = use[(key, l, g)]
                        b = psum[:, b, :].rearrange("p (u t) -> p u t", t=CR)
                        tt(x[:, us, :], x[:, us, :], b, ALU.add).then_inc(*v.empties((key, l, g)))
            for c in range(NCR - 1):
                key = ("state", c)
                eng.wait_ge(*filled_at(key))
                ps = bank_of(key).rearrange("p (i t) -> p i t", t=CR)[:, 0:NBR, :]
                end = cum7[:, :, CR * (c + 1) - 1:CR * (c + 1)].to_broadcast([P, NBR, CR])
                S, S1 = state7[c % 2], state7[(c + 1) % 2]
                if c:
                    eng.wait_ge(*filled_at(("y7", c - 1)))
                    tt(S1, ps, S, ALU.add).then_inc(*v.empties(key))
                    eng.wait_ge(*v.last)
                    tt(S1, S1, end, ALU.mult).then_inc(*v.signals("state_ready"))
                else:
                    tt(S1, ps, end, ALU.mult).then_inc(*v.empties(key))
            attend(memory(0))
            for i in range(3):
                key, two = ("mean7", i), slice(2 * i, 2 * i + 2)
                eng.wait_ge(*filled_at(key))
                ps = bank_of(key)
                stt(flat(yc7[:, two, :]), ps, -1.0 / HD, flat(yT7[:, two, :]), ALU.mult, ALU.add)\
                    .then_inc(*v.empties(key))
            for i in range(3):
                key, two = ("var7", i), slice(2 * i, 2 * i + 2)
                eng.wait_ge(*filled_at(key))
                ps = bank_of(key)
                ts(flat(y_sq7[:, two, :]), ps, 1.0 / HD, LNX_EPS, ALU.mult, ALU.add).then_inc(*v.empties(key))
            eng.wait_ge(done("y7_root"), 1)
            V.reciprocal(flat(y_sq7), flat(y_sq7)).then_inc(*v.step())
            eng.wait_ge(*v.last)
            tt(yc7, yc7, y_sq7, ALU.mult).then_inc(*v.step())
            eng.wait_ge(*v.last)
            for c in range(NBR):
                ts(yc7[:, c, :], yc7[:, c, :], col("a_lnx_w_2", c), col("a_lnx_b_2", c), ALU.mult, ALU.add)\
                    .then_inc(*v.step())
            for i in range(3):
                key, two = ("bonus", i), slice(2 * i, 2 * i + 2)
                eng.wait_ge(*filled_at(key))
                ps = bank_of(key)
                tt(flat(v7[:, two, :]), flat(v7[:, two, :]), ps, ALU.mult).then_inc(*v.empties(key))
                eng.wait_ge(*v.last)
                tt(yc7[:, two, :], yc7[:, two, :], v7[:, two, :], ALU.add).then_inc(*v.step())
                eng.wait_ge(*v.last)
                for c in (2 * i, 2 * i + 1):
                    tt(hT3[:, c, :], yc7[:, c, :], gateT[:, c, :], ALU.mult).then_inc(*v.signals("mixed"))

            def finish(l):
                at = memory(l)
                eng.wait_ge(*emptied_at(("o", at.name, at.n - 1)))
                for c in range(NBR, KC):
                    tt(hT3[:, c, :], hT3[:, c, :], gateT[:, c, :], ALU.mult).then_inc(*v.signals("mixed"))
                inverse_root(("ms_out", l), D)
                for c in range(KC):
                    stt(yP[:, c, :], yP[:, c, :], cols("post_norm_2", l * KC, KC)[:, c:c + 1], rstd, ALU.mult, ALU.mult)\
                        .then_inc(*v.step())
                    eng.wait_ge(*v.last)
                    tt(xT3[:, c, :], xT3[:, c, :], yP[:, c, :], ALU.add).then_inc(*v.signals("post_added"))

            finish(0)
            for i in range(2):
                tt(columns2[:, 32 + i:33 + i], col(f"b_lam_q{i + 1}_2", 0), col(f"b_lam_k{i + 1}_2", 0), ALU.mult)\
                    .then_inc(*v.signals("lam_products"))
            subln = columns2[:, 37:38]
            ts(subln, col("b_subln_2", 0), 1.0 - LAM_INIT, None, ALU.mult).then_inc(*v.step())
            inverse_root(("ms", 5), D)
            scale_chunks(h_kv, cols("kv_norm_2", 0, KC), "h_scaled")
            scale_chunks(hT3, cols("pre_norm_2", KC, KC), "h_scaled")
            minus_lam = columns2[:, 36:37]
            eng.wait_ge(*emptied_at("lam2"))
            stt(minus_lam, columns2[:, 34:35], -1.0, columns2[:, 35:36], ALU.mult, ALU.add).then_inc(*v.step())
            eng.wait_ge(*v.last)
            ts(minus_lam, minus_lam, -LAM_INIT, None, ALU.add).then_inc(*v.step())
            eng.wait_ge(done("alibi_landed"), 16)
            for u in range(ND + 1):
                if u < ND:
                    h, b = u // 2, u % 2
                    w = P * (b + 1)
                    if u >= 3:
                        eng.wait_ge(*filled_at(("dpt", u - 3)))
                    for c in range(2):
                        x = both[:, u % 3, c, 0:w]
                        eng.wait_ge(*filled_at(("ds", u, c)))
                        ps = bank_of(("ds", u, c))
                        stt(x, ps[:, 0:w], HD ** -0.5, alibi[:, h, b, 0:w], ALU.mult, ALU.add)\
                            .then_inc(*v.empties(("ds", u, c)))
                    eng.wait_ge(*v.last)
                    V.tensor_reduce(soft2[:, 0:2, u], both[:, u % 3, :, 0:w], AX_X, ALU.max, negate=True)\
                        .then_inc(*v.signals("max_diff"))
                if u:
                    u -= 1
                    w = P * (u % 2 + 1)
                    eng.wait_ge(done("exp_diff"), 2 * u + 2)
                    V.reciprocal(soft2[:, 2:4, u], sums2[:, 0:2, u]).then_inc(*v.step())
                    eng.wait_ge(*v.last)
                    tt(soft2[:, 3, u:u + 1], soft2[:, 3, u:u + 1], minus_lam, ALU.mult).then_inc(*v.step())
                    x = both[:, u % 3, :, 0:w]
                    ts(x[:, 0], x[:, 0], soft2[:, 2, u:u + 1], None, ALU.mult).then_inc(*v.step())
                    eng.wait_ge(*v.last)
                    stt(x[:, 0], x[:, 1], soft2[:, 3, u:u + 1], x[:, 0], ALU.mult, ALU.add)\
                        .then_inc(*v.signals("prob_diff"))
            attend(memory(1))
            for i in range(3):
                key, two = ("sub", i), slice(2 * i, 2 * i + 2)
                eng.wait_ge(*filled_at(key))
                ps = bank_of(key)
                ts(flat(o_sq[:, two, :]), ps, 1.0 / P, EPS, ALU.mult, ALU.add).then_inc(*v.empties(key))
            eng.wait_ge(done("sub_root"), 1)
            V.reciprocal(flat(o_sq), flat(o_sq)).then_inc(*v.step())
            for h in range(HB):
                eng.wait_ge(*v.last)
                stt(hT3[:, h, :], hT3[:, h, :], subln, o_sq[:, h, :], ALU.mult, ALU.mult).then_inc(*v.step())
                eng.wait_ge(*v.last)
                tt(hT3[:, h, :], hT3[:, h, :], gateT[:, h, :], ALU.mult).then_inc(*v.signals("mixed"))
            finish(1)
            for i in range(0, 4, 2):
                eng.wait_ge(*filled_at(("rows", i)))
                ps = bank_of(("rows", i))
                V.tensor_copy(out_rows[:, i // 2, 0:512], ps).then_inc(*v.empties(("rows", i)))

        @block.scalar
        def _(eng):
            s = Program("scalar")

            def act(dst, x, f, **k):
                return eng.activation(dst, x, f, **k)

            def vector_sources(name, n):
                x = a[name]
                if name == "a_r_k_2":
                    x = x.rearrange("l h n -> l (h n)")
                if len(x.shape) == 2:
                    x = x.rearrange("l n -> (l n)")
                if name.startswith("b_lam"):
                    return [(x.rearrange("(o n) -> o n", o=1), 0, HD)]
                return [(x.rearrange("(r p) -> r p", p=P), 0, P)]

            def load_s5():
                groups = [a["norm1_g"][0], a["ada_b"][0, 0:D], a["ada_b"][0, D:2 * D], a["s5_d"][0]]
                loads = [(lam_rows[:, 0, :], a["s5_lam_re"][0].rearrange("(j r) n -> j (r n)", r=2)),
                         (lam_rows[:, 1, :], a["s5_lam_im"][0].rearrange("(j r) n -> j (r n)", r=2)),
                         (lam_rows[:, 2, 0:2], a["s5_log_dt"][0].rearrange("(j r) -> j r", r=2))]
                loads += [(group_rows[:, m, :], x.rearrange("(g q) -> g q", q=P5)) for m, x in enumerate(groups)]
                loads += [(raw[:, m, :, :].rearrange("j r n -> j (r n)"),
                           a[x][0].rearrange("(j r) n q -> j (r n q)", r=2))
                          for m, x in enumerate(("s5_b_re", "s5_b_im", "s5_c_re", "s5_c_im"))]
                for dst, src in loads:
                    eng.dma_start(dst, src).then_inc(done("s5_landed"), 16)

            eng.dma_start(const_sb[:, :], constants[:, 0:CONST_KEEP]).then_inc(done("const_landed"), 16)
            eng.wait_ge(done("rows_clear"), 1)
            for name, (tile, r, n) in VEC_AT.items():
                for src, lo, hi in vector_sources(name, n):
                    eng.dma_start(rows[r:r + n, tile * P + lo:tile * P + hi], src)\
                       .then_inc(done(f"vectors{tile}_landed"), 16)
                if name == "kv_ada_b":
                    load_s5()
            eng.wait_ge(*emptied_at(("vec", 0)))
            act(c_act[:, :], cols("c", 0, KC), ACT.Silu).then_inc(*s.signals("c_act_ready"))
            for i in range(4):
                eng.wait_ge(*filled_at(("xT", i)))
                ps = bank_of(("xT", i))
                act(xT[:, i * 512:(i + 1) * 512], ps, ACT.Copy).then_inc(*s.empties(("xT", i)))
            eng.wait_ge(done("xc_landed"), 16)
            for t in range(L5):
                if t:
                    eng.wait_ge(*s.last)
                else:
                    eng.wait_ge(*filled_at(("xT", 3)))
                act(sq[0:C5, 0:D], xC_in[:, t, :], ACT.Square, accum_out=ss[:, 0, t:t + 1])\
                    .then_inc(*s.signals("xc_squares"))
            eng.wait_ge(done("xc_mean"), 1)
            act(ss[:, 2, :], ss[:, 1, :], ACT.Sqrt).then_inc(*s.signals("xc_root"))
            eng.wait_ge(done("log_dt_ready"), 1)
            act(small[:, 3, :], small[:, 4, :], ACT.Exp).then_inc(*s.signals("dt_ready"))
            eng.wait_ge(done("decay_ready"), 1)
            act(small[:, 9, :], small[:, 5, :], ACT.Exp).then_inc(*s.signals("poles_ready"))
            eng.wait_ge(done("angles_ready"), 1)
            act(small[:, 10, :], small[:, 6, :], ACT.Sin).then_inc(*s.signals("poles_ready"))
            act(small[:, 11, :], small[:, 7, :], ACT.Sin).then_inc(*s.signals("poles_ready"))
            for m, dst in enumerate((bt[:, 0], bt[:, 1], ct[:, 0], ct[:, 1])):
                eng.wait_ge(*filled_at(("raw", m)))
                ps = bank_of(("raw", m)).rearrange("p (q j) -> p j q", j=J5)
                act(dst, ps, ACT.Copy).then_inc(*s.empties(("raw", m)))
            for i in range(4):
                eng.wait_ge(*filled_at(("U", i)))
                ps = bank_of(("U", i))
                act(hT[:, i * 512:(i + 1) * 512], ps, ACT.Copy).then_inc(*s.empties(("U", i)))
            for b in range(NB5):
                for i in range(2):
                    eng.wait_ge(*filled_at(("w", b, i)))
                    ps = bank_of(("w", b, i)).rearrange("p (j n) -> p j n", n=P)
                    if b:
                        eng.wait_ge(*filled_at(("bu", b - 1)))
                    act(wT[:, :, i, :], ps, ACT.Copy).then_inc(*s.empties(("w", b, i)))
                for i in range(2):
                    eng.wait_ge(*filled_at(("kern", b, i)))
                    ps = bank_of(("kern", b, i))
                    if b > 1:
                        eng.wait_ge(done(f"toeplitz{b % 2}_landed"), 16 * L5 * (b // 2))
                    act(kern[:, b % 2, i::2, :], ps[64 * i:64 * i + P5].rearrange("p (g n) -> p g n", n=P), ACT.Copy)\
                        .then_inc(*s.empties(("kern", b, i)))
                eng.wait_ge(*filled_at(("bu", b)))
                ps = bank_of(("bu", b)).rearrange("p (j i c) -> p c i j", j=BJ, i=2)[:, 0:C5]
                act(BU[:, :, :, b * BJ:(b + 1) * BJ], ps, ACT.Copy).then_inc(*s.empties(("bu", b)))
            gC4 = gC.rearrange("c t (g q) -> c t g q", q=P5)
            for i in range(16):
                eng.wait_ge(*filled_at(("y5", i)))
                r = 64 * (i % 2)
                ps = bank_of(("y5", i))[r:r + C5, :].rearrange("c (m t q) -> c t m q", t=L5, q=P5)
                gg = 8 * (i // 2) + i % 2
                act(gC4[:, :, gg:gg + 7:2, :], ps, ACT.Gelu_apprx_tanh).then_inc(*s.empties(("y5", i)))
            for i in range(4):
                eng.wait_ge(*filled_at(("gt", i)))
                ps = bank_of(("gt", i)).rearrange("p (k t c) -> p k c t", k=2, t=L5)
                for k in range(2):
                    act(hT3[:, 2 * i + k, :].rearrange("p (c t) -> p c t", t=L5), ps[:, k], ACT.Copy)\
                        .then_inc(*(s.empties(("gt", i)) if k else s.step()))
            for i in range(4):
                eng.wait_ge(*filled_at(("glu", i)))
                ps = bank_of(("glu", i)).rearrange("p (m t) -> p m t", t=T)
                for m in range(2):
                    k = 2 * i + m
                    act(sq3[:, k, :], ps[:, m, :], ACT.Sigmoid, bias=col("s5_b_glu", k))\
                        .then_inc(*(s.empties(("glu", i)) if m else s.step()))

            def squares(r):
                for i in range(2):
                    for pair in (2 * i, 2 * i + 1):
                        if r == 0:
                            eng.wait_ge(done("x_ready"), 2 * (pair + 1))
                        elif r >= len(UPDATES):
                            eng.wait_ge(done("post_added"), KC * (r - len(UPDATES)) + 2 * (pair + 1))
                        else:
                            key = UPDATES[r]
                            eng.wait_ge(*emptied_at((*key, pair)))
                    act(sq[:, i * 4 * T:(i + 1) * 4 * T], xT[:, i * 4 * T:(i + 1) * 4 * T], ACT.Square)\
                        .then_inc(*s.signals("squares"))

            def root(key, width=T, rows=slice(0, P)):
                eng.wait_ge(*emptied_at(key))
                act(stat[rows, T:T + width], stat[rows, 0:width], ACT.Sqrt).then_inc(*s.signals("root_ready"))

            def shift(dst, layer, which, base):
                for k in range(KC):
                    eng.wait_ge(done("h_scaled"), base + k + 1)
                    act(dst[:, k, :], dst[:, k, :], ACT.Identity, bias=ada_cols(layer, which)[:, k:k + 1])\
                        .then_inc(*s.signals("h_ready"))

            def swiglu(l):
                for c in range(NGU):
                    eng.wait_ge(*filled_at(("gu", l, c)))
                    ps = bank_of(("gu", l, c))
                    act(hid[:, c, :], ps[:, 0:T], ACT.Silu).then_inc(*s.signals("silu_ready"))

            def attend(at):
                for u in range(at.n + LAG + 1):
                    if u < at.n:
                        eng.wait_ge(done("max_" + at.name), u + 1)
                        x = at.pslots[:, u % SLOTS, 0:at.keys(u)]
                        act(x, x, ACT.Exp, bias=at.soft[:, 0, u:u + 1], accum_out=at.soft[:, 1, u:u + 1])\
                            .then_inc(*s.signals("exp_" + at.name))
                    if LAG <= u < at.n + LAG:
                        w = u - LAG
                        eng.wait_ge(*filled_at(("pt", at.name, w)))
                        ps = bank_of(("pt", at.name, w))
                        if w >= 4:
                            eng.wait_ge(*filled_at(("o", at.name, w - 4)))
                        act(at.tslots[:, w % 4, 0:at.keys(w)], ps[:, 0:at.keys(w)], ACT.Copy)\
                            .then_inc(*s.empties(("pt", at.name, w)))
                    if u > LAG:
                        w = u - LAG - 1
                        eng.wait_ge(*filled_at(("o", at.name, w)))
                        ps = bank_of(("o", at.name, w))
                        r, m = at.width(w)
                        act(at.dst(w), ps[r:r + m, 0:P], ACT.Copy).then_inc(*s.empties(("o", at.name, w)))

            squares(0)
            root(("ms", 1))
            shift(hT3, 0, 3, 0)
            swiglu(0)
            for i in range(4):
                eng.wait_ge(*filled_at(("memT", i)))
                act(memT[:, 2 * i:2 * i + 2, :].rearrange("p k t -> p (k t)"), bank_of(("memT", i)), ACT.Copy)\
                    .then_inc(*s.empties(("memT", i)))
            squares(1)
            eng.dma_start(pos_i.bitcast(I32), a["positions"][0].rearrange("(b p) -> p b", p=P),
                          allow_slow_non_contiguous=True)\
               .then_inc(done("positions_landed"), 16)
            for m, names in enumerate((("k_nope_norm_g", "k_rope_norm_g"), ("mla_q_nope_norm_g", "mla_q_rope_norm_g"))):
                for name, lo, hi in zip(names, (0, DN), (DN, DQK)):
                    x = a[name] if m == 0 else a[name][0]
                    eng.dma_start(gain_rows[:, m, lo:hi], x.partition_broadcast(P)).then_inc(done("gain_rows_landed"), 16)
            eng.dma_start(mask1, constants[:, CONST_KEEP:CONST_MASK].rearrange("p (b t) -> p b t", t=T))\
               .then_inc(done("mask_landed"), 16)
            root(("ms", 2))
            shift(hT3, "kv", 0, KC)
            shift(h2, 1, 0, 2 * KC)
            eng.wait_ge(*emptied_at(("ada", 6)))
            act(flat(mem_sq), flat(memT), ACT.Square).then_inc(*s.signals("mem_squares"))
            eng.wait_ge(*filled_at(("ms", 2)))
            parts = [(("kva", b), 0, RKV, b) for b in range(2)] + [(("kva", b), RKV, RKV + DR, 2 + b) for b in range(2)]
            parts += [(("cqt", b), 0, RQ, 4 + b) for b in range(2)]
            for key, lo, hi, i in parts:
                eng.wait_ge(*filled_at(key))
                act(sq[:, i * 256:i * 256 + hi - lo], bank_of(key)[:, lo:hi], ACT.Square, accum_out=latent_ss[:, 0, i:i + 1])\
                    .then_inc(*s.signals("latent_squares"))
            eng.wait_ge(done("latent_mean"), 3)
            act(latent_ss[:, 2, :], latent_ss[:, 1, :], ACT.Sqrt).then_inc(*s.signals("latent_root"))
            eng.wait_ge(done("latent_rstd"), 1)
            for b in range(2):
                ps = bank_of(("kva", b))
                act(latent_tok[0][:, b, :], ps[:, 0:RKV], ACT.Identity, scale=latent_ss[:, 0, b:b + 1])\
                    .then_inc(*s.step())
                act(krope_tok[:, b, :], ps[:, RKV:RKV + DR], ACT.Identity, scale=latent_ss[:, 0, 2 + b:3 + b])\
                    .then_inc(*s.empties(("kva", b)))
            for b in range(2):
                act(latent_tok[1][:, b, :], bank_of(("cqt", b))[:, 0:RQ], ACT.Identity, scale=latent_ss[:, 0, 4 + b:5 + b])\
                    .then_inc(*s.empties(("cqt", b)))
            root("ms_mem")
            eng.wait_ge(done("rotary_angles"), 1)
            act(angle[:, 0:2], angle[:, 0:2], ACT.Sin).then_inc(*s.signals("rotary_ready"))

            def memory_kv(l):
                for dst, key in ((k_mem[l], ("k_mem", l, 0)), (v_mem[l], ("v_mem", l, 0))):
                    eng.wait_ge(*filled_at(key))
                    act(flat(dst), bank_of(key), ACT.Copy).then_inc(*s.empties(key))

            memory_kv(0)
            for i, (key, gain) in enumerate((("ckvT", "kv_a_norm_g"), ("cqT", "mla_q_norm_g"))):
                eng.wait_ge(*filled_at(key))
                ps = bank_of(key).rearrange("p (k t) -> p k t", t=T)
                for k in range(2):
                    act(latent[i][:, k, :], ps[:, k, :], ACT.Identity, scale=col(gain, k))\
                        .then_inc(*(s.empties(key) if k else s.step()))
            for hh in range(2):
                for b in range(2):
                    for n in range(2):
                        key, hs = ("kv", hh, b, n), slice(8 * hh + 4 * n, 8 * hh + 4 * n + 4)
                        eng.wait_ge(*filled_at(key))
                        ps = bank_of(key).rearrange("p (h n) -> p h n", n=P)
                        act(k_sq[:, b, hs, :], ps[:, :, 0:DN], ACT.Square).then_inc(*s.step())
                        act(k_tok1[:, b, hs, 0:DN], ps[:, :, 0:DN], ACT.Copy).then_inc(*s.step())
                        act(v1[:, b, :].rearrange("p (h n) -> p h n", n=DV)[:, hs, :], ps[:, :, DN:], ACT.Copy)\
                            .then_inc(*s.empties(key))
            for hh in range(2):
                for b in range(2):
                    for n in range(2):
                        key, hs = ("q1", hh, b, n), slice(8 * hh + 4 * n, 8 * hh + 4 * n + 4)
                        eng.wait_ge(*filled_at(key))
                        ps = bank_of(key)[:, 0:4 * DQK].rearrange("p (h n) -> p h n", n=DQK)
                        act(q_sq[:, b, hs, :], ps, ACT.Square).then_inc(*s.step())
                        act(q_tok1[:, b, hs, :], ps, ACT.Copy).then_inc(*s.empties(key))
                if hh == 0:
                    eng.wait_ge(done("k1_mean"), 1)
                    act(head_ss[:, 2, :, 0:H1], head_ss[:, 1, :, 0:H1], ACT.Sqrt).then_inc(*s.signals("k1_root"))
            eng.wait_ge(done("q1_mean"), 2)
            act(head_ss[:, 2, :, H1:], head_ss[:, 1, :, H1:], ACT.Sqrt).then_inc(*s.signals("q1_root"))
            memory_kv(1)
            for b in range(2):
                for g in range(H1 // 4):
                    key = ("kT1", b, g)
                    eng.wait_ge(*filled_at(key))
                    ps = bank_of(key).rearrange("p (h t) -> p h t", t=P)
                    act(kh[0:DQK, 4 * g:4 * g + 4, b * P:(b + 1) * P], ps[0:DQK], ACT.Copy).then_inc(*s.empties(key))
            attend(mla)
            squares(2)
            root(("ms", 3))
            shift(hT3, 1, 3, 3 * KC)
            swiglu(1)
            squares(3)
            for r, x in ((0, "a_w2_2"), (64, "a_a2_2")):
                eng.dma_start(w2a2[r:r + 64, :], a[x][0]).then_inc(done("w2_landed"), 16)
            eng.dma_start(masks7, constants[:, CONST_MASK:CONST_ALIBI]).then_inc(done("masks7_landed"), 16)
            root(("ms", 4))
            eng.wait_ge(done("shift_clear"), 1)
            for c in range(A_IN // P):
                i, m = c // 2, c % 2
                key = ("a_in", i)
                eng.wait_ge(*filled_at(key))
                ps = bank_of(key).rearrange("p (m t) -> p m t", t=T)[:, m, :]
                if c < 19:
                    if m == 0 and i > 1:
                        eng.wait_ge(*emptied_at(("a_in", i - 2)))
                    act(shifted[:, i % 2, m, 1:T + 1], ps, ACT.Identity, scale=col("a_shift_mu_2", c))\
                        .then_inc(*s.signals("shift_ready"))
                    if c == 18:
                        eng.wait_ge(done("lora_shifted"), 1)
                elif c < 19 + NBR or c >= 27:
                    k = c - 19 if c < 25 else c - 21
                    act(gateT[:, k, :], ps, ACT.Silu).then_inc(*(s.empties(key) if m or c == 28 else s.step()))
                else:
                    act(q_mem[:, c - 25, :], ps, ACT.Copy).then_inc(*(s.empties(key) if m else s.step()))
            act(lora_in[0:64, :], lora_in[0:64, :], ACT.Tanh).then_inc(*s.signals("tanh_ready"))
            eng.wait_ge(*emptied_at(("a_in", 5)))
            for c in range(NBR):
                act(tmp7[:, c, :], k7[:, c, :], ACT.Square, scale=col("a_k_k_2", c)).then_inc(*s.signals("kk_squares"))
            for i in range(NBR // 2):
                for key, bias, dst in ((("decay", i), "a_w0_2", sig7), (("rate", i), "a_a0_2", a7)):
                    eng.wait_ge(*filled_at(key))
                    ps = bank_of(key).rearrange("p (m t) -> p m t", t=T)
                    for m in range(2):
                        act(dst[:, 2 * i + m, :], ps[:, m, :], ACT.Sigmoid, bias=col(bias, 2 * i + m))\
                            .then_inc(*(s.empties(key) if m else s.step()))
            for i in range(3):
                eng.wait_ge(*emptied_at(("kks", i)))
            act(flat(tmp7), flat(tmp7), ACT.Sqrt).then_inc(*s.signals("kk_root"))
            eng.wait_ge(done("cum_ready"), 1)
            act(flat(grow7), flat(cum7), ACT.Exp, scale=math.exp(-0.5)).then_inc(*s.signals("exp7"))
            eng.wait_ge(*s.last)
            act(flat(cum7), flat(cum7), ACT.Exp, scale=-math.exp(-0.5)).then_inc(*s.signals("exp7"))
            act(flat(at7), flat(at7), ACT.Exp, scale=-math.exp(-0.5)).then_inc(*s.signals("exp7"))
            for name, dst in (("b_tok", b_tok), ("k_tok", k_tok), ("v_tok", v_tok)):
                for g in range(3):
                    key = (name, g)
                    eng.wait_ge(*filled_at(key))
                    ps = bank_of(key)
                    act(flat(dst[:, 8 * g:8 * g + 8, :]), ps, ACT.Copy).then_inc(*s.empties(key))
            for l in range(1, 6):
                for g in range(3):
                    key = ("lt", l, g)
                    eng.wait_ge(*filled_at(key))
                    ps = bank_of(key)
                    act(flat(lt_t7[:, 8 * g:8 * g + 8, :]), ps, ACT.Copy).then_inc(*s.empties(key))
            for c in range(NCR):
                for name, dst in (("rhs", rhs7), ("sa", sa7)):
                    eng.wait_ge(*filled_at((name, c)))
                    ps = bank_of((name, c))
                    act(flat(dst), ps[:, 0:NBR * CR], ACT.Copy).then_inc(*s.empties((name, c)))
                eng.wait_ge(*filled_at(("y7", c)))
                ps = bank_of(("y7", c)).rearrange("p (i t) -> p i t", t=CR)[:, 0:NBR, :]
                act(yT7[:, :, c * CR:(c + 1) * CR], ps, ACT.Copy).then_inc(*s.empties(("y7", c)))
            attend(memory(0))
            for i in range(3):
                eng.wait_ge(*emptied_at(("mean7", i)))
                act(flat(y_sq7[:, 2 * i:2 * i + 2, :]), flat(yc7[:, 2 * i:2 * i + 2, :]), ACT.Square)\
                    .then_inc(*s.signals("y7_squares"))
            for i in range(3):
                eng.wait_ge(*emptied_at(("var7", i)))
            act(flat(y_sq7), flat(y_sq7), ACT.Sqrt).then_inc(*s.signals("y7_root"))

            def output(l):
                for i in range(4):
                    key = ("out", l, i)
                    eng.wait_ge(*filled_at(key))
                    ps = bank_of(key)
                    act(flat(out_sq[l][:, 2 * i:2 * i + 2, :]), ps, ACT.Square).then_inc(*s.signals("out_squares"))
                    act(flat(yP[:, 2 * i:2 * i + 2, :]), ps, ACT.Copy).then_inc(*s.empties(key))
                root(("ms_out", l))

            output(0)
            squares(4)
            eng.dma_start(alibi, constants[:, CONST_ALIBI:].rearrange("p (h b t) -> p h b t", b=2, t=T))\
               .then_inc(done("alibi_landed"), 16)
            root(("ms", 5))
            for i in range(3):
                eng.wait_ge(*filled_at(("k_sh", i)))
                ps = bank_of(("k_sh", i))
                act(flat(kT[:, 2 * i:2 * i + 2, :]), ps, ACT.Copy).then_inc(*s.empties(("k_sh", i)))
            for i in range(3):
                eng.wait_ge(*filled_at(("v_sh", i)))
                ps = bank_of(("v_sh", i)).rearrange("p (b n) -> p b n", n=256)
                act(v_sh[:, :, i * 256:(i + 1) * 256], ps, ACT.Copy).then_inc(*s.empties(("v_sh", i)))
            for i in range(8):
                eng.wait_ge(*filled_at(("b_in", i)))
                ps = bank_of(("b_in", i))
                dst, f = ((qT[:, 2 * i:2 * i + 2, :], ACT.Copy) if i < 3 else
                          (gateT[:, 2 * i - 6:2 * i - 4, :], ACT.Silu) if i < 6 else
                          (q_mem, ACT.Copy) if i == 6 else (gateT[:, 6:8, :], ACT.Silu))
                act(flat(dst), ps, f).then_inc(*s.empties(("b_in", i)))
            eng.wait_ge(*filled_at("lam2"))
            ps = bank_of("lam2")
            act(columns2[:, 34:36], ps[:, 0:2], ACT.Exp).then_inc(*s.empties("lam2"))
            for u in range(ND + 3):
                if u < ND:
                    eng.wait_ge(done("max_diff"), u + 1)
                    for c in range(2):
                        x = both[:, u % 3, c, 0:P * (u % 2 + 1)]
                        act(x, x, ACT.Exp, bias=soft2[:, c, u:u + 1], accum_out=sums2[:, c, u:u + 1])\
                            .then_inc(*s.signals("exp_diff"))
                if 1 <= u <= ND:
                    w = u - 1
                    eng.wait_ge(*filled_at(("dpt", w)))
                    ps = bank_of(("dpt", w))
                    if w >= 4:
                        eng.wait_ge(*filled_at(("do", w - 4)))
                    n = P * (w % 2 + 1)
                    act(tslots2[:, w % 4, 0:n], ps[:, 0:n], ACT.Copy).then_inc(*s.empties(("dpt", w)))
                if 2 <= u <= ND + 1:
                    w = u - 2
                    eng.wait_ge(*filled_at(("do", w)))
                    ps = bank_of(("do", w))
                    act(hT3[:, w // 2, w % 2 * P:(w % 2 + 1) * P], ps[:, 0:P], ACT.Copy)\
                        .then_inc(*s.empties(("do", w)))
            attend(memory(1))
            eng.wait_ge(*emptied_at(("do", ND - 1)))
            for i in range(3):
                two = slice(2 * i, 2 * i + 2)
                act(flat(o_sq[:, two, :]), flat(hT3[:, two, :]), ACT.Square).then_inc(*s.signals("o_squares"))
            for i in range(3):
                eng.wait_ge(*emptied_at(("sub", i)))
            act(flat(o_sq), flat(o_sq), ACT.Sqrt).then_inc(*s.signals("sub_root"))
            output(1)
            for i in range(1, 4, 2):
                eng.wait_ge(*filled_at(("rows", i)))
                ps = bank_of(("rows", i))
                act(out_rows[:, i // 2, 512:1024], ps, ACT.Copy).then_inc(*s.empties(("rows", i)))

        @block.gpsimd
        def _(eng):
            g = Program("gpsimd")
            w = [a["ada_w"][l].rearrange("(k p) n -> k p n", p=P) for l in range(2)]
            kv = a["kv_ada_w"].rearrange("(k p) n -> k p n", p=P)
            src = [w[l][k, :, m * PANEL:(m + 1) * PANEL] for l in range(2) for m in range(3) for k in range(KC)]
            src += [kv[k] for k in range(KC)]
            def ada_load(i):
                if i >= ARING:
                    eng.wait_ge(done("ada_used"), i - ARING + 1)
                eng.dma_start(aring[:, (i % ARING) * PANEL:(i % ARING + 1) * PANEL], src[i])\
                   .then_inc(ada_landed[i % ARING], 16)

            for i in range(8):
                ada_load(i)
            G = nc.gpsimd
            for m in range(4):
                eng.wait_ge(*emptied_at(("raw", m)))
            G.memset(toep, 0.0).then_inc(*g.signals("toeplitz_clear"))
            eng.wait_ge(done("powers_ready"), 1)
            eng.wait_ge(done("bb_ready"), 2)
            eng.wait_ge(*filled_at(("U", 3)))
            for b in range(NB5):
                js = slice(b * BJ, (b + 1) * BJ)

                def power(x):
                    return x[:, :, js].rearrange("p k j -> p j k").unsqueeze(3).to_broadcast([P, BJ, 9, P5])

                def coefficient(i):
                    return ct[:, i, js, :].unsqueeze(2).to_broadcast([P, BJ, 9, P5])
                for dst, x0, x1 in ((ca_re, powr, powi), (ca_im, negi, powr)):
                    q = [tmp_c[:, n * 576:(n + 1) * 576].rearrange("p (j k q) -> p j k q", k=9, q=P5)
                         for n in range(2)]
                    if g.last:
                        eng.wait_ge(*g.last)
                    G.tensor_tensor(q[0], power(x0), coefficient(0), ALU.mult).then_inc(*g.step())
                    G.tensor_tensor(q[1], power(x1), coefficient(1), ALU.mult).then_inc(*g.step())
                    eng.wait_ge(*g.last)
                    G.tensor_tensor(dst[:, js, :, :], q[0], q[1], ALU.subtract).then_inc(*g.signals("ca_ready"))
                ada_load(8 + b)
            for i in range(16, len(src)):
                ada_load(i)
            eng.wait_ge(done("ada_used"), len(src))
            eng.dma_start(mem_nat, a["mem_2"][0].rearrange("(b p) d -> p b d", p=P)).then_inc(done("mem_landed"), 16)


def kernel(**inputs):
    import concourse.bacc as bacc
    from concourse.bass_utils import run_bass_kernel_spmd

    nc = bacc.Bacc("TRN2", target_bir_lowering=False, num_devices=1)
    arrays = {"in_" + name: np.ascontiguousarray(x) for name, x in inputs.items()}
    arrays["in_constants"] = CONSTANTS
    drams = {name: nc.dram_tensor(name, x.shape, mybir.dt.from_np(x.dtype), kind="ExternalInput").ap()
             for name, x in arrays.items()}
    constants = drams.pop("in_constants")
    out = nc.dram_tensor("out_0", (1, T, D), F32, kind="ExternalOutput").ap()
    blocks_kernel(nc, {name[3:]: x for name, x in drams.items()}, constants, out)
    r = run_bass_kernel_spmd(nc, [arrays], core_ids=[0])
    return r.results[0]["out_0"]
```

```python
from contextlib import ExitStack
import math

import numpy as np

import concourse.bass as bass
from concourse import mybir

F32 = mybir.dt.float32
I32 = mybir.dt.int32
ALU = mybir.AluOpType
ACT = mybir.ActivationFunctionType
AX_X = mybir.AxisListType.X

P = 128
T = 256
D = 1024
KC = D // P
FF = 2816
EPS = 1e-6
NEG = -1e30

G5, P5, N5 = 64, 16, 64
L5 = 8
C5 = T // L5
J5 = G5 // 2
BJ = 4
NB5 = J5 // BJ

H1, DN, DR, DV = 16, 64, 32, 64
DQK = DN + DR
RKV = RQ = 256
SCALE1 = 1.0 / math.sqrt(DQK)
THETA = 10000.0
CHUNK = 64

HD = 64
MW = 256
BR = 768
NBR = BR // P
A_SHIFT = 3 * BR + 128
A_IN = A_SHIFT + BR + 2 * MW
B_IN = 2 * BR + 2 * MW
HB = 6
LNX_EPS = 64e-5
CR = 64
NCR = T // CR
NU = NBR * NCR
LAM_INIT = 0.8 - 0.6 * math.exp(-0.3)

SLOTS = 6
LAG = 3
RING = 4
PANEL = 2048
ARING = 2
ARENA = 30000
TWO_PI = 2.0 * math.pi
ROUND = 1.5 * 2.0 ** 23
PI2_A = 6.28125
PI2_B = float((np.float32(TWO_PI - PI2_A).view(np.uint32) & np.uint32(0xFFFFF000)).view(np.float32))
PI2_C = float(np.float32(TWO_PI - PI2_A - PI2_B))


def alibi_slopes(n):
    def pow2(m):
        start = 2.0 ** (-8.0 / m)
        return [start ** (i + 1) for i in range(m)]
    if math.log2(n).is_integer():
        return pow2(n)
    c = 2 ** int(math.floor(math.log2(n)))
    return pow2(c) + pow2(2 * c)[0::2][: n - c]


def shape_constants():
    p = np.arange(P)
    parts = {}
    parts["ident"] = np.eye(P)
    parts["ones"] = np.ones((P, P))
    half = (p[:, None] // 64) == (p[None, :] // 64)
    parts["half"] = half * 1.0
    parts["diag16"] = ((p[:, None] % P5) == np.arange(P5)[None, :]) * 1.0
    inv = 1.0 / (np.float32(THETA) ** (np.arange(0, DR, 2, dtype=np.float32) / np.float32(DR)))
    parts["inv_freq"] = np.broadcast_to(inv[None, :], (P, DR // 2))
    parts["pick1"] = np.zeros((P, 2 * HB - 1))
    parts["pick1"][:, HB - 1] = 1.0
    parts["pick2"] = np.zeros((P, 4 * NBR - 2))
    parts["pick2"][:P // 2, 2 * NBR - 2] = 1.0
    parts["pick2"][P // 2:, 2 * NBR - 1] = 1.0
    mask = np.zeros((P, 2, T))
    for b in range(2):
        q = (b * P + p) // CHUNK
        mask[:, b, :] = np.where(q[:, None] >= (np.arange(T) // CHUNK)[None, :], 0.0, NEG)
    hidden = np.zeros((P, 2, T))
    for b in range(2):
        hidden[b, 0, b * P:b * P + CHUNK] = 1.0
        hidden[b, 1, b * P + CHUNK:(b + 1) * P] = NEG
    parts["hidden"] = hidden.reshape(P, -1)
    t = np.arange(CR)
    row = p % CR
    parts["strict_t"] = (row[:, None] < t[None, :]) * 1.0
    parts["causal_t"] = (row[:, None] <= t[None, :]) * 1.0
    parts["eye64"] = (row[:, None] == t[None, :]) * 1.0
    lev = []
    for l in range(6):
        b = 1 << l
        hi, lo = t[None, :], row[:, None]
        lev.append(((hi // (2 * b)) == (lo // (2 * b))) & ((hi // b) % 2 == 1) & ((lo // b) % 2 == 0))
    parts["levels_t"] = np.concatenate(lev, axis=1) * 1.0
    parts["level0"] = (((row[:, None] // 2) == (t[None, :] // 2)) & (row[:, None] % 2 == 1) & (t[None, :] % 2 == 0)) * 1.0
    parts["restart"] = np.broadcast_to((np.arange(T) % CR != 0) * 1.0, (P, T))
    bias = np.zeros((P, HB, 2, T), np.float32)
    for h, s in enumerate(np.array(alibi_slopes(HB), np.float32)):
        for b in range(2):
            dist = np.abs((b * P + p)[:, None] - np.arange(T)[None, :]).astype(np.float32)
            bias[:, h, b, :] = -s * dist + mask[:, b, :].astype(np.float32)
    parts["alibi"] = bias.reshape(P, -1)
    at, cols = {}, 0
    for n, a in parts.items():
        at[n] = (cols, a.shape[1])
        cols += a.shape[1]
    return at, np.concatenate([np.asarray(a, np.float32) for a in parts.values()], axis=1)


CONST_AT, CONSTANTS = shape_constants()
CONST_KEEP = CONST_AT["hidden"][0]
CONST_MASK = CONST_AT["strict_t"][0]
CONST_ALIBI = CONST_AT["alibi"][0]


def vector_rows():
    tiles = [
        [("c", 8), ("ada_b", 96), ("kv_ada_b", 16)],
        [("norm1_g", 16), ("norm2_g", 16), ("s5_b_glu", 8), ("kv_norm_g", 8), ("kv_a_norm_g", 2),
         ("mla_q_norm_g", 2), ("pre_norm_2", 16), ("post_norm_2", 16), ("mem_norm_2", 16), ("kv_norm_2", 8),
         ("b_subln_2", 1)],
        [("a_shift_mu_2", 19), ("a_w0_2", 6), ("a_a0_2", 6), ("a_k_k_2", 6), ("a_k_a_2", 6), ("a_r_k_2", 6),
         ("a_lnx_w_2", 6), ("a_lnx_b_2", 6),
         ("b_lam_q1_2", 1), ("b_lam_k1_2", 1), ("b_lam_q2_2", 1), ("b_lam_k2_2", 1)],
    ]
    at, counts = {}, []
    for i, rows in enumerate(tiles):
        n = 0
        for name, k in rows:
            at[name] = (i, n, k)
            n += k
        counts.append(n)
    return at, counts


def blocks_kernel(nc, a, constants, out):
    ctx = ExitStack()
    with ctx:
        def sb(name, n):
            return ctx.enter_context(nc.sbuf_tensor(name, [P, n], F32))

        const_sb = sb("const_sb", CONST_KEEP)
        rows = sb("rows", 3 * P)
        vec = sb("vec", 3 * P)
        ada = sb("ada", 7 * 16)
        c_act = sb("c_act", KC)
        gains = sb("gains", 8 * KC)
        xT = sb("xT", KC * T)
        hT = sb("hT", KC * T)
        sq = sb("sq", KC * T)
        stat = sb("stat", 4 * T)
        ring = sb("ring", RING * PANEL)
        aring = sb("aring", ARING * PANEL)
        acc = sb("acc", PANEL)
        arena = sb("arena", ARENA)
        eps_column = sb("eps_column", 1)[:, :]
        psum = ctx.enter_context(nc.psum_tensor("psum", [P, 8, 512], F32))

        sems = {}

        def done(name):
            if name not in sems:
                sems[name] = ctx.enter_context(nc.semaphore(name))
            return sems[name]

        filled = [done(f"bank{b}_filled") for b in range(8)]
        emptied = [done(f"bank{b}_emptied") for b in range(8)]
        panel_landed = [done(f"panel{i}_landed") for i in range(2 * RING)]
        ada_landed = [done(f"ada_panel{i}_landed") for i in range(ARING)]

        turns = {"a": 0, "b": 0}
        use = {}
        made = {}

        class Program:

            def __init__(self, name):
                self.name, self.n, self.last = name + "_step", 0, None

            def step(self):
                self.n += 1
                self.last = (done(self.name), self.n)
                return done(self.name), 1

            def signals(self, name):
                made[name] = made.get(name, 0) + 1
                self.last = (done(name), made[name])
                return done(name), 1

            def empties(self, key):
                b, n = use[key]
                self.last = (emptied[b], n)
                return emptied[b], 1

        def next_bank(key, pool="a"):
            q = turns[pool]
            turns[pool] += 1
            b, n = (0 if pool == "a" else 4) + q % 4, q // 4
            use[key] = (b, n + 1)
            return emptied[b], n

        def fills(key):
            return filled[use[key][0]], 1

        def filled_at(key):
            b, n = use[key]
            return filled[b], n

        def emptied_at(key):
            b, n = use[key]
            return emptied[b], n

        def bank_of(key):
            return psum[:, use[key][0], :]

        def carve(base, n):
            return arena[:, base:base + n]

        def con(name):
            at, n = CONST_AT[name]
            return const_sb[:, at:at + n]

        ident, ones, half = con("ident"), con("ones"), con("half")
        VEC_AT, VEC_N = vector_rows()
        VEC_LOADS = [sum(x[0] == i for x in VEC_AT.values()) for i in range(3)]

        def col(name, j):
            i, r, _ = VEC_AT[name]
            return vec[:, i * P + r + j:i * P + r + j + 1]

        def cols(name, j, k):
            i, r, _ = VEC_AT[name]
            return vec[:, i * P + r + j:i * P + r + j + k]

        def ada_cols(layer, which):
            if layer == "kv":
                return ada[:, 96 + which * 8:96 + which * 8 + 8]
            return ada[:, layer * 48 + which * 8:layer * 48 + which * 8 + 8]

        ADA_ORDER = [0, 1, 2, 3, 6, 4, 5]
        rstd = stat[:, 2 * T:3 * T]
        xT3 = xT[:, :].rearrange("p (k t) -> p k t", t=T)
        hT3 = hT[:, :].rearrange("p (k t) -> p k t", t=T)
        sq3 = sq[:, :].rearrange("p (k t) -> p k t", t=T)

        o = 0
        CA_N = J5 * 9 * P5
        xC_in = ring[0:C5, 0:8 * D].rearrange("c (s d) -> c s d", d=D)
        xC = carve(0, 8 * D)[0:C5, :].rearrange("c (g s q) -> c g s q", s=L5, q=P5)
        ca_re = carve(0, CA_N).rearrange("p (j k q) -> p j k q", k=9, q=P5)
        ca_im = carve(CA_N, CA_N).rearrange("p (j k q) -> p j k q", k=9, q=P5)
        o = 2 * CA_N
        toep = carve(o, G5 * P).rearrange("p (g n) -> p g n", n=P)
        raw = carve(o, 4 * 2048)[0:J5, :].rearrange("j (m r n) -> j m r n", m=4, r=2)
        o += G5 * P
        gC = carve(o, 8 * D)[0:C5, :].rearrange("c (t d) -> c t d", d=D)
        wT = carve(o, BJ * 2 * P).rearrange("p (j i n) -> p j i n", i=2, n=P)
        o += BJ * 2 * P
        aB = carve(o, BJ * 2 * P).rearrange("p (i j n) -> p i j n", i=2, n=P)
        o += BJ * 2 * P
        kern = carve(o, 2 * 2 * BJ * P)[0:P5, :].rearrange("q (i g n) -> q i g n", i=2, n=P)
        lam_rows = carve(o, 3 * P)[0:J5, :].rearrange("j (m n) -> j m n", n=P)
        group_rows = carve(o + 3 * P, 4 * P5)[0:G5, :].rearrange("g (m n) -> g m n", n=P5)
        group_rep = carve(o + 3 * P + 64, 4 * P)[0:G5, :].rearrange("g (m n) -> g m n", n=P)
        o += 4 * BJ * P
        bb = carve(o, 2 * J5 * P5).rearrange("p (i j q) -> p i j q", i=2, q=P5)
        ct = carve(o + 1024, 2 * J5 * P5).rearrange("p (i j q) -> p i j q", i=2, q=P5)
        bt = carve(o + 2048, 2 * J5 * P5).rearrange("p (i j q) -> p i j q", i=2, q=P5)
        tmp_c = carve(o + 2048, 2 * BJ * 9 * P5)
        o += 2048 + 2 * BJ * 9 * P5
        tmp5 = carve(o, 1024)
        pick = tmp5
        o += 1024
        st = carve(o, (C5 + 1) * 64).rearrange("p (c i j) -> p c i j", i=2, j=J5)
        o += (C5 + 1) * 64
        powr = carve(o, 9 * J5).rearrange("p (k j) -> p k j", j=J5)
        powi = carve(o + 9 * J5, 9 * J5).rearrange("p (k j) -> p k j", j=J5)
        prv = carve(o + 18 * J5, 16 * J5).rearrange("p (i j s) -> p i j s", i=2, s=L5)
        o += 34 * J5
        negi = carve(o, 9 * J5).rearrange("p (k j) -> p k j", j=J5)
        o += 9 * J5
        small = stat[:, 0:24 * J5].rearrange("p (m j) -> p m j", j=J5)
        skip = stat[0:P5, 24 * J5:24 * J5 + 8 * P5].rearrange("q (g p) -> q g p", p=P5)
        step4 = rows[:, 0:4 * J5].rearrange("p (e i j) -> p e i j", e=2, i=2)
        part4 = rows[:, 4 * J5:8 * J5].rearrange("p (e i j) -> p e i j", e=2, i=2)
        part2 = rows[:, 8 * J5:10 * J5].rearrange("p (e j) -> p e j", e=2)
        grp = carve(o, 4 * G5).rearrange("p (m g) -> p m g", g=G5)
        gmod = carve(o + 4 * G5, 2 * G5).rearrange("p (m g) -> p m g", g=G5)
        o += 6 * G5
        ss = carve(o, 24)[0:C5, :].rearrange("c (m s) -> c m s", s=L5)
        o += 24
        assert o <= ARENA, o
        U = hT[:, :].rearrange("p (g c) -> p g c", c=C5)
        BU = sq[:, :].rearrange("p (c i j) -> p c i j", i=2, j=J5)
        xN = sq[:, :].rearrange("p (b d) -> p b d", d=D)

        class Carver:
            def __init__(self, base=0):
                self.o = base

            def __call__(self, n):
                self.o += n
                assert self.o <= ARENA, self.o
                return carve(self.o - n, n)

        NGU = FF // P
        NDN = NGU // 2
        hid = carve(ARENA - FF // P * T, FF // P * T).rearrange("p (n t) -> p n t", t=T)
        m1 = Carver(2 * (2 * T + 2 * MW))
        h2 = m1(KC * T).rearrange("p (k t) -> p k t", t=T)
        latent = [m1(2 * T).rearrange("p (k t) -> p k t", t=T) for _ in range(2)]
        latent_tok = [m1(2 * RKV).rearrange("p (b n) -> p b n", n=RKV) for _ in range(2)]
        krope_tok = m1(2 * DR).rearrange("p (b n) -> p b n", n=DR)
        k_tok1, q_tok1 = [m1(2 * H1 * DQK).rearrange("p (b h n) -> p b h n", b=2, n=DQK) for _ in range(2)]
        v1 = m1(2 * D).rearrange("p (b n) -> p b n", n=D)
        HEADS_AT = m1.o
        qh = m1(H1 * T).rearrange("p (h t) -> p h t", t=T)
        kh = m1(H1 * T).rearrange("p (h t) -> p h t", t=T)
        k_sq = kh[:, :, :].rearrange("p h t -> p (h t)")[:, 0:2 * H1 * DN].rearrange("p (b h n) -> p b h n", b=2, n=DN)
        q_sq = qh[:, :, :].rearrange("p h t -> p (h t)")[:, 0:2 * H1 * DQK].rearrange("p (b h n) -> p b h n", b=2, n=DQK)
        o1 = m1(KC * T).rearrange("p (k t) -> p k t", t=T)
        gain_rows = m1(2 * DQK).rearrange("p (m n) -> p m n", n=DQK)
        angle = m1(4 * DR).rearrange("p (m b n) -> p m b n", b=2, n=DR // 2)
        pos_i = m1(2)
        pos_f = m1(2)
        turned = m1(2 * H1 * DR).rearrange("p (m h n) -> p m h n", m=2, n=DR)
        latent_ss = m1(3 * 6).rearrange("p (m n) -> p m n", n=6)
        head_ss = m1(3 * 96).rearrange("p (m b n) -> p m b n", b=2, n=48)
        pslots = m1(SLOTS * T).rearrange("p (i t) -> p i t", t=T)
        tslots = m1(4 * T).rearrange("p (i t) -> p i t", t=T)
        soft = m1(3 * 32).rearrange("p (m u) -> p m u", u=32)

        e2 = Carver()
        mem_nat = aring[:, 0:2 * D].rearrange("p (b d) -> p b d", d=D)
        memT = aring[:, 2 * D:4 * D].rearrange("p (k t) -> p k t", t=T)
        mem_sq = acc[:, :].rearrange("p (k t) -> p k t", t=T)
        memn = [mem_sq, aring[:, 0:2 * D].rearrange("p (k t) -> p k t", t=T)]
        k_mem = [e2(2 * T).rearrange("p (m t) -> p m t", t=T) for _ in range(2)]
        v_mem = [e2(2 * MW).rearrange("p (b n) -> p b n", n=MW) for _ in range(2)]
        gateT = e2(KC * T).rearrange("p (k t) -> p k t", t=T)
        q_mem = e2(2 * T).rearrange("p (m t) -> p m t", t=T)
        pslots2 = e2(SLOTS * T).rearrange("p (i t) -> p i t", t=T)
        tslots2 = aring[:, 2 * NBR * T:2 * NBR * T + 4 * T].rearrange("p (i t) -> p i t", t=T)
        soft2 = e2(5 * 32).rearrange("p (m u) -> p m u", u=32)
        sums2 = e2(64).rearrange("p (m u) -> p m u", u=32)
        columns2 = e2(64)
        r7 = Carver(e2.o)
        lora_in = r7(T)
        w2a2 = r7(BR)
        masks7 = r7(CONST_ALIBI - CONST_MASK)
        NB = NBR * T

        def con7(name):
            at, n = CONST_AT[name]
            return masks7[:, at - CONST_MASK:at - CONST_MASK + n]

        def tokens(x):
            return x.rearrange("p (i t) -> p i t", t=T)

        def units(x):
            return x.rearrange("p (u t) -> p u t", t=CR)

        ar7 = r7(2 * NB).rearrange("p (x i t) -> p x i t", x=2, t=T)
        at7, rt7 = ar7[:, 0], ar7[:, 1]
        k7, a7, v7, cum7, grow7, sig7, kk7, tmp7 = [tokens(r7(NB)) for _ in range(8)]
        lt7, x7, y7 = [units(r7(NB)) for _ in range(3)]
        lrb7, lak7 = [units(aring[:, i * NB:(i + 1) * NB]) for i in range(2)]
        v_tok = units(hT[:, 0:NB])
        k_tok = units(acc[:, 0:NB])
        flat = lambda x: x.rearrange("p i t -> p (i t)")
        b_tok, lt_t7 = units(flat(kk7)), units(flat(sig7))
        lt_m7 = [units(flat(a7)), units(flat(grow7))]
        lrk7 = units(r7(NB))
        grown7 = tokens(y7.rearrange("p u t -> p (u t)"))
        yT7 = tokens(x7.rearrange("p u t -> p (u t)"))
        yc7 = tokens(lt7.rearrange("p u t -> p (u t)"))
        chain = sq[:, 0:4 * NBR * CR].rearrange("p (n i t) -> p n i t", n=4, t=CR)
        state7, rhs7, sa7 = [chain[:, 0], chain[:, 1]], chain[:, 2], chain[:, 3]
        shifted = sq[:, 0:4 * (T + 1)].rearrange("p (s m t) -> p s m t", s=2, t=T + 1)
        y_sq7 = tokens(flat(sig7))
        kk_gain = grow7
        y_rows = sq[:, :].rearrange("p (b d) -> p b d", d=D)
        yP = sq3
        out_sq = [ar7.rearrange("p x i t -> p (x i t)")[:, 0:KC * T].rearrange("p (k t) -> p k t", t=T)]

        f2 = Carver(e2.o)
        alibi = f2(HB * 2 * T).rearrange("p (h b t) -> p h b t", b=2, t=T)
        kT, qT = [tokens(f2(NB)) for _ in range(2)]
        v_sh = f2(2 * BR).rearrange("p (b n) -> p b n", n=BR)
        h_kv = f2(KC * T).rearrange("p (k t) -> p k t", t=T)
        post_gain = f2(D)
        row_sq = f2(D)
        row_ss = f2(2 * 4).rearrange("p (b i) -> p b i", b=2)
        row_rms = f2(3 * 2).rearrange("p (m b) -> p m b", m=3)
        o_sq = tokens(f2(NB))
        mixT = [hT3, f2(KC * T).rearrange("p (k t) -> p k t", t=T)]
        both = f2(SLOTS * 2 * T).rearrange("p (s c t) -> p s c t", c=2, t=T)
        out_rows = f2(2 * D).rearrange("p (b d) -> p b d", d=D)
        A_ORDER = [9, 3, 4, 5, 0, 1, 2, 6, 7, 8, 10, 11, 12, 13, 14]
        SHIFTED = [[c for c in (2 * i, 2 * i + 1) if c < A_SHIFT // P] for i in range(15)]
        B_FIRST = [0, 1, 2, 6]
        PLAN = [("diff", range(0, 4)), ("panel", 3), ("diff", range(4, 8)), ("panel", 4), ("diff", range(8, 12)),
                ("panel", 5), ("diff", range(12, 16)), ("memory", range(0, 4)), ("panel", 7), ("memory", range(4, 12))]
        ND = 2 * HB

        def head(u):
            h = u // 2
            return slice(h % 2 * HD, h % 2 * HD + HD), h // 2, slice(u % 2 * P, u % 2 * P + P)

        def memory(l):
            def query(u):
                r, c, t = head(u)
                return q_mem[r, c, t]

            def key(u):
                r, c, _ = head(u)
                return k_mem[l][r, c, :]

            def dst(u):
                r, c, t = head(u)
                return mixT[l][r, NBR + c, t]
            return Attention(
                f"memory{l}", 2 * MW // HD, query, key, lambda u: T,
                lambda u, kb: v_mem[l][:, kb, u // 2 * HD:u // 2 * HD + HD], dst, lambda u: (u // 2 % 2 * HD, HD),
                (pslots2, tslots2, soft2))

        UPDATES = [None, ("dn", 0), ("wo1",), ("dn", 1)]

        class Attention:

            def __init__(self, name, n, query, key, keys, value, dst, width, buffers):
                self.pslots, self.tslots, self.soft = buffers
                self.name, self.n, self.query, self.key, self.keys = name, n, query, key, keys
                self.value, self.dst, self.width = value, dst, width

        mla = Attention(
            "mla", 2 * H1,
            lambda u: qh[0:DQK + 2, u // 2, (u % 2) * P:(u % 2 + 1) * P],
            lambda u: kh[0:DQK + 2, u // 2, 0:P * (u % 2 + 1)],
            lambda u: P * (u % 2 + 1),
            lambda u, kb: v1[:, kb, (u // 2) * DV:(u // 2 + 1) * DV],
            lambda u: o1[(u // 2 % 2) * DV:(u // 2 % 2 + 1) * DV, u // 4, (u % 2) * P:(u % 2 + 1) * P],
            lambda u: ((u // 2 % 2) * DV, DV), (pslots, tslots, soft))

        taken = [0]
        weights = []

        def in_columns(name, w, n_cols, order=None):
            rows_ = w.rearrange("(k p) n -> p k n", p=P)
            for i in order or range((n_cols + 255) // 256):
                m = min(256, n_cols - 256 * i)
                weights.append((rows_[:, :, 256 * i:256 * i + m], (rows_.shape[1], m), (*name, i)))

        def swiglu_weights(l):
            wg, wu = [a[x][l].rearrange("(k p) n -> p k n", p=P) for x in ("ffn_w_gate", "ffn_w_up")]
            wd = a["ffn_w_down"][l].rearrange("(j k p) n -> j p k n", k=2, p=P)
            for j in range(NDN + 1):
                if j < NDN:
                    for w in (wg, wu):
                        weights.append((w[:, :, j * 256:(j + 1) * 256], (KC, 256), ("gu", l, 2 * j + 1)))
                if j:
                    weights.append((wd[j - 1], (2, D), ("down", l, j - 1) if j < NDN else ("dn", l, 3)))

        in_columns(("glu",), a["s5_w_glu"][0], D)
        swiglu_weights(0)
        w_kva = a["w_kv_a"].rearrange("(k p) n -> p k n", p=P)
        weights.append((w_kva[:, :, 0:RKV], (KC, RKV), ("kva", 1)))
        weights.append((w_kva[:, :, RKV:], (KC, DR), ("kva", 1)))
        weights.append((a["mla_w_dq"][0].rearrange("(k p) n -> p k n", p=P), (KC, RQ), ("cqt", 1)))

        def memory_weights(l):
            in_columns(("k_mem", l), a["w_mem_kv_2"][l][:, 0:MW], MW)
            in_columns(("v_mem", l), a["w_mem_kv_2"][l][:, MW:], MW)

        memory_weights(0)
        for i in range(2):
            weights.append((a["w_kv_b"].rearrange("(k p) n -> p k n", p=P)[:, :, i * D:(i + 1) * D], (2, D),
                            ("kv", i, 1, 1)))
        for i in range(2):
            weights.append((a["mla_w_uq"][0].rearrange("(k p) n -> p k n", p=P)[:, :, i * 8 * DQK:(i + 1) * 8 * DQK],
                            (2, 8 * DQK), ("q1", i, 1, 1)))
        memory_weights(1)
        in_columns(("wo1",), a["mla_w_o"][0], D)
        swiglu_weights(1)
        in_columns(("a_in",), a["a_w_in_2"][0], A_IN, A_ORDER)
        in_columns(("out", 0), a["w_out_2"][0], D)
        in_columns(("k_sh",), a["w_kv_2"][:, 0:BR], BR)
        in_columns(("v_sh",), a["w_kv_2"][:, BR:], BR)
        in_columns(("b_in",), a["b_w_in_2"][0], B_IN, B_FIRST + [x for what, x in PLAN if what == "panel"])
        in_columns(("out", 1), a["w_out_2"][1], D)

        places = [ring[:, i * PANEL:(i + 1) * PANEL] for i in range(RING)]
        places += [carve(HEADS_AT + i * PANEL, PANEL) for i in range(RING)]
        order = list(range(2 * RING))
        uses = [[] for _ in places]
        place, turn, before = [], [], []
        for i, (_, _, key) in enumerate(weights):
            wide = key[0] in ("gu", "down", "dn")
            p = next(p for p in order if wide or p < RING)
            order.remove(p)
            order.append(p)
            place.append(p)
            turn.append(len(uses[p]) + 1)
            before.append(uses[p][-1] if uses[p] else None)
            uses[p].append(i)

        def slot(i):
            shape = weights[i][1]
            return places[place[i]][:, 0:shape[0] * shape[1]].rearrange("p (k n) -> p k n", n=shape[1])

        block = ctx.enter_context(nc.Block())

        @block.tensor
        def _(eng):
            pe = Program("tensor")

            def mm(dst, w, x, first=True, last=True):
                return eng.matmul(dst, w, x, start=first, stop=last)

            def panel():
                i = taken[0]
                taken[0] += 1
                return slot(i), (panel_landed[place[i]], 16 * turn[i])

            def vector_columns(i):
                eng.wait_ge(done(f"vectors{i}_landed"), 16 * VEC_LOADS[i])
                eng.wait_ge(*next_bank(("vec", i)))
                eng.transpose(bank_of(("vec", i))[:, 0:VEC_N[i]], rows[0:VEC_N[i], i * P:(i + 1) * P],
                              ident[0:VEC_N[i], 0:VEC_N[i]]).then_inc(*fills(("vec", i)))

            eng.wait_ge(done("const_landed"), 16)
            vector_columns(0)

            eng.wait_ge(done("poles_landed"), 16 * 3)
            eng.wait_ge(*next_bank("lam"))
            ps = bank_of("lam").rearrange("p (m j) -> p m j", j=J5)
            for m in range(2):
                mm(ps[:, m, :], lam_rows[:, m, :], ident[0:J5, 0:J5])
            for r in range(2):
                last = mm(ps[r * N5:(r + 1) * N5, 2, :], lam_rows[:, 2, r:r + 1].to_broadcast([J5, N5]),
                          ident[0:J5, 0:J5])
            last.then_inc(*fills("lam"))
            eng.wait_ge(done("group_rows_ready"), 1)
            eng.wait_ge(*next_bank("grp"))
            ps = bank_of("grp").rearrange("p (m g) -> p m g", g=G5)
            for m in range(4):
                last = mm(ps[:, m, :], group_rep[:, m, :], ident[0:G5, 0:G5])
            last.then_inc(*fills("grp"))
            eng.wait_ge(done("s5_landed"), 16 * 4)
            for m in range(4):
                eng.wait_ge(*next_bank(("raw", m), "b"))
                ps = bank_of(("raw", m)).rearrange("p (q j) -> p q j", j=J5)
                for q in range(P5):
                    if m < 2:
                        src = raw[:, m, :, :].rearrange("j r (n q) -> j (r n) q", q=P5)[:, :, q]
                        last = eng.transpose(ps[:, q, :], src, ident[0:J5, 0:J5])
                    else:
                        for r in range(2):
                            last = mm(ps[r * N5:(r + 1) * N5, q, :], raw[:, m, r, q * N5:(q + 1) * N5],
                                      ident[0:J5, 0:J5])
                last.then_inc(*fills(("raw", m)))

            eng.wait_ge(done("xc_scaled"), 8)
            for i in range(4):
                eng.wait_ge(*next_bank(("U", i)))
                ps = bank_of(("U", i)).rearrange("p (g c) -> p g c", c=C5)
                for g in range(16):
                    gg = 16 * i + g
                    last = eng.transpose(ps[:, g, :], xC[:, gg, :, :].rearrange("c s q -> c (s q)"), ident[0:C5, 0:C5])
                last.then_inc(*fills(("U", i)))

            eng.wait_ge(done("x_landed"), 16)
            for i in range(4):
                eng.wait_ge(*next_bank(("xT", i)))
                ps = bank_of(("xT", i)).rearrange("p (k b t) -> p k b t", k=2, b=2)
                for k in range(2):
                    for b in range(2):
                        last = eng.transpose(ps[:, k, b, :], xN[:, b, (2 * i + k) * P:(2 * i + k + 1) * P], ident)
                last.then_inc(*fills(("xT", i)))
            vector_columns(1)
            vector_columns(2)

            def ada_columns(blk):
                eng.wait_ge(done("ada_used"), 8 * (blk + 1))
                eng.wait_ge(*next_bank(("ada", blk), "b" if blk < 3 else "a"))
                ps = bank_of(("ada", blk))
                for j in range(16):
                    last = mm(ps[:, j:j + 1], acc[:, j * P:(j + 1) * P], ones[:, 0:1])
                last.then_inc(*fills(("ada", blk)))

            eng.wait_ge(done("ada_used"), 8)
            for i in range(4):
                eng.wait_ge(*next_bank(("ada0", i), "b"))
                ps = bank_of(("ada0", i))
                mm(ps, ones, acc[:, i * 512:(i + 1) * 512]).then_inc(*fills(("ada0", i)))

            for b in range(NB5):
                eng.wait_ge(done("ab_ready"), 2 * (b + 1))
                for i in range(2):
                    eng.wait_ge(*next_bank(("w", b, i)))
                    ps = bank_of(("w", b, i)).rearrange("p (j n) -> p j n", n=P)
                    for j in range(BJ):
                        last = eng.transpose(ps[:, j, :], aB[:, i, j, :], ident)
                    last.then_inc(*fills(("w", b, i)))
                eng.wait_ge(done("ca_ready"), 2 * (b + 1))
                for i in range(2):
                    eng.wait_ge(*next_bank(("kern", b, i), "b"))
                for g in range(4):
                    j = BJ * b + g
                    for m, c in ((0, ca_re), (1, ca_im)):
                        for i in range(2):
                            n5 = slice(i * N5, (i + 1) * N5)
                            ps = bank_of(("kern", b, i)).rearrange("p (g n) -> p g n", n=P)
                            last = mm(ps[64 * i:64 * i + P5, g, :], bb[n5, m, j, :], c[n5, j, 0:L5, :], m == 0, m == 1)
                            if g == 3 and m == 1:
                                last.then_inc(*fills(("kern", b, i)))
                eng.wait_ge(*emptied_at(("w", b, 0)))
                eng.wait_ge(*emptied_at(("w", b, 1)))
                if b == 0:
                    eng.wait_ge(done("u_ready"), 1)
                eng.wait_ge(*next_bank(("bu", b)))
                ps = bank_of(("bu", b)).rearrange("p (j i c) -> p j i c", j=BJ, i=2)[:, :, :, 0:C5]
                for j in range(BJ):
                    for i in range(2):
                        for r in range(2):
                            last = mm(ps[r * N5:(r + 1) * N5, j, i, :], wT[:, j, i, r * N5:(r + 1) * N5],
                                      U[:, 2 * (BJ * b + j) + r, :])
                last.then_inc(*fills(("bu", b)))
            ada_columns(1)

            for i in range(2):
                eng.wait_ge(done(f"toeplitz{i}_landed"), 16 * L5 * NB5 // 2)

            def y5_bank(q, r):
                return bank_of(("y5", 2 * q + r))[64 * r:64 * r + C5, :].rearrange("c (m n) -> c m n", n=P)

            def own_inputs(q):
                for r in range(2):
                    eng.wait_ge(*next_bank(("y5", 2 * q + r), "ab"[r]))
                    for m in range(4):
                        j = 4 * q + m
                        eng.matmul(y5_bank(q, r)[:, m, :], U[:, 2 * j + r, :], toep[:, 2 * j + r, :], start=m == 0,
                                   stop=False, skip_group_check=True)

            for q in range(4):
                own_inputs(q)
            eng.wait_ge(done("states_ready"), 1)
            for q in range(8):
                if q >= 4:
                    own_inputs(q)
                for m in range(4):
                    j = 4 * q + m
                    for i, c in enumerate((ca_re, ca_im)):
                        for r in range(2):
                            n5 = slice(r * N5, (r + 1) * N5)
                            last = eng.matmul(y5_bank(q, r)[:, m, :], st[n5, 0:C5, i, j], c[n5, j, 1:9, :], start=False,
                                              stop=i == 1, skip_group_check=True)
                            if m == 3 and i == 1:
                                last.then_inc(*fills(("y5", 2 * q + r)))
            ada_columns(2)
            for i in range(4):
                eng.wait_ge(*emptied_at(("y5", 4 * i + 3)))
                eng.wait_ge(*next_bank(("gt", i)))
                ps = bank_of(("gt", i)).rearrange("p (k t c) -> p k t c", k=2, t=L5)
                for k in range(2):
                    for t in range(L5):
                        last = eng.transpose(ps[:, k, t, :], gC[:, t, (2 * i + k) * P:(2 * i + k + 1) * P],
                                             ident[0:C5, 0:C5])
                last.then_inc(*fills(("gt", i)))

            for i in range(4):
                eng.wait_ge(*emptied_at(("gt", i)))
            for i in range(4):
                w, landed = panel()
                eng.wait_ge(*landed)
                eng.wait_ge(*next_bank(("glu", i)))
                ps = bank_of(("glu", i)).rearrange("p (m t) -> p m t", t=T)
                for m in range(2):
                    for k in range(KC):
                        last = mm(ps[:, m, :], w[:, k, m * P:(m + 1) * P], hT3[:, k, :], k == 0, k == KC - 1)
                last.then_inc(*fills(("glu", i)))

            def mean_square(key, chunks, src, sig, count, pool="a"):
                eng.wait_ge(*next_bank(key, pool))
                ps = bank_of(key)
                for k in range(chunks):
                    eng.wait_ge(done(sig), count(k))
                    last = mm(ps[:, 0:T], ones, src[:, k, :], k == 0, k == chunks - 1)
                last.then_inc(*fills(key))

            def project(name, x, n_cols, chunks=KC, ready=None, pool="a", order=None):
                order = order or range((n_cols + 255) // 256)
                for i in order:
                    m = min(256, n_cols - 256 * i)
                    w, landed = panel()
                    eng.wait_ge(*landed)
                    key = (*name, i) if isinstance(name, tuple) else (name, i)
                    eng.wait_ge(*next_bank(key, pool))
                    ps = bank_of(key).rearrange("p (m t) -> p m t", t=T)
                    for j in range(m // P):
                        for k in range(chunks):
                            if ready and i == order[0] and j == 0:
                                eng.wait_ge(done(ready[0]), ready[1] + k + 1)
                            last = mm(ps[:, j, :], w[:, k, j * P:(j + 1) * P], x[:, k, :], k == 0, k == chunks - 1)
                    last.then_inc(*fills(key))

            def swiglu(l, h_base, extra):
                for i in range(4):
                    eng.wait_ge(*next_bank(("dn", l, i), "b"))
                dn = [bank_of(("dn", l, i)).rearrange("p (m t) -> p m t", t=T) for i in range(4)]

                def down(j):
                    w, landed = panel()
                    eng.wait_ge(*landed)
                    for kk in range(2):
                        eng.wait_ge(*emptied_at(("gu", l, 2 * j + kk)))
                        for c in range(KC):
                            last = eng.matmul(dn[c // 2][:, c % 2, :], w[:, kk, c * P:(c + 1) * P],
                                              hid[:, 2 * j + kk, :], start=(j == 0 and kk == 0 and c % 2 == 0),
                                              stop=(j == NDN - 1 and kk == 1), skip_group_check=True)
                            if j == NDN - 1 and kk == 1 and c % 2:
                                last.then_inc(*fills(("dn", l, c // 2)))
                    if j < NDN - 1:
                        last.then_inc(*pe.signals("down_used"))

                for j in range(NDN):
                    g, landed = panel()
                    eng.wait_ge(*landed)
                    u, landed = panel()
                    eng.wait_ge(*landed)
                    for m in range(2):
                        c = 2 * j + m
                        eng.wait_ge(*next_bank(("gu", l, c)))
                        ps = bank_of(("gu", l, c)).rearrange("p (m t) -> p m t", t=T)
                        for i, w in enumerate((g, u)):
                            for k in range(KC):
                                if c == 0 and i == 0:
                                    eng.wait_ge(done("h_ready"), h_base + k + 1)
                                last = mm(ps[:, i, :], w[:, k, m * P:(m + 1) * P], hT3[:, k, :], k == 0, k == KC - 1)
                        last.then_inc(*fills(("gu", l, c)))
                    extra(j)
                    if j:
                        down(j - 1)
                down(NDN - 1)

            def attend(at, steps=None):
                def scores(u):
                    key = ("s", at.name, u)
                    eng.wait_ge(*next_bank(key))
                    ps = bank_of(key)
                    mm(ps[:, 0:at.keys(u)], at.query(u), at.key(u)).then_inc(*fills(key))

                def transposes(u):
                    key = ("pt", at.name, u)
                    eng.wait_ge(done("prob_" + at.name), u + 1)
                    eng.wait_ge(*next_bank(key, "b"))
                    ps = bank_of(key).rearrange("p (b q) -> p b q", q=P)
                    for kb in range(at.keys(u) // P):
                        last = eng.transpose(ps[:, kb, :], at.pslots[:, u % SLOTS, kb * P:(kb + 1) * P], ident)
                    last.then_inc(*fills(key))

                def values(u):
                    key = ("o", at.name, u)
                    eng.wait_ge(*emptied_at(("pt", at.name, u)))
                    eng.wait_ge(*next_bank(key, "b"))
                    ps = bank_of(key)
                    r, m = at.width(u)
                    nb = at.keys(u) // P
                    for kb in range(nb):
                        last = mm(ps[r:r + m, 0:P], at.value(u, kb), at.tslots[:, u % 4, kb * P:(kb + 1) * P],
                                  kb == 0, kb == nb - 1)
                    last.then_inc(*fills(key))

                for u in steps or range(at.n + LAG + 1):
                    if u < at.n:
                        scores(u)
                    if LAG <= u < at.n + LAG:
                        transposes(u - LAG)
                    if u > LAG:
                        values(u - LAG - 1)

            ada_columns(3)
            mean_square(("ms", 1), KC, sq3, "squares", lambda k: 4 * 0 + k // 2 + 1)
            swiglu(0, 0, lambda j: ada_columns({3: 4, 7: 5}[j]) if j in (3, 7) else None)
            eng.wait_ge(done("mem_landed"), 16)
            for i in range(4):
                eng.wait_ge(*next_bank(("memT", i)))
                ps = bank_of(("memT", i)).rearrange("p (k b t) -> p k b t", k=2, b=2)
                for k in range(2):
                    for b in range(2):
                        last = eng.transpose(ps[:, k, b, :], mem_nat[:, b, (2 * i + k) * P:(2 * i + k + 1) * P], ident)
                last.then_inc(*fills(("memT", i)))

            def memory_kv(l):
                project(("k_mem", l), memn[l], MW, ready=("memn_ready", KC * l))
                w, landed = panel()
                eng.wait_ge(*landed)
                eng.wait_ge(*next_bank(("v_mem", l, 0)))
                ps = bank_of(("v_mem", l, 0)).rearrange("p (b n) -> p b n", n=MW)
                for b in range(2):
                    for k in range(KC):
                        last = mm(ps[:, b, :], memn[l][:, k, b * P:(b + 1) * P], w[:, k, :], k == 0, k == KC - 1)
                last.then_inc(*fills(("v_mem", l, 0)))

            mean_square(("ms", 2), KC, sq3, "squares", lambda k: 4 * 1 + k // 2 + 1)
            ada_columns(6)
            for b in range(2):
                eng.wait_ge(*next_bank(("kva", b)))
            w, landed = panel()
            eng.wait_ge(*landed)
            for b in range(2):
                ps = bank_of(("kva", b))
                for k in range(KC):
                    if b == 0:
                        eng.wait_ge(done("h_ready"), KC + k + 1)
                    mm(ps[:, 0:RKV], hT3[:, k, b * P:(b + 1) * P], w[:, k, :], k == 0, k == KC - 1)
            w, landed = panel()
            eng.wait_ge(*landed)
            for b in range(2):
                ps = bank_of(("kva", b))
                for k in range(KC):
                    last = mm(ps[:, RKV:RKV + DR], hT3[:, k, b * P:(b + 1) * P], w[:, k, :], k == 0, k == KC - 1)
                last.then_inc(*fills(("kva", b)))
            w, landed = panel()
            eng.wait_ge(*landed)
            for b in range(2):
                eng.wait_ge(*next_bank(("cqt", b)))
                ps = bank_of(("cqt", b))
                for k in range(KC):
                    if b == 0:
                        eng.wait_ge(done("h_ready"), 2 * KC + k + 1)
                    last = mm(ps[:, 0:RQ], h2[:, k, b * P:(b + 1) * P], w[:, k, :], k == 0, k == KC - 1)
                last.then_inc(*fills(("cqt", b)))
            mean_square("ms_mem", KC, mem_sq, "mem_squares", lambda k: 1, "b")
            for i, (name, src) in enumerate((("ckvT", "kva"), ("cqT", "cqt"))):
                if i == 0:
                    memory_kv(0)
                eng.wait_ge(*next_bank(name, "b"))
                ps = bank_of(name).rearrange("p (k b t) -> p k b t", k=2, b=2)
                for b in range(2):
                    eng.wait_ge(*emptied_at((src, b)))
                    for k in range(2):
                        last = eng.transpose(ps[:, k, b, :], latent_tok[i][:, b, k * P:(k + 1) * P], ident)
                last.then_inc(*fills(name))
            eng.wait_ge(*emptied_at("ckvT"))
            for name, x, width, pool in (("kv", latent[0], 4 * P, "a"), ("q1", latent[1], 4 * DQK, "b")):
                if name == "q1":
                    eng.wait_ge(*emptied_at("cqT"))
                for hh in range(2):
                    w, landed = panel()
                    eng.wait_ge(*landed)
                    for b in range(2):
                        for n in range(2):
                            key = (name, hh, b, n)
                            eng.wait_ge(*next_bank(key, pool))
                            ps = bank_of(key)
                            for k in range(2):
                                last = mm(ps[:, 0:width], x[:, k, b * P:(b + 1) * P], w[:, k, n * width:(n + 1) * width],
                                          k == 0, k == 1)
                            last.then_inc(*fills(key))
            memory_kv(1)
            for name, x, pool in (("kT1", k_tok1, "a"), ("qT1", q_tok1, "b")):
                for b in range(2):
                    eng.wait_ge(done(name + "_ready"), b + 1)
                    for g in range(H1 // 4):
                        key = (name, b, g)
                        eng.wait_ge(*next_bank(key, pool))
                        ps = bank_of(key).rearrange("p (h t) -> p h t", t=P)
                        for h in range(4):
                            last = eng.transpose(ps[0:DQK, h, :], x[:, b, 4 * g + h, :], ident)
                        last.then_inc(*fills(key))
            for name in ("kT1", "qT1"):
                for g in range(H1 // 4):
                    eng.wait_ge(*emptied_at((name, 1, g)))
            eng.wait_ge(done("hidden_landed"), 32)
            attend(mla)
            eng.wait_ge(*emptied_at(("o", "mla", mla.n - 1)))
            project("wo1", o1, D)
            mean_square(("ms", 3), KC, sq3, "squares", lambda k: 4 * 2 + k // 2 + 1)
            swiglu(1, 3 * KC, lambda j: None)
            mean_square(("ms", 4), KC, sq3, "squares", lambda k: 4 * 3 + k // 2 + 1)
            project("a_in", hT3, A_IN, ready=("h_scaled", 4 * KC), order=A_ORDER[0:4])
            eng.wait_ge(done("w2_landed"), 32)
            eng.wait_ge(done("tanh_ready"), 1)
            for i in range(NBR // 2):
                for r, key in ((0, "decay"), (64, "rate")):
                    eng.wait_ge(*next_bank((key, i), "b"))
                    ps = bank_of((key, i)).rearrange("p (m t) -> p m t", t=T)
                    for m in range(2):
                        c = 2 * i + m
                        last = mm(ps[:, m, :], w2a2[r:r + 64, c * P:(c + 1) * P], lora_in[r:r + 64, :])
                    last.then_inc(*fills((key, i)))
            project("a_in", hT3, A_IN, order=A_ORDER[4:7])
            for i in range(NBR // 2):
                eng.wait_ge(done("kk_squares"), 2 * i + 2)
                eng.wait_ge(*next_bank(("kks", i), "b"))
                ps = bank_of(("kks", i))
                mm(ps, half, flat(tmp7[:, 2 * i:2 * i + 2, :])).then_inc(*fills(("kks", i)))
            project("a_in", hT3, A_IN, order=A_ORDER[7:])

            def chunk(x, u, r):
                return x[r:r + HD, u // NCR, u % NCR * CR:(u % NCR + 1) * CR]

            eng.wait_ge(done("scaled7"), 3)
            for g in range(NU // 8):
                eng.wait_ge(*next_bank(("l", g)))
                ps = bank_of(("l", g)).rearrange("p (u t) -> p u t", t=CR)
                for uu in range(8):
                    for r in (0, HD):
                        u = 8 * g + uu
                        last = mm(ps[r:r + CR, uu, :], chunk(at7, u, r), chunk(a7, u, r))
                last.then_inc(*fills(("l", g)))
                for h in range(2):
                    for key, x in (("lb", a7), ("lk", k7)):
                        eng.wait_ge(*next_bank((key, g, h), "b"))
                        ps = bank_of((key, g, h)).rearrange("p (u x t) -> p u x t", x=2, t=CR)
                        for uu in range(4):
                            for r in (0, HD):
                                u = 8 * g + 4 * h + uu
                                last = mm(ps[r:r + CR, uu, :, :], chunk(x, u, r),
                                          ar7[r:r + HD, :, u // NCR, u % NCR * CR:(u % NCR + 1) * CR])
                        last.then_inc(*fills((key, g, h)))
            for key, x in (("b_tok", a7), ("k_tok", k7), ("v_tok", v7)):
                for g in range(NU // 8):
                    eng.wait_ge(*next_bank((key, g)))
                    ps = bank_of((key, g)).rearrange("p (u t) -> p u t", t=CR)
                    for uu in range(8):
                        for r in (0, HD):
                            last = mm(ps[r:r + CR, uu, :], chunk(x, 8 * g + uu, r), ident[r:r + HD, r:r + HD])
                    last.then_inc(*fills((key, g)))
            for l in range(1, 6):
                for g in range(NU // 8):
                    if l == 1:
                        eng.wait_ge(done("level_mask"), g + 1)
                    else:
                        eng.wait_ge(done("level_mask_ahead"), l - 1)
                    if l == 1:
                        eng.wait_ge(done("inverse_ready"), 2 * g + 2)
                    else:
                        eng.wait_ge(*emptied_at(("lx", l - 1, g)))
                        eng.wait_ge(*emptied_at(("ly", l - 1, g)))
                    eng.wait_ge(*next_bank(("lt", l, g)))
                    ps = bank_of(("lt", l, g)).rearrange("p (u t) -> p u t", t=CR)
                    for uu in range(8):
                        for r in (0, HD):
                            u, rr = 8 * g + uu, slice(r, r + CR)
                            last = mm(ps[rr, uu, :], lt_m7[l % 2][rr, u, :], x7[rr, u, :])
                    last.then_inc(*fills(("lt", l, g)))
                for g in range(NU // 8):
                    eng.wait_ge(*emptied_at(("lt", l, g)))
                    for key, w, x in (("lx", y7, lt_t7), ("ly", lt_t7, y7)):
                        if key == "lx" and l == 5:
                            continue
                        eng.wait_ge(*next_bank((key, l, g), "b"))
                        ps = bank_of((key, l, g)).rearrange("p (u t) -> p u t", t=CR)
                        for uu in range(8):
                            for r in (0, HD):
                                u, rr = 8 * g + uu, slice(r, r + CR)
                                last = mm(ps[rr, uu, :], w[rr, u, :], x[rr, u, :])
                        last.then_inc(*fills((key, l, g)))
            for i in range(3):
                eng.wait_ge(*next_bank(("bonus", i), "b"))
                ps = bank_of(("bonus", i))
                mm(ps, half, flat(tmp7[:, 2 * i:2 * i + 2, :])).then_inc(*fills(("bonus", i)))
            for g in range(3):
                eng.wait_ge(*emptied_at(("ly", 5, g)))
                eng.wait_ge(*emptied_at(("b_tok", g)))
                eng.wait_ge(*emptied_at(("k_tok", g)))
                eng.wait_ge(*emptied_at(("v_tok", g)))
            for c in range(NCR):
                S = state7[c % 2]
                if c == 1:
                    eng.wait_ge(*emptied_at(("state", 0)))
                elif c:
                    eng.wait_ge(done("state_ready"), c - 1)
                eng.wait_ge(*next_bank(("rhs", c)))
                ps = bank_of(("rhs", c)).rearrange("p (i t) -> p i t", t=CR)[:, 0:NBR, :]
                for i in range(NBR):
                    for r in (0, HD):
                        u, rr = NCR * i + c, slice(r, r + CR)
                        if c:
                            mm(ps[rr, i, :], chunk(at7, u, r), S[rr, i, :], True, False)
                        last = mm(ps[rr, i, :], lak7[rr, u, :], v_tok[rr, u, :], c == 0, True)
                last.then_inc(*fills(("rhs", c)))
                attend(memory(0), [3 * c])
                eng.wait_ge(*emptied_at(("rhs", c)))
                eng.wait_ge(*next_bank(("sa", c), "b"))
                ps = bank_of(("sa", c)).rearrange("p (i t) -> p i t", t=CR)[:, 0:NBR, :]
                for i in range(NBR):
                    for r in (0, HD):
                        u, rr = NCR * i + c, slice(r, r + CR)
                        last = mm(ps[rr, i, :], y7[rr, u, :], rhs7[rr, i, :])
                last.then_inc(*fills(("sa", c)))
                attend(memory(0), [3 * c + 1])
                eng.wait_ge(*emptied_at(("sa", c)))
                if c < NCR - 1:
                    eng.wait_ge(*next_bank(("state", c)))
                    ps = bank_of(("state", c)).rearrange("p (i t) -> p i t", t=CR)[:, 0:NBR, :]
                    for i in range(NBR):
                        for r in (0, HD):
                            u, rr = NCR * i + c, slice(r, r + CR)
                            mm(ps[rr, i, :], b_tok[rr, u, :], sa7[rr, i, :], True, False)
                            last = mm(ps[rr, i, :], k_tok[rr, u, :], v_tok[rr, u, :], False, True)
                    last.then_inc(*fills(("state", c)))
                eng.wait_ge(*next_bank(("y7", c), "b"))
                ps = bank_of(("y7", c)).rearrange("p (i t) -> p i t", t=CR)[:, 0:NBR, :]
                for i in range(NBR):
                    for r in (0, HD):
                        u, rr = NCR * i + c, slice(r, r + CR)
                        if c:
                            mm(ps[rr, i, :], S[rr, i, :], chunk(rt7, u, r), True, False)
                        mm(ps[rr, i, :], sa7[rr, i, :], lrb7[rr, u, :], c == 0, False)
                        last = mm(ps[rr, i, :], v_tok[rr, u, :], lrk7[rr, u, :], False, True)
                last.then_inc(*fills(("y7", c)))
                attend(memory(0), [3 * c + 2])
            eng.wait_ge(*emptied_at(("y7", NCR - 1)))
            for i in range(3):
                eng.wait_ge(*next_bank(("mean7", i)))
                ps = bank_of(("mean7", i))
                mm(ps, half, flat(yT7[:, 2 * i:2 * i + 2, :])).then_inc(*fills(("mean7", i)))
            eng.wait_ge(*next_bank("var7"))
            ps = bank_of("var7")
            for c in range(NBR):
                eng.wait_ge(done("y7_squares"), c // 2 + 1)
                at = 2 * (NBR - 1 - c)
                last = mm(ps[0:2 * NBR, 0:T], con("pick2")[:, at:at + 2 * NBR], y_sq7[:, c, :], c == 0, c == NBR - 1)
            last.then_inc(*fills("var7"))
            eng.wait_ge(done("y7_rstd"), 1)
            for i in range(3):
                eng.wait_ge(*next_bank(("rstd7", i), "b"))
                ps = bank_of(("rstd7", i)).rearrange("p (m t) -> p m t", t=T)
                for m in range(2):
                    for r in range(2):
                        h = 4 * i + 2 * m + r
                        last = mm(ps[r * HD:(r + 1) * HD, m, :], ident[0:2 * NBR, h:h + 1].to_broadcast([2 * NBR, HD]),
                                  rstd[0:2 * NBR])
                last.then_inc(*fills(("rstd7", i)))

            def output(l):
                project(("out", l), mixT[l], D, ready=("mixed", KC * l))
                mean_square(("ms_out", l), KC, out_sq[l], "out_squares", lambda k: 4 * l + k // 2 + 1)

            output(0)
            mean_square(("ms", 5), KC, sq3, "squares", lambda k: 4 * 4 + k // 2 + 1)
            project("k_sh", h_kv, BR, ready=("h_scaled", 5 * KC))
            for i in range(3):
                w, landed = panel()
                eng.wait_ge(*landed)
                eng.wait_ge(*next_bank(("v_sh", i)))
                ps = bank_of(("v_sh", i)).rearrange("p (b n) -> p b n", n=256)
                for b in range(2):
                    for k in range(KC):
                        last = mm(ps[:, b, :], h_kv[:, k, b * P:(b + 1) * P], w[:, k, :], k == 0, k == KC - 1)
                last.then_inc(*fills(("v_sh", i)))
            project("b_in", hT3, B_IN, ready=("h_scaled", 6 * KC), order=B_FIRST)
            eng.wait_ge(done("lam_products"), 2)
            eng.wait_ge(*next_bank("lam2"))
            ps = bank_of("lam2")
            mm(ps[:, 0:2], ones, columns2[:, 32:34]).then_inc(*fills("lam2"))
            for i in range(3):
                eng.wait_ge(*emptied_at(("v_sh", i)))
                eng.wait_ge(*emptied_at(("b_in", i)))
            def diff_steps(steps):
                for u in steps:
                    if u < ND:
                        h, b = u // 2, u % 2
                        for c in range(2):
                            r = slice(c * HD, (c + 1) * HD)
                            eng.wait_ge(*next_bank(("ds", u, c)))
                            ps = bank_of(("ds", u, c))
                            mm(ps[:, 0:P * (b + 1)], qT[r, h, b * P:(b + 1) * P], kT[r, h, 0:P * (b + 1)])\
                                .then_inc(*fills(("ds", u, c)))
                    if LAG <= u < ND + LAG:
                        w = u - LAG
                        eng.wait_ge(done("prob_diff"), w + 1)
                        eng.wait_ge(*next_bank(("dpt", w), "b"))
                        ps = bank_of(("dpt", w)).rearrange("p (b q) -> p b q", q=P)
                        for kb in range(w % 2 + 1):
                            last = eng.transpose(ps[:, kb, :], both[:, w % SLOTS, 0, kb * P:(kb + 1) * P], ident)
                        last.then_inc(*fills(("dpt", w)))
                    if u > LAG:
                        w = u - LAG - 1
                        eng.wait_ge(*emptied_at(("dpt", w)))
                        eng.wait_ge(*next_bank(("do", w), "b"))
                        ps = bank_of(("do", w))
                        for kb in range(w % 2 + 1):
                            last = mm(ps[:, 0:P], v_sh[:, kb, w // 2 * P:(w // 2 + 1) * P], tslots2[:, w % 4, kb * P:(kb + 1) * P],
                                      kb == 0, kb == w % 2)
                        last.then_inc(*fills(("do", w)))

            for what, x in PLAN:
                if what == "diff":
                    diff_steps(x)
                elif what == "memory":
                    attend(memory(1), x)
                else:
                    project("b_in", hT3, B_IN, order=[x])
            eng.wait_ge(*next_bank("sub"))
            ps = bank_of("sub")
            for h in range(HB):
                eng.wait_ge(done("o_squares"), h // 2 + 1)
                last = mm(ps[0:HB, 0:T], con("pick1")[:, HB - 1 - h:2 * HB - 1 - h], o_sq[:, h, :], h == 0, h == HB - 1)
            last.then_inc(*fills("sub"))
            eng.wait_ge(done("post_added"), KC)
            for i in range(4):
                eng.wait_ge(*next_bank(("rows", i)))
                ps = bank_of(("rows", i)).rearrange("p (k n) -> p k n", n=P)
                for k in range(4):
                    last = eng.transpose(ps[:, k, :], xT3[:, i % 2 * 4 + k, i // 2 * P:(i // 2 + 1) * P], ident)
                last.then_inc(*fills(("rows", i)))
            eng.wait_ge(done("sub_rstd"), 1)
            for i in range(3):
                eng.wait_ge(*next_bank(("rstd_o", i), "b"))
                ps = bank_of(("rstd_o", i)).rearrange("p (m t) -> p m t", t=T)
                for m in range(2):
                    last = mm(ps[:, m, :], ident[0:HB, 2 * i + m:2 * i + m + 1].to_broadcast([HB, P]), rstd[0:HB])
                last.then_inc(*fills(("rstd_o", i)))
            for i in range(4):
                w, landed = panel()
                eng.wait_ge(*landed)
                eng.wait_ge(*next_bank(("out", 1, i)))
                ps = bank_of(("out", 1, i)).rearrange("p (b n) -> p b n", b=2)
                for b in range(2):
                    for k in range(KC):
                        if i == 0 and b == 0:
                            eng.wait_ge(done("mixed"), KC + k + 1)
                        last = mm(ps[:, b, :], mixT[1][:, k, b * P:(b + 1) * P], w[:, k, :], k == 0, k == KC - 1)
                last.then_inc(*fills(("out", 1, i)))

        @block.sync
        def _(sp):
            def vector_source(name):
                x = a[name]
                if name == "a_r_k_2":
                    x = x.rearrange("l h n -> l (h n)")
                if len(x.shape) == 2:
                    x = x.rearrange("l n -> (l n)")
                n = min(P, x.shape[0])
                return x.rearrange("(r p) -> r p", p=n), n

            def load_vectors(tiles):
                for name, (tile, r, n) in VEC_AT.items():
                    if tile in tiles:
                        src, width = vector_source(name)
                        sp.dma_start(rows[r:r + n, tile * P:tile * P + width], src)\
                          .then_inc(done(f"vectors{tile}_landed"), 16)

            sp.wait_ge(done("rows_clear"), 1)
            load_vectors((0,))
            sp.wait_ge(done("vectors0_landed"), 16 * VEC_LOADS[0])
            sp.dma_start(xC_in, a["x"][0].rearrange("(c s) d -> c s d", s=L5)).then_inc(done("xc_landed"), 16)
            groups = [a["norm1_g"][0], a["ada_b"][0, 0:D], a["ada_b"][0, D:2 * D], a["s5_d"][0]]
            for dst, src in ((lam_rows[:, 0, :], a["s5_lam_re"][0].rearrange("(j r) n -> j (r n)", r=2)),
                             (lam_rows[:, 1, :], a["s5_lam_im"][0].rearrange("(j r) n -> j (r n)", r=2)),
                             (lam_rows[:, 2, 0:2], a["s5_log_dt"][0].rearrange("(j r) -> j r", r=2))):
                sp.dma_start(dst, src).then_inc(done("poles_landed"), 16)
            for m, x in enumerate(groups):
                sp.dma_start(group_rows[:, m, :], x.rearrange("(g q) -> g q", q=P5)).then_inc(done("groups_landed"), 16)
            for m, x in enumerate(("s5_b_re", "s5_b_im", "s5_c_re", "s5_c_im")):
                sp.dma_start(raw[:, m, :, :].rearrange("j r n -> j (r n)"),
                             a[x][0].rearrange("(j r) n q -> j (r n q)", r=2)).then_inc(done("s5_landed"), 16)
            sp.dma_start(xN, a["x"][0].rearrange("(b p) d -> p b d", p=P)).then_inc(done("x_landed"), 16)
            load_vectors((1, 2))

            def load(i):
                if before[i] is not None:
                    key = weights[before[i]][2]
                    if key[0] == "down":
                        sp.wait_ge(done("down_used"), (NDN - 1) * key[1] + key[2] + 1)
                    else:
                        sp.wait_ge(*filled_at(key))
                if place[i] >= RING:
                    key = weights[i][2]
                    sp.wait_ge(*filled_at(("gt", 3) if key[1] == 0 else ("s", "mla", mla.n - 1)))
                    if key[1] == 0:
                        sp.wait_ge(done("ada_used"), 4 * KC - 1)
                sp.dma_start(slot(i), weights[i][0]).then_inc(panel_landed[place[i]], 16)

            first = RING
            sp.wait_ge(done("xc_scaled"), 8)
            for i in range(first):
                load(i)
            sp.wait_ge(done("toeplitz_clear"), 1)
            for b in range(NB5):
                sp.wait_ge(done("kern_ready"), b + 1)
                for s in range(L5):
                    sp.dma_start(toep[s * P5:(s + 1) * P5, 8 * b:8 * b + 8, s * P5:P],
                                 kern[:, b % 2, :, 0:P - s * P5]).then_inc(done(f"toeplitz{b % 2}_landed"), 16)
            for i in range(first, len(weights)):
                load(i)
            for i in range(4):
                sp.wait_ge(done("result_ready"), i + 1)
                sp.dma_start(out[0][i // 2 * P:(i // 2 + 1) * P, i % 2 * 512:i % 2 * 512 + 512],
                             out_rows[:, i // 2, i % 2 * 512:i % 2 * 512 + 512]).then_inc(done("out_written"), 16)
            sp.wait_ge(done("out_written"), 16 * 4)

        @block.vector
        def _(eng):
            v = Program("vector")
            V = nc.vector

            def tt(dst, x, y, op):
                return V.tensor_tensor(dst, x, y, op)

            def ts(dst, x, s1, s2, op0, op1=ALU.bypass):
                return V.tensor_scalar(dst, x, s1, s2, op0, op1)

            def stt(dst, x, s, y, op0, op1):
                return V.scalar_tensor_tensor(dst, x, s, y, op0, op1)

            ada_next = [0]

            def ada_panel():
                i = ada_next[0]
                ada_next[0] += 1
                blk, k = i // 8, i % 8
                eng.wait_ge(ada_landed[i % ARING], 16 * (i // ARING + 1))
                w = aring[:, (i % ARING) * PANEL:(i % ARING + 1) * PANEL]
                if i == 0:
                    eng.wait_ge(done("c_act_ready"), 1)
                if k == 0:
                    if blk:
                        eng.wait_ge(*filled_at(("ada", blk - 1) if blk > 1 else ("ada0", 3)))
                    ts(acc[:, :], w, c_act[:, 0:1], None, ALU.mult).then_inc(*v.signals("ada_used"))
                else:
                    eng.wait_ge(done("ada_used"), i)
                    stt(acc[:, :], w, c_act[:, k:k + 1], acc[:, :], ALU.mult, ALU.add).then_inc(*v.signals("ada_used"))

            def ada_bias(blk):
                to = ADA_ORDER[blk]
                eng.wait_ge(*filled_at(("ada", blk)))
                ps = bank_of(("ada", blk))
                name, at = ("ada_b", 16 * to) if to < 6 else ("kv_ada_b", 0)
                tt(ada[:, to * 16:to * 16 + 16], ps[:, 0:16], cols(name, at, 16), ALU.add)\
                    .then_inc(*v.empties(("ada", blk)))

            V.memset(eps_column, EPS).then_inc(*v.step())
            V.memset(rows[:, :], 0.0).then_inc(*v.signals("rows_clear"))
            def vector_columns(i):
                eng.wait_ge(*filled_at(("vec", i)))
                V.tensor_copy(vec[:, i * P:i * P + VEC_N[i]], bank_of(("vec", i))[:, 0:VEC_N[i]])\
                    .then_inc(*v.empties(("vec", i)))

            vector_columns(0)
            ada_panel()
            ada_panel()
            eng.wait_ge(done("xc_squares"), 8)
            ts(ss[:, 1, :], ss[:, 0, :], 1.0 / D, EPS, ALU.mult, ALU.add).then_inc(*v.signals("xc_mean"))
            eng.wait_ge(done("xc_root"), 1)
            V.reciprocal(ss[:, 0, :], ss[:, 2, :]).then_inc(*v.step())
            eng.wait_ge(*v.last)
            for s in range(L5):
                ts(xC[:, :, s, :], xC_in[:, s, :].rearrange("c (g q) -> c g q", q=P5), ss[:, 0, s:s + 1], None, ALU.mult)\
                    .then_inc(*v.signals("xc_scaled"))

            ada_panel()
            eng.wait_ge(done("groups_landed"), 16 * 4)
            for m in range(4):
                V.tensor_copy(group_rep[:, m, :].rearrange("g (s q) -> g s q", q=P5),
                              group_rows[:, m, :].unsqueeze(1).to_broadcast([G5, L5, P5]))\
                    .then_inc(*(v.signals("group_rows_ready") if m == 3 else v.step()))
            eng.wait_ge(*filled_at("lam"))
            ps = bank_of("lam").rearrange("p (m j) -> p m j", j=J5)
            V.tensor_copy(small[:, 0:3, :], ps[:, 0:3, :]).then_inc(*v.empties("lam"))
            lr, li, dt = small[:, 0, :], small[:, 1, :], small[:, 3, :]
            eng.wait_ge(*v.last)
            V.tensor_copy(small[:, 4, :], small[:, 2, :]).then_inc(*v.signals("log_dt_ready"))
            ada_panel()
            eng.wait_ge(done("dt_ready"), 1)
            tt(small[:, 5, :], lr, dt, ALU.mult).then_inc(*v.signals("decay_ready"))
            tt(small[:, 6, :], li, dt, ALU.mult).then_inc(*v.step())
            eng.wait_ge(*v.last)
            ts(small[:, 7, :], small[:, 6, :], 1.0 / TWO_PI, ROUND, ALU.mult, ALU.add).then_inc(*v.step())
            eng.wait_ge(*v.last)
            ts(small[:, 8, :], small[:, 7, :], -ROUND, None, ALU.add).then_inc(*v.step())
            for part in (PI2_A, PI2_B, PI2_C):
                eng.wait_ge(*v.last)
                stt(small[:, 6, :], small[:, 8, :], -part, small[:, 6, :], ALU.mult, ALU.add).then_inc(*v.step())
            eng.wait_ge(*v.last)
            ts(small[:, 6, :], small[:, 6, :], math.pi * (1 - 1e-7), -math.pi * (1 - 1e-7), ALU.min, ALU.max)\
                .then_inc(*v.step())
            eng.wait_ge(*v.last)
            ts(small[:, 7, :], small[:, 6, :], math.pi / 2, None, ALU.add).then_inc(*v.step())
            eng.wait_ge(*v.last)
            ts(small[:, 8, :], small[:, 7, :], math.pi, -TWO_PI, ALU.is_gt, ALU.mult).then_inc(*v.step())
            eng.wait_ge(*v.last)
            tt(small[:, 7, :], small[:, 7, :], small[:, 8, :], ALU.add).then_inc(*v.step())
            eng.wait_ge(*v.last)
            ts(small[:, 7, :], small[:, 7, :], math.pi * (1 - 1e-7), -math.pi * (1 - 1e-7), ALU.min, ALU.max)\
                .then_inc(*v.signals("angles_ready"))
            eng.wait_ge(*filled_at("grp"))
            ps = bank_of("grp").rearrange("p (m g) -> p m g", g=G5)
            V.tensor_copy(grp, ps[:, 0:4, :]).then_inc(*v.empties("grp"))
            ada_panel()
            eng.wait_ge(done("poles_ready"), 3)
            tt(powr[:, 1, :], small[:, 9, :], small[:, 11, :], ALU.mult).then_inc(*v.step())
            tt(powi[:, 1, :], small[:, 9, :], small[:, 10, :], ALU.mult).then_inc(*v.step())
            V.memset(powr[:, 0, :], 1.0).then_inc(*v.step())
            V.memset(powi[:, 0, :], 0.0).then_inc(*v.step())
            eng.wait_ge(*v.last)
            tt(small[:, 12, :], lr, lr, ALU.mult).then_inc(*v.step())
            tt(small[:, 13, :], li, li, ALU.mult).then_inc(*v.step())
            ts(small[:, 14, :], powr[:, 1, :], -1.0, None, ALU.add).then_inc(*v.step())
            eng.wait_ge(*v.last)
            tt(small[:, 12, :], small[:, 12, :], small[:, 13, :], ALU.add).then_inc(*v.step())
            eng.wait_ge(*v.last)
            V.reciprocal(small[:, 13, :], small[:, 12, :]).then_inc(*v.step())
            tt(small[:, 15, :], small[:, 14, :], lr, ALU.mult).then_inc(*v.step())
            tt(small[:, 16, :], powi[:, 1, :], li, ALU.mult).then_inc(*v.step())
            tt(small[:, 17, :], powi[:, 1, :], lr, ALU.mult).then_inc(*v.step())
            tt(small[:, 18, :], small[:, 14, :], li, ALU.mult).then_inc(*v.step())
            eng.wait_ge(*v.last)
            tt(small[:, 15, :], small[:, 15, :], small[:, 16, :], ALU.add).then_inc(*v.step())
            tt(small[:, 17, :], small[:, 17, :], small[:, 18, :], ALU.subtract).then_inc(*v.step())
            eng.wait_ge(*v.last)
            tt(small[:, 19, :], small[:, 15, :], small[:, 13, :], ALU.mult).then_inc(*v.step())
            tt(small[:, 20, :], small[:, 17, :], small[:, 13, :], ALU.mult).then_inc(*v.step())
            for m in (1, 2, 4):
                pr = powr[:, m, :].unsqueeze(1).to_broadcast([P, m, J5])
                pi = powi[:, m, :].unsqueeze(1).to_broadcast([P, m, J5])
                xr, xi = powr[:, 1:m + 1, :], powi[:, 1:m + 1, :]
                q = [tmp5[:, n * 128:n * 128 + m * J5].rearrange("p (k j) -> p k j", j=J5) for n in range(4)]
                eng.wait_ge(*v.last)
                tt(q[0], xr, pr, ALU.mult).then_inc(*v.step())
                tt(q[1], xi, pi, ALU.mult).then_inc(*v.step())
                tt(q[2], xr, pi, ALU.mult).then_inc(*v.step())
                tt(q[3], xi, pr, ALU.mult).then_inc(*v.step())
                eng.wait_ge(*v.last)
                tt(powr[:, m + 1:2 * m + 1, :], q[0], q[1], ALU.subtract).then_inc(*v.step())
                tt(powi[:, m + 1:2 * m + 1, :], q[2], q[3], ALU.add).then_inc(*v.step())
            eng.wait_ge(*v.last)
            ts(negi, powi, -1.0, None, ALU.mult).then_inc(*v.signals("powers_ready"))
            for s in range(L5):
                V.tensor_copy(prv[:, 0, :, s], powr[:, L5 - 1 - s, :]).then_inc(*v.step())
                V.tensor_copy(prv[:, 1, :, s], powi[:, L5 - 1 - s, :]).then_inc(*v.step())
            vector_columns(1)
            vector_columns(2)
            V.tensor_copy(step4[:, 0, 0, :], powr[:, L5, :]).then_inc(*v.step())
            ts(step4[:, 0, 1, :], powi[:, L5, :], -1.0, None, ALU.mult).then_inc(*v.step())
            V.tensor_copy(step4[:, 1, 0, :], powi[:, L5, :]).then_inc(*v.step())
            V.tensor_copy(step4[:, 1, 1, :], powr[:, L5, :]).then_inc(*v.step())
            for m in range(4):
                eng.wait_ge(*emptied_at(("raw", m)))
            fr = small[:, 19, :].unsqueeze(2).to_broadcast([P, J5, P5])
            fi = small[:, 20, :].unsqueeze(2).to_broadcast([P, J5, P5])
            q = [tmp5[:, n * 512:(n + 1) * 512].rearrange("p (j q) -> p j q", q=P5) for n in range(2)]
            for i, (f0, f1, op) in enumerate(((fr, fi, ALU.subtract), (fi, fr, ALU.add))):
                eng.wait_ge(*v.last)
                tt(q[0], bt[:, 0, :, :], f0, ALU.mult).then_inc(*v.step())
                tt(q[1], bt[:, 1, :, :], f1, ALU.mult).then_inc(*v.step())
                eng.wait_ge(*v.last)
                tt(bb[:, i, :, :], q[0], q[1], op).then_inc(*v.signals("bb_ready"))
            for k in range(3):
                ada_panel()
            for i in range(4):
                eng.wait_ge(*filled_at(("ada0", i)))
                ps = bank_of(("ada0", i)).rearrange("p (g q) -> p g q", q=P5)
                pk = pick[:, 0:512].rearrange("p (g q) -> p g q", q=P5)
                eng.wait_ge(*v.last)
                tt(pk, ps, con("diag16").unsqueeze(1).to_broadcast([P, 32, P5]), ALU.mult)\
                    .then_inc(*v.empties(("ada0", i)))
                eng.wait_ge(*v.last)
                V.tensor_reduce(gmod[:, i // 2, (i % 2) * 32:(i % 2) * 32 + 32], pk, AX_X, ALU.add).then_inc(*v.step())
            eng.wait_ge(*v.last)
            tt(gmod, gmod, grp[:, 1:3, :], ALU.add).then_inc(*v.step())
            eng.wait_ge(*v.last)
            stt(gmod[:, 1, :], gmod[:, 1, :], 1.0, grp[:, 0, :], ALU.add, ALU.mult).then_inc(*v.step())
            for i in range(4):
                eng.wait_ge(*emptied_at(("U", i)))
            eng.wait_ge(*v.last)
            tt(U, U, gmod[:, 1, :].unsqueeze(2).to_broadcast([P, G5, C5]), ALU.mult).then_inc(*v.step())
            eng.wait_ge(*v.last)
            tt(U, U, gmod[:, 0, :].unsqueeze(2).to_broadcast([P, G5, C5]), ALU.add).then_inc(*v.signals("u_ready"))

            def add_skip(b):
                for i in range(2):
                    eng.wait_ge(*emptied_at(("kern", b, i)))
                x = kern[:, b % 2, :, 0:P5]
                eng.wait_ge(*v.last)
                tt(skip, grp[0:P5, 3, 8 * b:8 * b + 8].unsqueeze(2).to_broadcast([P5, 8, P5]),
                   con("diag16")[0:P5].unsqueeze(1).to_broadcast([P5, 8, P5]), ALU.mult).then_inc(*v.step())
                eng.wait_ge(*v.last)
                tt(x, x, skip, ALU.add).then_inc(*v.signals("kern_ready"))

            for b in range(NB5):
                js = slice(b * BJ, (b + 1) * BJ)
                if b:
                    eng.wait_ge(*filled_at(("w", b - 1, 1)))
                for i, (n0, n1, op) in enumerate(((0, 1, ALU.subtract), (1, 0, ALU.add))):
                    w0 = prv[:, n0, js, :].unsqueeze(3).to_broadcast([P, BJ, L5, P5])
                    w1 = prv[:, n1, js, :].unsqueeze(3).to_broadcast([P, BJ, L5, P5])
                    q = [tmp5[:, n * 512:(n + 1) * 512].rearrange("p (j s q) -> p j s q", s=L5, q=P5)
                         for n in range(2)]
                    eng.wait_ge(*v.last)
                    tt(q[0], w0, bb[:, 0, js, :].unsqueeze(2).to_broadcast([P, BJ, L5, P5]), ALU.mult)\
                        .then_inc(*v.step())
                    tt(q[1], w1, bb[:, 1, js, :].unsqueeze(2).to_broadcast([P, BJ, L5, P5]), ALU.mult)\
                        .then_inc(*v.step())
                    eng.wait_ge(*v.last)
                    tt(aB[:, i, :, :].rearrange("p j (s q) -> p j s q", q=P5), q[0], q[1], op)\
                        .then_inc(*v.signals("ab_ready"))
                ada_panel()
                if b:
                    add_skip(b - 1)
            add_skip(NB5 - 1)

            for b in range(4, NB5):
                eng.wait_ge(*emptied_at(("bu", b)))
            V.memset(st[:, 0, :, :], 0.0).then_inc(*v.step())
            for c in range(C5 - 1):
                eng.wait_ge(*v.last)
                tt(part4, step4, st[:, c, :, :].unsqueeze(1).to_broadcast([P, 2, 2, J5]), ALU.mult).then_inc(*v.step())
                eng.wait_ge(*v.last)
                tt(part2, part4[:, :, 0, :], BU[:, c, :, :], ALU.add).then_inc(*v.step())
                eng.wait_ge(*v.last)
                tt(st[:, c + 1, :, :], part2, part4[:, :, 1, :], ALU.add)\
                    .then_inc(*(v.signals("states_ready") if c == C5 - 2 else v.step()))
            ada_bias(1)
            for k in range(8):
                ada_panel()
            ada_bias(2)
            for k in range(8):
                ada_panel()
            for i in range(4):
                eng.wait_ge(*emptied_at(("glu", i)))
                for m in range(2):
                    k = 2 * i + m
                    tt(sq3[:, k, :], sq3[:, k, :], hT3[:, k, :], ALU.mult).then_inc(*v.step())
                    eng.wait_ge(*v.last)
                    stt(xT3[:, k, :], sq3[:, k, :], ada_cols(0, 2)[:, k:k + 1], xT3[:, k, :], ALU.mult, ALU.add)\
                        .then_inc(*v.signals("x_ready"))

            def inverse_root(key):
                eng.wait_ge(*emptied_at(key))
                V.reciprocal(rstd, stat[:, T:2 * T]).then_inc(*v.step())
                eng.wait_ge(*v.last)

            def scale_chunks(dst, gain, sig, chunks=KC, src=xT3):
                for k in range(chunks):
                    stt(dst[:, k, :], src[:, k, :], gain[:, k:k + 1], rstd, ALU.mult, ALU.mult)\
                        .then_inc(*v.signals(sig))

            def modulation(slot, layer, which, gain):
                g = gains[:, slot * KC:(slot + 1) * KC]
                stt(g, ada_cols(layer, which), 1.0, gain, ALU.add, ALU.mult).then_inc(*v.step())
                eng.wait_ge(*v.last)
                return g

            def swiglu(l, extra):
                for c in range(NGU):
                    eng.wait_ge(*filled_at(("gu", l, c)))
                    ps = bank_of(("gu", l, c))
                    eng.wait_ge(done("silu_ready"), l * NGU + c + 1)
                    tt(hid[:, c, :], hid[:, c, :], ps[:, T:2 * T], ALU.mult).then_inc(*v.empties(("gu", l, c)))
                    extra(c)
                for c in range(KC):
                    eng.wait_ge(*filled_at(("dn", l, c // 2)))
                    ps = bank_of(("dn", l, c // 2)).rearrange("p (m t) -> p m t", t=T)
                    stt(xT3[:, c, :], ps[:, c % 2, :], ada_cols(l, 5)[:, c:c + 1], xT3[:, c, :], ALU.mult, ALU.add)\
                        .then_inc(*(v.empties(("dn", l, c // 2)) if c % 2 else v.step()))

            def attend(at, steps=None):
                for u in steps or range(at.n + LAG + 1):
                    if u < at.n:
                        key = ("s", at.name, u)
                        eng.wait_ge(*filled_at(key))
                        V.tensor_reduce(at.soft[:, 0, u:u + 1], bank_of(key)[:, 0:at.keys(u)], AX_X, ALU.max, negate=True)\
                            .then_inc(*v.signals("max_" + at.name))
                    if 1 <= u <= at.n:
                        w = u - 1
                        eng.wait_ge(*emptied_at(("s", at.name, w)))
                        V.reciprocal(at.soft[:, 2, w:w + 1], at.soft[:, 1, w:w + 1]).then_inc(*v.step())
                        eng.wait_ge(*v.last)
                        x = at.pslots[:, w % SLOTS, 0:at.keys(w)]
                        ts(x, x, at.soft[:, 2, w:w + 1], None, ALU.mult).then_inc(*v.signals("prob_" + at.name))
                    if u > LAG:
                        w = u - LAG - 1
                        eng.wait_ge(*filled_at(("o", at.name, w)))
                        ps = bank_of(("o", at.name, w))
                        r, m = at.width(w)
                        V.tensor_copy(at.dst(w), ps[r:r + m, 0:P]).then_inc(*v.empties(("o", at.name, w)))

            ada_bias(3)
            g = modulation(0, 0, 4, cols("norm2_g", 0, KC))
            inverse_root(("ms", 1))
            scale_chunks(hT3, g, "h_scaled")

            def ada_beside(c):
                for _ in range(2 if c < 2 else 1):
                    ada_panel()
                if c in (7, 15):
                    ada_bias({7: 4, 15: 5}[c])
            swiglu(0, ada_beside)
            eng.wait_ge(*v.last)
            gk = modulation(1, "kv", 1, cols("kv_norm_g", 0, KC))
            gq = modulation(2, 1, 1, cols("norm1_g", KC, KC))
            inverse_root(("ms", 2))
            scale_chunks(hT3, gk, "h_scaled")
            ada_bias(6)
            scale_chunks(h2, gq, "h_scaled")
            eng.wait_ge(done("positions_landed"), 16)
            V.tensor_copy(pos_f, pos_i.bitcast(I32)).then_inc(*v.step())
            eng.wait_ge(*v.last)
            for b in range(2):
                ts(angle[:, 0, b, :], con("inv_freq"), pos_f[:, b:b + 1], None, ALU.mult).then_inc(*v.step())
            ang = [angle[:, i, :, :] for i in range(3)]
            eng.wait_ge(*v.last)
            ts(ang[1], ang[0], 1.0 / TWO_PI, ROUND, ALU.mult, ALU.add).then_inc(*v.step())
            eng.wait_ge(*v.last)
            ts(ang[1], ang[1], -ROUND, None, ALU.add).then_inc(*v.step())
            for part in (PI2_A, PI2_B, PI2_C):
                eng.wait_ge(*v.last)
                stt(ang[0], ang[1], -part, ang[0], ALU.mult, ALU.add).then_inc(*v.step())
            eng.wait_ge(*v.last)
            ts(ang[0], ang[0], math.pi * (1 - 1e-7), -math.pi * (1 - 1e-7), ALU.min, ALU.max).then_inc(*v.step())
            eng.wait_ge(*v.last)
            ts(ang[1], ang[0], math.pi / 2, None, ALU.add).then_inc(*v.step())
            eng.wait_ge(*v.last)
            ts(ang[2], ang[1], math.pi, -TWO_PI, ALU.is_gt, ALU.mult).then_inc(*v.step())
            eng.wait_ge(*v.last)
            tt(ang[1], ang[1], ang[2], ALU.add).then_inc(*v.step())
            eng.wait_ge(*v.last)
            ts(ang[1], ang[1], math.pi * (1 - 1e-7), -math.pi * (1 - 1e-7), ALU.min, ALU.max)\
                .then_inc(*v.signals("rotary_angles"))
            eng.wait_ge(done("latent_squares"), 6)
            for i, n in enumerate((RKV, DR, RQ)):
                x = slice(2 * i, 2 * i + 2)
                ts(latent_ss[:, 1, x], latent_ss[:, 0, x], 1.0 / n, EPS, ALU.mult, ALU.add)\
                    .then_inc(*v.signals("latent_mean"))
            eng.wait_ge(done("latent_root"), 1)
            V.reciprocal(latent_ss[:, 0, :], latent_ss[:, 2, :]).then_inc(*v.signals("latent_rstd"))
            inverse_root("ms_mem")
            for l in range(2):
                scale_chunks(memn[l], cols("mem_norm_2", l * KC, KC), "memn_ready", src=memT)

            def turn(x, n, b, tells=None):
                x4 = x.rearrange("p h (s m) -> p h s m", s=2)
                t = [turned[:, i, 0:n, :].rearrange("p h (s m) -> p h s m", s=2) for i in range(2)]
                for i in range(2):
                    f = angle[:, i, b, :].unsqueeze(1).unsqueeze(1).to_broadcast([P, n, 2, DR // 2])
                    tt(t[i], x4, f, ALU.mult).then_inc(*v.step())
                eng.wait_ge(*v.last)
                tt(x4[:, :, 0, :], t[1][:, :, 0, :], t[0][:, :, 1, :], ALU.subtract).then_inc(*v.step())
                tt(x4[:, :, 1, :], t[1][:, :, 1, :], t[0][:, :, 0, :], ALU.add)\
                    .then_inc(*(v.signals(tells) if tells else v.step()))
                eng.wait_ge(*v.last)

            def over_tokens(x, n):
                return x.unsqueeze(1).to_broadcast([P, n, x.shape[1]])

            eng.wait_ge(done("gain_rows_landed"), 16 * 4)
            eng.wait_ge(done("rotary_ready"), 1)
            eng.wait_ge(*emptied_at(("kva", 1)))
            tt(krope_tok, krope_tok, over_tokens(gain_rows[:, 0, DN:], 2), ALU.mult).then_inc(*v.step())
            eng.wait_ge(*v.last)
            for b in range(2):
                turn(krope_tok[:, b:b + 1, :], 1, b)
                V.tensor_copy(k_tok1[:, b, :, DN:], krope_tok[:, b:b + 1, :].to_broadcast([P, H1, DR]))\
                    .then_inc(*v.step())
            for hh in range(2):
                for b in range(2):
                    hs = slice(8 * hh, 8 * hh + 8)
                    eng.wait_ge(*emptied_at(("kv", hh, b, 1)))
                    V.tensor_reduce(head_ss[:, 0, b, hs], k_sq[:, b, hs, :], AX_X, ALU.add).then_inc(*v.step())
            eng.wait_ge(*v.last)
            ts(head_ss[:, 1, :, 0:H1], head_ss[:, 0, :, 0:H1], 1.0 / DN, EPS, ALU.mult, ALU.add)\
                .then_inc(*v.signals("k1_mean"))
            eng.wait_ge(done("k1_root"), 1)
            V.reciprocal(head_ss[:, 0, :, 0:H1], head_ss[:, 2, :, 0:H1]).then_inc(*v.step())
            for b in range(2):
                x = k_tok1[:, b, :, 0:DN]
                eng.wait_ge(*v.last)
                tt(x, x, head_ss[:, 0, b, 0:H1].unsqueeze(2).to_broadcast([P, H1, DN]), ALU.mult).then_inc(*v.step())
                eng.wait_ge(*v.last)
                tt(x, x, over_tokens(gain_rows[:, 0, 0:DN], H1), ALU.mult).then_inc(*v.signals("kT1_ready"))
            ts(gain_rows[:, 1, :], gain_rows[:, 1, :], SCALE1, None, ALU.mult).then_inc(*v.step())
            for hh in range(2):
                for b in range(2):
                    hs = slice(8 * hh, 8 * hh + 8)
                    eng.wait_ge(*emptied_at(("q1", hh, b, 1)))
                    for at, lo, hi in ((H1, 0, DN), (2 * H1, DN, DQK)):
                        V.tensor_reduce(head_ss[:, 0, b, at + 8 * hh:at + 8 * hh + 8], q_sq[:, b, hs, lo:hi], AX_X, ALU.add)\
                            .then_inc(*v.step())
            eng.wait_ge(*v.last)
            for at, n in ((H1, DN), (2 * H1, DR)):
                ts(head_ss[:, 1, :, at:at + H1], head_ss[:, 0, :, at:at + H1], 1.0 / n, EPS, ALU.mult, ALU.add)\
                    .then_inc(*v.signals("q1_mean"))
            eng.wait_ge(done("q1_root"), 1)
            V.reciprocal(head_ss[:, 0, :, H1:], head_ss[:, 2, :, H1:]).then_inc(*v.step())
            eng.wait_ge(*v.last)
            for b in range(2):
                for at, lo, hi in ((H1, 0, DN), (2 * H1, DN, DQK)):
                    x = q_tok1[:, b, :, lo:hi]
                    tt(x, x, head_ss[:, 0, b, at:at + H1].unsqueeze(2).to_broadcast([P, H1, hi - lo]), ALU.mult)\
                        .then_inc(*v.step())
                eng.wait_ge(*v.last)
                x = q_tok1[:, b, :, :]
                tt(x, x, over_tokens(gain_rows[:, 1, :], H1), ALU.mult).then_inc(*v.step())
                eng.wait_ge(*v.last)
                turn(q_tok1[:, b, :, DN:], H1, b, "qT1_ready")
            for b in range(2):
                for g in range(H1 // 4):
                    key = ("qT1", b, g)
                    eng.wait_ge(*filled_at(key))
                    ps = bank_of(key).rearrange("p (h t) -> p h t", t=P)
                    V.tensor_copy(qh[0:DQK, 4 * g:4 * g + 4, b * P:(b + 1) * P], ps[0:DQK]).then_inc(*v.empties(key))
            attend(mla)
            for c in range(KC):
                eng.wait_ge(*filled_at(("wo1", c // 2)))
                ps = bank_of(("wo1", c // 2)).rearrange("p (m t) -> p m t", t=T)
                stt(xT3[:, c, :], ps[:, c % 2, :], ada_cols(1, 2)[:, c:c + 1], xT3[:, c, :], ALU.mult, ALU.add)\
                    .then_inc(*(v.empties(("wo1", c // 2)) if c % 2 else v.step()))
            g = modulation(0, 1, 4, cols("norm2_g", KC, KC))
            inverse_root(("ms", 3))
            scale_chunks(hT3, g, "h_scaled")
            swiglu(1, lambda c: None)
            eng.wait_ge(*v.last)
            keep = columns2[:, 0:19]
            ts(keep, cols("a_shift_mu_2", 0, 19), -1.0, 1.0, ALU.mult, ALU.add).then_inc(*v.step())
            keep_k = columns2[:, 19:25]
            ts(keep_k, cols("a_k_a_2", 0, 6), -1.0, 1.0, ALU.mult, ALU.add).then_inc(*v.step())
            inverse_root(("ms", 4))
            V.memset(shifted[:, :, :, 0:1], 0.0).then_inc(*v.signals("shift_clear"))
            scale_chunks(hT3, cols("pre_norm_2", 0, KC), "h_scaled")
            shifts = [0]

            def add_shifted(panels):
                for i in panels:
                    key, pos = ("a_in", i), A_ORDER.index(i)
                    eng.wait_ge(*filled_at(key))
                    ps = bank_of(key).rearrange("p (m t) -> p m t", t=T)
                    shifts[0] += len(SHIFTED[i])
                    eng.wait_ge(done("shift_ready"), shifts[0])
                    for c in SHIFTED[i]:
                        dst = (rt7[:, c, :] if c < 6 else k7[:, c - 6, :] if c < 12 else v7[:, c - 12, :] if c < 18
                               else lora_in)
                        stt(dst, ps[:, c % 2, :], keep[:, c:c + 1], shifted[:, pos % 2, c % 2, 0:T], ALU.mult, ALU.add)\
                            .then_inc(*(v.signals("lora_shifted") if c == 18 else v.empties(key) if c % 2 else v.step()))

            add_shifted(A_ORDER[0:4])
            eng.wait_ge(*v.last)
            for c in range(NBR):
                ts(kk7[:, c, :], k7[:, c, :], col("a_k_k_2", c), None, ALU.mult).then_inc(*v.step())
            add_shifted(A_ORDER[4:5])
            eng.wait_ge(done("masks7_landed"), 16)
            for c in range(NBR):
                eng.wait_ge(*emptied_at(("decay", c // 2)))
                V.tensor_tensor_scan(cum7[:, c, :], con7("restart"), sig7[:, c, :], 0.0, ALU.mult, ALU.add)\
                    .then_inc(*v.step())
            eng.wait_ge(*v.last)
            tt(at7, cum7, sig7, ALU.subtract).then_inc(*v.signals("cum_ready"))
            add_shifted(A_ORDER[5:7])
            eng.wait_ge(*emptied_at(("rate", 2)))
            for c in range(NBR):
                ts(grown7[:, c, :], a7[:, c, :], col("a_k_a_2", c), keep_k[:, c:c + 1], ALU.mult, ALU.add)\
                    .then_inc(*v.step())
            for i in range(3):
                key = ("kks", i)
                eng.wait_ge(*filled_at(key))
                ps = bank_of(key)
                ts(flat(tmp7[:, 2 * i:2 * i + 2, :]), ps, 1e-12, None, ALU.max).then_inc(*v.empties(key))
            eng.wait_ge(*v.last)
            tt(k7, k7, grown7, ALU.mult).then_inc(*v.step())
            eng.wait_ge(done("kk_root"), 1)
            V.reciprocal(flat(tmp7), flat(tmp7)).then_inc(*v.step())
            add_shifted(A_ORDER[7:8])
            eng.wait_ge(*v.last)
            tt(kk7, kk7, tmp7, ALU.mult).then_inc(*v.step())
            eng.wait_ge(*v.last)
            tt(a7, a7, kk7, ALU.mult).then_inc(*v.step())
            add_shifted(A_ORDER[8:9])
            for c in range(NBR):
                stt(tmp7[:, c, :], rt7[:, c, :], col("a_r_k_2", c), k7[:, c, :], ALU.mult, ALU.mult)\
                    .then_inc(*v.step())
            add_shifted(A_ORDER[9:10])
            eng.wait_ge(*v.last)
            eng.wait_ge(done("exp7"), 3)
            tt(a7, a7, grow7, ALU.mult).then_inc(*v.signals("scaled7"))
            tt(k7, k7, grow7, ALU.mult).then_inc(*v.step())
            stt(flat(at7), flat(kk7), -1.0, flat(at7), ALU.mult, ALU.mult).then_inc(*v.signals("scaled7"))
            tt(rt7, rt7, cum7, ALU.mult).then_inc(*v.signals("scaled7"))

            def spread(name, n, i=0):
                return con7(name)[:, i * CR:(i + 1) * CR].unsqueeze(1).to_broadcast([P, n, CR])

            for g in range(NU // 8):
                us = slice(8 * g, 8 * g + 8)
                key = ("l", g)
                eng.wait_ge(done("masks7_landed"), 16)
                eng.wait_ge(*filled_at(key))
                ps = bank_of(key).rearrange("p (u t) -> p u t", t=CR)
                tt(x7[:, us, :], ps, spread("level0", 8), ALU.mult).then_inc(*v.empties(key))
                for h in range(2):
                    for key, s_dst, c_dst in (("lb", lt7, lrb7), ("lk", lak7, lrk7)):
                        key = (key, g, h)
                        eng.wait_ge(*filled_at(key))
                        ps = bank_of(key).rearrange("p (u x t) -> p u x t", x=2, t=CR)
                        uh = slice(8 * g + 4 * h, 8 * g + 4 * h + 4)
                        tt(s_dst[:, uh, :], ps[:, :, 0, :], spread("strict_t", 4), ALU.mult).then_inc(*v.step())
                        tt(c_dst[:, uh, :], ps[:, :, 1, :], spread("causal_t", 4), ALU.mult).then_inc(*v.empties(key))
                eng.wait_ge(*v.last)
                tt(y7[:, us, :], lt7[:, us, :], spread("levels_t", 8), ALU.mult).then_inc(*v.step())
                tt(lt_m7[1][:, us, :], lt7[:, us, :], spread("levels_t", 8, 1), ALU.mult).then_inc(*v.signals("level_mask"))
                tt(x7[:, us, :], x7[:, us, :], spread("eye64", 8), ALU.add).then_inc(*v.signals("inverse_ready"))
                eng.wait_ge(*v.last)
                tt(y7[:, us, :], y7[:, us, :], spread("eye64", 8), ALU.add).then_inc(*v.signals("inverse_ready"))
            for l in range(1, 6):
                for g in range(NU // 8):
                    us = slice(8 * g, 8 * g + 8)
                    pair = [(key, x) for key, x in (("lx", x7), ("ly", y7)) if not (key == "lx" and l == 5)]
                    for key, _ in pair:
                        eng.wait_ge(*filled_at((key, l, g)))
                    for key, x in pair:
                        b, _ = use[(key, l, g)]
                        b = psum[:, b, :].rearrange("p (u t) -> p u t", t=CR)
                        tt(x[:, us, :], x[:, us, :], b, ALU.add).then_inc(*v.empties((key, l, g)))
            for i in range(3):
                key, two = ("bonus", i), slice(2 * i, 2 * i + 2)
                eng.wait_ge(*filled_at(key))
                tt(flat(v7[:, two, :]), flat(v7[:, two, :]), bank_of(key), ALU.mult).then_inc(*v.empties(key))
            eng.wait_ge(*v.last)
            for c in range(NBR):
                stt(v7[:, c, :], v7[:, c, :], col("a_lnx_b_2", c), gateT[:, c, :], ALU.add, ALU.mult).then_inc(*v.step())
                ts(kk_gain[:, c, :], gateT[:, c, :], col("a_lnx_w_2", c), None, ALU.mult).then_inc(*v.step())
            for c in range(NCR):
                attend(memory(0), [3 * c])
                attend(memory(0), [3 * c + 1])
                if c < NCR - 1:
                    key = ("state", c)
                    eng.wait_ge(*filled_at(key))
                    ps = bank_of(key).rearrange("p (i t) -> p i t", t=CR)[:, 0:NBR, :]
                    end = cum7[:, :, CR * (c + 1) - 1:CR * (c + 1)].to_broadcast([P, NBR, CR])
                    S, S1 = state7[c % 2], state7[(c + 1) % 2]
                    if c:
                        eng.wait_ge(*filled_at(("y7", c - 1)))
                        tt(S1, ps, S, ALU.add).then_inc(*v.empties(key))
                        eng.wait_ge(*v.last)
                        tt(S1, S1, end, ALU.mult).then_inc(*v.signals("state_ready"))
                    else:
                        tt(S1, ps, end, ALU.mult).then_inc(*v.empties(key))
                attend(memory(0), [3 * c + 2])
            for i in range(3):
                key, two = ("mean7", i), slice(2 * i, 2 * i + 2)
                eng.wait_ge(*filled_at(key))
                ps = bank_of(key)
                stt(flat(yc7[:, two, :]), ps, -1.0 / HD, flat(yT7[:, two, :]), ALU.mult, ALU.add)\
                    .then_inc(*v.empties(key))
            eng.wait_ge(*filled_at("var7"))
            h12 = slice(0, 2 * NBR)
            ts(stat[h12, 0:T], bank_of("var7")[h12, 0:T], 1.0 / HD, LNX_EPS, ALU.mult, ALU.add).then_inc(*v.empties("var7"))
            eng.wait_ge(done("y7_root"), 1)
            V.reciprocal(rstd[h12], stat[h12, T:2 * T]).then_inc(*v.signals("y7_rstd"))
            for i in range(3):
                key, two = ("rstd7", i), slice(2 * i, 2 * i + 2)
                eng.wait_ge(*filled_at(key))
                tt(flat(yc7[:, two, :]), flat(yc7[:, two, :]), bank_of(key), ALU.mult).then_inc(*v.empties(key))
                eng.wait_ge(*v.last)
                tt(yc7[:, two, :], yc7[:, two, :], kk_gain[:, two, :], ALU.mult).then_inc(*v.step())
                for c in (2 * i, 2 * i + 1):
                    eng.wait_ge(*v.last)
                    tt(hT3[:, c, :], yc7[:, c, :], v7[:, c, :], ALU.add).then_inc(*v.signals("mixed"))

            def memory_gate(l):
                at = memory(l)
                eng.wait_ge(*emptied_at(("o", at.name, at.n - 1)))
                for c in range(NBR, KC):
                    tt(mixT[l][:, c, :], mixT[l][:, c, :], gateT[:, c, :], ALU.mult).then_inc(*v.signals("mixed"))

            memory_gate(0)
            inverse_root(("ms_out", 0))
            for c in range(KC + 1):
                if c < KC:
                    stt(yP[:, c, :], yP[:, c, :], cols("post_norm_2", 0, KC)[:, c:c + 1], rstd, ALU.mult, ALU.mult)\
                        .then_inc(*v.signals("post_scaled"))
                if c:
                    eng.wait_ge(done("post_scaled"), c)
                    tt(xT3[:, c - 1, :], xT3[:, c - 1, :], yP[:, c - 1, :], ALU.add).then_inc(*v.signals("post_added"))
            for i in range(2):
                tt(columns2[:, 32 + i:33 + i], col(f"b_lam_q{i + 1}_2", 0), col(f"b_lam_k{i + 1}_2", 0), ALU.mult)\
                    .then_inc(*v.signals("lam_products"))
            subln = columns2[:, 37:38]
            ts(subln, col("b_subln_2", 0), 1.0 - LAM_INIT, None, ALU.mult).then_inc(*v.step())
            inverse_root(("ms", 5))
            scale_chunks(h_kv, cols("kv_norm_2", 0, KC), "h_scaled")
            scale_chunks(hT3, cols("pre_norm_2", KC, KC), "h_scaled")
            minus_lam = columns2[:, 36:37]
            eng.wait_ge(*emptied_at("lam2"))
            stt(minus_lam, columns2[:, 34:35], -1.0, columns2[:, 35:36], ALU.mult, ALU.add).then_inc(*v.step())
            eng.wait_ge(*v.last)
            ts(minus_lam, minus_lam, -LAM_INIT, None, ALU.add).then_inc(*v.step())
            eng.wait_ge(done("alibi_landed"), 16)
            def diff_steps(steps):
                for u in steps:
                    if u < ND:
                        h, b = u // 2, u % 2
                        w = P * (b + 1)
                        if u >= SLOTS:
                            eng.wait_ge(*filled_at(("dpt", u - SLOTS)))
                        for c in range(2):
                            x = both[:, u % SLOTS, c, 0:w]
                            eng.wait_ge(*filled_at(("ds", u, c)))
                            ps = bank_of(("ds", u, c))
                            stt(x, ps[:, 0:w], HD ** -0.5, alibi[:, h, b, 0:w], ALU.mult, ALU.add)\
                                .then_inc(*v.empties(("ds", u, c)))
                        eng.wait_ge(*v.last)
                        V.tensor_reduce(soft2[:, 0:2, u], both[:, u % SLOTS, :, 0:w], AX_X, ALU.max, negate=True)\
                            .then_inc(*v.signals("max_diff"))
                    if 1 <= u <= ND:
                        u -= 1
                        w = P * (u % 2 + 1)
                        eng.wait_ge(done("exp_diff"), 2 * u + 2)
                        V.reciprocal(soft2[:, 2:4, u], sums2[:, 0:2, u]).then_inc(*v.step())
                        eng.wait_ge(*v.last)
                        tt(soft2[:, 3, u:u + 1], soft2[:, 3, u:u + 1], minus_lam, ALU.mult).then_inc(*v.step())
                        x = both[:, u % SLOTS, :, 0:w]
                        ts(x[:, 0], x[:, 0], soft2[:, 2, u:u + 1], None, ALU.mult).then_inc(*v.step())
                        eng.wait_ge(*v.last)
                        stt(x[:, 0], x[:, 1], soft2[:, 3, u:u + 1], x[:, 0], ALU.mult, ALU.add)\
                            .then_inc(*v.signals("prob_diff"))

            for what, x in PLAN:
                if what == "diff":
                    diff_steps(x)
                elif what == "memory":
                    attend(memory(1), x)
            eng.wait_ge(*filled_at("sub"))
            ts(stat[0:HB, 0:T], bank_of("sub")[0:HB, 0:T], 1.0 / P, EPS, ALU.mult, ALU.add).then_inc(*v.empties("sub"))
            eng.wait_ge(done("sub_root"), 1)
            V.reciprocal(rstd[0:HB], stat[0:HB, T:2 * T]).then_inc(*v.signals("sub_rstd"))
            eng.wait_ge(done("gate_ready"), 1)
            for i in range(3):
                key = ("rstd_o", i)
                eng.wait_ge(*filled_at(key))
                for h in (2 * i, 2 * i + 1):
                    stt(mixT[1][:, h, :], mixT[1][:, h, :], subln, bank_of(key)[:, h % 2 * T:(h % 2 + 1) * T],
                        ALU.mult, ALU.mult).then_inc(*(v.empties(key) if h % 2 else v.step()))
                for h in (2 * i, 2 * i + 1):
                    eng.wait_ge(*v.last)
                    tt(mixT[1][:, h, :], mixT[1][:, h, :], gateT[:, h, :], ALU.mult).then_inc(*v.signals("mixed"))
            memory_gate(1)
            eng.wait_ge(done("post_gain_landed"), 16)
            for i in range(4):
                eng.wait_ge(done("row_squares"), 2 * i + 2)
                ps = bank_of(("out", 1, i)).rearrange("p (b n) -> p b n", b=2)
                tt(y_rows[:, :, i * 256:(i + 1) * 256], ps,
                   post_gain[:, i * 256:(i + 1) * 256].unsqueeze(1).to_broadcast([P, 2, 256]), ALU.mult)\
                    .then_inc(*v.empties(("out", 1, i)))
            V.tensor_reduce(row_rms[:, 0, :], row_ss, AX_X, ALU.add).then_inc(*v.signals("row_sums"))
            eng.wait_ge(done("row_root"), 1)
            V.reciprocal(row_rms[:, 2, :], row_rms[:, 1, :]).then_inc(*v.step())
            eng.wait_ge(*v.last)
            eng.wait_ge(*emptied_at(("rows", 3)))
            for i in range(4):
                n = slice(i % 2 * 512, i % 2 * 512 + 512)
                stt(out_rows[:, i // 2, n], y_rows[:, i // 2, n], row_rms[:, 2, i // 2:i // 2 + 1], out_rows[:, i // 2, n],
                    ALU.mult, ALU.add).then_inc(*v.signals("result_ready"))

        @block.scalar
        def _(eng):
            s = Program("scalar")

            def act(dst, x, f, **k):
                return eng.activation(dst, x, f, **k)

            eng.dma_start(const_sb[:, :], constants[:, 0:CONST_KEEP]).then_inc(done("const_landed"), 16)
            eng.wait_ge(*emptied_at(("vec", 0)))
            act(c_act[:, :], cols("c", 0, KC), ACT.Silu).then_inc(*s.signals("c_act_ready"))
            eng.wait_ge(done("xc_landed"), 16)
            for t in range(L5):
                if t:
                    eng.wait_ge(*s.last)
                act(hT[0:C5, 0:D], xC_in[:, t, :], ACT.Square, accum_out=ss[:, 0, t:t + 1])\
                    .then_inc(*s.signals("xc_squares"))
            eng.wait_ge(done("xc_mean"), 1)
            act(ss[:, 2, :], ss[:, 1, :], ACT.Sqrt).then_inc(*s.signals("xc_root"))
            eng.wait_ge(done("log_dt_ready"), 1)
            act(small[:, 3, :], small[:, 4, :], ACT.Exp).then_inc(*s.signals("dt_ready"))
            eng.wait_ge(done("decay_ready"), 1)
            act(small[:, 9, :], small[:, 5, :], ACT.Exp).then_inc(*s.signals("poles_ready"))
            eng.wait_ge(done("angles_ready"), 1)
            act(small[:, 10, :], small[:, 6, :], ACT.Sin).then_inc(*s.signals("poles_ready"))
            act(small[:, 11, :], small[:, 7, :], ACT.Sin).then_inc(*s.signals("poles_ready"))
            for m, dst in enumerate((bt[:, 0], bt[:, 1], ct[:, 0], ct[:, 1])):
                eng.wait_ge(*filled_at(("raw", m)))
                ps = bank_of(("raw", m)).rearrange("p (q j) -> p j q", j=J5)
                act(dst, ps, ACT.Copy).then_inc(*s.empties(("raw", m)))
            for i in range(4):
                eng.wait_ge(*filled_at(("U", i)))
                ps = bank_of(("U", i))
                act(hT[:, i * 512:(i + 1) * 512], ps, ACT.Copy).then_inc(*s.empties(("U", i)))
            for i in range(4):
                eng.wait_ge(*filled_at(("xT", i)))
                ps = bank_of(("xT", i))
                act(xT[:, i * 512:(i + 1) * 512], ps, ACT.Copy).then_inc(*s.empties(("xT", i)))
            for b in range(NB5):
                for i in range(2):
                    eng.wait_ge(*filled_at(("w", b, i)))
                    ps = bank_of(("w", b, i)).rearrange("p (j n) -> p j n", n=P)
                    if b:
                        eng.wait_ge(*filled_at(("bu", b - 1)))
                    act(wT[:, :, i, :], ps, ACT.Copy).then_inc(*s.empties(("w", b, i)))
                for i in range(2):
                    eng.wait_ge(*filled_at(("kern", b, i)))
                    ps = bank_of(("kern", b, i))
                    if b > 1:
                        eng.wait_ge(done(f"toeplitz{b % 2}_landed"), 16 * L5 * (b // 2))
                    act(kern[:, b % 2, i::2, :], ps[64 * i:64 * i + P5].rearrange("p (g n) -> p g n", n=P), ACT.Copy)\
                        .then_inc(*s.empties(("kern", b, i)))
                eng.wait_ge(*filled_at(("bu", b)))
                ps = bank_of(("bu", b)).rearrange("p (j i c) -> p c i j", j=BJ, i=2)[:, 0:C5]
                act(BU[:, :, :, b * BJ:(b + 1) * BJ], ps, ACT.Copy).then_inc(*s.empties(("bu", b)))
            gC4 = gC.rearrange("c t (g q) -> c t g q", q=P5)
            for i in range(16):
                eng.wait_ge(*filled_at(("y5", i)))
                r = 64 * (i % 2)
                ps = bank_of(("y5", i))[r:r + C5, :].rearrange("c (m t q) -> c t m q", t=L5, q=P5)
                gg = 8 * (i // 2) + i % 2
                act(gC4[:, :, gg:gg + 7:2, :], ps, ACT.Gelu_apprx_tanh).then_inc(*s.empties(("y5", i)))
            for i in range(4):
                eng.wait_ge(*filled_at(("gt", i)))
                ps = bank_of(("gt", i)).rearrange("p (k t c) -> p k c t", k=2, t=L5)
                for k in range(2):
                    act(hT3[:, 2 * i + k, :].rearrange("p (c t) -> p c t", t=L5), ps[:, k], ACT.Copy)\
                        .then_inc(*(s.empties(("gt", i)) if k else s.step()))
            for i in range(4):
                eng.wait_ge(*filled_at(("glu", i)))
                ps = bank_of(("glu", i)).rearrange("p (m t) -> p m t", t=T)
                for m in range(2):
                    k = 2 * i + m
                    act(sq3[:, k, :], ps[:, m, :], ACT.Sigmoid, bias=col("s5_b_glu", k))\
                        .then_inc(*(s.empties(("glu", i)) if m else s.step()))

            def squares(r):
                for pair in range(4):
                    if r == 0:
                        eng.wait_ge(done("x_ready"), 2 * (pair + 1))
                    elif r >= len(UPDATES):
                        eng.wait_ge(done("post_added"), KC * (r - len(UPDATES)) + 2 * (pair + 1))
                    else:
                        key = UPDATES[r]
                        eng.wait_ge(*emptied_at((*key, pair)))
                    act(sq[:, pair * 2 * T:(pair + 1) * 2 * T], xT[:, pair * 2 * T:(pair + 1) * 2 * T], ACT.Square)\
                        .then_inc(*s.signals("squares"))

            def root(key):
                eng.wait_ge(*filled_at(key))
                act(stat[:, T:2 * T], bank_of(key)[:, 0:T], ACT.Sqrt, bias=eps_column, scale=1.0 / D)\
                    .then_inc(*s.empties(key))

            def shift(dst, layer, which, base):
                for k in range(KC):
                    eng.wait_ge(done("h_scaled"), base + k + 1)
                    act(dst[:, k, :], dst[:, k, :], ACT.Identity, bias=ada_cols(layer, which)[:, k:k + 1])\
                        .then_inc(*s.signals("h_ready"))

            def swiglu(l):
                for c in range(NGU):
                    eng.wait_ge(*filled_at(("gu", l, c)))
                    ps = bank_of(("gu", l, c))
                    act(hid[:, c, :], ps[:, 0:T], ACT.Silu).then_inc(*s.signals("silu_ready"))

            def attend(at, steps=None):
                for u in steps or range(at.n + LAG):
                    if u < at.n:
                        eng.wait_ge(done("max_" + at.name), u + 1)
                        if u >= SLOTS:
                            eng.wait_ge(*filled_at(("pt", at.name, u - SLOTS)))
                        key = ("s", at.name, u)
                        act(at.pslots[:, u % SLOTS, 0:at.keys(u)], bank_of(key)[:, 0:at.keys(u)], ACT.Exp,
                            bias=at.soft[:, 0, u:u + 1], accum_out=at.soft[:, 1, u:u + 1]).then_inc(*s.empties(key))
                    if LAG <= u < at.n + LAG:
                        w = u - LAG
                        eng.wait_ge(*filled_at(("pt", at.name, w)))
                        ps = bank_of(("pt", at.name, w))
                        if w >= 4:
                            eng.wait_ge(*filled_at(("o", at.name, w - 4)))
                        act(at.tslots[:, w % 4, 0:at.keys(w)], ps[:, 0:at.keys(w)], ACT.Copy)\
                            .then_inc(*s.empties(("pt", at.name, w)))

            squares(0)
            root(("ms", 1))
            shift(hT3, 0, 3, 0)
            swiglu(0)
            for i in range(4):
                eng.wait_ge(*filled_at(("memT", i)))
                act(memT[:, 2 * i:2 * i + 2, :].rearrange("p k t -> p (k t)"), bank_of(("memT", i)), ACT.Copy)\
                    .then_inc(*s.empties(("memT", i)))
            squares(1)
            eng.dma_start(pos_i.bitcast(I32), a["positions"][0].rearrange("(b p) -> p b", p=P),
                          allow_slow_non_contiguous=True)\
               .then_inc(done("positions_landed"), 16)
            for m, names in enumerate((("k_nope_norm_g", "k_rope_norm_g"), ("mla_q_nope_norm_g", "mla_q_rope_norm_g"))):
                for name, lo, hi in zip(names, (0, DN), (DN, DQK)):
                    x = a[name] if m == 0 else a[name][0]
                    eng.dma_start(gain_rows[:, m, lo:hi], x.partition_broadcast(P)).then_inc(done("gain_rows_landed"), 16)
            root(("ms", 2))
            shift(hT3, "kv", 0, KC)
            shift(h2, 1, 0, 2 * KC)
            eng.wait_ge(*emptied_at(("ada", 6)))
            act(flat(mem_sq), flat(memT), ACT.Square).then_inc(*s.signals("mem_squares"))
            eng.wait_ge(*filled_at(("ms", 2)))
            parts = [(("kva", b), 0, RKV, b) for b in range(2)] + [(("kva", b), RKV, RKV + DR, 2 + b) for b in range(2)]
            parts += [(("cqt", b), 0, RQ, 4 + b) for b in range(2)]
            for key, lo, hi, i in parts:
                eng.wait_ge(*filled_at(key))
                act(sq[:, i * 256:i * 256 + hi - lo], bank_of(key)[:, lo:hi], ACT.Square, accum_out=latent_ss[:, 0, i:i + 1])\
                    .then_inc(*s.signals("latent_squares"))
            eng.wait_ge(done("latent_mean"), 3)
            act(latent_ss[:, 2, :], latent_ss[:, 1, :], ACT.Sqrt).then_inc(*s.signals("latent_root"))
            eng.wait_ge(done("latent_rstd"), 1)
            for b in range(2):
                ps = bank_of(("kva", b))
                act(latent_tok[0][:, b, :], ps[:, 0:RKV], ACT.Identity, scale=latent_ss[:, 0, b:b + 1])\
                    .then_inc(*s.step())
                act(krope_tok[:, b, :], ps[:, RKV:RKV + DR], ACT.Identity, scale=latent_ss[:, 0, 2 + b:3 + b])\
                    .then_inc(*s.empties(("kva", b)))
            for b in range(2):
                act(latent_tok[1][:, b, :], bank_of(("cqt", b))[:, 0:RQ], ACT.Identity, scale=latent_ss[:, 0, 4 + b:5 + b])\
                    .then_inc(*s.empties(("cqt", b)))
            root("ms_mem")
            eng.wait_ge(done("rotary_angles"), 1)
            act(angle[:, 0:2], angle[:, 0:2], ACT.Sin).then_inc(*s.signals("rotary_ready"))

            def memory_kv(l):
                for dst, key, scale in ((k_mem[l], ("k_mem", l, 0), HD ** -0.5), (v_mem[l], ("v_mem", l, 0), 1.0)):
                    eng.wait_ge(*filled_at(key))
                    act(flat(dst), bank_of(key), ACT.Copy, scale=scale).then_inc(*s.empties(key))

            memory_kv(0)
            for i, (key, gain) in enumerate((("ckvT", "kv_a_norm_g"), ("cqT", "mla_q_norm_g"))):
                eng.wait_ge(*filled_at(key))
                ps = bank_of(key).rearrange("p (k t) -> p k t", t=T)
                for k in range(2):
                    act(latent[i][:, k, :], ps[:, k, :], ACT.Identity, scale=col(gain, k))\
                        .then_inc(*(s.empties(key) if k else s.step()))
            for hh in range(2):
                for b in range(2):
                    for n in range(2):
                        key, hs = ("kv", hh, b, n), slice(8 * hh + 4 * n, 8 * hh + 4 * n + 4)
                        eng.wait_ge(*filled_at(key))
                        ps = bank_of(key).rearrange("p (h n) -> p h n", n=P)
                        act(k_sq[:, b, hs, :], ps[:, :, 0:DN], ACT.Square).then_inc(*s.step())
                        act(k_tok1[:, b, hs, 0:DN], ps[:, :, 0:DN], ACT.Copy).then_inc(*s.step())
                        act(v1[:, b, :].rearrange("p (h n) -> p h n", n=DV)[:, hs, :], ps[:, :, DN:], ACT.Copy)\
                            .then_inc(*s.empties(key))
            for hh in range(2):
                for b in range(2):
                    for n in range(2):
                        key, hs = ("q1", hh, b, n), slice(8 * hh + 4 * n, 8 * hh + 4 * n + 4)
                        eng.wait_ge(*filled_at(key))
                        ps = bank_of(key)[:, 0:4 * DQK].rearrange("p (h n) -> p h n", n=DQK)
                        act(q_sq[:, b, hs, :], ps, ACT.Square).then_inc(*s.step())
                        act(q_tok1[:, b, hs, :], ps, ACT.Copy).then_inc(*s.empties(key))
                if hh == 0:
                    eng.wait_ge(done("k1_mean"), 1)
                    act(head_ss[:, 2, :, 0:H1], head_ss[:, 1, :, 0:H1], ACT.Sqrt).then_inc(*s.signals("k1_root"))
            eng.wait_ge(done("q1_mean"), 2)
            act(head_ss[:, 2, :, H1:], head_ss[:, 1, :, H1:], ACT.Sqrt).then_inc(*s.signals("q1_root"))
            memory_kv(1)
            for x, at in ((qh, CONST_KEEP), (kh, CONST_KEEP + T)):
                eng.dma_start(x[DQK:DQK + 2], constants[0:2, at:at + T].unsqueeze(1).to_broadcast([2, H1, T]))\
                   .then_inc(done("hidden_landed"), 16)
            for b in range(2):
                for g in range(H1 // 4):
                    key = ("kT1", b, g)
                    eng.wait_ge(*filled_at(key))
                    ps = bank_of(key).rearrange("p (h t) -> p h t", t=P)
                    act(kh[0:DQK, 4 * g:4 * g + 4, b * P:(b + 1) * P], ps[0:DQK], ACT.Copy).then_inc(*s.empties(key))
            attend(mla)
            squares(2)
            root(("ms", 3))
            shift(hT3, 1, 3, 3 * KC)
            swiglu(1)
            squares(3)
            for r, x in ((0, "a_w2_2"), (64, "a_a2_2")):
                eng.dma_start(w2a2[r:r + 64, :], a[x][0]).then_inc(done("w2_landed"), 16)
            eng.dma_start(masks7, constants[:, CONST_MASK:CONST_ALIBI]).then_inc(done("masks7_landed"), 16)
            root(("ms", 4))
            eng.wait_ge(done("shift_clear"), 1)
            def shift_panels(panels):
                for i in panels:
                    key, pos = ("a_in", i), A_ORDER.index(i)
                    eng.wait_ge(*filled_at(key))
                    ps = bank_of(key).rearrange("p (m t) -> p m t", t=T)
                    if pos > 1:
                        eng.wait_ge(*emptied_at(("a_in", A_ORDER[pos - 2])))
                    for c in SHIFTED[i]:
                        act(shifted[:, pos % 2, c % 2, 1:T + 1], ps[:, c % 2, :], ACT.Identity,
                            scale=col("a_shift_mu_2", c)).then_inc(*s.signals("shift_ready"))

            def gate(c):
                key, k = ("a_in", c // 2), c - 19 if c < 25 else c - 21
                act(gateT[:, k, :], bank_of(key)[:, c % 2 * T:(c % 2 + 1) * T], ACT.Silu)\
                    .then_inc(*(s.empties(key) if c % 2 or c == 28 else s.step()))

            shift_panels(A_ORDER[0:1])
            eng.wait_ge(done("lora_shifted"), 1)
            gate(19)
            act(lora_in[0:64, :], lora_in[0:64, :], ACT.Tanh).then_inc(*s.signals("tanh_ready"))
            shift_panels(A_ORDER[1:4])
            for c in range(NBR):
                eng.wait_ge(*emptied_at(("a_in", 3 + c // 2)))
                act(tmp7[:, c, :], k7[:, c, :], ACT.Square, scale=col("a_k_k_2", c)).then_inc(*s.signals("kk_squares"))
            for i in range(NBR // 2):
                for key, bias, dst in ((("decay", i), "a_w0_2", sig7), (("rate", i), "a_a0_2", a7)):
                    eng.wait_ge(*filled_at(key))
                    ps = bank_of(key).rearrange("p (m t) -> p m t", t=T)
                    for m in range(2):
                        act(dst[:, 2 * i + m, :], ps[:, m, :], ACT.Sigmoid, bias=col(bias, 2 * i + m))\
                            .then_inc(*(s.empties(key) if m else s.step()))
            shift_panels(A_ORDER[4:7])
            for i in range(3):
                eng.wait_ge(*emptied_at(("kks", i)))
            act(flat(tmp7), flat(tmp7), ACT.Sqrt).then_inc(*s.signals("kk_root"))
            shift_panels(A_ORDER[7:8])
            eng.wait_ge(done("cum_ready"), 1)
            act(flat(grow7), flat(cum7), ACT.Exp, scale=math.exp(-0.5)).then_inc(*s.signals("exp7"))
            eng.wait_ge(*s.last)
            act(flat(cum7), flat(cum7), ACT.Exp, scale=-math.exp(-0.5)).then_inc(*s.signals("exp7"))
            act(flat(at7), flat(at7), ACT.Exp, scale=-math.exp(-0.5)).then_inc(*s.signals("exp7"))
            shift_panels(A_ORDER[8:10])
            for i in A_ORDER[10:]:
                eng.wait_ge(*filled_at(("a_in", i)))
                for c in (2 * i, 2 * i + 1):
                    if c in (25, 26):
                        ps = bank_of(("a_in", i))[:, c % 2 * T:(c % 2 + 1) * T]
                        act(q_mem[:, c - 25, :], ps, ACT.Copy).then_inc(*(s.empties(("a_in", i)) if c % 2 else s.step()))
                    elif c < A_IN // P:
                        gate(c)
            for name, dst in (("b_tok", b_tok), ("k_tok", k_tok), ("v_tok", v_tok)):
                for g in range(3):
                    key = (name, g)
                    eng.wait_ge(*filled_at(key))
                    ps = bank_of(key)
                    act(flat(dst[:, 8 * g:8 * g + 8, :]), ps, ACT.Copy).then_inc(*s.empties(key))
            for l in range(1, 6):
                for g in range(3):
                    key = ("lt", l, g)
                    eng.wait_ge(*filled_at(key))
                    ps = bank_of(key)
                    act(flat(lt_t7[:, 8 * g:8 * g + 8, :]), ps, ACT.Copy).then_inc(*s.empties(key))
            for c in range(NCR):
                for name, dst in (("rhs", rhs7), ("sa", sa7)):
                    eng.wait_ge(*filled_at((name, c)))
                    ps = bank_of((name, c))
                    act(flat(dst), ps[:, 0:NBR * CR], ACT.Copy).then_inc(*s.empties((name, c)))
                    attend(memory(0), [3 * c + (name == "sa")])
                eng.wait_ge(*filled_at(("y7", c)))
                ps = bank_of(("y7", c)).rearrange("p (i t) -> p i t", t=CR)[:, 0:NBR, :]
                act(yT7[:, :, c * CR:(c + 1) * CR], ps, ACT.Copy).then_inc(*s.empties(("y7", c)))
                attend(memory(0), [3 * c + 2])
            for i in range(3):
                eng.wait_ge(*emptied_at(("mean7", i)))
                act(flat(y_sq7[:, 2 * i:2 * i + 2, :]), flat(yc7[:, 2 * i:2 * i + 2, :]), ACT.Square)\
                    .then_inc(*s.signals("y7_squares"))
            eng.wait_ge(*emptied_at("var7"))
            act(stat[0:2 * NBR, T:2 * T], stat[0:2 * NBR, 0:T], ACT.Sqrt).then_inc(*s.signals("y7_root"))

            def output(l):
                for i in range(4):
                    key = ("out", l, i)
                    eng.wait_ge(*filled_at(key))
                    ps = bank_of(key)
                    act(flat(out_sq[l][:, 2 * i:2 * i + 2, :]), ps, ACT.Square).then_inc(*s.signals("out_squares"))
                    act(flat(yP[:, 2 * i:2 * i + 2, :]), ps, ACT.Copy).then_inc(*s.empties(key))
                root(("ms_out", l))

            output(0)
            squares(4)
            eng.dma_start(alibi, constants[:, CONST_ALIBI:].rearrange("p (h b t) -> p h b t", b=2, t=T))\
               .then_inc(done("alibi_landed"), 16)
            eng.dma_start(post_gain, a["post_norm_2"][1].partition_broadcast(P)).then_inc(done("post_gain_landed"), 16)
            root(("ms", 5))
            for i in range(3):
                eng.wait_ge(*filled_at(("k_sh", i)))
                ps = bank_of(("k_sh", i))
                act(flat(kT[:, 2 * i:2 * i + 2, :]), ps, ACT.Copy).then_inc(*s.empties(("k_sh", i)))
            for i in range(3):
                eng.wait_ge(*filled_at(("v_sh", i)))
                ps = bank_of(("v_sh", i)).rearrange("p (b n) -> p b n", n=256)
                act(v_sh[:, :, i * 256:(i + 1) * 256], ps, ACT.Copy).then_inc(*s.empties(("v_sh", i)))
            def take_panel(i):
                key, two = ("b_in", i), slice(2 * i, 2 * i + 2)
                dst = (qT[:, two, :] if i < 3 else gateT[:, 2 * i - 6:2 * i - 4, :] if i < 6 else q_mem if i == 6
                       else gateT[:, NBR:, :])
                eng.wait_ge(*filled_at(key))
                act(flat(dst), bank_of(key), ACT.Copy).then_inc(*s.empties(key))

            for i in B_FIRST:
                take_panel(i)
            eng.wait_ge(*filled_at("lam2"))
            ps = bank_of("lam2")
            act(columns2[:, 34:36], ps[:, 0:2], ACT.Exp).then_inc(*s.empties("lam2"))
            def diff_steps(steps):
                for u in steps:
                    if u < ND:
                        eng.wait_ge(done("max_diff"), u + 1)
                        for c in range(2):
                            x = both[:, u % SLOTS, c, 0:P * (u % 2 + 1)]
                            act(x, x, ACT.Exp, bias=soft2[:, c, u:u + 1], accum_out=sums2[:, c, u:u + 1])\
                                .then_inc(*s.signals("exp_diff"))
                    if LAG <= u < ND + LAG:
                        w = u - LAG
                        eng.wait_ge(*filled_at(("dpt", w)))
                        ps = bank_of(("dpt", w))
                        if w >= 4:
                            eng.wait_ge(*filled_at(("do", w - 4)))
                        n = P * (w % 2 + 1)
                        act(tslots2[:, w % 4, 0:n], ps[:, 0:n], ACT.Copy).then_inc(*s.empties(("dpt", w)))
                    if u > LAG:
                        w = u - LAG - 1
                        eng.wait_ge(*filled_at(("do", w)))
                        ps = bank_of(("do", w))
                        act(mixT[1][:, w // 2, w % 2 * P:(w % 2 + 1) * P], ps[:, 0:P], ACT.Copy)\
                            .then_inc(*s.empties(("do", w)))

            for what, x in PLAN:
                if what == "diff":
                    diff_steps(x)
                elif what == "memory":
                    attend(memory(1), x)
                else:
                    take_panel(x)
            eng.wait_ge(*emptied_at(("do", ND - 1)))
            for i in range(3):
                two = slice(2 * i, 2 * i + 2)
                act(flat(o_sq[:, two, :]), flat(mixT[1][:, two, :]), ACT.Square).then_inc(*s.signals("o_squares"))
            act(flat(gateT), flat(gateT), ACT.Silu).then_inc(*s.signals("gate_ready"))
            eng.wait_ge(*emptied_at("sub"))
            act(stat[0:HB, T:2 * T], stat[0:HB, 0:T], ACT.Sqrt).then_inc(*s.signals("sub_root"))
            for i in range(4):
                eng.wait_ge(*filled_at(("rows", i)))
                act(out_rows[:, i // 2, i % 2 * 512:i % 2 * 512 + 512], bank_of(("rows", i)), ACT.Copy)\
                    .then_inc(*s.empties(("rows", i)))
            for i in range(4):
                eng.wait_ge(*filled_at(("out", 1, i)))
                ps = bank_of(("out", 1, i))
                if i > 1:
                    eng.wait_ge(done("row_squares"), 2 * i - 2)
                for b in range(2):
                    at = (2 * i + b) % 4 * 256
                    act(row_sq[:, at:at + 256], ps[:, b * 256:(b + 1) * 256], ACT.Square,
                        accum_out=row_ss[:, b, i:i + 1]).then_inc(*s.signals("row_squares"))
            eng.wait_ge(done("row_sums"), 1)
            act(row_rms[:, 1, :], row_rms[:, 0, :], ACT.Sqrt, bias=eps_column, scale=1.0 / D).then_inc(*s.signals("row_root"))

        @block.gpsimd
        def _(eng):
            g = Program("gpsimd")
            w = [a["ada_w"][l].rearrange("(k p) n -> k p n", p=P) for l in range(2)]
            kv = a["kv_ada_w"].rearrange("(k p) n -> k p n", p=P)
            src = [kv[k] if b == 6 else w[b // 3][k, :, b % 3 * PANEL:(b % 3 + 1) * PANEL]
                   for b in ADA_ORDER for k in range(KC)]

            def ada_load(i):
                if i >= ARING:
                    eng.wait_ge(done("ada_used"), i - ARING + 1)
                eng.dma_start(aring[:, (i % ARING) * PANEL:(i % ARING + 1) * PANEL], src[i])\
                   .then_inc(ada_landed[i % ARING], 16)

            eng.wait_ge(done("vectors0_landed"), 16 * VEC_LOADS[0])
            for i in range(8):
                ada_load(i)
            G = nc.gpsimd
            for m in range(4):
                eng.wait_ge(*emptied_at(("raw", m)))
            G.memset(toep, 0.0).then_inc(*g.signals("toeplitz_clear"))
            eng.wait_ge(done("powers_ready"), 1)
            eng.wait_ge(done("bb_ready"), 2)
            eng.wait_ge(*filled_at(("U", 3)))
            for b in range(NB5):
                js = slice(b * BJ, (b + 1) * BJ)

                def power(x):
                    return x[:, :, js].rearrange("p k j -> p j k").unsqueeze(3).to_broadcast([P, BJ, 9, P5])

                def coefficient(i):
                    return ct[:, i, js, :].unsqueeze(2).to_broadcast([P, BJ, 9, P5])
                for dst, x0, x1 in ((ca_re, powr, powi), (ca_im, negi, powr)):
                    q = [tmp_c[:, n * 576:(n + 1) * 576].rearrange("p (j k q) -> p j k q", k=9, q=P5)
                         for n in range(2)]
                    if g.last:
                        eng.wait_ge(*g.last)
                    G.tensor_tensor(q[0], power(x0), coefficient(0), ALU.mult).then_inc(*g.step())
                    G.tensor_tensor(q[1], power(x1), coefficient(1), ALU.mult).then_inc(*g.step())
                    eng.wait_ge(*g.last)
                    G.tensor_tensor(dst[:, js, :, :], q[0], q[1], ALU.subtract).then_inc(*g.signals("ca_ready"))
                ada_load(8 + b)
            for i in range(16, len(src)):
                ada_load(i)
            eng.wait_ge(done("ada_used"), len(src))
            eng.dma_start(mem_nat, a["mem_2"][0].rearrange("(b p) d -> p b d", p=P)).then_inc(done("mem_landed"), 16)
            for l in range(2, 6):
                if l == 2:
                    eng.wait_ge(done("inverse_ready"), 6)
                    eng.wait_ge(*filled_at(("b_tok", 2)))
                else:
                    eng.wait_ge(*filled_at(("lt", l - 2, 2)))
                at, _ = CONST_AT["levels_t"]
                mask = masks7[:, at - CONST_MASK + l * CR:at - CONST_MASK + (l + 1) * CR]
                G.tensor_tensor(lt_m7[l % 2], lt7, mask.unsqueeze(1).to_broadcast([P, NU, CR]), ALU.mult)\
                    .then_inc(*g.signals("level_mask_ahead"))


def kernel(**inputs):
    import concourse.bacc as bacc
    from concourse.bass_utils import run_bass_kernel_spmd

    nc = bacc.Bacc("TRN2", target_bir_lowering=False, num_devices=1)
    arrays = {"in_" + name: np.ascontiguousarray(x) for name, x in inputs.items()}
    arrays["in_constants"] = CONSTANTS
    drams = {name: nc.dram_tensor(name, x.shape, mybir.dt.from_np(x.dtype), kind="ExternalInput").ap()
             for name, x in arrays.items()}
    constants = drams.pop("in_constants")
    out = nc.dram_tensor("out_0", (1, T, D), F32, kind="ExternalOutput").ap()
    blocks_kernel(nc, {name[3:]: x for name, x in drams.items()}, constants, out)
    r = run_bass_kernel_spmd(nc, [arrays], core_ids=[0])
    return r.results[0]["out_0"]
```
